# Optimizing a Trainium2 kernel written in Bass

```python
import jax, jax.numpy as jnp
from jax import lax
import numpy as np
import math

D_MODEL = 1024
BATCH = 1
SEQ = 1024
DEPTH = 1

GRID_W = 64
CTX_LEN = 256
D_MIX = D_MODEL
RET_DIM = 64
RET_WIDTH = D_MIX // 2
RET_HEADS = RET_WIDTH // RET_DIM
RWKV_DIM = 64
RWKV_WIDTH = D_MIX - RET_WIDTH
RWKV_HEADS = RWKV_WIDTH // RWKV_DIM
DECAY_LORA = 64
ICLR_LORA = 64
GATE_LORA = 128
CHUNK = 128
CONV_W = 3
N_EXPERTS = 16
EC_CAPACITY = 2
D_EXPERT = D_MODEL
ROPE_BASE = 10000.0
NORM_EPS = 1e-6
RWKV_GN_EPS = 64e-5
RET_COLS = 5 * RET_WIDTH
RWKV_SPLITS = (RWKV_WIDTH, RWKV_WIDTH, RWKV_WIDTH, DECAY_LORA, DECAY_LORA, ICLR_LORA, GATE_LORA, GATE_LORA)
RWKV_COLS = sum(RWKV_SPLITS)
D_IN = RET_COLS + RWKV_COLS


def split_cols(u, sizes):
    outs, start = [], 0
    for s in sizes:
        outs.append(u[..., start:start + s])
        start += s
    return outs

def flip(t):
    return jnp.flip(t, axis=1)

def rms_norm(x, g):
    xf = x.astype(jnp.float32)
    y = xf * lax.rsqrt(jnp.mean(xf * xf, axis=-1, keepdims=True) + NORM_EPS)
    return (y * g.astype(jnp.float32)).astype(x.dtype)

def head_rms(y):
    y = y * lax.rsqrt(jnp.mean(y * y, axis=-1, keepdims=True) + NORM_EPS)
    return y.reshape(y.shape[0], y.shape[1], -1)

def depthwise_conv(x, w):
    return lax.conv_general_dilated(x, w[:, None, :].astype(x.dtype), window_strides=(1,), padding='SAME',
                                    dimension_numbers=('NWC', 'WIO', 'NWC'), feature_group_count=x.shape[-1])

def axial_rope(x):
    n_tok, d = x.shape[1], x.shape[-1]
    rows = n_tok // GRID_W
    row = jnp.repeat(jnp.arange(rows, dtype=jnp.float32), GRID_W)
    col = jnp.tile(jnp.arange(GRID_W, dtype=jnp.float32), rows)
    n_freq = d // 4
    freq = ROPE_BASE ** (-jnp.arange(n_freq, dtype=jnp.float32) / n_freq)
    ang = jnp.concatenate([row[:, None] * freq, col[:, None] * freq], axis=-1)[None, :, None, :]
    cos, sin = jnp.cos(ang), jnp.sin(ang)
    x1, x2 = x[..., : d // 2], x[..., d // 2:]
    return jnp.concatenate([x1 * cos - x2 * sin, x2 * cos + x1 * sin], axis=-1)

def retention_scan(q, k, v, log_gamma, s0):
    B, T, H, d = q.shape
    n = T // CHUNK
    to_chunks = lambda t: t.reshape(B, n, CHUNK, H, d).transpose(1, 0, 3, 2, 4)
    idx = jnp.arange(CHUNK, dtype=jnp.float32)
    rel = idx[:, None] - idx[None, :]
    decay_in = jnp.where(rel >= 0, jnp.exp(jnp.maximum(rel, 0.0) * log_gamma[:, None, None]), 0.0)
    q_dec = jnp.exp((idx + 1.0) * log_gamma[:, None])[..., None]
    k_dec = jnp.exp((CHUNK - 1.0 - idx) * log_gamma[:, None])[..., None]
    chunk_dec = jnp.exp(CHUNK * log_gamma)[:, None, None]

    def step(S, inp):
        qc, kc, vc = inp
        scores = jnp.einsum('bhid,bhjd->bhij', qc, kc) * decay_in
        out = jnp.einsum('bhij,bhjd->bhid', scores, vc) + jnp.einsum('bhid,bhde->bhie', qc * q_dec, S)
        S = S * chunk_dec + jnp.einsum('bhjd,bhje->bhde', kc * k_dec, vc)
        return S, out

    S_fin, ys = lax.scan(step, s0, (to_chunks(q), to_chunks(k), to_chunks(v)))
    return ys.transpose(1, 0, 3, 2, 4).reshape(B, T, H, d), S_fin

def retention_group(u, uc, need_ctx):
    def split_heads(t):
        q, k, v, gf, gb = split_cols(t.astype(jnp.float32), (RET_WIDTH,) * 5)
        hd = lambda a: a.reshape(a.shape[0], a.shape[1], RET_HEADS, RET_DIM)
        return hd(q), hd(k) * RET_DIM ** -0.5, hd(v), gf, gb

    q, k, v, gf, gb = split_heads(u)
    qc, kc, vc, gfc, gbc = split_heads(uc)
    q, k = axial_rope(q), axial_rope(k)
    log_gamma = jnp.log1p(-jnp.exp2(-5.0 - jnp.arange(RET_HEADS, dtype=jnp.float32)))
    s0 = jnp.zeros((u.shape[0], RET_HEADS, RET_DIM, RET_DIM), jnp.float32)
    yc_f, sc_f = retention_scan(qc, kc, vc, log_gamma, s0)
    yc_b, sc_b = retention_scan(flip(qc), flip(kc), flip(vc), log_gamma, s0)
    y_f, _ = retention_scan(q, k, v, log_gamma, sc_f)
    y_b, _ = retention_scan(flip(q), flip(k), flip(v), log_gamma, sc_b)
    lat = jax.nn.silu(gf) * head_rms(y_f) + jax.nn.silu(gb) * head_rms(flip(y_b))
    if not need_ctx:
        return lat, None
    ctx_out = jax.nn.silu(gfc) * head_rms(yc_f) + jax.nn.silu(gbc) * head_rms(flip(yc_b))
    return lat, ctx_out

def rwkv_prepare(u, w0, w2, a0, a2, g2, k_k, k_a, r_k):
    u = u.astype(jnp.float32)
    B, T, _ = u.shape
    r, k, v, wl_f, wl_b, al, gl_f, gl_b = split_cols(u, RWKV_SPLITS)
    heads = lambda t: t.reshape(B, T, RWKV_HEADS, RWKV_DIM)

    def decay(wl, w0_d, w2_d):
        w_log = -jax.nn.softplus(-(w0_d + jnp.tanh(wl) @ w2_d)) - 0.5
        return heads(jnp.exp(-jnp.exp(w_log)))

    iclr = jax.nn.sigmoid(a0 + al @ a2)
    kk = heads(k * k_k)
    kk = kk / jnp.maximum(jnp.linalg.norm(kk, axis=-1, keepdims=True), 1e-12)
    k_mod = heads(k * (1.0 + (iclr - 1.0) * k_a))
    r, v = heads(r), heads(v)
    bonus = (jnp.sum(r * k_mod * r_k.reshape(RWKV_HEADS, RWKV_DIM), axis=-1, keepdims=True) * v).reshape(B, T, -1)
    g_f = jax.nn.sigmoid(gl_f) @ g2[0]
    g_b = jax.nn.sigmoid(gl_b) @ g2[1]
    return (r, decay(wl_f, w0[0], w2[0]), decay(wl_b, w0[1], w2[1]), k_mod, v, -kk, kk * heads(iclr), g_f, g_b, bonus)

def rwkv7_scan(r, w, k, v, a, b, s0):
    def step(S, inp):
        r_t, w_t, k_t, v_t, a_t, b_t = inp
        sa = jnp.einsum('bhvk,bhk->bhv', S, a_t)
        S = S * w_t[:, :, None, :] + sa[..., None] * b_t[:, :, None, :] + v_t[..., None] * k_t[:, :, None, :]
        return S, jnp.einsum('bhvk,bhk->bhv', S, r_t)

    xs = tuple(jnp.moveaxis(t, 1, 0) for t in (r, w, k, v, a, b))
    S_fin, ys = lax.scan(step, s0, xs)
    return jnp.moveaxis(ys, 0, 1), S_fin

def rwkv_group_norm(y, w, b):
    mu = jnp.mean(y, axis=-1, keepdims=True)
    var = jnp.mean((y - mu) ** 2, axis=-1, keepdims=True)
    yn = ((y - mu) * lax.rsqrt(var + RWKV_GN_EPS)).reshape(y.shape[0], y.shape[1], -1)
    return yn * w + b

def rwkv_group(rw, rwc, w0, w2, a0, a2, g2, k_k, k_a, r_k, lnx_w, lnx_b, need_ctx):
    r, w_f, w_b, k, v, a, b, g_f, g_b, bonus = rwkv_prepare(rw, w0, w2, a0, a2, g2, k_k, k_a, r_k)
    rc, wc_f, wc_b, kc, vc, ac, bc, gc_f, gc_b, bonus_c = rwkv_prepare(rwc, w0, w2, a0, a2, g2, k_k, k_a, r_k)
    s0 = jnp.zeros((rw.shape[0], RWKV_HEADS, RWKV_DIM, RWKV_DIM), jnp.float32)
    yc_f, sc_f = rwkv7_scan(rc, wc_f, kc, vc, ac, bc, s0)
    yc_b, sc_b = rwkv7_scan(*[flip(t) for t in (rc, wc_b, kc, vc, ac, bc)], s0)
    y_f, _ = rwkv7_scan(r, w_f, k, v, a, b, sc_f)
    y_b, _ = rwkv7_scan(*[flip(t) for t in (r, w_b, k, v, a, b)], sc_b)
    lat = g_f * (rwkv_group_norm(y_f, lnx_w, lnx_b) + bonus) + g_b * (rwkv_group_norm(flip(y_b), lnx_w, lnx_b) + bonus)
    if not need_ctx:
        return lat, None
    ctx_out = (gc_f * (rwkv_group_norm(yc_f, lnx_w, lnx_b) + bonus_c)
               + gc_b * (rwkv_group_norm(flip(yc_b), lnx_w, lnx_b) + bonus_c))
    return lat, ctx_out

def token_mix(h, hc, w_in, conv_w, w0, w2, a0, a2, g2, k_k, k_a, r_k, lnx_w, lnx_b, w_out, need_ctx):
    u, uc = h @ w_in, hc @ w_in
    ret_lat, ret_ctx = retention_group(u[..., :RET_COLS], uc[..., :RET_COLS], need_ctx)
    rw = depthwise_conv(u[..., RET_COLS:], conv_w)
    rwc = depthwise_conv(uc[..., RET_COLS:], conv_w)
    rwkv_lat, rwkv_ctx = rwkv_group(rw, rwc, w0, w2, a0, a2, g2, k_k, k_a, r_k, lnx_w, lnx_b, need_ctx)
    lat = jnp.concatenate([ret_lat, rwkv_lat], axis=-1).astype(h.dtype) @ w_out
    if not need_ctx:
        return lat, None
    ctx_out = jnp.concatenate([ret_ctx, rwkv_ctx], axis=-1).astype(hc.dtype) @ w_out
    return lat, ctx_out

def ec_moe(h, w_router, w_gate, w_up, w_down):
    B, T, D = h.shape
    cap = max(1, EC_CAPACITY * T // N_EXPERTS)
    affinity = jax.nn.softmax((h @ w_router).astype(jnp.float32), axis=-1)
    gate_vals, tok_idx = lax.top_k(jnp.swapaxes(affinity, 1, 2), cap)
    xs = jax.vmap(lambda hb, ib: hb[ib])(h, tok_idx)
    hid = jax.nn.silu(jnp.einsum('becd,edf->becf', xs, w_gate)) * jnp.einsum('becd,edf->becf', xs, w_up)
    ye = jnp.einsum('becf,efd->becd', hid, w_down) * gate_vals[..., None].astype(h.dtype)
    return jax.vmap(lambda yb, ib: jnp.zeros((T, D), yb.dtype).at[ib.reshape(-1)].add(yb.reshape(-1, D)))(ye, tok_idx)

def first_inputs(seed: int = 0) -> dict:
    key = jax.random.key(seed)
    ks = jax.random.split(key, 24)
    nrm = lambda k, shape, s: s * jax.random.normal(k, shape, jnp.float32)
    L, D, W, E, F = DEPTH, D_MODEL, RWKV_WIDTH, N_EXPERTS, D_EXPERT
    return {
        'x': nrm(ks[0], (BATCH, SEQ, D), 1.0),
        'c': nrm(ks[1], (BATCH, D), 1.0),
        'ctx': nrm(ks[2], (BATCH, CTX_LEN, D), 1.0),
        'c_ctx': nrm(ks[3], (D,), 1.0),
        'w_mod': nrm(ks[4], (L, D, 6 * D), 0.5 * D ** -0.5),
        'b_mod': nrm(ks[5], (L, 6 * D), 0.02),
        'norm_gains': 1.0 + nrm(ks[6], (L, 4, D), 0.1),
        'w_in': nrm(ks[7], (L, D, D_IN), D ** -0.5),
        'rwkv_conv': jnp.array([0.3, 1.0, 0.3], jnp.float32)[None, :, None] + nrm(ks[8], (L, CONV_W, RWKV_COLS), 0.05),
        'rwkv_w0': jnp.linspace(-6.0, -1.0, W, dtype=jnp.float32) + nrm(ks[9], (L, 2, W), 0.1),
        'rwkv_w2': nrm(ks[10], (L, 2, DECAY_LORA, W), 0.5 * DECAY_LORA ** -0.5),
        'rwkv_a0': nrm(ks[11], (L, W), 0.1),
        'rwkv_a2': nrm(ks[12], (L, ICLR_LORA, W), 0.5 * ICLR_LORA ** -0.5),
        'rwkv_g2': nrm(ks[13], (L, 2, GATE_LORA, W), GATE_LORA ** -0.5),
        'rwkv_k_k': 0.85 + nrm(ks[14], (L, W), 0.05),
        'rwkv_k_a': 1.0 + nrm(ks[15], (L, W), 0.05),
        'rwkv_r_k': nrm(ks[16], (L, W), 0.1),
        'rwkv_lnx_w': 1.0 + nrm(ks[17], (L, W), 0.1),
        'rwkv_lnx_b': nrm(ks[18], (L, W), 0.02),
        'w_out': nrm(ks[19], (L, D_MIX, D), D_MIX ** -0.5),
        'w_router': nrm(ks[20], (L, D, E), D ** -0.5),
        'w_gate': nrm(ks[21], (L, E, D, F), D ** -0.5),
        'w_up': nrm(ks[22], (L, E, D, F), D ** -0.5),
        'w_down': nrm(ks[23], (L, E, F, D), F ** -0.5),
    }

def first_block(x, c, ctx, c_ctx, w_mod, b_mod, norm_gains, w_in, rwkv_conv, rwkv_w0, rwkv_w2, rwkv_a0, rwkv_a2,
              rwkv_g2, rwkv_k_k, rwkv_k_a, rwkv_r_k, rwkv_lnx_w, rwkv_lnx_b, w_out, w_router, w_gate, w_up, w_down):
    for i in range(DEPTH):
        need_ctx = i < DEPTH - 1
        sh1, sc1, gt1, sh2, sc2, gt2 = jnp.split((jax.nn.silu(c) @ w_mod[i] + b_mod[i])[:, None, :], 6, axis=-1)
        csh1, csc1, cgt1, csh2, csc2, cgt2 = jnp.split(jax.nn.silu(c_ctx) @ w_mod[i] + b_mod[i], 6, axis=-1)
        g_pre_mix, g_post_mix, g_pre_ffn, g_post_ffn = norm_gains[i]
        h = rms_norm(x, g_pre_mix) * (1.0 + sc1) + sh1
        hc = rms_norm(ctx, g_pre_mix) * (1.0 + csc1) + csh1
        mix, mix_c = token_mix(h, hc, w_in[i], rwkv_conv[i], rwkv_w0[i], rwkv_w2[i], rwkv_a0[i], rwkv_a2[i],
                               rwkv_g2[i], rwkv_k_k[i], rwkv_k_a[i], rwkv_r_k[i], rwkv_lnx_w[i], rwkv_lnx_b[i],
                               w_out[i], need_ctx)
        x = x + gt1 * rms_norm(mix, g_post_mix)
        h2 = rms_norm(x, g_pre_ffn) * (1.0 + sc2) + sh2
        x = x + gt2 * rms_norm(ec_moe(h2, w_router[i], w_gate[i], w_up[i], w_down[i]), g_post_ffn)
        if need_ctx:
            ctx = ctx + cgt1 * rms_norm(mix_c, g_post_mix)
            hc2 = rms_norm(ctx, g_pre_ffn) * (1.0 + csc2) + csh2
            ctx = ctx + cgt2 * rms_norm(ec_moe(hc2, w_router[i], w_gate[i], w_up[i], w_down[i]), g_post_ffn)
    return x


CHUNK_2 = 64
Q_BLOCK = 128
MAX_STREAM_OFFSET = 65536

LRU_WIDTH = D_MODEL
LRU_BLOCKS = 8
CONV_WIDTH = 4
LRU_C = 8.0

ATTN_HEADS = 8
ATTN_HEAD_DIM = D_MODEL // (2 * ATTN_HEADS)
ATTN_V_DIM = 2 * ATTN_HEAD_DIM
ATTN_QK_WIDTH = ATTN_HEADS * 2 * ATTN_HEAD_DIM
ATTN_WIDTH = ATTN_HEADS * ATTN_V_DIM
ROPE_THETA = 500000.0
ROT_DIMS = ATTN_HEAD_DIM // 4

MEM_TOKENS = 256
MEM_HEADS = 4
MEM_HEAD_DIM = 128
MEM_WIDTH = MEM_HEADS * MEM_HEAD_DIM

N_GROUPS = 4
EXPERTS_PER_GROUP = 8
N_EXPERTS_2 = N_GROUPS * EXPERTS_PER_GROUP
TOP_K = 2
EXPERT_FF = 512
EXPERT_BLOCK = 128

IN_WIDTHS = (LRU_WIDTH, LRU_WIDTH, ATTN_QK_WIDTH, ATTN_QK_WIDTH, ATTN_WIDTH, D_MODEL, D_MODEL)
EPS = 1e-6
NEG_INF = -1e30


def rms_norm_2(x, g):
    xf = x.astype(jnp.float32)
    y = xf * lax.rsqrt(jnp.mean(xf * xf, axis=-1, keepdims=True) + EPS)
    return (y * g.astype(jnp.float32)).astype(x.dtype)

def rotary_tables(positions):
    half = ROT_DIMS // 2
    inv_freq = jnp.exp(-math.log(ROPE_THETA) * jnp.arange(half, dtype=jnp.float32) / half)
    ang = positions.astype(jnp.float32)[..., None] * inv_freq
    return jnp.cos(ang)[:, :, None, None, :], jnp.sin(ang)[:, :, None, None, :]

def rope_partial(x, cos, sin):
    half = ROT_DIMS // 2
    xr = x[..., :ROT_DIMS].astype(jnp.float32)
    x1, x2 = xr[..., :half], xr[..., half:]
    rot = jnp.concatenate([x1 * cos - x2 * sin, x2 * cos + x1 * sin], axis=-1)
    return jnp.concatenate([rot.astype(x.dtype), x[..., ROT_DIMS:]], axis=-1)

def causal_depthwise_conv(x, w, b):
    k = w.shape[0]
    y = lax.conv_general_dilated(x, w[:, None, :].astype(x.dtype), window_strides=(1,),
                                 padding=((k - 1, 0),), dimension_numbers=('NWC', 'WIO', 'NWC'),
                                 feature_group_count=x.shape[-1])
    return y + b

def block_diag_linear(x, w, b):
    bsz, s, c = x.shape
    nb, bw, _ = w.shape
    y = jnp.einsum('bsnc,ncd->bsnd', x.reshape(bsz, s, nb, bw), w).reshape(bsz, s, c)
    return y + b

def rg_lru(x, wa, ba, wx, bx, lam):
    r = jax.nn.sigmoid(block_diag_linear(x, wa, ba).astype(jnp.float32))
    i = jax.nn.sigmoid(block_diag_linear(x, wx, bx).astype(jnp.float32))
    log_a = -LRU_C * r * jax.nn.softplus(-lam.astype(jnp.float32))
    a = jnp.exp(log_a)
    b = jnp.sqrt(-jnp.expm1(2.0 * log_a)) * i * x.astype(jnp.float32)

    def combine(left, right):
        a_l, b_l = left
        a_r, b_r = right
        return a_l * a_r, a_r * b_l + b_r

    _, h = lax.associative_scan(combine, (a, b), axis=1)
    return h.astype(x.dtype)

def diff_attention(q, k, v, cos, sin, q_norm, k_norm, lam, lambda_init, subln):
    bsz, s, _ = q.shape
    q = q.reshape(bsz, s, ATTN_HEADS, 2, ATTN_HEAD_DIM)
    k = k.reshape(bsz, s, ATTN_HEADS, 2, ATTN_HEAD_DIM)
    v = v.reshape(bsz, s, ATTN_HEADS, ATTN_V_DIM)
    q = rope_partial(rms_norm_2(q, q_norm), cos, sin) * (ATTN_HEAD_DIM ** -0.5)
    k = rope_partial(rms_norm_2(k, k_norm), cos, sin)
    outs = []
    for blk in range(s // Q_BLOCK):
        q0, q1 = blk * Q_BLOCK, (blk + 1) * Q_BLOCK
        sc = jnp.einsum('bqhmd,bkhmd->bhmqk', q[:, q0:q1], k[:, :q1]).astype(jnp.float32)
        mask = (jnp.arange(q1) // CHUNK_2)[None, :] <= (jnp.arange(q0, q1) // CHUNK_2)[:, None]
        p = jax.nn.softmax(jnp.where(mask, sc, NEG_INF), axis=-1)
        w = p[:, :, 0] - lam * p[:, :, 1]
        outs.append(jnp.einsum('bhqk,bkhd->bqhd', w.astype(v.dtype), v[:, :q1]))
    o = jnp.concatenate(outs, axis=1)
    o = rms_norm_2(o, subln) * (1.0 - lambda_init)
    return o.reshape(bsz, s, ATTN_WIDTH)

def memory_cross_attention(x, mem, norm_cx, norm_mem, w_cq, w_ckv, cq_norm, ck_norm, w_co):
    bsz, s, _ = x.shape
    m = mem.shape[1]
    q = (rms_norm_2(x, norm_cx) @ w_cq).reshape(bsz, s, MEM_HEADS, MEM_HEAD_DIM)
    kv = rms_norm_2(mem, norm_mem) @ w_ckv
    k = kv[..., :MEM_WIDTH].reshape(bsz, m, MEM_HEADS, MEM_HEAD_DIM)
    v = kv[..., MEM_WIDTH:].reshape(bsz, m, MEM_HEADS, MEM_HEAD_DIM)
    q = rms_norm_2(q, cq_norm) * (MEM_HEAD_DIM ** -0.5)
    k = rms_norm_2(k, ck_norm)
    p = jax.nn.softmax(jnp.einsum('bqhd,bkhd->bhqk', q, k).astype(jnp.float32), axis=-1)
    o = jnp.einsum('bhqk,bkhd->bqhd', p.astype(v.dtype), v).reshape(bsz, s, MEM_WIDTH)
    return o @ w_co

def hierarchical_moe(h, w_group, b_group, w_router, b_router, w_gate_up, w_down):
    bsz, s, d = h.shape
    n = bsz * s
    a_tot = n * TOP_K
    hf = h.reshape(n, d)
    gp = jax.nn.softmax((hf @ w_group).astype(jnp.float32) + b_group.astype(jnp.float32), axis=-1)
    gval, gidx = lax.top_k(gp, 1)
    el = ((hf @ w_router).astype(jnp.float32) + b_router.astype(jnp.float32))
    el = el.reshape(n, N_GROUPS, EXPERTS_PER_GROUP)
    el = jnp.take_along_axis(el, gidx[:, :, None], axis=1)[:, 0]
    ev, eidx = lax.top_k(el, TOP_K)
    ew = jax.nn.softmax(ev, axis=-1) * gval
    expert_id = (gidx * EXPERTS_PER_GROUP + eidx).reshape(-1)
    token_id = jnp.repeat(jnp.arange(n, dtype=jnp.int32), TOP_K)
    weight = ew.reshape(-1)
    order = jnp.argsort(expert_id)
    sorted_e = expert_id[order]
    counts = jnp.bincount(expert_id, length=N_EXPERTS_2)
    padded = (counts + EXPERT_BLOCK - 1) // EXPERT_BLOCK * EXPERT_BLOCK
    start = jnp.cumsum(counts) - counts
    pend = jnp.cumsum(padded)
    pstart = pend - padded
    dest = pstart[sorted_e] + jnp.arange(a_tot) - start[sorted_e]
    p_rows = a_tot + N_EXPERTS_2 * EXPERT_BLOCK
    n_blk = p_rows // EXPERT_BLOCK
    buf_tok = jnp.full((p_rows,), n, jnp.int32).at[dest].set(token_id[order])
    buf_w = jnp.zeros((p_rows,), jnp.float32).at[dest].set(weight[order])
    blk_e = jnp.minimum(jnp.searchsorted(pend, jnp.arange(n_blk) * EXPERT_BLOCK, side='right'),
                        N_EXPERTS_2 - 1)
    h_pad = jnp.concatenate([hf, jnp.zeros((1, d), hf.dtype)], axis=0)
    xs = h_pad[buf_tok].reshape(n_blk, EXPERT_BLOCK, d)

    def expert_block(args):
        xb, e = args
        gu = xb @ w_gate_up[e]
        return (jax.nn.silu(gu[:, :EXPERT_FF]) * gu[:, EXPERT_FF:]) @ w_down[e]

    ys = lax.map(expert_block, (xs, blk_e)).reshape(p_rows, d)
    out = jnp.zeros((n + 1, d), ys.dtype).at[buf_tok].add(ys * buf_w[:, None].astype(ys.dtype))
    return out[:n].reshape(bsz, s, d)

def second_inputs(seed: int = 0) -> dict:
    key = jax.random.key(seed)
    keys = iter(jax.random.split(key, 48))

    def normal(shape, scale):
        return jax.random.normal(next(keys), shape, jnp.float32) * scale

    def gain(n):
        return 1.0 + normal((DEPTH, n), 0.02)

    bw = LRU_WIDTH // LRU_BLOCKS
    u = jax.random.uniform(next(keys), (DEPTH, LRU_WIDTH), jnp.float32, 0.9, 0.999)
    p = u ** (1.0 / LRU_C)
    lru_lambda = jnp.log(p) - jnp.log1p(-p)
    offset = jax.random.randint(next(keys), (BATCH, 1), 0, MAX_STREAM_OFFSET, jnp.int32)
    positions = offset + jnp.arange(SEQ, dtype=jnp.int32)[None, :]
    return {
        "x": normal((BATCH, SEQ, D_MODEL), 1.0),
        "mem": normal((BATCH, MEM_TOKENS, D_MODEL), 1.0),
        "positions": positions,
        "norm_mix": gain(D_MODEL),
        "w_in": normal((DEPTH, D_MODEL, sum(IN_WIDTHS)), D_MODEL ** -0.5),
        "conv_w": normal((DEPTH, CONV_WIDTH, LRU_WIDTH), CONV_WIDTH ** -0.5),
        "conv_b": normal((DEPTH, LRU_WIDTH), 0.01),
        "lru_wa": normal((DEPTH, LRU_BLOCKS, bw, bw), bw ** -0.5),
        "lru_ba": normal((DEPTH, LRU_WIDTH), 0.01),
        "lru_wx": normal((DEPTH, LRU_BLOCKS, bw, bw), bw ** -0.5),
        "lru_bx": normal((DEPTH, LRU_WIDTH), 0.01),
        "lru_lambda": lru_lambda,
        "w_lru_o": normal((DEPTH, LRU_WIDTH, D_MODEL), LRU_WIDTH ** -0.5),
        "q_norm": gain(ATTN_HEAD_DIM),
        "k_norm": gain(ATTN_HEAD_DIM),
        "lambda_q1": normal((DEPTH, ATTN_HEAD_DIM), 0.1),
        "lambda_k1": normal((DEPTH, ATTN_HEAD_DIM), 0.1),
        "lambda_q2": normal((DEPTH, ATTN_HEAD_DIM), 0.1),
        "lambda_k2": normal((DEPTH, ATTN_HEAD_DIM), 0.1),
        "subln": gain(ATTN_V_DIM),
        "w_attn_o": normal((DEPTH, ATTN_WIDTH, D_MODEL), ATTN_WIDTH ** -0.5),
        "w_out": normal((DEPTH, D_MODEL, D_MODEL), D_MODEL ** -0.5),
        "norm_cx": gain(D_MODEL),
        "norm_mem": gain(D_MODEL),
        "w_cq": normal((DEPTH, D_MODEL, MEM_WIDTH), D_MODEL ** -0.5),
        "w_ckv": normal((DEPTH, D_MODEL, 2 * MEM_WIDTH), D_MODEL ** -0.5),
        "cq_norm": gain(MEM_HEAD_DIM),
        "ck_norm": gain(MEM_HEAD_DIM),
        "w_co": normal((DEPTH, MEM_WIDTH, D_MODEL), MEM_WIDTH ** -0.5),
        "norm_ffn": gain(D_MODEL),
        "w_group": normal((DEPTH, D_MODEL, N_GROUPS), D_MODEL ** -0.5),
        "b_group": normal((DEPTH, N_GROUPS), 0.01),
        "w_router": normal((DEPTH, D_MODEL, N_EXPERTS_2), D_MODEL ** -0.5),
        "b_router": normal((DEPTH, N_EXPERTS_2), 0.01),
        "w_gate_up": normal((DEPTH, N_EXPERTS_2, D_MODEL, 2 * EXPERT_FF), D_MODEL ** -0.5),
        "w_down": normal((DEPTH, N_EXPERTS_2, EXPERT_FF, D_MODEL), EXPERT_FF ** -0.5),
    }

def second_block(x, mem, positions, norm_mix, w_in, conv_w, conv_b, lru_wa, lru_ba, lru_wx, lru_bx,
              lru_lambda, w_lru_o, q_norm, k_norm, lambda_q1, lambda_k1, lambda_q2, lambda_k2,
              subln, w_attn_o, w_out, norm_cx, norm_mem, w_cq, w_ckv, cq_norm, ck_norm, w_co,
              norm_ffn, w_group, b_group, w_router, b_router, w_gate_up, w_down):
    cos, sin = rotary_tables(positions)
    splits = np.cumsum(IN_WIDTHS)[:-1].tolist()
    for layer in range(DEPTH):
        lambda_init = 0.8 - 0.6 * math.exp(-0.3 * layer)
        h = rms_norm_2(x, norm_mix[layer])
        proj = h @ w_in[layer]
        lru_in, lru_gate, q, k, v, g_lru, g_attn = jnp.split(proj, splits, axis=-1)
        xc = causal_depthwise_conv(lru_in, conv_w[layer], conv_b[layer])
        hr = rg_lru(xc, lru_wa[layer], lru_ba[layer], lru_wx[layer], lru_bx[layer], lru_lambda[layer])
        y_lru = (jax.nn.gelu(lru_gate) * hr) @ w_lru_o[layer]
        lam = (jnp.exp(jnp.sum(lambda_q1[layer].astype(jnp.float32) * lambda_k1[layer].astype(jnp.float32)))
               - jnp.exp(jnp.sum(lambda_q2[layer].astype(jnp.float32) * lambda_k2[layer].astype(jnp.float32)))
               + lambda_init)
        o_attn = diff_attention(q, k, v, cos, sin, q_norm[layer], k_norm[layer], lam, lambda_init,
                                subln[layer])
        y_attn = o_attn @ w_attn_o[layer]
        mixed = jax.nn.sigmoid(g_lru) * y_lru + jax.nn.sigmoid(g_attn) * y_attn
        x = x + mixed @ w_out[layer]
        x = x + memory_cross_attention(x, mem, norm_cx[layer], norm_mem[layer], w_cq[layer],
                                       w_ckv[layer], cq_norm[layer], ck_norm[layer], w_co[layer])
        x = x + hierarchical_moe(rms_norm_2(x, norm_ffn[layer]), w_group[layer], b_group[layer],
                                 w_router[layer], b_router[layer], w_gate_up[layer], w_down[layer])
    return x


def setup_inputs(seed=0):
    out = dict(first_inputs(seed))
    for name, value in second_inputs(seed + 1).items():
        if name != "x":
            out[name + "_2"] = value
    return out


def reference(
    x, c, ctx, c_ctx, w_mod, b_mod, norm_gains, w_in, rwkv_conv, rwkv_w0, rwkv_w2, rwkv_a0,
    rwkv_a2, rwkv_g2, rwkv_k_k, rwkv_k_a, rwkv_r_k, rwkv_lnx_w, rwkv_lnx_b, w_out, w_router,
    w_gate, w_up, w_down, mem_2, positions_2, norm_mix_2, w_in_2, conv_w_2, conv_b_2, lru_wa_2,
    lru_ba_2, lru_wx_2, lru_bx_2, lru_lambda_2, w_lru_o_2, q_norm_2, k_norm_2, lambda_q1_2,
    lambda_k1_2, lambda_q2_2, lambda_k2_2, subln_2, w_attn_o_2, w_out_2, norm_cx_2, norm_mem_2,
    w_cq_2, w_ckv_2, cq_norm_2, ck_norm_2, w_co_2, norm_ffn_2, w_group_2, b_group_2, w_router_2,
    b_router_2, w_gate_up_2, w_down_2,
):
    x = first_block(
        x, c, ctx, c_ctx, w_mod, b_mod, norm_gains, w_in, rwkv_conv, rwkv_w0, rwkv_w2, rwkv_a0,
        rwkv_a2, rwkv_g2, rwkv_k_k, rwkv_k_a, rwkv_r_k, rwkv_lnx_w, rwkv_lnx_b, w_out, w_router,
        w_gate, w_up, w_down,
    )
    return second_block(
        x, mem_2, positions_2, norm_mix_2, w_in_2, conv_w_2, conv_b_2, lru_wa_2, lru_ba_2,
        lru_wx_2, lru_bx_2, lru_lambda_2, w_lru_o_2, q_norm_2, k_norm_2, lambda_q1_2,
        lambda_k1_2, lambda_q2_2, lambda_k2_2, subln_2, w_attn_o_2, w_out_2, norm_cx_2,
        norm_mem_2, w_cq_2, w_ckv_2, cq_norm_2, ck_norm_2, w_co_2, norm_ffn_2, w_group_2,
        b_group_2, w_router_2, b_router_2, w_gate_up_2, w_down_2,
    )


_drawn_inputs = setup_inputs


def setup_inputs(seed=0):
    import zlib

    import numpy as np

    out = dict(_drawn_inputs(seed))
    spreads = {}
    factors = {'lru_ba_2': 24.692,
     'lru_bx_2': 8.0,
     'q_norm_2': 3.174,
     'k_norm_2': 3.111,
     'lambda_q1_2': 8.0,
     'lambda_k1_2': 8.0,
     'subln_2': 3.581,
     'norm_cx_2': 6.627,
     'norm_mem_2': 5.928,
     'cq_norm_2': 8.0,
     'ck_norm_2': 8.0,
     'b_group_2': 30.192,
     'b_router_2': 37.12,
     'lambda_q2_2': 8.0,
     'lambda_k2_2': 8.0,
     'norm_ffn_2': 8.0}
    for name, (base, spread) in spreads.items():
        noise = np.random.default_rng([zlib.crc32(name.encode()), seed]).standard_normal(out[name].shape)
        drawn = base * np.exp(spread * noise) if base else spread * noise
        out[name] = __import__('jax').numpy.asarray(drawn.astype(out[name].dtype))
    for name, factor in factors.items():
        out[name] = (out[name] * factor).astype(out[name].dtype)
    return out
```

```python
import math
from contextlib import ExitStack

import numpy as np

import concourse.bass as bass
from concourse import mybir

F32 = mybir.dt.float32
I32 = mybir.dt.int32
U32 = mybir.dt.uint32
ALU = mybir.AluOpType
ACT = mybir.ActivationFunctionType
AX_X = mybir.AxisListType.X
ds = bass.ds

P = 128
BANK = 512
D = 1024
KD = D // P
T = 1024
TC = 256
TT = T + TC
NT, NTC = T // P, TC // P
EPS = 1e-6

RET_HEADS, RET_DIM, GRID_W = 8, 64, 64
RW = 512
PAIRS = RW // P
GN_EPS = 64e-5
D_IN = 5 * RW + 3 * RW + 64 * 3 + 128 * 2
CH = 64
LEVELS = (2, 4, 8, 16, 32)
E1, CAP = 16, 128

HEADS2, HD2 = 8, 64
CHUNK2 = 64
MEM, MH = 256, 4
PROJ2 = 7 * D
GROUPS, EPG = 4, 8
E2 = GROUPS * EPG
FF2 = 512


def fill(n, parts):
    at, out = n, {}
    for name, width in parts:
        out[name] = at
        at += width
    return out, at


CONST, CW = fill(0, [("ident", 128), ("pair", 128), ("pairx", 128), ("ones", 128), ("lower", 128),
                     ("axrot", 128), ("rot2", 128), ("st_f", 256), ("st_b", 256),
                     ("ident2", 256), ("hm", 256), ("cmask", 128), ("idc", 64),
                     ("invf", 1), ("e32", 32), ("tok", 8)])
COLS, VW = fill(0, [("conv", 3 * 16), ("a0", 4), ("w0", 8), ("k_k", 4), ("k_a", 4), ("r_k", 4),
                    ("lnw", 4), ("lnb", 4),
                    ("norm_mix", 8), ("conv2", 32), ("conv2b", 8), ("ba", 8), ("bx", 8), ("lam", 8),
                    ("qn", 1), ("kn", 1), ("subln", 1), ("norm_cx", 8), ("norm_mem", 8),
                    ("cqn", 1), ("ckn", 1)])
MOD_G1, MOD_S1, MOD_CG1, MOD_CS1, MOD_GT1, MOD_G2, MOD_S2, MOD_GT2 = range(8)


class Stage:

    def __init__(self, nc, name):
        self.nc, self.name, self.ctx, self.sems = nc, name, ExitStack(), []

    def __enter__(self):
        return self

    def sb(self, name, shape, dt=F32):
        return self.ctx.enter_context(self.nc.sbuf_tensor(f"{self.name}_{name}", shape, dt))

    def sem(self, name):
        s = self.ctx.enter_context(self.nc.semaphore(f"{self.name}_{name}"))
        self.sems.append(s)
        return s

    def __exit__(self, *exc):
        if exc[0] is None:
            with self.nc.Block() as block:
                @block.gpsimd
                def _(pool):
                    for s in self.sems:
                        pool.sem_clear(s)
        self.ctx.close()
        return False


class Steps:

    def __init__(self, sem, base=0):
        self.sem, self.n = sem, base

    def __call__(self, instruction):
        instruction.then_inc(self.sem, 1)
        self.n = self.n + 1
        return self.n


def modulation(nc, bank, w_mod, b_mod, c, c_ctx, gains, mod):
    N = 6 * D
    NG = N // BANK
    with Stage(nc, "mod") as st:
        cc = st.sb("cc", [P, KD, 2])
        sc = st.sb("sc", [P, KD, 2])
        w = st.sb("w", [P, 2, KD, BANK])
        bias = st.sb("bias", [2, N])
        m = st.sb("m", [2, N])
        g = st.sb("g", [2, 4 * D])
        o = st.sb("o", [2, 4, D])
        c_in, g_in, w_in = st.sem("c_in"), st.sem("g_in"), [st.sem("w_in0"), st.sem("w_in1")]
        silu, mm, added, vec, out = st.sem("silu"), st.sem("mm"), st.sem("added"), st.sem("vec"), st.sem("out")
        with nc.Block() as block:
            @block.sync
            def _(sp):
                with nc.allow_non_contiguous_dma("vectors as columns"):
                    sp.dma_start(cc[:, :, 0], c.rearrange("o (k p) -> p (o k)", p=P)).then_inc(c_in, 16)
                    sp.dma_start(cc[:, :, 1], c_ctx.rearrange("(k p) -> p k", p=P)).then_inc(c_in, 16)
                for r in range(2):
                    sp.dma_start(bias[r:r + 1, :], b_mod[0:1, :]).then_inc(g_in, 16)
                    sp.dma_start(g[r:r + 1, :], gains.rearrange("o a d -> o (a d)")).then_inc(g_in, 16)
                for n in range(NG):
                    if n >= 2:
                        sp.wait_ge(mm, n - 1)
                    sp.dma_start(w[:, n % 2], w_mod[0, :, n * BANK:(n + 1) * BANK]
                                 .rearrange("(k p) n -> p k n", p=P)).then_inc(w_in[n % 2], 16)
                sp.wait_ge(vec, 4)
                rows = [(MOD_G1, o[0:1, 0]), (MOD_CG1, o[1:2, 0]), (MOD_S1, m[0:1, 0:D]), (MOD_CS1, m[1:2, 0:D]),
                        (MOD_GT1, o[0:1, 1]), (MOD_G2, o[0:1, 2]), (MOD_S2, m[0:1, 3 * D:4 * D]),
                        (MOD_GT2, o[0:1, 3])]
                for r, src in rows:
                    sp.dma_start(mod[r:r + 1, :], src).then_inc(out, 16)
                sp.wait_ge(out, 16 * len(rows))

            @block.scalar
            def _(act):
                act.wait_ge(c_in, 32)
                nc.scalar.activation(sc[:, :, :], cc[:, :, :], ACT.Silu).then_inc(silu, 1)

            @block.tensor
            def _(pe):
                pe.wait_ge(silu, 1)
                for n in range(NG):
                    pe.wait_ge(w_in[n % 2], 16 * (n // 2 + 1))
                    if n >= 2:
                        pe.wait_ge(added, n - 1)
                    for k in range(KD):
                        last = nc.tensor.matmul(bank[n % 2][0:2, :], sc[:, k, :], w[:, n % 2, k, :],
                                                start=(k == 0), stop=(k == KD - 1))
                    last.then_inc(mm, 1)

            @block.vector
            def _(dve):
                dve.wait_ge(g_in, 64)
                for n in range(NG):
                    dve.wait_ge(mm, n + 1)
                    c0 = n * BANK
                    nc.vector.tensor_tensor(m[:, c0:c0 + BANK], bank[n % 2][0:2, :], bias[:, c0:c0 + BANK],
                                            ALU.add).then_inc(added, 1)
                dve.wait_ge(added, NG)
                sh1, sc1, gt1, sh2, sc2, gt2 = (m[:, j * D:(j + 1) * D] for j in range(6))
                gain = [g[:, j * D:(j + 1) * D] for j in range(4)]
                nc.vector.scalar_tensor_tensor(o[:, 0], sc1, 1.0, gain[0], ALU.add, ALU.mult).then_inc(vec, 1)
                nc.vector.tensor_tensor(o[:, 1], gt1, gain[1], ALU.mult).then_inc(vec, 1)
                nc.vector.scalar_tensor_tensor(o[:, 2], sc2, 1.0, gain[2], ALU.add, ALU.mult).then_inc(vec, 1)
                nc.vector.tensor_tensor(o[:, 3], gt2, gain[3], ALU.mult).then_inc(vec, 1)


def norm_T(nc, bank, name, cst, x, ntok, actT, at, gcol=None, scol=None, gvec=None, svec=None,
           grow=None, srow=None, rows_out=None):
    n = ntok // P
    by_rows = grow is not None
    per = 2 if by_rows and srow is not None else 1
    with Stage(nc, name) as st:
        xt = st.sb("x", [P, n, D])
        sq = st.sb("sq", [P, D])
        ss = st.sb("ss", [P, n, 3])
        gs = st.sb("gs", [P, 2, KD])
        gb = st.sb("gb", [P, 2, D]) if by_rows else None
        x_in = [st.sem(f"x_in{i}") for i in range(4)]
        g_in, ssq, ms, root, rstd, scaled, stored = (st.sem(s) for s in
                                                     ("g_in", "ssq", "ms", "root", "rstd", "scaled", "stored"))
        tr, ev = st.sem("transposed"), [st.sem("ev_act"), st.sem("ev_dve")]
        ident = cst[:, CONST["ident"]:CONST["ident"] + P]
        if gcol is None:
            gcol, scol = gs[:, 0, :], gs[:, 1, :]
        has_s = scol is not None
        with nc.Block() as block:
            @block.sync
            def _(sp):
                if gvec is not None:
                    with nc.allow_non_contiguous_dma("vectors as columns"):
                        sp.dma_start(gs[:, 0, :], gvec.rearrange("o (k p) -> p (o k)", p=P)).then_inc(g_in, 16)
                        sp.dma_start(gs[:, 1, :], svec.rearrange("o (k p) -> p (o k)", p=P)).then_inc(g_in, 16)
                if by_rows:
                    sp.dma_start(gb[:, 0, :], grow.partition_broadcast(P).rearrange("p o d -> p (o d)"))\
                        .then_inc(g_in, 16)
                    if srow is not None:
                        sp.dma_start(gb[:, 1, :], srow.partition_broadcast(P).rearrange("p o d -> p (o d)"))\
                            .then_inc(g_in, 16)
                for i in range(n):
                    if i >= 4:
                        sp.wait_ge(ssq, i - 3)
                    sp.dma_start(xt[:, i, :], x[i * P:(i + 1) * P, :]).then_inc(x_in[i % 4], 16)
                if rows_out is not None:
                    for i in range(n):
                        sp.wait_ge(scaled, per * (i + 1))
                        sp.dma_start(rows_out[i * P:(i + 1) * P, :], xt[:, i, :]).then_inc(stored, 16)
                    sp.wait_ge(stored, 16 * n)

            def evac_act(act, i):
                act.wait_ge(tr, 2 * i + 1)
                if i == 0 and gvec is not None:
                    act.wait_ge(g_in, 32)
                for k in range(4):
                    dst, src = actT[:, k, at + i * P:at + (i + 1) * P], bank[2 * (i % 2)][:, k * P:(k + 1) * P]
                    if by_rows:
                        ins = nc.scalar.activation(dst, src, ACT.Copy)
                    elif has_s:
                        ins = nc.scalar.activation(dst, src, ACT.Identity, scale=gcol[:, k:k + 1], bias=scol[:, k:k + 1])
                    else:
                        ins = nc.scalar.activation(dst, src, ACT.Copy, scale=gcol[:, k:k + 1])
                    ins.then_inc(ev[0], 1)

            def evac_dve(dve, i):
                dve.wait_ge(tr, 2 * i + 2)
                if i == 0 and gvec is not None:
                    dve.wait_ge(g_in, 32)
                for k in range(4, 8):
                    dst = actT[:, k, at + i * P:at + (i + 1) * P]
                    src = bank[2 * (i % 2) + 1][:, (k - 4) * P:(k - 3) * P]
                    if by_rows:
                        ins = nc.vector.tensor_copy(dst, src)
                    elif has_s:
                        ins = nc.vector.tensor_scalar(dst, src, gcol[:, k:k + 1], scol[:, k:k + 1], ALU.mult, ALU.add)
                    else:
                        ins = nc.vector.tensor_scalar(dst, src, gcol[:, k:k + 1], None, ALU.mult)
                    ins.then_inc(ev[1], 1)

            @block.scalar
            def _(act):
                for i in range(n):
                    act.wait_ge(x_in[i % 4], 16 * (i // 4 + 1))
                    if i:
                        act.wait_ge(ssq, i)
                    nc.scalar.activation(sq[:, :], xt[:, i, :], ACT.Square, accum_out=ss[:, i, 0:1]).then_inc(ssq, 1)
                    act.wait_ge(ms, i + 1)
                    nc.scalar.activation(ss[:, i, 2:3], ss[:, i, 1:2], ACT.Sqrt).then_inc(root, 1)
                    if i:
                        evac_act(act, i - 1)
                evac_act(act, n - 1)

            @block.vector
            def _(dve):
                for i in range(n):
                    dve.wait_ge(ssq, i + 1)
                    nc.vector.tensor_scalar(ss[:, i, 1:2], ss[:, i, 0:1], 1.0 / D, EPS, ALU.mult, ALU.add)\
                        .then_inc(ms, 1)
                    dve.wait_ge(root, i + 1)
                    nc.vector.reciprocal(ss[:, i, 0:1], ss[:, i, 2:3]).then_inc(rstd, 1)
                    dve.wait_ge(rstd, i + 1)
                    if by_rows:
                        if i == 0:
                            dve.wait_ge(g_in, 32 if srow is not None else 16)
                        nc.vector.scalar_tensor_tensor(xt[:, i, :], xt[:, i, :], ss[:, i, 0:1], gb[:, 0, :],
                                                       ALU.mult, ALU.mult).then_inc(scaled, 1)
                        if srow is not None:
                            dve.wait_ge(scaled, 2 * i + 1)
                            nc.vector.tensor_tensor(xt[:, i, :], xt[:, i, :], gb[:, 1, :], ALU.add).then_inc(scaled, 1)
                    else:
                        nc.vector.tensor_scalar(xt[:, i, :], xt[:, i, :], ss[:, i, 0:1], None, ALU.mult)\
                            .then_inc(scaled, 1)
                    if i:
                        evac_dve(dve, i - 1)
                evac_dve(dve, n - 1)

            @block.tensor
            def _(pe):
                for i in range(n):
                    pe.wait_ge(scaled, per * (i + 1))
                    if i >= 2:
                        pe.wait_ge(ev[0], 4 * (i - 1))
                        pe.wait_ge(ev[1], 4 * (i - 1))
                    for k in range(KD):
                        ins = nc.tensor.transpose(bank[2 * (i % 2) + k // 4][:, (k % 4) * P:(k % 4 + 1) * P],
                                                  xt[:, i, k * P:(k + 1) * P], ident)
                        if k % 4 == 3:
                            ins.then_inc(tr, 1)


def gemm_T(nc, bank, name, actT, tok, w, col0, groups, tail, dst):
    chunks = [(a, min(BANK, tok - a)) for a in range(0, tok, BANK)]
    nch = len(chunks)
    blocks = BANK // P
    with Stage(nc, name) as st:
        wt = st.sb("w", [P, 2, KD, BANK])
        ob = st.sb("out", [P, 2, tok])
        w_in = [st.sem("w_in0"), st.sem("w_in1")]
        mm = [st.sem("mm_act"), st.sem("mm_dve")]
        ev = [st.sem("ev_act"), st.sem("ev_dve")]
        stored = [st.sem("stored0"), st.sem("stored1")]
        its = groups // 2

        def load(sp, c0, slot, width=BANK):
            sp.dma_start(wt[:, slot, :, 0:width], w[:, ds(c0, width)].rearrange("(k p) n -> p k n", p=P))\
                .then_inc(w_in[slot], 16)

        with nc.Block() as block:
            @block.sync
            def _(sp):
                def store(e, q, row, width):
                    sp.wait_ge(ev[e], q * nch + (nch + 1))
                    sp.dma_start(dst[ds(row, width), :], ob[0:width, e, :]).then_inc(stored[e], 16)

                def store_group(g, s, row):
                    for b in range(blocks):
                        store(b % 2, g * 2 + b // 2, row + b * P, P)

                for e in range(2):
                    sp.sem_inc(stored[e], 1)
                load(sp, col0, 0)
                load(sp, col0 + BANK, 1)
                if its > 1:
                    with sp.Fori(0, its - 1) as it:
                        for s in range(2):
                            store_group(it * 2 + s, s, it * (2 * BANK) + s * BANK)
                            load(sp, it * (2 * BANK) + (col0 + (2 + s) * BANK), s)
                for s in range(2):
                    store_group(groups - 2 + s, s, (groups - 2 + s) * BANK)
                    if s == 0 and tail:
                        load(sp, col0 + groups * BANK, 0, sum(tail))
                for b, width in enumerate(tail):
                    store(b % 2, its * 4 + b // 2, groups * BANK + b * P, width)
                for e in range(2):
                    n = its * 4 + sum(1 for b in range(len(tail)) if b % 2 == e)
                    sp.wait_ge(stored[e], 16 * n + 1)

            def products(pe, e, q, slot, c0, width):
                pe.wait_ge(ev[e], q * nch + 1)
                for c, (a, n) in enumerate(chunks):
                    for k in range(KD):
                        last = nc.tensor.matmul(bank[e * nch + c][0:width, 0:n], wt[:, slot, k, c0:c0 + width],
                                                actT[:, k, a:a + n], start=(k == 0), stop=(k == KD - 1))
                    last.then_inc(mm[e], 1)

            @block.tensor
            def _(pe):
                with pe.Fori(0, its) as it:
                    for s in range(2):
                        pe.wait_ge(w_in[s], it * 16 + 16)
                        for b in range(blocks):
                            products(pe, b % 2, it * 4 + (2 * s + b // 2), s, b * P, P)
                if tail:
                    pe.wait_ge(w_in[0], its * 16 + 16)
                    for b, width in enumerate(tail):
                        products(pe, b % 2, its * 4 + b // 2, 0, b * P, width)

            def evac(eng, e, q, width):
                eng.wait_ge(stored[e], q * 16 + 1)
                for c, (a, n) in enumerate(chunks):
                    eng.wait_ge(mm[e], q * nch + (c + 1))
                    o, i = ob[0:width, e, a:a + n], bank[e * nch + c][0:width, 0:n]
                    ins = nc.scalar.activation(o, i, ACT.Copy) if e == 0 else nc.vector.tensor_copy(o, i)
                    ins.then_inc(ev[e], 1)

            def drain_banks(eng, e):
                eng.sem_inc(ev[e], 1)
                with eng.Fori(0, its) as it:
                    for b in range(4):
                        evac(eng, e, it * 4 + b, P)
                for b, width in enumerate(tail):
                    if b % 2 == e:
                        evac(eng, e, its * 4 + b // 2, width)

            @block.scalar
            def _(act):
                drain_banks(act, 0)

            @block.vector
            def _(dve):
                drain_banks(dve, 1)


class Loop:

    def __init__(self, sem, turn, per):
        self.sem, self.base, self.per, self.k = sem, turn * per, per, 0

    def __call__(self, instruction):
        instruction.then_inc(self.sem, 1)
        self.k += 1
        return self.base + self.k

    def end(self):
        assert self.k == self.per, f"{self.sem}: {self.k} a turn, not {self.per}"


def retention(nc, bank, cst, tabs, uT, latT):
    NB = TT // P
    with Stage(nc, "ret") as st:
        q, k, v = st.sb("q", [P, TT]), st.sb("k", [P, TT]), st.sb("v", [P, TT])
        g = st.sb("g", [P, 2, T])
        din = st.sb("din", [P, 2, 2, P])
        qd, kd, cd = st.sb("qd", [P, 2, P]), st.sb("kd", [P, 2, P]), st.sb("cd", [P, 1])
        ax = st.sb("ax", [P, 2, T])
        kz = st.sb("kz", [P, 2, T])
        vz = st.sb("vz", [P, NB, 2, P])
        vr = st.sb("vr", [P, 2, P])
        tmp = st.sb("tmp", [P, 2, T])
        qs = st.sb("qs", [P, 2, T])
        kfb = st.sb("kfb", [P, 2, 2, P])
        kvm = st.sb("kvm", [P, 2, NB, P])
        S = st.sb("S", [P, 2, NT + 3, P])
        sc = st.sb("sc", [P, 2, 2, 2, P])
        y = st.sb("y", [P, 2, T])
        lat = st.sb("lat", [P, T])
        names = ("tab_in", "q_in", "k_in", "v_in", "g_in", "zeroed", "rot", "cosed", "roped", "halved", "tr",
                 "k_rows", "v_rows", "v_copied", "kv", "kv_kept", "scan", "states", "q_scaled", "scores", "sc_ready",
                 "y_mm", "y_ready", "squared", "sums", "ms", "root", "chain", "silu", "lat_ready", "stored")
        s = {n: st.sem(n) for n in names}
        ident, pair = (cst[:, CONST[n]:CONST[n] + P] for n in ("ident", "pair"))
        axrot = cst[:, CONST["axrot"]:CONST["axrot"] + P]
        LAT = slice(TC, TT)
        CHAIN = 10
        with nc.Block() as block:
            @block.sync
            def _(sp):
                sp.dma_start(ax[:, :, :], tabs["ax"].rearrange("a p t -> p a t")).then_inc(s["tab_in"], 16)
                sp.sem_inc(s["stored"], 1)
                with sp.Fori(0, PAIRS) as p:
                    for n, (t, a) in enumerate(((q, 0), (k, RW), (v, 2 * RW))):
                        sp.dma_start(t[:, :], uT[ds(p * P + a, P), :]).then_inc(s["qkv"[n] + "_in"], 16)
                    for d in range(2):
                        sp.dma_start(g[:, d, :], uT[ds(p * P + (3 + d) * RW, P), LAT]).then_inc(s["g_in"], 16)
                    for d in range(2):
                        sp.dma_start(din[:, d], tabs["din"][d, ds(p * 2, 2)].rearrange("h j i -> j h i"))\
                            .then_inc(s["tab_in"], 16)
                    for t, n in ((qd, "qd"), (kd, "kd")):
                        sp.dma_start(t[:, :, :], tabs[n][:, ds(p, 1)].rearrange("d o p t -> p (d o) t"))\
                            .then_inc(s["tab_in"], 16)
                    sp.dma_start(cd[:, :], tabs["cdec"][ds(p, 1)].rearrange("o p t -> p (o t)"))\
                        .then_inc(s["tab_in"], 16)
                    sp.wait_ge(s["lat_ready"], p + 1)
                    sp.dma_start(latT[ds(p * P, P), :], lat[:, :]).then_inc(s["stored"], 16)
                sp.wait_ge(s["stored"], 16 * PAIRS + 1)

            TAB = 80

            @block.gpsimd
            def _(pool):
                nc.gpsimd.memset(kz[:, :, :], 0.0).then_inc(s["zeroed"], 1)
                nc.gpsimd.memset(vz[:, :, :, :], 0.0).then_inc(s["zeroed"], 1)
                nc.gpsimd.memset(S[:, :, 0, :], 0.0).then_inc(s["zeroed"], 1)
                pool.wait_ge(s["zeroed"], 3)
                with pool.Fori(0, PAIRS) as p:
                    pool.wait_ge(s["tab_in"], p * TAB + (TAB + 16))
                    for i, t in enumerate((q, k)):
                        pool.wait_ge(s["rot"], p * 4 + (2 * i + 2))
                        nc.gpsimd.tensor_tensor(t[:, LAT], t[:, LAT], ax[:, 0, :], ALU.mult).then_inc(s["cosed"], 1)
                    pool.wait_ge(s["roped"], p * 4 + 4)
                    for d in range(2):
                        nc.gpsimd.tensor_tensor(qs[:, d, :].rearrange("p (n t) -> p n t", t=P),
                                                q[:, LAT].rearrange("p (n t) -> p n t", t=P),
                                                qd[:, d, :].unsqueeze(1).to_broadcast([P, NT, P]),
                                                ALU.mult).then_inc(s["q_scaled"], 1)

            @block.tensor
            def _(pe):
                pe.wait_ge(s["zeroed"], 3)
                with pe.Fori(0, PAIRS) as p:
                    for n, (t, nm) in enumerate(((q, "q_in"), (k, "k_in"))):
                        pe.wait_ge(s[nm], p * 16 + 16)
                        for c in range(2):
                            nc.tensor.matmul(bank[2 * n + c][:, :], axrot, t[:, TC + c * BANK:TC + (c + 1) * BANK],
                                             start=True, stop=True).then_inc(s["rot"], 1)
                    pe.wait_ge(s["v_in"], p * 16 + 16)
                    pe.wait_ge(s["roped"], p * 4 + 4)

                    def rows(j):
                        if j >= 2:
                            pe.wait_ge(s["k_rows"], p * (2 * NB) + 2 * (j - 1))
                            pe.wait_ge(s["v_rows"], p * NB + (j - 1))
                        b = bank[4 + j % 2]
                        nc.tensor.transpose(b[:, 0:P], k[:, j * P:(j + 1) * P], ident)
                        nc.tensor.transpose(bank[j % 2][:, 0:P], v[:, j * P:(j + 1) * P], ident).then_inc(s["tr"], 1)

                    rows(0)
                    for j in range(NB):
                        if j + 1 < NB:
                            rows(j + 1)
                        pe.wait_ge(s["k_rows"], p * (2 * NB) + 2 * (j + 1))
                        pe.wait_ge(s["v_rows"], p * NB + (j + 1))
                        if j >= 2:
                            pe.wait_ge(s["kv_kept"], p * NB + (j - 1))
                        for d in range(2):
                            ins = nc.tensor.matmul(bank[6 + j % 2][:, d * P:(d + 1) * P], kfb[:, j % 2, d, :],
                                                   vr[:, j % 2, :], start=True, stop=True)
                        ins.then_inc(s["kv"], 1)
                    pe.wait_ge(s["halved"], p * 2 + 2)
                    pe.wait_ge(s["v_copied"], p * (2 * NB) + 2 * NB)
                    pe.wait_ge(s["q_scaled"], p * 2 + 2)

                    def scores(j):
                        if j >= 2:
                            pe.wait_ge(s["sc_ready"], p * (2 * NT) + 2 * (j - 1))
                        t = slice(j * P, (j + 1) * P)
                        for h in range(2):
                            ins = nc.tensor.matmul(bank[j % 2][:, h * P:(h + 1) * P], kz[:, h, t], q[:, TC + j * P:TC + (j + 1) * P],
                                                   start=True, stop=True)
                        ins.then_inc(s["scores"], 1)

                    scores(0)
                    for j in range(NT):
                        if j + 1 < NT:
                            scores(j + 1)
                        if j == 0:
                            pe.wait_ge(s["states"], p + 1)
                        pe.wait_ge(s["sc_ready"], p * (2 * NT) + 2 * (j + 1))
                        if j >= 2:
                            pe.wait_ge(s["y_ready"], p * NT + (j - 1))
                        for d in range(2):
                            o = bank[2 + j % 2][:, d * P:(d + 1) * P]
                            nc.tensor.matmul(o, S[:, d, 2 + j, :], qs[:, d, j * P:(j + 1) * P], start=True, stop=False)
                            for h in range(2):
                                ins = nc.tensor.matmul(o, vz[:, 2 + j, h, :], sc[:, j % 2, d, h, :],
                                                       start=False, stop=(h == 1))
                        ins.then_inc(s["y_mm"], 1)
                    for d in range(2):
                        pe.wait_ge(s["squared"], p * 2 + (d + 1))
                        for c in range(2):
                            nc.tensor.matmul(bank[4 + 2 * d + c][:, :], pair, tmp[:, d, c * BANK:(c + 1) * BANK],
                                             start=True, stop=True).then_inc(s["sums"], 1)

            @block.scalar
            def _(act):
                act.wait_ge(s["zeroed"], 3)
                with act.Fori(0, PAIRS) as p:
                    act.wait_ge(s["roped"], p * 4 + 4)
                    for h in range(2):
                        r = slice(64 * h, 64 * h + 64)
                        nc.scalar.activation(kz[r, h, :], k[r, LAT], ACT.Copy).then_inc(s["halved"], 1)
                    for j in range(NB):
                        act.wait_ge(s["tr"], p * NB + (j + 1))
                        if j >= 2:
                            act.wait_ge(s["kv"], p * NB + (j - 1))
                        nc.scalar.activation(vr[:, j % 2, :], bank[j % 2][:, 0:P], ACT.Copy)\
                            .then_inc(s["v_rows"], 1)
                        act.wait_ge(s["v_rows"], p * NB + (j + 1))
                        for h in range(2):
                            c = slice(64 * h, 64 * h + 64)
                            nc.scalar.activation(vz[:, j, h, c], vr[:, j % 2, c], ACT.Copy).then_inc(s["v_copied"], 1)
                    for j in range(NT):
                        act.wait_ge(s["y_mm"], p * NT + (j + 1))
                        nc.scalar.activation(y[:, :, j * P:(j + 1) * P],
                                             bank[2 + j % 2][:, 0:2 * P].rearrange("p (d t) -> p d t", d=2),
                                             ACT.Copy).then_inc(s["y_ready"], 1)
                    act.wait_ge(s["y_ready"], p * NT + NT)
                    for d in range(2):
                        nc.scalar.activation(tmp[:, d, :], y[:, d, :], ACT.Square).then_inc(s["squared"], 1)
                    act.wait_ge(s["ms"], p * 4 + 4)
                    nc.scalar.activation(tmp[:, :, :], tmp[:, :, :], ACT.Sqrt).then_inc(s["root"], 1)
                    act.wait_ge(s["g_in"], p * 32 + 32)
                    for d in range(2):
                        nc.scalar.activation(g[:, d, :], g[:, d, :], ACT.Silu).then_inc(s["silu"], 1)

            def keep(dve, p, j):
                dve.wait_ge(s["kv"], p * NB + (j + 1))
                nc.vector.tensor_tensor(kvm[:, :, j, :], bank[6 + j % 2][:, 0:2 * P].rearrange("p (d e) -> p d e", d=2),
                                        pair.unsqueeze(1).to_broadcast([P, 2, P]), ALU.mult).then_inc(s["kv_kept"], 1)

            @block.vector
            def _(dve):
                dve.wait_ge(s["zeroed"], 3)
                with dve.Fori(0, PAIRS) as p:
                    link = Loop(s["chain"], p, CHAIN)
                    dve.wait_ge(s["tab_in"], p * TAB + (TAB + 16))
                    for n, t in enumerate((q, k)):
                        for c in range(2):
                            tc = slice(c * BANK, (c + 1) * BANK)
                            dve.wait_ge(s["rot"], p * 4 + (2 * n + c + 1))
                            dve.wait_ge(s["chain"], link(nc.vector.tensor_tensor(
                                tmp[:, n, tc], bank[2 * n + c][:, :], ax[:, 1, tc], ALU.mult)))
                            dve.wait_ge(s["cosed"], p * 2 + (n + 1))
                            o = t[:, TC + c * BANK:TC + (c + 1) * BANK]
                            nc.vector.tensor_tensor(o, o, tmp[:, n, tc], ALU.add).then_inc(s["roped"], 1)
                    for j in range(NB):
                        dve.wait_ge(s["tr"], p * NB + (j + 1))
                        if j >= 2:
                            dve.wait_ge(s["kv"], p * NB + (j - 1))
                        for d in range(2):
                            nc.vector.tensor_tensor(kfb[:, j % 2, d, :], bank[4 + j % 2][:, 0:P], kd[:, d, :],
                                                    ALU.mult).then_inc(s["k_rows"], 1)
                        if j:
                            keep(dve, p, j - 1)
                    keep(dve, p, NB - 1)
                    dve.wait_ge(s["kv_kept"], p * NB + NB)
                    n = 0
                    for d in range(2):
                        order = list(range(NB)) if d == 0 else [1, 0] + list(range(NB - 1, 1, -1))
                        before = 0
                        for i, j in enumerate(order[:-1]):
                            after = order[i + 1] if i >= 1 else NT + 2
                            nc.vector.scalar_tensor_tensor(S[:, d, after, :], S[:, d, before, :], cd[:, 0:1],
                                                           kvm[:, d, j, :], ALU.mult, ALU.add)\
                                .then_inc(s["scan"] if not (d == 1 and i == NB - 2) else s["states"], 1)
                            if not (d == 1 and i == NB - 2):
                                n += 1
                                dve.wait_ge(s["scan"], p * (2 * NB - 3) + n)
                            before = after
                    for j in range(NT):
                        dve.wait_ge(s["scores"], p * NT + (j + 1))
                        if j >= 2:
                            dve.wait_ge(s["y_mm"], p * NT + (j - 1))
                        for d in range(2):
                            nc.vector.tensor_tensor(sc[:, j % 2, d], bank[j % 2][:, 0:2 * P].rearrange("p (h i) -> p h i", h=2),
                                                    din[:, d], ALU.mult).then_inc(s["sc_ready"], 1)
                    for d in range(2):
                        for c in range(2):
                            dve.wait_ge(s["sums"], p * 4 + (2 * d + c + 1))
                            nc.vector.tensor_scalar(tmp[:, d, c * BANK:(c + 1) * BANK], bank[4 + 2 * d + c][:, :],
                                                    1.0 / RET_DIM, EPS, ALU.mult, ALU.add).then_inc(s["ms"], 1)
                    dve.wait_ge(s["root"], p + 1)
                    for d in range(2):
                        dve.wait_ge(s["chain"], link(nc.vector.reciprocal(tmp[:, d, :], tmp[:, d, :])))
                    for d in range(2):
                        dve.wait_ge(s["chain"], link(nc.vector.tensor_tensor(y[:, d, :], y[:, d, :], tmp[:, d, :], ALU.mult)))
                    for d in range(2):
                        dve.wait_ge(s["silu"], p * 2 + (d + 1))
                        dve.wait_ge(s["chain"], link(nc.vector.tensor_tensor(y[:, d, :], y[:, d, :], g[:, d, :], ALU.mult)))
                    dve.wait_ge(s["stored"], p * 16 + 1)
                    nc.vector.tensor_tensor(lat[:, :], y[:, 0, :], y[:, 1, :], ALU.add).then_inc(s["lat_ready"], 1)
                    link.end()


NC = TT // CH
DECAY = math.exp(-0.5)
PCOL, PW = fill(0, [("conv_r", 3), ("conv_k", 3), ("conv_v", 3), ("a0", 1), ("w0", 2), ("k_k", 1), ("k_a", 1),
                    ("r_k", 1), ("lnw", 1), ("lnb", 1)])
PRIMED = ("a_f", "r_f", "a_b", "r_b", "b_f", "b_b", "k_f", "k_b")


def rwkv_prepare(nc, bank, cst, col, tabs, x, uT, prim, vT, wc, bonus, gate):
    U0 = 5 * RW
    NBK = TT // P
    CHS = [(0, BANK), (BANK, BANK), (2 * BANK, TT - 2 * BANK)]
    SEG = ((0, TC), (TC, TT))
    LAT = slice(TC, TT)
    w2, a2, g2 = x["rwkv_w2"][0], x["rwkv_a2"][0], x["rwkv_g2"][0]
    with Stage(nc, "prep") as st:
        raw = st.sb("raw", [P, 3, TT])
        u = st.sb("u", [P, 3, TT])
        wl, al = st.sb("wl", [P, TT]), st.sb("al", [64, TT])
        gl = st.sb("gl", [P, 2, T])
        keep = st.sb("keep", [P, TT])
        sig = st.sb("sig", [P, 2, TT])
        iclr = st.sb("iclr", [P, TT])
        cum = st.sb("cum", [P, 2, TT])
        ex = st.sb("ex", [P, 3, 2, TT])
        kk = st.sb("kk", [P, TT])
        prod = st.sb("prod", [P, TT])
        out = st.sb("out", [P, 2, TT])
        gt = st.sb("gt", [P, 3, T])
        pc = st.sb("pc", [P, PW])
        w2t, a2t, g2t = st.sb("w2t", [P, P]), st.sb("a2t", [64, P]), st.sb("g2t", [P, 2, P])
        names = ("lora_in", "lora", "u_in", "w_in", "z_mm", "sig_ready", "chain", "cum_ready", "exp_ready",
                 "kx_ready", "kx_sq", "ss_mm", "norm", "bonus_in", "bonus_mm", "g_mm", "g_ready", "out_ready",
                 "stored0", "stored1", "gt_ready", "gt_stored", "wc_stored", "pair_done")
        s = {n: st.sem(n) for n in names}
        stored = [s["stored0"], s["stored1"]]
        pair, pairx = (cst[:, CONST[n]:CONST[n] + P] for n in ("pair", "pairx"))
        chunked = [P, NC, CH]

        def conv(dst, src, w, rows, link, wait, segments):
            lo, hi = segments[0][0], segments[-1][1]
            o = lo
            wait(link(nc.vector.tensor_scalar(dst[:, 0:hi - o], src[:, lo:hi], w[1], None, ALU.mult)))
            for a, b in segments:
                wait(link(nc.vector.scalar_tensor_tensor(dst[:, a + 1 - o:b - o], src[:, a:b - 1], w[0],
                                                         dst[:, a + 1 - o:b - o], ALU.mult, ALU.add)))
                wait(link(nc.vector.scalar_tensor_tensor(dst[:, a - o:b - 1 - o], src[:, a + 1:b], w[2],
                                                         dst[:, a - o:b - 1 - o], ALU.mult, ALU.add)))

        with nc.Block() as block:
            @block.sync
            def _(sp):
                l0 = U0 + 3 * RW
                sp.dma_start(raw[:, 0, :], uT[l0:l0 + 128, :]).then_inc(s["lora_in"], 16)
                sp.dma_start(raw[0:64, 1, :], uT[l0 + 128:l0 + 192, :]).then_inc(s["lora_in"], 16)
                sp.dma_start(raw[:, 2, :], uT[l0 + 192:l0 + 320, :]).then_inc(s["lora_in"], 16)
                sp.dma_start(ex[:, 0, 0, :], uT[l0 + 320:l0 + 448, :]).then_inc(s["lora_in"], 16)

            @block.vector
            def _(dve):
                link = Steps(s["lora"])

                def wait(n):
                    dve.wait_ge(s["lora"], n)

                link(nc.vector.memset(keep[:, :], 1.0))
                wait(link.n)
                link(nc.vector.memset(keep[:, :].rearrange("p (n c) -> p n c", c=CH)[:, :, 0:1], 0.0))
                dve.wait_ge(s["lora_in"], 64)
                for n, (dst, src, rows, seg) in enumerate(((wl, raw[:, 0, :], P, SEG), (al, raw[0:64, 1, :], 64, SEG),
                                                           (gl[:, 0, :], raw[:, 2, :], P, SEG[1:]),
                                                           (gl[:, 1, :], ex[:, 0, 0, :], P, SEG[1:]))):
                    c0 = COLS["conv"] + 12 + n
                    conv(dst, src, [col[0:rows, c0 + 16 * t:c0 + 16 * t + 1] for t in range(3)], rows, link, wait, seg)
                assert link.n == LORA

            @block.scalar
            def _(act):
                act.wait_ge(s["lora"], LORA)
                nc.scalar.activation(wl[:, :], wl[:, :], ACT.Tanh).then_inc(s["g_ready"], 1)
                nc.scalar.activation(gl[:, :, :], gl[:, :, :], ACT.Sigmoid).then_inc(s["g_ready"], 1)
                act.wait_ge(s["g_ready"], 2)

        with nc.Block() as block:
            @block.sync
            def _(sp):
                for n in ("stored0", "stored1", "gt_stored"):
                    sp.sem_inc(s[n], 1)
                with sp.Fori(0, PAIRS) as p:
                    for n in range(2):
                        sp.dma_start(raw[:, n, :], uT[ds(p * P + (U0 + n * RW), P), :]).then_inc(s["u_in"], 16)
                    for h in range(2):
                        r = slice(64 * h, 64 * h + 64)
                        sp.dma_start(raw[r, 2, :], uT[ds(p * P + (U0 + 2 * RW + 64 * (1 - h)), 64), :])\
                            .then_inc(s["u_in"], 16)
                        sp.dma_start(w2t[r, :], w2[h, :, ds(p * P, P)]).then_inc(s["w_in"], 16)
                        for d in range(2):
                            sp.dma_start(g2t[:, d, r], g2[d, :, ds(p * P + 64 * (1 - h), 64)]).then_inc(s["w_in"], 16)
                    sp.dma_start(a2t[:, :], a2[:, ds(p * P, P)]).then_inc(s["w_in"], 16)
                    sp.dma_start(pc[:, :], tabs["pcols"][ds(p, 1)].rearrange("o p c -> p (o c)")).then_inc(s["w_in"], 16)
                    sp.wait_ge(s["kx_ready"], p + 1)
                    sp.dma_start(vT[ds(p * NBK, NBK)].rearrange("b c t -> c b t"),
                                 u[:, 2, :].rearrange("p (b t) -> p b t", t=P)).then_inc(s["wc_stored"], 16)
                    for n in range(8):
                        sp.wait_ge(s["out_ready"], p * 8 + (n + 1))
                        sp.dma_start(prim[ds(p * NBK, NBK), n].rearrange("b c t -> c b t"),
                                     out[:, n % 2, :].rearrange("p (b t) -> p b t", t=P))\
                            .then_inc(stored[n % 2], 16)
                    for d in range(2):
                        at = CH - 1 if d == 0 else 0
                        with nc.allow_non_contiguous_dma("one value in a chunk"):
                            for n in range(2):
                                sp.dma_start(wc[ds(p * NBK, NBK), d, :, n].rearrange("b c -> c b"),
                                             ex[:, 0, d, :].rearrange("p (b n c) -> p b n c", n=2, c=CH)[:, :, n, at])\
                                    .then_inc(s["wc_stored"], 16)
                    sp.wait_ge(s["gt_ready"], p * 3 + 3)
                    sp.dma_start(bonus[ds(p * P, P), :], gt[:, 2, :]).then_inc(s["gt_stored"], 16)
                    sp.dma_start(gate[:, ds(p * P, P), :].rearrange("d c t -> c d t"), gt[:, 0:2, :])\
                        .then_inc(s["gt_stored"], 16)
                    sp.wait_ge(s["wc_stored"], p * 80 + 80)
                    sp.wait_ge(s["gt_stored"], p * 32 + 33)
                    sp.wait_ge(stored[0], p * 64 + 65)
                    sp.wait_ge(stored[1], p * 64 + 65)
                    sp.sem_inc(s["pair_done"], 1)

            @block.tensor
            def _(pe):
                with pe.Fori(0, PAIRS) as p:
                    pe.wait_ge(s["w_in"], p * 128 + 128)
                    for n in range(3):
                        for c, (a, m) in enumerate(CHS):
                            if n == 2:
                                pe.wait_ge(s["sig_ready"], p * 9 + (c + 1))
                            lhsT, rhs = ((w2t[0:64, :], wl[0:64, a:a + m]), (w2t[64:128, :], wl[64:128, a:a + m]),
                                         (a2t[:, :], al[:, a:a + m]))[n]
                            nc.tensor.matmul(bank[3 * (n % 2) + c][:, 0:m], lhsT, rhs, start=True, stop=True)\
                                .then_inc(s["z_mm"], 1)
                    pe.wait_ge(s["sig_ready"], p * 9 + 9)
                    pe.wait_ge(s["kx_sq"], p + 1)
                    for c, (a, m) in enumerate(CHS):
                        nc.tensor.matmul(bank[c][:, 0:m], pair, prod[:, a:a + m], start=True, stop=True)\
                            .then_inc(s["ss_mm"], 1)
                    for d in range(2):
                        for c in range(2):
                            nc.tensor.matmul(bank[3 + 2 * d + c][:, :], g2t[:, d, :], gl[:, d, c * BANK:(c + 1) * BANK],
                                             start=True, stop=True).then_inc(s["g_mm"], 1)
                    pe.wait_ge(s["norm"], p * 3 + 3)
                    pe.wait_ge(s["bonus_in"], p + 1)
                    for c in range(2):
                        nc.tensor.matmul(bank[c][:, :], pairx, prod[:, TC + c * BANK:TC + (c + 1) * BANK],
                                         start=True, stop=True).then_inc(s["bonus_mm"], 1)

            @block.scalar
            def _(act):
                with act.Fori(0, PAIRS) as p:
                    act.wait_ge(s["w_in"], p * 128 + 128)
                    for n in range(3):
                        for c, (a, m) in enumerate(CHS):
                            act.wait_ge(s["z_mm"], p * 9 + (3 * n + c + 1))
                            o = (sig[:, 0, a:a + m], sig[:, 1, a:a + m], iclr[:, a:a + m])[n]
                            b = pc[:, PCOL["w0"] + n:PCOL["w0"] + n + 1] if n < 2 else pc[:, PCOL["a0"]:PCOL["a0"] + 1]
                            nc.scalar.activation(o, bank[3 * (n % 2) + c][:, 0:m], ACT.Sigmoid, bias=b)\
                                .then_inc(s["sig_ready"], 1)
                    act.wait_ge(s["kx_ready"], p + 1)
                    nc.scalar.activation(prod[:, :], kk[:, :], ACT.Square).then_inc(s["kx_sq"], 1)
                    for d in range(2):
                        for c in range(2):
                            act.wait_ge(s["g_mm"], p * 4 + (2 * d + c + 1))
                            nc.scalar.activation(gt[:, d, c * BANK:(c + 1) * BANK], bank[3 + 2 * d + c][:, :], ACT.Copy)\
                                .then_inc(s["g_ready"] if 2 * d + c < 3 else s["gt_ready"], 1)
                    for c, (a, m) in enumerate(CHS):
                        act.wait_ge(s["ss_mm"], p * 3 + (c + 1))
                        nc.scalar.activation(prod[:, a:a + m], bank[c][:, 0:m], ACT.Sqrt).then_inc(s["norm"], 1)
                    act.wait_ge(s["cum_ready"], p + 1)
                    nc.scalar.activation(ex[:, 2], cum[:, :, :], ACT.Exp, scale=-DECAY).then_inc(s["exp_ready"], 1)
                    nc.scalar.activation(ex[:, 0], raw[:, 0:2, :], ACT.Exp, scale=-DECAY).then_inc(s["exp_ready"], 1)
                    nc.scalar.activation(ex[:, 1], raw[:, 0:2, :], ACT.Exp, scale=DECAY).then_inc(s["exp_ready"], 1)

            @block.vector
            def _(dve):
                dve.sem_inc(s["pair_done"], 1)
                with dve.Fori(0, PAIRS) as p:
                    link = Loop(s["chain"], p, CHAIN)

                    def wait(n):
                        dve.wait_ge(s["chain"], n)

                    def c_(name, i=0):
                        return pc[:, PCOL[name] + i:PCOL[name] + i + 1]

                    dve.wait_ge(s["u_in"], p * 64 + 64)
                    dve.wait_ge(s["w_in"], p * 128 + 128)
                    dve.wait_ge(s["pair_done"], p + 1)
                    for n, nm in enumerate(("conv_r", "conv_k", "conv_v")):
                        conv(u[:, n, :], raw[:, n, :], [c_(nm, t) for t in range(3)], P, link, wait, SEG)
                    nc.vector.tensor_scalar(kk[:, :], u[:, 1, :], c_("k_k"), None, ALU.mult).then_inc(s["kx_ready"], 1)
                    dve.wait_ge(s["sig_ready"], p * 9 + 9)
                    wait(link(nc.vector.tensor_tensor_scan(raw[:, 0, :], keep[:, :], sig[:, 0, :], 0.0, ALU.mult, ALU.add)))
                    wait(link(nc.vector.tensor_tensor_scan(raw[:, 2, :], keep[:, :], sig[:, 1, :], 0.0, ALU.mult, ALU.add)))
                    link(nc.vector.tensor_tensor(cum[:, 0, :], raw[:, 0, :], sig[:, 0, :], ALU.subtract))
                    c2 = raw[:, 2, :].rearrange("p (n c) -> p n c", c=CH)
                    wait(link(nc.vector.tensor_tensor(cum[:, 1, :].rearrange("p (n c) -> p n c", c=CH),
                                                      c2[:, :, CH - 1:CH].to_broadcast(chunked), c2, ALU.subtract)))
                    nc.vector.tensor_tensor(raw[:, 1, :], cum[:, 1, :], sig[:, 1, :], ALU.add).then_inc(s["cum_ready"], 1)
                    wait(link(nc.vector.tensor_scalar(raw[:, 2, :], iclr[:, :], 1.0, c_("k_a"), ALU.subtract, ALU.mult)))
                    wait(link(nc.vector.scalar_tensor_tensor(raw[:, 2, :], raw[:, 2, :], 1.0, u[:, 1, :], ALU.add, ALU.mult)))
                    dve.wait_ge(s["norm"], p * 3 + 3)
                    wait(link(nc.vector.tensor_scalar(prod[:, :], prod[:, :], 1e-12, None, ALU.max)))
                    wait(link(nc.vector.reciprocal(prod[:, :], prod[:, :])))
                    wait(link(nc.vector.tensor_tensor(kk[:, :], kk[:, :], prod[:, :], ALU.mult)))
                    nc.vector.scalar_tensor_tensor(prod[:, :], u[:, 0, :], c_("r_k"), raw[:, 2, :], ALU.mult, ALU.mult)\
                        .then_inc(s["bonus_in"], 1)
                    wait(link(nc.vector.tensor_tensor(iclr[:, :], kk[:, :], iclr[:, :], ALU.mult)))
                    dve.wait_ge(s["exp_ready"], p * 3 + 3)
                    for n, nm in enumerate(PRIMED):
                        d = 0 if nm.endswith("f") else 1
                        dve.wait_ge(stored[n % 2], p * 64 + (n // 2 * 16 + 1))
                        o = out[:, n % 2, :]
                        if nm[0] == "a":
                            ins = nc.vector.scalar_tensor_tensor(o, kk[:, :], -1.0, ex[:, 2, d, :], ALU.mult, ALU.mult)
                        else:
                            a, e = {"r": (u[:, 0, :], 0), "b": (iclr[:, :], 1), "k": (raw[:, 2, :], 1)}[nm[0]]
                            ins = nc.vector.tensor_tensor(o, a, ex[:, e, d, :], ALU.mult)
                        ins.then_inc(s["out_ready"], 1)
                    for c in range(2):
                        dve.wait_ge(s["bonus_mm"], p * 2 + (c + 1))
                        nc.vector.tensor_tensor(gt[:, 2, c * BANK:(c + 1) * BANK], bank[c][:, :],
                                                u[:, 2, TC + c * BANK:TC + (c + 1) * BANK], ALU.mult)\
                            .then_inc(s["gt_ready"], 1)
                    link.end()


LORA = 18
CHAIN = 25


def rwkv_chunks(nc, bank, cst, tabs, prim, vT, wc, mt, nn, re, yi):
    NBK = TT // P
    UN = 4
    NL = len(LEVELS)
    with Stage(nc, "chunks") as st:
        ar = st.sb("ar", [P, 2, 2, 2, P])
        bk = st.sb("bk", [P, 2, 2, 2, 2, P])
        vt = st.sb("vt", [P, 2, P])
        wct = st.sb("wct", [P, 2, 2, 2])
        msk = st.sb("msk", [P, 2, NL + 1, 2 * P], I32)
        vrow = st.sb("vrow", [P, P])
        vz = st.sb("vz", [P, 2, P])
        vm = st.sb("vm", [P, 2, 2, CH])
        LL = st.sb("LL", [P, UN, 2, 2 * P])
        X = st.sb("X", [P, UN, 2 * P])
        T1 = st.sb("T1", [P, UN, P])
        rows = st.sb("rows", [P, UN, 2, P])
        bm = st.sb("bm", [P, UN, 2, CH])
        Y0 = st.sb("Y0", [P, UN, P])
        TT_ = st.sb("TT", [P, UN, P])
        tvm = st.sb("tvm", [P, UN, 2, CH])
        mts, nns = st.sb("mts", [P, 2, 2, CH]), st.sb("nns", [P, 2, 2, CH])
        res, yis = st.sb("res", [P, 2, P]), st.sb("yis", [P, 2, P])
        names = ("msk_in", "zeroed", "in0", "in1", "v_mm", "v_ev", "vz_ready", "g_mm", "g_ev", "x_init", "lab_mm", "lab_ev",
                 "x_one", "rows_mm", "rows_ev", "a_ev", "bm_ready", "lakv_mm", "lakv_ev", "t1_mm", "t1_ev", "p_mm", "x_ev",
                 "ta_mm", "ta_ev", "tvm_ready", "y_mm", "re_ev", "yi_ev", "m_mm", "mt_ev", "n_ev", "stored", "turns")
        s = {n: st.sem(n) for n in names}
        s_in = [s["in0"], s["in1"]]
        ident = cst[:, CONST["ident"]:CONST["ident"] + P]
        ident2 = cst[:, CONST["ident2"]:CONST["ident2"] + 2 * P]
        hm = [cst[:, CONST["hm"] + P * h:CONST["hm"] + P * (h + 1)] for h in range(2)]
        cmask = cst[:, CONST["cmask"]:CONST["cmask"] + P].rearrange("p (c k) -> p c k", c=2)
        idc = cst[:, CONST["idc"]:CONST["idc"] + CH]
        stm = [cst[:, CONST[n]:CONST[n] + 2 * P] for n in ("st_f", "st_b")]
        A = lambda u_: bank[u_]
        B = lambda u_: bank[4 + u_]
        ITS = PAIRS * NBK // 2

        def each(fn):
            for u_ in range(UN):
                fn(u_, u_ // 2, u_ % 2)

        with nc.Block() as block:
            @block.sync
            def _(sp):
                sp.sem_inc(s["stored"], 1)
                sp.dma_start(msk[:, :, :, :], tabs["msk"].rearrange("d l p c -> p d l c")).then_inc(s["msk_in"], 16)
                sp.wait_ge(s["zeroed"], 1)

                def load(q, k):
                    for d in range(2):
                        sp.dma_start(ar[:, k, d], prim[ds(q, 1), 2 * d:2 * d + 2].rearrange("o n c t -> c (o n) t"))\
                            .then_inc(s_in[k], 16)
                        for h in range(2):
                            r = slice(64 * h, 64 * h + 64)
                            for n in range(2):
                                sp.dma_start(bk[r, k, d, h, n, :], prim[ds(q, 1), 4 + 2 * n + d, r]
                                             .rearrange("o c t -> c (o t)")).then_inc(s_in[k], 16)
                    with nc.allow_non_contiguous_dma("four values a channel"):
                        sp.dma_start(wct[:, k], wc[ds(q, 1)].rearrange("o d c n -> c (o d) n")).then_inc(s_in[k], 16)
                    sp.dma_start(vt[:, k, :], vT[ds(q, 1)].rearrange("o c t -> c (o t)")).then_inc(s_in[k], 16)

                def store(q, k):
                    sp.wait_ge(s["mt_ev"], q * 2 + 3)
                    sp.wait_ge(s["n_ev"], q * 4 + 5)
                    sp.wait_ge(s["re_ev"], q * 4 + 5)
                    sp.wait_ge(s["yi_ev"], q * 4 + 5)
                    for dst, src in ((mt, mts), (nn, nns)):
                        sp.dma_start(dst[ds(q, 1)].rearrange("o d c n k -> n (o d) c k"), src[:, :, :, :])\
                            .then_inc(s["stored"], 16)
                    for dst, src in ((re, res), (yi, yis)):
                        sp.dma_start(dst[ds(q, 1)].rearrange("o d c t -> c (o d) t"), src[:, :, :])\
                            .then_inc(s["stored"], 16)

                for k in range(2):
                    load(k, k)
                with sp.Fori(0, ITS - 1) as it:
                    for k in range(2):
                        store(it * 2 + k, k)
                        load(it * 2 + (2 + k), k)
                for k in range(2):
                    store(2 * (ITS - 1) + k, k)
                sp.wait_ge(s["stored"], 64 * 2 * ITS + 1)

            INC = 16 * 12

            @block.gpsimd
            def _(pool):
                nc.gpsimd.memset(bk[:, :, :, :, :, :], 0.0).then_inc(s["zeroed"], 1)
                with pool.Fori(0, ITS) as it:
                    for k in range(2):
                        q = it * 2 + k
                        pool.wait_ge(s["m_mm"], q * 2 + 1)
                        for u_ in range(UN):
                            nc.gpsimd.tensor_tensor(X[:, u_, :], ident2, ident2, ALU.mult).then_inc(s["x_init"], 1)
                        pool.wait_ge(s["v_ev"], q + 1)
                        for h in range(2):
                            nc.gpsimd.tensor_tensor(vz[:, h, :], vrow[:, :], hm[1 - h], ALU.mult).then_inc(s["vz_ready"], 1)
                            vh = vrow[:, CH * (1 - h):CH * (1 - h) + CH]
                            nc.gpsimd.tensor_tensor(vm[:, h], vh.unsqueeze(1).to_broadcast([P, 2, CH]), cmask, ALU.mult)\
                                .then_inc(s["vz_ready"], 1)
                        for u_ in range(UN):
                            h = u_ % 2
                            pool.wait_ge(s["rows_ev"], q * 4 + (u_ + 1))
                            bh = rows[:, u_, 0, CH * h:CH * h + CH]
                            nc.gpsimd.tensor_tensor(bm[:, u_], bh.unsqueeze(1).to_broadcast([P, 2, CH]), cmask, ALU.mult)\
                                .then_inc(s["bm_ready"], 1)
                        for u_ in range(UN):
                            h = u_ % 2
                            pool.wait_ge(s["ta_ev"], q * 4 + (u_ + 1))
                            tv = TT_[:, u_, CH * (1 - h):CH * (1 - h) + CH]
                            nc.gpsimd.tensor_tensor(tvm[:, u_], tv.unsqueeze(1).to_broadcast([P, 2, CH]), cmask, ALU.mult)\
                                .then_inc(s["tvm_ready"], 1)

            @block.tensor
            def _(pe):
                pe.sem_inc(s["m_mm"], 1)
                with pe.Fori(0, ITS) as it:
                    for k in range(2):
                        q = it * 2 + k
                        pe.wait_ge(s_in[k], it * INC + INC)
                        pe.wait_ge(s["mt_ev"], q * 2 + 1)
                        pe.wait_ge(s["n_ev"], q * 4 + 1)

                        def g(u_, d, h):
                            for n in range(2):
                                ins = nc.tensor.matmul(A(u_)[:, n * 256:n * 256 + 256], bk[:, k, d, h, n, :],
                                                       ar[:, k, d].rearrange("p a t -> p (a t)"), start=True, stop=True)
                            ins.then_inc(s["g_mm"], 1)
                        each(g)
                        pe.wait_ge(s["re_ev"], q * 4 + 1)
                        pe.wait_ge(s["yi_ev"], q * 4 + 1)

                        def lab(u_, d, h):
                            nc.tensor.matmul(B(u_)[:, 0:P], ar[:, k, d, 0, :], bk[:, k, d, h, 0, :], start=True, stop=True)\
                                .then_inc(s["lab_mm"], 1)
                        each(lab)

                        def by_rows(u_, d, h):
                            pe.wait_ge(s["g_ev"], q * 4 + (u_ + 1))
                            nc.tensor.transpose(A(u_)[:, 0:P], bk[:, k, d, h, 0, :], ident)
                            nc.tensor.transpose(A(u_)[:, P:2 * P], bk[:, k, d, h, 1, :], ident)
                            nc.tensor.transpose(A(u_)[:, 2 * P:3 * P], ar[:, k, d, 0, :], ident).then_inc(s["rows_mm"], 1)
                        each(by_rows)
                        pe.wait_ge(s["x_one"], q * 4 + 1)
                        nc.tensor.transpose(B(0)[:, 0:P], vt[:, k, :], ident).then_inc(s["v_mm"], 1)
                        pe.wait_ge(s["v_ev"], q + 1)

                        def lakv(u_, d, h):
                            pe.wait_ge(s["x_one"], q * 4 + (u_ + 1))
                            nc.tensor.matmul(B(u_)[:, 0:P], LL[:, u_, 1, 0:P], vrow[:, :], start=True, stop=True)\
                                .then_inc(s["lakv_mm"], 1)
                        each(lakv)
                        for l in range(NL):
                            def t1(u_, d, h):
                                if l == 0:
                                    pe.wait_ge(s["rows_ev"], q * 4 + (u_ + 1))
                                    pe.wait_ge(s["a_ev"], q * 4 + (u_ + 1))
                                else:
                                    pe.wait_ge(s["x_ev"], q * 20 + (4 * (l - 1) + u_ + 1))
                                nc.tensor.matmul(A(u_)[:, 0:P], LL[:, u_, 0, 0:P], X[:, u_, 0:P], start=True, stop=True)\
                                    .then_inc(s["t1_mm"], 1)
                            each(t1)

                            def pp(u_, d, h):
                                pe.wait_ge(s["t1_ev"], q * 20 + (4 * l + u_ + 1))
                                if l == 0:
                                    pe.wait_ge(s["lakv_ev"], q * 4 + (u_ + 1))
                                nc.tensor.matmul(B(u_)[:, 0:P], X[:, u_, P:2 * P], T1[:, u_, :], start=True, stop=True)
                                nc.tensor.matmul(B(u_)[:, P:2 * P], T1[:, u_, :], X[:, u_, P:2 * P], start=True, stop=True)\
                                    .then_inc(s["p_mm"], 1)
                            each(pp)

                        def ta(u_, d, h):
                            pe.wait_ge(s["x_ev"], q * 20 + (4 * (NL - 1) + u_ + 1))
                            nc.tensor.matmul(A(u_)[:, 0:P], X[:, u_, P:2 * P], Y0[:, u_, :], start=True, stop=True)\
                                .then_inc(s["ta_mm"], 1)
                        each(ta)
                        pe.wait_ge(s["vz_ready"], q * 4 + 4)

                        def yy(u_, d, h):
                            pe.wait_ge(s["ta_ev"], q * 4 + (u_ + 1))
                            nc.tensor.matmul(B(u_)[:, 0:P], TT_[:, u_, :], LL[:, u_, 0, P:2 * P], start=True, stop=False)
                            nc.tensor.matmul(B(u_)[:, 0:P], vz[:, h, :], LL[:, u_, 1, P:2 * P], start=False, stop=True)\
                                .then_inc(s["y_mm"], 1)
                        each(yy)
                        pe.wait_ge(s["bm_ready"], q * 4 + 4)
                        pe.wait_ge(s["tvm_ready"], q * 4 + 4)
                        for d in range(2):
                            for h in range(2):
                                u_ = 2 * d + h
                                nc.tensor.matmul(A(2 * d)[64 * h:64 * h + 64, 0:P], TT_[:, u_, CH * h:CH * h + CH],
                                                 bm[:, u_].rearrange("p c k -> p (c k)"), start=True, stop=True)
                            for h in range(2):
                                u_ = 2 * d + h
                                nc.tensor.matmul(A(2 * d + 1)[:, 0:P], rows[:, u_, 0, :],
                                                 tvm[:, u_].rearrange("p c k -> p (c k)"), start=(h == 0), stop=False)
                                ins = nc.tensor.matmul(A(2 * d + 1)[:, 0:P], rows[:, u_, 1, :],
                                                       vm[:, h].rearrange("p c k -> p (c k)"), start=False, stop=(h == 1))
                            ins.then_inc(s["m_mm"], 1)

            @block.scalar
            def _(act):
                act.sem_inc(s["n_ev"], 1)
                act.sem_inc(s["yi_ev"], 1)
                with act.Fori(0, ITS) as it:
                    for k in range(2):
                        q = it * 2 + k

                        def by_rows(u_, d, h):
                            act.wait_ge(s["rows_mm"], q * 4 + (u_ + 1))
                            nc.scalar.activation(rows[:, u_].rearrange("p a t -> p (a t)"), A(u_)[:, 0:2 * P], ACT.Copy)\
                                .then_inc(s["rows_ev"], 1)
                            nc.scalar.activation(Y0[:, u_, CH * h:CH * h + CH],
                                                 A(u_)[:, 2 * P + CH * h:2 * P + CH * h + CH], ACT.Copy)\
                                .then_inc(s["a_ev"], 1)
                        each(by_rows)
                        act.wait_ge(s["v_mm"], q + 1)
                        nc.scalar.activation(vrow[:, :], B(0)[:, 0:P], ACT.Copy).then_inc(s["v_ev"], 1)

                        def lakv(u_, d, h):
                            c = slice(CH * (1 - h), CH * (1 - h) + CH)
                            act.wait_ge(s["lakv_mm"], q * 4 + (u_ + 1))
                            nc.scalar.activation(Y0[:, u_, c], B(u_)[:, c], ACT.Copy).then_inc(s["lakv_ev"], 1)
                        each(lakv)
                        for l in range(NL):
                            def t1(u_, d, h):
                                act.wait_ge(s["t1_mm"], q * 20 + (4 * l + u_ + 1))
                                nc.scalar.activation(T1[:, u_, :], A(u_)[:, 0:P], ACT.Copy).then_inc(s["t1_ev"], 1)
                            each(t1)

                        def ta(u_, d, h):
                            act.wait_ge(s["ta_mm"], q * 4 + (u_ + 1))
                            nc.scalar.activation(TT_[:, u_, :], A(u_)[:, 0:P], ACT.Copy).then_inc(s["ta_ev"], 1)
                        each(ta)
                        act.wait_ge(s["stored"], q * 64 + 1)

                        def yy(u_, d, h):
                            r = slice(64 * (1 - h), 64 * (1 - h) + 64)
                            act.wait_ge(s["y_mm"], q * 4 + (u_ + 1))
                            nc.scalar.activation(yis[r, d, :], B(u_)[r, 0:P], ACT.Copy).then_inc(s["yi_ev"], 1)
                        each(yy)
                        for d in range(2):
                            act.wait_ge(s["m_mm"], q * 2 + (d + 2))
                            for c in range(2):
                                nc.scalar.activation(nns[:, d, c, :], A(2 * d + 1)[:, CH * c:CH * c + CH], ACT.Copy,
                                                     scale=wct[:, k, d, c:c + 1]).then_inc(s["n_ev"], 1)

            @block.vector
            def _(dve):
                dve.sem_inc(s["mt_ev"], 1)
                dve.sem_inc(s["re_ev"], 1)
                dve.wait_ge(s["msk_in"], 16)
                with dve.Fori(0, ITS) as it:
                    for k in range(2):
                        q = it * 2 + k

                        def g(u_, d, h):
                            dve.wait_ge(s["g_mm"], q * 4 + (u_ + 1))
                            nc.vector.tensor_tensor(LL[:, u_], A(u_)[:, :].rearrange("p (a t) -> p a t", a=2),
                                                    stm[d].unsqueeze(1).to_broadcast([P, 2, 2 * P]), ALU.mult)\
                                .then_inc(s["g_ev"], 1)
                        each(g)
                        dve.wait_ge(s["x_init"], q * 4 + 4)

                        def one(u_, d, h):
                            dve.wait_ge(s["lab_mm"], q * 4 + (u_ + 1))
                            dve.sem_inc(s["turns"], 1)
                            nc.vector.copy_predicated(X[:, u_, 0:P], msk[:, d, 0, 0:P], B(u_)[:, 0:P]).then_inc(s["lab_ev"], 1)
                            dve.wait_ge(s["g_ev"], q * 4 + (u_ + 1))
                            dve.sem_inc(s["turns"], 1)
                            nc.vector.copy_predicated(X[:, u_, P:2 * P], msk[:, d, 0, P:2 * P], LL[:, u_, 0, 0:P])\
                                .then_inc(s["x_one"], 1)
                        each(one)
                        dve.wait_ge(s["lab_ev"], q * 4 + 4)
                        for l in range(NL):
                            def pp(u_, d, h):
                                dve.wait_ge(s["p_mm"], q * 20 + (4 * l + u_ + 1))
                                if l:
                                    dve.wait_ge(s["x_ev"], q * 20 + (4 * (l - 1) + u_ + 1))
                                dve.sem_inc(s["turns"], 1)
                                nc.vector.copy_predicated(X[:, u_, :], msk[:, d, 1 + l, :], B(u_)[:, 0:2 * P])\
                                    .then_inc(s["x_ev"], 1)
                            each(pp)
                        dve.wait_ge(s["stored"], q * 64 + 1)

                        def yy(u_, d, h):
                            r = slice(64 * h, 64 * h + 64)
                            dve.wait_ge(s["y_mm"], q * 4 + (u_ + 1))
                            nc.vector.tensor_tensor(res[r, d, :], B(u_)[r, 0:P], ar[r, k, d, 1, :], ALU.add)\
                                .then_inc(s["re_ev"], 1)
                        each(yy)
                        for d in range(2):
                            dve.wait_ge(s["m_mm"], q * 2 + (d + 2))
                            nc.vector.tensor_tensor(mts[:, d], A(2 * d)[:, 0:P].rearrange("p (c k) -> p c k", c=2),
                                                    idc.unsqueeze(1).to_broadcast([P, 2, CH]), ALU.add)\
                                .then_inc(s["mt_ev"], 1)


def rwkv_states(nc, bank, wc, mt, nn, re, yi, yT):
    RING = 4
    NBK = TT // P
    with Stage(nc, "states") as st:
        m = st.sb("m", [P, RING, 2, PAIRS, P])
        n_ = st.sb("n", [P, RING, 2, PAIRS, P])
        w = st.sb("w", [P, 2, PAIRS * NBK, 2])
        S = st.sb("S", [P, 2, 2, PAIRS, P])
        r = st.sb("r", [P, 2, PAIRS, NT, P])
        y = st.sb("y", [P, 2, PAIRS, NT, P])
        mn_in = [st.sem(f"mn_in{i}") for i in range(RING)]
        zeroed, ry_in, w_in = st.sem("zeroed"), st.sem("ry_in"), st.sem("w_in")
        p_mm, s_ready, y_mm, y_ready, stored = (st.sem(x) for x in ("p_mm", "s_ready", "y_mm", "y_ready", "stored"))
        C0 = TC // CH
        order = [list(range(NC)), list(range(C0))[::-1] + list(range(C0, NC))[::-1]]
        with nc.Block() as block:
            @block.gpsimd
            def _(pool):
                nc.gpsimd.memset(m[:, :, :, :, :], 0.0).then_inc(zeroed, 1)
                nc.gpsimd.memset(n_[:, :, :, :, :], 0.0).then_inc(zeroed, 1)
                nc.gpsimd.memset(S[:, :, :, :, :], 0.0).then_inc(zeroed, 1)

            def loads(eng, d, i):
                slot, c = i % RING, order[d][i]
                for h in range(2):
                    rr = slice(64 * h, 64 * h + 64)
                    eng.dma_start(m[rr, slot, d, :, 64 * h:64 * h + 64],
                                  mt[c // 2::NBK, d, c % 2, rr].rearrange("p r k -> r p k")).then_inc(mn_in[slot], 16)
                    eng.dma_start(n_[rr, slot, d, :, 64 * (1 - h):64 * (1 - h) + 64],
                                  nn[c // 2::NBK, d, c % 2, rr].rearrange("p r k -> r p k")).then_inc(mn_in[slot], 16)

            @block.sync
            def _(sp):
                sp.wait_ge(zeroed, 3)
                with nc.allow_non_contiguous_dma("four values a channel"):
                    for d in range(2):
                        sp.dma_start(w[:, d], wc[:, d].rearrange("q c n -> c q n")).then_inc(w_in, 16)
                for i in range(NC - 1):
                    if i >= RING:
                        sp.wait_ge(s_ready, 8 * (i - RING + 1))
                    loads(sp, 0, i)
                    if i == 1:
                        for d in range(2):
                            for p in range(PAIRS):
                                b = slice(p * NBK + NTC, (p + 1) * NBK)
                                sp.dma_start(r[:, d, p], re[b, d].rearrange("b c t -> c b t")).then_inc(ry_in, 16)
                                sp.dma_start(y[:, d, p], yi[b, d].rearrange("b c t -> c b t")).then_inc(ry_in, 16)
                for d in range(2):
                    sp.wait_ge(y_ready, 2 * (NC - C0))
                    for p in range(PAIRS):
                        sp.dma_start(yT[d, p * P:(p + 1) * P, :], y[:, d, p].rearrange("c b t -> c (b t)"))\
                            .then_inc(stored, 16)
                sp.wait_ge(stored, 16 * 2 * PAIRS)

            @block.tensor
            def _(pe):
                pe.wait_ge(zeroed, 3)
                for i in range(NC):
                    for d in range(2):
                        c = order[d][i]
                        if i:
                            pe.wait_ge(s_ready, 8 * (i - 1) + 4 * (d + 1))
                        if i < NC - 1:
                            pe.wait_ge(mn_in[i % RING], 128 * (i // RING + 1))
                            for p in range(PAIRS):
                                ins = nc.tensor.matmul(bank[d][:, p * P:(p + 1) * P], m[:, i % RING, d, p, :],
                                                       S[:, i % 2, d, p, :], start=True, stop=True)
                            ins.then_inc(p_mm, 1)
                        if c >= C0:
                            if i == C0 and d == 0:
                                pe.wait_ge(ry_in, 16 * 4 * PAIRS)
                            if i > C0:
                                pe.wait_ge(y_ready, 2 * (i - C0 - 1) + d + 1)
                            for p in range(PAIRS):
                                ins = nc.tensor.matmul(bank[2 + d][:, p * P:(p + 1) * P], S[:, i % 2, d, p, :],
                                                       r[:, d, p, c // 2 - NTC, :], start=True, stop=True)
                            ins.then_inc(y_mm, 1)

            @block.scalar
            def _(act):
                act.wait_ge(zeroed, 3)
                for i in range(NC - 1):
                    if i >= RING:
                        act.wait_ge(s_ready, 8 * (i - RING + 1))
                    loads(act, 1, i)

            @block.vector
            def _(dve):
                dve.wait_ge(zeroed, 3)
                dve.wait_ge(w_in, 32)
                for i in range(NC):
                    for d in range(2):
                        c = order[d][i]
                        if i < NC - 1:
                            dve.wait_ge(p_mm, 2 * i + d + 1)
                            if i:
                                dve.wait_ge(s_ready, 8 * (i - 1) + 4 * (d + 1))
                            if d == 0 and i > C0:
                                dve.wait_ge(y_mm, 2 * (i - C0))
                            dve.wait_ge(mn_in[i % RING], 128 * (i // RING + 1))
                            for p in range(PAIRS):
                                nc.vector.scalar_tensor_tensor(S[:, (i + 1) % 2, d, p, :], bank[d][:, p * P:(p + 1) * P],
                                                               w[:, d, p * NBK + c // 2, c % 2:c % 2 + 1],
                                                               n_[:, i % RING, d, p, :], ALU.mult, ALU.add)\
                                    .then_inc(s_ready, 1)
                        if c >= C0:
                            dve.wait_ge(y_mm, 2 * (i - C0) + d + 1)
                            if i == C0 and d == 0:
                                dve.wait_ge(ry_in, 16 * 4 * PAIRS)
                            t = slice(CH * (c % 2), CH * (c % 2) + CH)
                            o = y[:, d, :, c // 2 - NTC, t]
                            nc.vector.tensor_tensor(o, bank[2 + d][:, :].rearrange("q (p t) -> q p t", p=PAIRS)[:, :, t], o,
                                                    ALU.add).then_inc(y_ready, 1)


def rwkv_combine(nc, bank, cst, tabs, yT, bonus, gate, latT):
    with Stage(nc, "comb") as st:
        y, g, b = st.sb("y", [P, 2, T]), st.sb("g", [P, 2, T]), st.sb("b", [P, T])
        sq = st.sb("sq", [P, 2, T])
        o = st.sb("o", [P, T])
        pc = st.sb("pc", [P, PW])
        names = ("y_in", "g_in", "mean_mm", "centred", "squared", "var_mm", "var", "root", "chain", "out", "stored")
        s = {n: st.sem(n) for n in names}
        pair = cst[:, CONST["pair"]:CONST["pair"] + P]
        CH_ = 10
        with nc.Block() as block:
            @block.sync
            def _(sp):
                sp.sem_inc(s["stored"], 1)
                with sp.Fori(0, PAIRS) as p:
                    rows = ds(p * P, P)
                    sp.dma_start(y[:, :, :], yT[:, rows, :].rearrange("d c t -> c d t")).then_inc(s["y_in"], 16)
                    sp.dma_start(g[:, :, :], gate[:, rows, :].rearrange("d c t -> c d t")).then_inc(s["g_in"], 16)
                    sp.dma_start(b[:, :], bonus[rows, :]).then_inc(s["g_in"], 16)
                    sp.dma_start(pc[:, :], tabs["pcols"][ds(p, 1)].rearrange("o p c -> p (o c)")).then_inc(s["g_in"], 16)
                    sp.wait_ge(s["out"], p + 1)
                    sp.dma_start(latT[ds(p * P + RW, P), :], o[:, :]).then_inc(s["stored"], 16)
                sp.wait_ge(s["stored"], 16 * PAIRS + 1)

            @block.tensor
            def _(pe):
                with pe.Fori(0, PAIRS) as p:
                    pe.wait_ge(s["y_in"], p * 16 + 16)
                    for d in range(2):
                        for c in range(2):
                            nc.tensor.matmul(bank[2 * d + c][:, :], pair, y[:, d, c * BANK:(c + 1) * BANK],
                                             start=True, stop=True).then_inc(s["mean_mm"], 1)
                    for d in range(2):
                        pe.wait_ge(s["squared"], p * 2 + (d + 1))
                        for c in range(2):
                            nc.tensor.matmul(bank[4 + 2 * d + c][:, :], pair, sq[:, d, c * BANK:(c + 1) * BANK],
                                             start=True, stop=True).then_inc(s["var_mm"], 1)

            @block.scalar
            def _(act):
                with act.Fori(0, PAIRS) as p:
                    for d in range(2):
                        act.wait_ge(s["centred"], p * 4 + 2 * (d + 1))
                        nc.scalar.activation(sq[:, d, :], y[:, d, :], ACT.Square).then_inc(s["squared"], 1)
                    act.wait_ge(s["var"], p * 4 + 4)
                    nc.scalar.activation(sq[:, :, :], sq[:, :, :], ACT.Sqrt).then_inc(s["root"], 1)

            @block.vector
            def _(dve):
                with dve.Fori(0, PAIRS) as p:
                    link = Loop(s["chain"], p, CH_)

                    def wait(n):
                        dve.wait_ge(s["chain"], n)

                    for d in range(2):
                        for c in range(2):
                            t = slice(c * BANK, (c + 1) * BANK)
                            dve.wait_ge(s["mean_mm"], p * 4 + (2 * d + c + 1))
                            nc.vector.scalar_tensor_tensor(y[:, d, t], bank[2 * d + c][:, :], -1.0 / RET_DIM, y[:, d, t],
                                                           ALU.mult, ALU.add).then_inc(s["centred"], 1)
                    for d in range(2):
                        for c in range(2):
                            t = slice(c * BANK, (c + 1) * BANK)
                            dve.wait_ge(s["var_mm"], p * 4 + (2 * d + c + 1))
                            nc.vector.tensor_scalar(sq[:, d, t], bank[4 + 2 * d + c][:, :], 1.0 / RET_DIM, GN_EPS,
                                                    ALU.mult, ALU.add).then_inc(s["var"], 1)
                    dve.wait_ge(s["root"], p + 1)
                    dve.wait_ge(s["g_in"], p * 48 + 48)
                    for d in range(2):
                        wait(link(nc.vector.reciprocal(sq[:, d, :], sq[:, d, :])))
                        wait(link(nc.vector.tensor_tensor(y[:, d, :], y[:, d, :], sq[:, d, :], ALU.mult)))
                        wait(link(nc.vector.tensor_scalar(y[:, d, :], y[:, d, :], pc[:, PCOL["lnw"]:PCOL["lnw"] + 1],
                                                          pc[:, PCOL["lnb"]:PCOL["lnb"] + 1], ALU.mult, ALU.add)))
                        wait(link(nc.vector.tensor_tensor(y[:, d, :], y[:, d, :], b[:, :], ALU.add)))
                        wait(link(nc.vector.tensor_tensor(y[:, d, :], y[:, d, :], g[:, d, :], ALU.mult)))
                    dve.wait_ge(s["stored"], p * 16 + 1)
                    nc.vector.tensor_tensor(o[:, :], y[:, 0, :], y[:, 1, :], ALU.add).then_inc(s["out"], 1)
                    link.end()


def rwkv(nc, bank, cst, col, tabs, x, uT, scratch, latT, upto=9):
    NBK = TT // P
    Q = PAIRS * NBK
    prim, vT = scratch("prim", Q, 8, P, P), scratch("vT", Q, P, P)
    wc, bonus, gate = scratch("wc", Q, 2, P, 2), scratch("bonus", RW, T), scratch("gate", 2, RW, T)
    rwkv_prepare(nc, bank, cst, col, tabs, x, uT, prim, vT, wc, bonus, gate)
    if upto < 2:
        return
    mt, nn = scratch("mt", Q, 2, 2, P, CH), scratch("nn", Q, 2, 2, P, CH)
    re, yi = scratch("re", Q, 2, P, P), scratch("yi", Q, 2, P, P)
    rwkv_chunks(nc, bank, cst, tabs, prim, vT, wc, mt, nn, re, yi)
    if upto < 3:
        return
    yT = scratch("yT", 2, RW, T)
    rwkv_states(nc, bank, wc, mt, nn, re, yi, yT)
    rwkv_combine(nc, bank, cst, tabs, yT, bonus, gate, latT)


def gemm_rows(nc, bank, name, actT, K, w, x, out, grow=None, exchanged=()):
    KK = K // P
    with Stage(nc, name) as st:
        wt = st.sb("w", [P, KK, D])
        xt = st.sb("x", [P, 4, D])
        sq = st.sb("sq", [P, D])
        ss = st.sb("ss", [P, NT, 5])
        gb, yt = st.sb("g", [P, D]), st.sb("y", [P, D])
        w_in, g_in, x_in = [st.sem(f"w_in{c}") for c in range(2)], st.sem("g_in"), [st.sem(f"x_in{i}") for i in range(4)]
        mm, ssq, ms, root, rstd, scaled, out_ready = (st.sem(n) for n in
                                                      ("mm", "ssq", "ms", "root", "rstd", "scaled", "out_ready"))
        stored = [st.sem(f"stored{i}") for i in range(4)]
        WIN = 16 * (KK - len(exchanged) + 2 * len(exchanged))
        with nc.Block() as block:
            @block.sync
            def _(sp):
                for c in range(2):
                    cc = slice(c * BANK, (c + 1) * BANK)
                    for k in range(KK):
                        if k in exchanged:
                            for h in range(2):
                                sp.dma_start(wt[64 * h:64 * h + 64, k, cc],
                                             w[k * P + 64 * (1 - h):k * P + 64 * (1 - h) + 64, cc]).then_inc(w_in[c], 16)
                        else:
                            sp.dma_start(wt[:, k, cc], w[k * P:(k + 1) * P, cc]).then_inc(w_in[c], 16)
                    if c == 0 and grow is not None:
                        sp.dma_start(gb[:, :], grow.partition_broadcast(P).rearrange("p o d -> p (o d)")).then_inc(g_in, 16)
                for i in range(4):
                    sp.dma_start(xt[:, i, :], x[i * P:(i + 1) * P, :]).then_inc(x_in[i], 16)
                for i in range(NT):
                    sp.wait_ge(out_ready, (i + 1) if grow is not None else 2 * (i + 1))
                    sp.dma_start(out[i * P:(i + 1) * P, :], xt[:, i % 4, :]).then_inc(stored[i % 4], 16)
                    if i + 4 < NT:
                        sp.wait_ge(stored[i % 4], 16 * (i // 4 + 1))
                        sp.dma_start(xt[:, i % 4, :], x[(i + 4) * P:(i + 5) * P, :]).then_inc(x_in[i % 4], 16)
                for i in range(4):
                    sp.wait_ge(stored[i], 16 * (NT // 4))

            @block.tensor
            def _(pe):
                for i in range(NT):
                    for c in range(2):
                        if i == 0:
                            pe.wait_ge(w_in[c], WIN)
                        if i >= 2 and c == 0:
                            pe.wait_ge(scaled if grow is not None else out_ready, 2 * (i - 1))
                        for k in range(KK):
                            last = nc.tensor.matmul(bank[2 * (i % 2) + c][:, :], actT[:, k, i * P:(i + 1) * P],
                                                    wt[:, k, c * BANK:(c + 1) * BANK], start=(k == 0), stop=(k == KK - 1))
                        last.then_inc(mm, 1)

            if grow is not None:
                @block.scalar
                def _(act):
                    for i in range(NT):
                        for c in range(2):
                            act.wait_ge(mm, 2 * i + c + 1)
                            if i or c:
                                act.wait_ge(ssq, 2 * i + c)
                            nc.scalar.activation(sq[:, c * BANK:(c + 1) * BANK], bank[2 * (i % 2) + c][:, :], ACT.Square,
                                                 accum_out=ss[:, i, c:c + 1]).then_inc(ssq, 1)
                        act.wait_ge(ms, i + 1)
                        nc.scalar.activation(ss[:, i, 3:4], ss[:, i, 2:3], ACT.Sqrt).then_inc(root, 1)

            @block.vector
            def _(dve):
                for i in range(NT):
                    xs = xt[:, i % 4, :]
                    if grow is not None:
                        dve.wait_ge(ssq, 2 * i + 2)
                        nc.vector.tensor_tensor(ss[:, i, 2:3], ss[:, i, 0:1], ss[:, i, 1:2], ALU.add).then_inc(rstd, 1)
                        dve.wait_ge(rstd, 2 * i + 1)
                        nc.vector.tensor_scalar(ss[:, i, 2:3], ss[:, i, 2:3], 1.0 / D, EPS, ALU.mult, ALU.add)\
                            .then_inc(ms, 1)
                        dve.wait_ge(root, i + 1)
                        nc.vector.reciprocal(ss[:, i, 4:5], ss[:, i, 3:4]).then_inc(rstd, 1)
                        dve.wait_ge(rstd, 2 * i + 2)
                        if i == 0:
                            dve.wait_ge(g_in, 16)
                        for c in range(2):
                            cc = slice(c * BANK, (c + 1) * BANK)
                            nc.vector.scalar_tensor_tensor(yt[:, cc], bank[2 * (i % 2) + c][:, :], ss[:, i, 4:5],
                                                           gb[:, cc], ALU.mult, ALU.mult).then_inc(scaled, 1)
                        dve.wait_ge(scaled, 2 * i + 2)
                        dve.wait_ge(x_in[i % 4], 16 * (i // 4 + 1))
                        nc.vector.tensor_tensor(xs, xs, yt[:, :], ALU.add).then_inc(out_ready, 1)
                        dve.wait_ge(out_ready, i + 1)
                    else:
                        dve.wait_ge(x_in[i % 4], 16 * (i // 4 + 1))
                        for c in range(2):
                            cc = slice(c * BANK, (c + 1) * BANK)
                            dve.wait_ge(mm, 2 * i + c + 1)
                            nc.vector.tensor_tensor(xs[:, cc], xs[:, cc], bank[2 * (i % 2) + c][:, :], ALU.add)\
                                .then_inc(out_ready, 1)


def add_normed(nc, name, x, y, grow, out):
    with Stage(nc, name) as st:
        xt, yt, gb = st.sb("x", [P, NT, D]), st.sb("y", [P, NT, D]), st.sb("g", [P, D])
        sq, ss = st.sb("sq", [P, D]), st.sb("ss", [P, NT, 4])
        x_in, y_in = [st.sem(f"x_in{i}") for i in range(2)], [st.sem(f"y_in{i}") for i in range(2)]
        g_in, ssq, ms, root, rstd, scaled, out_ready, stored = (
            st.sem(n) for n in ("g_in", "ssq", "ms", "root", "rstd", "scaled", "out_ready", "stored"))
        H = NT // 2
        with nc.Block() as block:
            @block.sync
            def _(sp):
                for i in range(2):
                    t = slice(i * H * P, (i + 1) * H * P)
                    sp.dma_start(yt[:, i * H:(i + 1) * H, :], y[t, :].rearrange("(n p) d -> p n d", p=P)).then_inc(y_in[i], 16)
                    if i == 0:
                        sp.dma_start(gb[:, :], grow.partition_broadcast(P).rearrange("p o d -> p (o d)")).then_inc(g_in, 16)
                    sp.dma_start(xt[:, i * H:(i + 1) * H, :], x[t, :].rearrange("(n p) d -> p n d", p=P)).then_inc(x_in[i], 16)
                for i in range(NT):
                    sp.wait_ge(out_ready, i + 1)
                    sp.dma_start(out[i * P:(i + 1) * P, :], xt[:, i, :]).then_inc(stored, 16)
                sp.wait_ge(stored, 16 * NT)

            @block.scalar
            def _(act):
                for i in range(NT):
                    act.wait_ge(y_in[i // H], 16)
                    if i:
                        act.wait_ge(ssq, i)
                    nc.scalar.activation(sq[:, :], yt[:, i, :], ACT.Square, accum_out=ss[:, i, 0:1]).then_inc(ssq, 1)
                    act.wait_ge(ms, i + 1)
                    nc.scalar.activation(ss[:, i, 2:3], ss[:, i, 1:2], ACT.Sqrt).then_inc(root, 1)

            @block.vector
            def _(dve):
                dve.wait_ge(g_in, 16)
                for i in range(NT):
                    dve.wait_ge(ssq, i + 1)
                    nc.vector.tensor_scalar(ss[:, i, 1:2], ss[:, i, 0:1], 1.0 / D, EPS, ALU.mult, ALU.add).then_inc(ms, 1)
                    dve.wait_ge(root, i + 1)
                    nc.vector.reciprocal(ss[:, i, 3:4], ss[:, i, 2:3]).then_inc(rstd, 1)
                    dve.wait_ge(rstd, i + 1)
                    nc.vector.scalar_tensor_tensor(yt[:, i, :], yt[:, i, :], ss[:, i, 3:4], gb[:, :], ALU.mult, ALU.mult)\
                        .then_inc(scaled, 1)
                    dve.wait_ge(scaled, i + 1)
                    dve.wait_ge(x_in[i // H], 16)
                    nc.vector.tensor_tensor(xt[:, i, :], xt[:, i, :], yt[:, i, :], ALU.add).then_inc(out_ready, 1)


def route1(nc, bank, cst, hT, w_router, acc, idx, gates):
    with Stage(nc, "route1") as st:
        wr = st.sb("wr", [P, KD, E1])
        lT = st.sb("lT", [E1, T])
        lg, ex = st.sb("lg", [P, NT, E1]), st.sb("ex", [P, NT, E1])
        mx, sm = st.sb("mx", [P, NT]), st.sb("sm", [P, 2, NT])
        af = [st.sb("af0", [E1, T]), st.sb("af1", [E1, T])]
        va, ix, ixf = st.sb("va", [E1, CAP]), st.sb("ix", [E1, CAP], U32), st.sb("ixf", [E1, CAP])
        zero = st.sb("zero", [P, D])
        w_in, l_mm, l_ev, tr, chain, e_ready, af_mm, af_ev, ixf_ready, fin_mm, fin = (
            st.sem(n) for n in ("w_in", "l_mm", "l_ev", "tr", "chain", "e_ready", "af_mm", "af_ev", "ixf_ready", "fin_mm", "fin"))
        zeroed, cleared, p_ready, d_ready = st.sem("zeroed"), st.sem("cleared"), st.sem("p_ready"), st.sem("d_ready")
        ident = cst[:, CONST["ident"]:CONST["ident"] + P]
        with nc.Block() as block:
            @block.sync
            def _(sp):
                sp.dma_start(wr[:, :, :], w_router.rearrange("(k p) e -> p k e", p=P)).then_inc(w_in, 16)
                sp.wait_ge(zeroed, 1)
                for i in range(NT):
                    sp.dma_start(acc[i * P:(i + 1) * P, :], zero[:, :]).then_inc(cleared, 16)
                sp.wait_ge(cleared, 16 * NT)

            @block.gpsimd
            def _(pool):
                nc.gpsimd.memset(zero[:, :], 0.0).then_inc(zeroed, 1)

            @block.tensor
            def _(pe):
                pe.wait_ge(w_in, 16)
                for c in range(2):
                    for k in range(KD):
                        last = nc.tensor.matmul(bank[c][0:E1, :], wr[:, k, :], hT[:, k, c * BANK:(c + 1) * BANK],
                                                start=(k == 0), stop=(k == KD - 1))
                    last.then_inc(l_mm, 1)
                pe.wait_ge(l_ev, 2)
                for i in range(NT):
                    last = nc.tensor.transpose(bank[2][:, i * E1:(i + 1) * E1], lT[:, i * P:(i + 1) * P], ident[0:E1, 0:E1])
                last.then_inc(tr, 1)
                pe.wait_ge(p_ready, 1)
                for i in range(NT):
                    last = nc.tensor.transpose(bank[3 + i // 4][0:E1, (i % 4) * P:(i % 4 + 1) * P], ex[:, i, :], ident)
                last.then_inc(af_mm, 1)
                pe.wait_ge(ixf_ready, 1)
                nc.tensor.transpose(bank[5][:, 0:E1], va[:, :], ident[0:E1, 0:E1])
                nc.tensor.transpose(bank[5][:, E1:2 * E1], ixf[:, :], ident[0:E1, 0:E1]).then_inc(fin_mm, 1)

            @block.scalar
            def _(act):
                for c in range(2):
                    act.wait_ge(l_mm, c + 1)
                    nc.scalar.activation(lT[:, c * BANK:(c + 1) * BANK], bank[c][0:E1, :], ACT.Copy).then_inc(l_ev, 1)
                act.wait_ge(d_ready, 1)
                nc.scalar.activation(ex[:, :, :], lg[:, :, :], ACT.Exp).then_inc(e_ready, 1)

            @block.vector
            def _(dve):
                link = Steps(chain)
                dve.wait_ge(tr, 1)
                lp = bank[2][:, 0:NT * E1].rearrange("p (n e) -> p n e", e=E1)
                dve.wait_ge(chain, link(nc.vector.tensor_reduce(mx[:, :], lp, AX_X, ALU.max)))
                nc.vector.tensor_tensor(lg[:, :, :], lp, mx[:, :].unsqueeze(2).to_broadcast([P, NT, E1]), ALU.subtract)\
                    .then_inc(d_ready, 1)
                dve.wait_ge(e_ready, 1)
                dve.wait_ge(chain, link(nc.vector.tensor_reduce(sm[:, 0, :], ex[:, :, :], AX_X, ALU.add)))
                dve.wait_ge(chain, link(nc.vector.reciprocal(sm[:, 1, :], sm[:, 0, :])))
                nc.vector.tensor_tensor(ex[:, :, :], ex[:, :, :], sm[:, 1, :].unsqueeze(2).to_broadcast([P, NT, E1]),
                                        ALU.mult).then_inc(p_ready, 1)
                dve.wait_ge(af_mm, 1)
                for c in range(2):
                    dve.wait_ge(chain, link(nc.vector.tensor_copy(af[0][:, c * BANK:(c + 1) * BANK], bank[3 + c][0:E1, :])))
                for r in range(CAP // 8):
                    v8, i8, a, b = va[:, 8 * r:8 * r + 8], ix[:, 8 * r:8 * r + 8], af[r % 2], af[(r + 1) % 2]
                    dve.wait_ge(chain, link(nc.vector.max(v8, a[:, :])))
                    link(nc.vector.max_index(i8, v8, a[:, :]))
                    dve.wait_ge(chain, link(nc.vector.match_replace(b[:, :], v8, a[:, :], -1.0)))
                nc.vector.tensor_copy(ixf[:, :], ix[:, :]).then_inc(ixf_ready, 1)
                dve.wait_ge(fin_mm, 1)
                nc.vector.tensor_copy(gates[:, :], bank[5][:, 0:E1]).then_inc(fin, 1)
                nc.vector.tensor_copy(idx[:, 0:E1], bank[5][:, E1:2 * E1]).then_inc(fin, 1)
                nc.vector.tensor_copy(idx[:, E1:E1 + 1], bank[5][:, E1:E1 + 1]).then_inc(fin, 1)


def experts1(nc, bank, cst, h2, w_gate, w_up, w_down, acc, idx, gates, xs_in, added):
    with Stage(nc, "moe1") as st:
        w = st.sb("w", [P, 6, 8 * BANK])
        xs, xT = st.sb("xs", [P, D]), st.sb("xT", [P, KD, P])
        cur = st.sb("cur", [P, 2], U32)
        sg = st.sb("sg", [P, 2, BANK])
        hid, hidT = st.sb("hid", [P, 2, BANK]), st.sb("hidT", [P, KD, P])
        ye = st.sb("ye", [P, D])
        w_in = [st.sem(f"w_in{i}") for i in range(6)]
        names = ("turns", "cur_ready", "x_tr", "xT_ev", "gu_mm", "sg_ready", "hid_ready", "h_tr", "hT_ev", "y_mm",
                 "ye_ready", "ye_free")
        s = {n: st.sem(n) for n in names}
        ident = cst[:, CONST["ident"]:CONST["ident"] + P]

        def load(sp, e, i):
            m = (w_gate, w_up, w_gate, w_up, w_down, w_down)[i]
            if i < 4:
                c = (i // 2) * BANK
                src = m[ds(e, 1), :, c:c + BANK].rearrange("o (k p) n -> p (o k) n", p=P)
                dst = w[:, i].rearrange("p (k n) -> p k n", k=8)
            else:
                r = (i - 4) * BANK
                src = m[ds(e, 1), r:r + BANK, :].rearrange("o (k p) n -> p (o k) n", p=P)
                dst = w[:, i].rearrange("p (k n) -> p k n", k=4)
            sp.dma_start(dst, src).then_inc(w_in[i], 16)

        with nc.Block() as block:
            @block.sync
            def _(sp):
                for i in range(6):
                    load(sp, 0, i)
                with sp.Fori(0, E1 - 1) as e:
                    for i in range(4):
                        sp.wait_ge(s["gu_mm"], e * 4 + (i + 1))
                        load(sp, e + 1, i)
                    for i in range(2):
                        sp.wait_ge(s["y_mm"], e * 2 + (i + 1))
                        load(sp, e + 1, 4 + i)

            @block.gpsimd
            def _(pool):
                def gather():
                    pool.indirect_dma_start(out=xs[:, :], out_offset=None, in_=h2[:, :],
                                            in_offset=bass.IndirectOffsetOnAxis(ap=cur[:, 0:1], axis=0))\
                        .then_inc(xs_in, 16)

                pool.sem_inc(s["ye_free"], 1)
                nc.gpsimd.tensor_copy(cur[:, 0:1], idx[:, 0:1]).then_inc(s["cur_ready"], 1)
                pool.wait_ge(s["cur_ready"], 1)
                gather()
                with pool.Fori(0, E1) as e:
                    pool.wait_ge(s["x_tr"], e * 2 + 2)
                    pool.sem_inc(s["turns"], 1)
                    nc.gpsimd.tensor_copy(cur[:, 1:2], cur[:, 0:1]).then_inc(s["cur_ready"], 1)
                    pool.wait_ge(s["cur_ready"], e * 2 + 2)
                    pool.sem_inc(s["turns"], 1)
                    nc.gpsimd.tensor_copy(cur[:, 0:1], idx[:, ds(e + 1, 1)]).then_inc(s["cur_ready"], 1)
                    pool.wait_ge(s["cur_ready"], e * 2 + 3)
                    pool.sem_inc(s["turns"], 1)
                    gather()
                    pool.wait_ge(s["ye_ready"], e * 2 + 3)
                    pool.sem_inc(s["turns"], 1)
                    pool.indirect_dma_start(out=acc[:, :], out_offset=bass.IndirectOffsetOnAxis(ap=cur[:, 1:2], axis=0),
                                            in_=ye[:, :], in_offset=None, compute_op=ALU.add).then_inc(added, 16)
                    pool.wait_ge(added, e * 16 + 16)
                    pool.sem_inc(s["ye_free"], 1)
                pool.wait_ge(xs_in, 16 * (E1 + 1))

            @block.tensor
            def _(pe):
                def take_tokens(e):
                    pe.wait_ge(xs_in, e * 16 + 16)
                    for k in range(KD):
                        ins = nc.tensor.transpose(bank[k // 4][:, (k % 4) * P:(k % 4 + 1) * P], xs[:, k * P:(k + 1) * P], ident)
                        if k % 4 == 3:
                            ins.then_inc(s["x_tr"], 1)

                take_tokens(0)
                with pe.Fori(0, E1) as e:
                    pe.wait_ge(s["xT_ev"], e * 2 + 2)
                    for i in range(4):
                        pe.wait_ge(w_in[i], e * 16 + 16)
                        wi = w[:, i].rearrange("p (k n) -> p k n", k=8)
                        for k in range(KD):
                            last = nc.tensor.matmul(bank[i][:, :], xT[:, k, :], wi[:, k, :], start=(k == 0), stop=(k == KD - 1))
                        last.then_inc(s["gu_mm"], 1)
                    for half in range(2):
                        pe.wait_ge(s["hid_ready"], e * 2 + (half + 1))
                        for j in range(4):
                            ins = nc.tensor.transpose(bank[4 + half][:, j * P:(j + 1) * P], hid[:, half, j * P:(j + 1) * P], ident)
                        ins.then_inc(s["h_tr"], 1)
                        if half == 0:
                            take_tokens(e + 1)
                        pe.wait_ge(s["hT_ev"], e * 2 + (half + 1))
                        pe.wait_ge(w_in[4 + half], e * 16 + 16)
                        if half == 0:
                            pe.wait_ge(s["ye_ready"], e * 2 + 1)
                        wi = w[:, 4 + half].rearrange("p (k n) -> p k n", k=4)
                        for c in range(2):
                            for j in range(4):
                                last = nc.tensor.matmul(bank[6 + c][:, :], hidT[:, 4 * half + j, :], wi[:, j, c * BANK:(c + 1) * BANK],
                                                        start=(half == 0 and j == 0), stop=(half == 1 and j == 3),
                                                        skip_group_check=True)
                        last.then_inc(s["y_mm"], 1)

            @block.scalar
            def _(act):
                def xT_evac(e):
                    for i in range(2):
                        act.wait_ge(s["x_tr"], e * 2 + (i + 1))
                        nc.scalar.activation(xT[:, 4 * i:4 * i + 4, :].rearrange("p k t -> p (k t)"), bank[i][:, :], ACT.Copy)\
                            .then_inc(s["xT_ev"], 1)

                xT_evac(0)
                with act.Fori(0, E1) as e:
                    for half in range(2):
                        act.wait_ge(s["gu_mm"], e * 4 + (2 * half + 1))
                        nc.scalar.activation(sg[:, half, :], bank[2 * half][:, :], ACT.Silu).then_inc(s["sg_ready"], 1)
                    xT_evac(e + 1)

            @block.vector
            def _(dve):
                dve.sem_inc(s["ye_ready"], 1)
                with dve.Fori(0, E1) as e:
                    for half in range(2):
                        dve.wait_ge(s["sg_ready"], e * 2 + (half + 1))
                        dve.wait_ge(s["gu_mm"], e * 4 + (2 * half + 2))
                        nc.vector.tensor_tensor(hid[:, half, :], sg[:, half, :], bank[2 * half + 1][:, :], ALU.mult)\
                            .then_inc(s["hid_ready"], 1)
                    for half in range(2):
                        dve.wait_ge(s["h_tr"], e * 2 + (half + 1))
                        nc.vector.tensor_copy(hidT[:, 4 * half:4 * half + 4, :].rearrange("p k t -> p (k t)"), bank[4 + half][:, :])\
                            .then_inc(s["hT_ev"], 1)
                    dve.wait_ge(s["y_mm"], e * 2 + 2)
                    dve.wait_ge(s["ye_free"], e + 1)
                    for c in range(2):
                        nc.vector.tensor_scalar(ye[:, c * BANK:(c + 1) * BANK], bank[6 + c][:, :], gates[:, ds(e, 1)], None,
                                                ALU.mult).then_inc(s["ye_ready"], 1)


def load_T(nc, name, src, dst, tiles=KD):
    with Stage(nc, name) as st:
        loaded = st.sem("loaded")
        with nc.Block() as block:
            @block.sync
            def _(sp):
                for k in range(tiles):
                    sp.dma_start(dst[:, k, :], src[k * P:(k + 1) * P, :]).then_inc(loaded, 16)
                sp.wait_ge(loaded, 16 * tiles)


LAMBDA_INIT = 0.8 - 0.6 * math.exp(-0.3 * 0)


def lru(nc, bank, col, wa, wx, uT, gT):
    LC = 2
    with Stage(nc, "lru") as st:
        x = st.sb("x", [P, LC, T + 4])
        gate = st.sb("gate", [P, LC, T])
        w = st.sb("w", [P, LC, 2, P])
        pc = st.sb("pc", [P, 3, KD])
        sp4 = st.sb("sp4", [P, 4, KD])
        xc = st.sb("xc", [P, LC, T])
        r, i_ = st.sb("r", [P, LC, T]), st.sb("i", [P, LC, T])
        a, t, u = st.sb("a", [P, LC, T]), st.sb("t", [P, LC, T]), st.sb("u", [P, LC, T])
        h = st.sb("h", [P, LC, T])
        names = ("zeroed", "x_in", "w_in", "g_in", "conv", "xc_ready", "mm", "r_ready", "i_ready", "a_ready", "t_ready",
                 "chain", "head", "head_act", "u_ready", "root", "ix_ready", "gelu", "h_used", "out")
        s = {n: st.sem(n) for n in names}
        stored = [st.sem(f"stored{k}") for k in range(LC)]
        c = lambda name, at, n=1: col[:, ds(at + COLS[name], n)]
        with nc.Block() as block:
            @block.sync
            def _(sp):
                sp.wait_ge(s["zeroed"], 1)
                for k in range(LC):
                    sp.sem_inc(stored[k], 1)
                with sp.Fori(0, KD // LC) as it:
                    for k in range(LC):
                        row = it * (LC * P) + k * P
                        sp.dma_start(x[:, k, 4:], uT[ds(row, P), :]).then_inc(s["x_in"], 16)
                        sp.dma_start(w[:, k, 0, :], wa[ds(it * LC + k, 1)].rearrange("o c d -> c (o d)")).then_inc(s["w_in"], 16)
                        sp.dma_start(w[:, k, 1, :], wx[ds(it * LC + k, 1)].rearrange("o c d -> c (o d)")).then_inc(s["w_in"], 16)
                        sp.dma_start(gate[:, k, :], uT[ds(row + D, P), :]).then_inc(s["g_in"], 16)
                    for k in range(LC):
                        sp.wait_ge(s["out"], it * LC + (k + 1))
                        sp.dma_start(gT[ds(it * (LC * P) + k * P, P), :], h[:, k, :]).then_inc(stored[k], 16)
                for k in range(LC):
                    sp.wait_ge(stored[k], 16 * (KD // LC) + 1)

            @block.gpsimd
            def _(pool):
                nc.gpsimd.memset(x[:, :, 0:4], 0.0).then_inc(s["zeroed"], 1)
                with pool.Fori(0, KD // LC) as it:
                    for k in range(LC):
                        pool.wait_ge(s["i_ready"], it * LC + (k + 1))
                        nc.gpsimd.tensor_tensor(i_[:, k, :], i_[:, k, :], xc[:, k, :], ALU.mult).then_inc(s["ix_ready"], 1)

            @block.tensor
            def _(pe):
                with pe.Fori(0, KD // LC) as it:
                    pe.wait_ge(s["w_in"], it * (32 * LC) + 32 * LC)
                    for k in range(LC):
                        pe.wait_ge(s["xc_ready"], it * LC + (k + 1))
                        for m in range(2):
                            for b in range(2):
                                ins = nc.tensor.matmul(bank[4 * k + 2 * m + b][:, :], w[:, k, m, :], xc[:, k, b * BANK:(b + 1) * BANK],
                                                       start=True, stop=True)
                            ins.then_inc(s["mm"], 1)

            @block.scalar
            def _(act):
                act.wait_ge(s["head"], 1)
                nc.scalar.activation(sp4[:, 1, :], sp4[:, 0, :], ACT.Exp, scale=-1.0).then_inc(s["head_act"], 1)
                act.wait_ge(s["head"], 2)
                nc.scalar.activation(sp4[:, 0, :], sp4[:, 2, :], ACT.Ln).then_inc(s["head_act"], 1)
                act.wait_ge(s["head"], 3)
                with act.Fori(0, KD // LC) as it:
                    for k in range(LC):
                        for m, (o, n, bias) in enumerate(((r, "r_ready", "ba"), (i_, "i_ready", "bx"))):
                            act.wait_ge(s["mm"], it * (2 * LC) + (2 * k + m + 1))
                            for b in range(2):
                                ins = nc.scalar.activation(o[:, k, b * BANK:(b + 1) * BANK], bank[4 * k + 2 * m + b][:, :],
                                                           ACT.Sigmoid, bias=c(bias, it * LC + k))
                            ins.then_inc(s[n], 1)
                    for k in range(LC):
                        act.wait_ge(s["r_ready"], it * LC + (k + 1))
                        nc.scalar.activation(t[:, k, :], r[:, k, :], ACT.Tanh, scale=pc[:, 0, ds(it * LC + k, 1)])\
                            .then_inc(s["t_ready"], 1)
                    for k in range(LC):
                        nc.scalar.activation(a[:, k, :], r[:, k, :], ACT.Exp, scale=pc[:, 1, ds(it * LC + k, 1)])\
                            .then_inc(s["a_ready"], 1)
                    for k in range(LC):
                        act.wait_ge(s["u_ready"], it * LC + (k + 1))
                        nc.scalar.activation(u[:, k, :], u[:, k, :], ACT.Sqrt).then_inc(s["root"], 1)
                    act.wait_ge(s["g_in"], it * (16 * LC) + 16 * LC)
                    for k in range(LC):
                        nc.scalar.activation(gate[:, k, :], gate[:, k, :], ACT.Gelu_apprx_tanh).then_inc(s["gelu"], 1)

            @block.vector
            def _(dve):
                head = Steps(s["chain"])
                lam = col[:, COLS["lam"]:COLS["lam"] + KD]
                dve.wait_ge(s["chain"], head(nc.vector.tensor_scalar(sp4[:, 2, :], lam, -1.0, None, ALU.mult)))
                dve.wait_ge(s["chain"], head(nc.vector.tensor_scalar(sp4[:, 3, :], sp4[:, 2, :], 0.0, None, ALU.max)))
                nc.vector.tensor_tensor(sp4[:, 0, :], lam, sp4[:, 2, :], ALU.max).then_inc(s["head"], 1)
                dve.wait_ge(s["head_act"], 1)
                nc.vector.tensor_scalar(sp4[:, 2, :], sp4[:, 1, :], 1.0, None, ALU.add).then_inc(s["head"], 1)
                dve.wait_ge(s["head_act"], 2)
                dve.wait_ge(s["chain"], head(nc.vector.tensor_scalar(pc[:, 2, :], sp4[:, 2, :], 1.0, None, ALU.is_equal)))
                dve.wait_ge(s["chain"], head(nc.vector.tensor_tensor(sp4[:, 0, :], sp4[:, 0, :], pc[:, 2, :], ALU.add)))
                dve.wait_ge(s["chain"], head(nc.vector.scalar_tensor_tensor(pc[:, 2, :], sp4[:, 2, :], -1.0, pc[:, 2, :],
                                                                            ALU.add, ALU.add)))
                dve.wait_ge(s["chain"], head(nc.vector.reciprocal(pc[:, 2, :], pc[:, 2, :])))
                dve.wait_ge(s["chain"], head(nc.vector.tensor_tensor(sp4[:, 0, :], sp4[:, 0, :], sp4[:, 1, :], ALU.mult)))
                dve.wait_ge(s["chain"], head(nc.vector.tensor_tensor(sp4[:, 0, :], sp4[:, 0, :], pc[:, 2, :], ALU.mult)))
                dve.wait_ge(s["chain"], head(nc.vector.tensor_tensor(sp4[:, 0, :], sp4[:, 0, :], sp4[:, 3, :], ALU.add)))
                dve.wait_ge(s["chain"], head(nc.vector.tensor_scalar(pc[:, 0, :], sp4[:, 0, :], 8.0, None, ALU.mult)))
                nc.vector.tensor_scalar(pc[:, 1, :], sp4[:, 0, :], -8.0, None, ALU.mult).then_inc(s["head"], 1)
                CHAIN = 3 * LC + 3 * LC + LC
                with dve.Fori(0, KD // LC) as it:
                    link = Loop(s["conv"], it, CHAIN)

                    def wait(n):
                        dve.wait_ge(s["conv"], n)

                    dve.wait_ge(s["x_in"], it * (16 * LC) + 16 * LC)
                    last = [None] * LC
                    for tap in range(4):
                        for k in range(LC):
                            n = it * LC + k
                            src = x[:, k, 1 + tap:1 + tap + T]
                            if tap == 0:
                                last[k] = link(nc.vector.tensor_scalar(xc[:, k, :], src, c("conv2", n), c("conv2b", n),
                                                                       ALU.mult, ALU.add))
                                continue
                            wait(last[k])
                            ins = nc.vector.scalar_tensor_tensor(xc[:, k, :], src, c("conv2", n + 8 * tap), xc[:, k, :],
                                                                 ALU.mult, ALU.add)
                            if tap < 3:
                                last[k] = link(ins)
                            else:
                                ins.then_inc(s["xc_ready"], 1)
                    for k in range(LC):
                        dve.wait_ge(s["t_ready"], it * LC + (k + 1))
                        last[k] = link(nc.vector.tensor_scalar(u[:, k, :], t[:, k, :], 1.0, None, ALU.add))
                    for k in range(LC):
                        wait(last[k])
                        last[k] = link(nc.vector.reciprocal(u[:, k, :], u[:, k, :]))
                    for k in range(LC):
                        wait(last[k])
                        nc.vector.scalar_tensor_tensor(u[:, k, :], t[:, k, :], 2.0, u[:, k, :], ALU.mult, ALU.mult)\
                            .then_inc(s["u_ready"], 1)
                    for k in range(LC):
                        dve.wait_ge(s["root"], it * LC + (k + 1))
                        dve.wait_ge(s["ix_ready"], it * LC + (k + 1))
                        last[k] = link(nc.vector.tensor_tensor(u[:, k, :], u[:, k, :], i_[:, k, :], ALU.mult))
                    for k in range(LC):
                        wait(last[k])
                        dve.wait_ge(s["a_ready"], it * LC + (k + 1))
                        dve.wait_ge(stored[k], it * 16 + 1)
                        last[k] = link(nc.vector.tensor_tensor_scan(h[:, k, :], a[:, k, :], u[:, k, :], 0.0, ALU.mult, ALU.add))
                    for k in range(LC):
                        wait(last[k])
                        dve.wait_ge(s["gelu"], it * LC + (k + 1))
                        nc.vector.tensor_tensor(h[:, k, :], h[:, k, :], gate[:, k, :], ALU.mult).then_inc(s["out"], 1)
                    link.end()


TWO_PI_HI, TWO_PI_MID = 6.28125, 0.00193500518798828125
TWO_PI_LO = 2 * math.pi - TWO_PI_HI - TWO_PI_MID
ROUND = 1.5 * 2.0 ** 23
PI_BELOW = 3.1415925


def qkv_heads(nc, bank, cst, col, positions, uT, qkT, v_rows):
    LH = 2
    Q0, K0, V0 = 2 * D, 3 * D, 4 * D
    with Stage(nc, "heads") as st:
        pos = st.sb("pos", [P, T], I32)
        tab = st.sb("tab", [P, 2, T])
        ang, turn = st.sb("ang", [P, T]), st.sb("turn", [P, T])
        g2 = st.sb("g2", [P, 2])
        x = st.sb("x", [P, LH, 2, T])
        v = st.sb("v", [P, LH, T])
        rs = st.sb("rs", [P, LH, 2, T])
        vr = st.sb("vr", [P, LH, NT, P])
        names = ("pos_in", "ang", "x_in", "v_in", "chain", "tables", "sin", "squared", "sums", "ms", "root", "normed", "rot",
                 "turns", "cosed", "rotated", "v_tr", "v_ev", "ready")
        s = {n: st.sem(n) for n in names}
        stored, v_stored = ([st.sem(f"{n}{k}") for k in range(LH)] for n in ("stored", "v_stored"))
        ident, pair, rot2 = (cst[:, CONST[n]:CONST[n] + P] for n in ("ident", "pair", "rot2"))
        N = 2 * LH
        with nc.Block() as block:
            @block.sync
            def _(sp):
                sp.dma_start(pos[:, :], positions.partition_broadcast(P).rearrange("p o t -> p (o t)")).then_inc(s["pos_in"], 16)
                for k in range(LH):
                    sp.sem_inc(stored[k], 1)
                    sp.sem_inc(v_stored[k], 1)
                with sp.Fori(0, HEADS2 // LH) as it:
                    for k in range(LH):
                        row = it * (LH * P) + k * P
                        sp.wait_ge(stored[k], it * 32 + 1)
                        sp.sem_inc(s["turns"], 1)
                        for n, r0 in enumerate((Q0, K0)):
                            sp.dma_start(x[:, k, n, :], uT[ds(row + r0, P), :]).then_inc(s["x_in"], 16)
                        sp.dma_start(v[:, k, :], uT[ds(row + V0, P), :]).then_inc(s["v_in"], 16)
                    for k in range(LH):
                        row = it * (LH * P) + k * P
                        sp.wait_ge(s["v_ev"], it * N + 2 * (k + 1))
                        sp.sem_inc(s["turns"], 1)
                        sp.dma_start(v_rows[:, ds(row, P)].rearrange("(n p) d -> p n d", p=P), vr[:, k, :, :])\
                            .then_inc(v_stored[k], 16)
                    for k in range(LH):
                        row = it * (LH * P) + k * P
                        for n in range(2):
                            sp.wait_ge(s["ready"], it * N + (2 * k + n + 1))
                            sp.sem_inc(s["turns"], 1)
                            sp.dma_start(qkT[n, ds(row, P), :], x[:, k, n, :]).then_inc(stored[k], 16)
                for k in range(LH):
                    sp.wait_ge(stored[k], 32 * (HEADS2 // LH) + 1)
                    sp.wait_ge(v_stored[k], 16 * (HEADS2 // LH) + 1)

            @block.gpsimd
            def _(pool):
                pool.wait_ge(s["sin"], 2)
                with pool.Fori(0, HEADS2 // LH) as it:
                    for k in range(LH):
                        for n in range(2):
                            pool.wait_ge(s["rot"], it * N + (2 * k + n + 1))
                            nc.gpsimd.tensor_tensor(x[:, k, n, :], x[:, k, n, :], tab[:, 0, :], ALU.mult)\
                                .then_inc(s["cosed"], 1)

            @block.tensor
            def _(pe):
                with pe.Fori(0, HEADS2 // LH) as it:
                    pe.wait_ge(s["v_in"], it * (16 * LH) + 16 * LH)
                    for k in range(LH):
                        for b in range(2):
                            if k:
                                pe.wait_ge(s["v_ev"], it * N + (b + 1))
                            for j in range(4):
                                t = slice((4 * b + j) * P, (4 * b + j + 1) * P)
                                ins = nc.tensor.transpose(bank[4 + b][:, j * P:(j + 1) * P], v[:, k, t], ident)
                            ins.then_inc(s["v_tr"], 1)

                    def sums(k, n):
                        i = 2 * k + n
                        pe.wait_ge(s["squared"], it * N + (i + 1))
                        if i >= 2:
                            pe.wait_ge(s["ms"], it * N + (i - 1))
                        for b in range(2):
                            ins = nc.tensor.matmul(bank[2 * n + b][:, :], pair, rs[:, k, n, b * BANK:(b + 1) * BANK],
                                                   start=True, stop=True)
                        ins.then_inc(s["sums"], 1)

                    for k in range(LH):
                        for n in range(2):
                            sums(k, n)
                    for k in range(LH):
                        for n in range(2):
                            i = 2 * k + n
                            pe.wait_ge(s["normed"], it * N + (i + 1))
                            if i >= 2:
                                pe.wait_ge(s["rotated"], it * N + (i - 1))
                            for b in range(2):
                                ins = nc.tensor.matmul(bank[2 * n + b][:, :], rot2, x[:, k, n, b * BANK:(b + 1) * BANK],
                                                       start=True, stop=True)
                            ins.then_inc(s["rot"], 1)

            @block.scalar
            def _(act):
                act.wait_ge(s["ang"], 1)
                nc.scalar.activation(tab[:, 1, :], turn[:, :], ACT.Sin).then_inc(s["sin"], 1)
                act.wait_ge(s["ang"], 2)
                nc.scalar.activation(tab[:, 0, :], ang[:, :], ACT.Sin).then_inc(s["sin"], 1)
                with act.Fori(0, HEADS2 // LH) as it:
                    act.wait_ge(s["x_in"], it * (32 * LH) + 32 * LH)
                    for k in range(LH):
                        for n in range(2):
                            nc.scalar.activation(rs[:, k, n, :], x[:, k, n, :], ACT.Square).then_inc(s["squared"], 1)
                    for k in range(LH):
                        act.wait_ge(v_stored[k], it * 16 + 1)
                        for b in range(2):
                            act.wait_ge(s["v_tr"], it * N + (2 * k + b + 1))
                            nc.scalar.activation(vr[:, k, 4 * b:4 * b + 4, :].rearrange("p n d -> p (n d)"), bank[4 + b][:, :],
                                                 ACT.Copy).then_inc(s["v_ev"], 1)
                    for k in range(LH):
                        act.wait_ge(s["ms"], it * N + 2 * (k + 1))
                        nc.scalar.activation(rs[:, k, :, :], rs[:, k, :, :], ACT.Sqrt).then_inc(s["root"], 1)

            @block.vector
            def _(dve):
                head = Steps(s["tables"])

                def wait_head(n):
                    dve.wait_ge(s["tables"], n)

                dve.wait_ge(s["pos_in"], 16)
                wait_head(head(nc.vector.tensor_copy(ang[:, :], pos[:, :])))
                wait_head(head(nc.vector.tensor_scalar(ang[:, :], ang[:, :], cst[:, CONST["invf"]:CONST["invf"] + 1], None,
                                                       ALU.mult)))
                wait_head(head(nc.vector.tensor_scalar(turn[:, :], ang[:, :], 1.0 / (2 * math.pi), ROUND, ALU.mult, ALU.add)))
                wait_head(head(nc.vector.tensor_scalar(turn[:, :], turn[:, :], -ROUND, None, ALU.add)))
                for part in (TWO_PI_HI, TWO_PI_MID, TWO_PI_LO):
                    wait_head(head(nc.vector.scalar_tensor_tensor(ang[:, :], turn[:, :], -part, ang[:, :], ALU.mult, ALU.add)))
                nc.vector.tensor_scalar(turn[:, :], ang[:, :], PI_BELOW, -PI_BELOW, ALU.min, ALU.max).then_inc(s["ang"], 1)
                wait_head(head(nc.vector.tensor_scalar(tab[:, 0, :], ang[:, :], -1.0, None, ALU.mult)))
                wait_head(head(nc.vector.tensor_tensor(ang[:, :], ang[:, :], tab[:, 0, :], ALU.max)))
                nc.vector.tensor_scalar(ang[:, :], ang[:, :], -1.0, math.pi / 2, ALU.mult, ALU.add).then_inc(s["ang"], 1)
                for n, (name, scale) in enumerate((("qn", HD2 ** -0.5), ("kn", 1.0))):
                    wait_head(head(nc.vector.tensor_scalar(g2[:, n:n + 1], col[:, COLS[name]:COLS[name] + 1], scale, None,
                                                           ALU.mult)))
                dve.wait_ge(s["sin"], 2)
                with dve.Fori(0, HEADS2 // LH) as it:
                    link = Loop(s["chain"], it, LH)
                    last = [None] * N
                    for k in range(LH):
                        for n in range(2):
                            dve.wait_ge(s["sums"], it * N + (2 * k + n + 1))
                            for b in range(2):
                                ins = nc.vector.tensor_scalar(rs[:, k, n, b * BANK:(b + 1) * BANK], bank[2 * n + b][:, :],
                                                              1.0 / HD2, EPS, ALU.mult, ALU.add)
                            ins.then_inc(s["ms"], 1)
                    for k in range(LH):
                        dve.wait_ge(s["root"], it * LH + (k + 1))
                        last[k] = link(nc.vector.reciprocal(rs[:, k, :, :], rs[:, k, :, :]))
                    for k in range(LH):
                        dve.wait_ge(s["chain"], last[k])
                        for n in range(2):
                            nc.vector.scalar_tensor_tensor(x[:, k, n, :], x[:, k, n, :], g2[:, n:n + 1], rs[:, k, n, :],
                                                           ALU.mult, ALU.mult).then_inc(s["normed"], 1)
                    for k in range(LH):
                        for n in range(2):
                            dve.wait_ge(s["rot"], it * N + (2 * k + n + 1))
                            for b in range(2):
                                t = slice(b * BANK, (b + 1) * BANK)
                                ins = nc.vector.tensor_tensor(rs[:, k, n, t], bank[2 * n + b][:, :], tab[:, 1, t], ALU.mult)
                            ins.then_inc(s["rotated"], 1)
                            dve.wait_ge(s["rotated"], it * N + (2 * k + n + 1))
                            dve.wait_ge(s["cosed"], it * N + (2 * k + n + 1))
                            nc.vector.tensor_tensor(x[:, k, n, :], x[:, k, n, :], rs[:, k, n, :], ALU.add).then_inc(s["ready"], 1)
                    link.end()


def diff_attention(nc, bank, cst, col, x, qkT, v_rows, oT):
    J = 2 * NT
    with Stage(nc, "attn") as st:
        q = st.sb("q", [P, 2, T])
        kz = st.sb("kz", [P, 2, 2, T])
        v = st.sb("v", [P, 2, NT, P])
        lv = st.sb("lv", [P, 4, HD2])
        lp = st.sb("lp", [P, 2, HD2])
        lm = st.sb("lm", [P, 8])
        sub = st.sb("sub", [P, 1])
        e = st.sb("e", [P, 2, 2, T])
        sm = st.sb("sm", [P, 2, 2, 8])
        w = st.sb("w", [P, 2, T])
        wT = st.sb("wT", [P, 2, NT, P])
        o, rs = st.sb("o", [P, 2, T]), st.sb("rs", [P, 2, T])
        names = ("zeroed", "lam_in", "lam", "lam_exp", "ready", "s_mm", "chain", "nm", "exp", "scaled", "rec", "w_ready",
                 "trA", "trB", "evA", "evB", "o_mm", "o_ev", "squared", "sums", "ms", "root", "out")
        s = {n: st.sem(n) for n in names}
        qkv_in = [st.sem(f"qkv_in{k}") for k in range(2)]
        stored = [st.sem(f"stored{k}") for k in range(2)]
        ident, ones = (cst[:, CONST[n]:CONST[n] + P] for n in ("ident", "ones"))
        TURNS = HEADS2 // 2
        LOADS = 4 * 16
        late = lambda j: (j // NT) * 4 + j % NT - 3

        def banks(i):
            n = (i + 1) * P
            return [(0, 0, min(n, BANK))] + ([(1, BANK, n)] if n > BANK else [])

        with nc.Block() as block:
            @block.sync
            def _(sp):
                for n, name in enumerate(("lambda_q1_2", "lambda_k1_2", "lambda_q2_2", "lambda_k2_2")):
                    sp.dma_start(lv[:, n, :], x[name].partition_broadcast(P).rearrange("p o d -> p (o d)")).then_inc(s["lam_in"], 16)

                def load(it, k):
                    rows = ds(it * (2 * P) + k * P, P)
                    sp.dma_start(q[:, k, :], qkT[0, rows, :]).then_inc(qkv_in[k], 16)
                    for m in range(2):
                        sp.dma_start(kz[64 * m:64 * m + 64, k, m, :], qkT[1, ds(it * (2 * P) + (k * P + 64 * m), 64), :])\
                            .then_inc(qkv_in[k], 16)
                    sp.dma_start(v[:, k, :, :], v_rows[:, rows].rearrange("(n p) d -> p n d", p=P)).then_inc(qkv_in[k], 16)

                def store(it, k):
                    sp.wait_ge(s["out"], it * 2 + (k + 1))
                    sp.dma_start(oT[ds(it * (2 * P) + k * P, P), :], o[:, k, :]).then_inc(stored[k], 16)

                for k in range(2):
                    sp.sem_inc(stored[k], 1)
                sp.wait_ge(s["zeroed"], 1)
                load(0, 0)
                load(0, 1)
                with sp.Fori(0, TURNS - 1) as it:
                    for k in range(2):
                        sp.wait_ge(s["o_mm"], it * J + NT * (k + 1))
                        load(it + 1, k)
                        store(it, k)
                for k in range(2):
                    store(TURNS - 1, k)
                    sp.wait_ge(stored[k], 16 * TURNS + 1)

            @block.gpsimd
            def _(pool):
                nc.gpsimd.memset(kz[:, :, :, :], 0.0).then_inc(s["zeroed"], 1)
                with pool.Fori(0, TURNS) as it:
                    for j in range(J):
                        i = j % NT
                        pool.wait_ge(s["rec"], it * J + (j + 1))
                        pool.sem_inc(s["ready"], 1)
                        nc.gpsimd.tensor_scalar(e[:, j % 2, 0, 0:(i + 1) * P], e[:, j % 2, 0, 0:(i + 1) * P],
                                                sm[:, j % 2, 0, 6:7], None, ALU.mult).then_inc(s["scaled"], 1)

            @block.tensor
            def _(pe):
                with pe.Fori(0, TURNS) as it:
                    def scores(j):
                        i, k = j % NT, j // NT
                        if i == 0:
                            pe.wait_ge(qkv_in[k], it * LOADS + LOADS)
                        for m in range(2):
                            if j:
                                pe.wait_ge(s["exp"], it * (2 * J) + (2 * (j - 1) + m + 1))
                            for b, c0, c1 in banks(i):
                                ins = nc.tensor.matmul(bank[2 * m + b][:, 0:c1 - c0], q[:, k, i * P:(i + 1) * P],
                                                       kz[:, k, m, c0:c1], start=True, stop=True)
                            ins.then_inc(s["s_mm"], 1)

                    def values(j):
                        i, k = j % NT, j // NT
                        pe.wait_ge(s["w_ready"], it * J + (j + 1))
                        for b, c0, c1 in banks(i):
                            for t in range(c0 // P, c1 // P):
                                ins = nc.tensor.transpose(bank[4 + b][:, (t % 4) * P:(t % 4 + 1) * P], w[:, j % 2, t * P:(t + 1) * P],
                                                          ident)
                            ins.then_inc(s["trB" if b else "trA"], 1)
                        if j >= 2:
                            pe.wait_ge(s["o_ev"], it * J + (j - 1))
                        if j == NT + 1:
                            pe.wait_ge(s["ms"], it * 2 + 1)
                        for t in range(i + 1):
                            if t % 4 == 0:
                                pe.wait_ge(*((s["evB"], it * 8 + late(j)) if t else (s["evA"], it * J + (j + 1))))
                            ins = nc.tensor.matmul(bank[6 + j % 2][:, 0:P], v[:, k, t, :], wT[:, j % 2, t, :],
                                                   start=(t == 0), stop=(t == i))
                        ins.then_inc(s["o_mm"], 1)

                    def sums(k, j):
                        pe.wait_ge(s["squared"], it * 2 + (k + 1))
                        pe.wait_ge(s["o_ev"], it * J + (j + 1))
                        for b in range(2):
                            ins = nc.tensor.matmul(bank[6 + b][:, :], ones, rs[:, k, b * BANK:(b + 1) * BANK], start=True, stop=True)
                        ins.then_inc(s["sums"], 1)

                    for j in range(J):
                        scores(j)
                        if j:
                            values(j - 1)
                        if j == NT + 1:
                            sums(0, NT)
                    values(J - 1)
                    sums(1, J - 1)

            @block.scalar
            def _(act):
                act.wait_ge(s["lam"], 1)
                nc.scalar.activation(lm[:, 2:4], lm[:, 0:2], ACT.Exp).then_inc(s["lam_exp"], 1)
                with act.Fori(0, TURNS) as it:
                    def evacuate(j):
                        i, k = j % NT, j // NT
                        n = min((i + 1) * P, BANK)
                        act.wait_ge(s["trA"], it * J + (j + 1))
                        nc.scalar.activation(wT[:, j % 2, 0:4, :].rearrange("p n d -> p (n d)")[:, 0:n], bank[4][:, 0:n], ACT.Copy)\
                            .then_inc(s["evA"], 1)
                        act.wait_ge(s["o_mm"], it * J + (j + 1))
                        if i == 0:
                            act.wait_ge(stored[k], it * 16 + 1)
                        nc.scalar.activation(o[:, k, i * P:(i + 1) * P], bank[6 + j % 2][:, 0:P], ACT.Copy).then_inc(s["o_ev"], 1)

                    def square(k):
                        act.wait_ge(s["o_ev"], it * J + (k + 1) * NT)
                        nc.scalar.activation(rs[:, k, :], o[:, k, :], ACT.Square).then_inc(s["squared"], 1)

                    def root(k):
                        act.wait_ge(s["ms"], it * 2 + (k + 1))
                        nc.scalar.activation(rs[:, k, :], rs[:, k, :], ACT.Sqrt).then_inc(s["root"], 1)

                    for j in range(J):
                        i = j % NT
                        if j >= 2:
                            act.wait_ge(s["w_ready"], it * J + (j - 1))
                        for m in range(2):
                            act.wait_ge(s["nm"], it * (2 * J) + (2 * j + m + 1))
                            for b, c0, c1 in banks(i):
                                ins = nc.scalar.activation(e[:, j % 2, m, c0:c1], bank[2 * m + b][:, 0:c1 - c0], ACT.Exp,
                                                           bias=sm[:, j % 2, m, 2:3], accum_out=sm[:, j % 2, m, 3 + b:4 + b])
                            ins.then_inc(s["exp"], 1)
                        if j:
                            evacuate(j - 1)
                        if j == NT:
                            square(0)
                        if j == NT + 2:
                            root(0)
                    evacuate(J - 1)
                    square(1)
                    root(1)

            @block.vector
            def _(dve):
                head = Steps(s["chain"])
                dve.wait_ge(s["lam_in"], 64)
                for n in range(2):
                    dve.wait_ge(s["chain"], head(nc.vector.tensor_tensor(lp[:, n, :], lv[:, 2 * n, :], lv[:, 2 * n + 1, :], ALU.mult)))
                nc.vector.tensor_reduce(lm[:, 0:2], lp[:, :, :], AX_X, ALU.add).then_inc(s["lam"], 1)
                dve.wait_ge(s["lam_exp"], 1)
                dve.wait_ge(s["chain"], head(nc.vector.tensor_tensor(lm[:, 4:5], lm[:, 2:3], lm[:, 3:4], ALU.subtract)))
                dve.wait_ge(s["chain"], head(nc.vector.tensor_scalar(lm[:, 5:6], lm[:, 4:5], LAMBDA_INIT, -1.0, ALU.add, ALU.mult)))
                dve.wait_ge(s["chain"], head(nc.vector.tensor_scalar(sub[:, :], col[:, COLS["subln"]:COLS["subln"] + 1],
                                                                     1.0 - LAMBDA_INIT, None, ALU.mult)))
                base = head.n
                per_tile = lambda i: 2 * (2 + (i >= 4)) + 1 + (i >= 4)
                CHAIN = 2 * sum(per_tile(i) for i in range(NT)) + 2
                with dve.Fori(0, TURNS) as it:
                    class Link(Loop):
                        def __call__(self, ins):
                            return Loop.__call__(self, ins) + base
                    link = Link(s["chain"], it, CHAIN)

                    def wait(n):
                        dve.wait_ge(s["chain"], n)

                    def maxima(j):
                        i = j % NT
                        for m in range(2):
                            c = sm[:, j % 2, m]
                            dve.wait_ge(s["s_mm"], it * (2 * J) + (2 * j + m + 1))
                            d = i % 4 * P
                            wait(link(nc.vector.memset(bank[2 * m + i // 4][0:CHUNK2, d + CHUNK2:d + P], -1e30)))
                            for b, c0, c1 in banks(i):
                                n = link(nc.vector.tensor_reduce(c[:, b:b + 1], bank[2 * m + b][:, 0:c1 - c0], AX_X, ALU.max))
                            wait(n)
                            if i >= 4:
                                nc.vector.tensor_scalar(c[:, 2:3], c[:, 0:1], c[:, 1:2], -1.0, ALU.max, ALU.mult).then_inc(s["nm"], 1)
                            else:
                                nc.vector.tensor_scalar(c[:, 2:3], c[:, 0:1], -1.0, None, ALU.mult).then_inc(s["nm"], 1)

                    def weights(j):
                        i = j % NT
                        both = sm[:, j % 2]
                        dve.wait_ge(s["exp"], it * (2 * J) + 2 * (j + 1))
                        if i >= 4:
                            wait(link(nc.vector.tensor_tensor(both[:, :, 5:6], both[:, :, 3:4], both[:, :, 4:5], ALU.add)))
                        total = 5 if i >= 4 else 3
                        nc.vector.reciprocal(both[:, :, 6:7], both[:, :, total:total + 1]).then_inc(s["rec"], 1)
                        dve.wait_ge(s["rec"], it * J + (j + 1))
                        wait(link(nc.vector.tensor_tensor(both[:, 1, 7:8], both[:, 1, 6:7], lm[:, 5:6], ALU.mult)))
                        dve.wait_ge(s["scaled"], it * J + (j + 1))
                        if j >= 2:
                            dve.wait_ge(s["trA"], it * J + (j - 1))
                        n = (i + 1) * P
                        nc.vector.scalar_tensor_tensor(w[:, j % 2, 0:n], e[:, j % 2, 1, 0:n], both[:, 1, 7:8], e[:, j % 2, 0, 0:n],
                                                       ALU.mult, ALU.add).then_inc(s["w_ready"], 1)

                    def evacuate(j):
                        i = j % NT
                        if i >= 4:
                            n = (i + 1) * P - BANK
                            dve.wait_ge(s["trB"], it * 8 + late(j))
                            nc.vector.tensor_copy(wT[:, j % 2, 4:8, :].rearrange("p n d -> p (n d)")[:, 0:n], bank[5][:, 0:n])\
                                .then_inc(s["evB"], 1)

                    def mean(k):
                        dve.wait_ge(s["sums"], it * 2 + (k + 1))
                        for b in range(2):
                            ins = nc.vector.tensor_scalar(rs[:, k, b * BANK:(b + 1) * BANK], bank[6 + b][:, :], 1.0 / P, EPS,
                                                          ALU.mult, ALU.add)
                        ins.then_inc(s["ms"], 1)

                    def norm(k):
                        dve.wait_ge(s["root"], it * 2 + (k + 1))
                        wait(link(nc.vector.reciprocal(rs[:, k, :], rs[:, k, :])))
                        nc.vector.scalar_tensor_tensor(o[:, k, :], o[:, k, :], sub[:, 0:1], rs[:, k, :], ALU.mult, ALU.mult)\
                            .then_inc(s["out"], 1)

                    for j in range(J):
                        maxima(j)
                        if j:
                            evacuate(j - 1)
                        weights(j)
                        if j == NT + 1:
                            mean(0)
                        if j == NT + 3:
                            norm(0)
                    evacuate(J - 1)
                    mean(1)
                    norm(1)
                    link.end()


def mixed_T(nc, bank, w_a, w_b, aT_dram, bT_dram, gates, mT):
    with Stage(nc, "mixed") as st:
        act_T = st.sb("act", [P, 2, KD, T])
        w = st.sb("w", [P, 2, 2, KD, 2 * P])
        g = st.sb("g", [P, 2, 2, T])
        y = st.sb("y", [P, 2, T])
        names = ("mm", "sig", "gated", "done", "ev")
        s = {n: st.sem(n) for n in names}
        a_in = [st.sem(f"a_in{n}") for n in range(2)]
        w_in, g_in = ([st.sem(f"{n}{k}") for k in range(2)] for n in ("w_in", "g_in"))
        TURNS = KD // 4
        with nc.Block() as block:
            @block.sync
            def _(sp):
                def load_w(slot, c0):
                    for n, m in enumerate((w_a, w_b)):
                        sp.dma_start(w[:, slot, n], m[:, ds(c0, 2 * P)].rearrange("(k p) n -> p k n", p=P)).then_inc(w_in[slot], 16)

                load_w(0, 0)
                for n, src in enumerate((aT_dram, bT_dram)):
                    sp.dma_start(act_T[:, n], src.rearrange("(k p) t -> p k t", p=P)).then_inc(a_in[n], 16)
                load_w(1, 2 * P)
                with sp.Fori(0, TURNS - 1) as it:
                    for k in range(2):
                        sp.wait_ge(s["mm"], it * 8 + 4 * (k + 1))
                        load_w(k, it * (4 * P) + ((4 + 2 * k) * P))

            @block.gpsimd
            def _(pool):
                with pool.Fori(0, TURNS) as it:
                    for c in range(4):
                        pool.wait_ge(s["gated"], it * 8 + 2 * (c + 1))
                        nc.gpsimd.tensor_tensor(mT[:, ds(it * 4 + c, 1), :].rearrange("p o t -> p (o t)"), y[:, 0, :], y[:, 1, :],
                                                ALU.add).then_inc(s["done"], 1)

            @block.tensor
            def _(pe):
                pe.wait_ge(a_in[0], 16)
                pe.wait_ge(a_in[1], 16)
                with pe.Fori(0, TURNS) as it:
                    for c in range(4):
                        if c % 2 == 0:
                            pe.wait_ge(w_in[c // 2], it * 32 + 32)
                        for n in range(2):
                            o = bank[4 * (c % 2) + 2 * n:4 * (c % 2) + 2 * n + 2]
                            if c >= 2:
                                pe.wait_ge(s["gated"], it * 8 + (2 * (c - 2) + n + 1))
                            elif c == 0 and n == 0:
                                pe.wait_ge(s["ev"], it * 2 + 1)
                            elif c == 1 and n == 0:
                                pe.wait_ge(s["ev"], it * 2 + 2)
                            for b in range(2):
                                for k in range(KD):
                                    last = nc.tensor.matmul(o[b][:, :], w[:, c // 2, n, k, (c % 2) * P:(c % 2 + 1) * P],
                                                            act_T[:, n, k, b * BANK:(b + 1) * BANK],
                                                            start=(k == 0), stop=(k == KD - 1))
                            last.then_inc(s["mm"], 1)

            @block.scalar
            def _(act):
                act.sem_inc(s["done"], 1)
                with act.Fori(0, TURNS) as it:
                    for c in range(4):
                        slot = c % 2
                        if c >= 2:
                            act.wait_ge(s["gated"], it * 8 + 2 * (c - 1))
                        elif c == 1:
                            act.wait_ge(s["ev"], it * 2 + 2)
                        else:
                            act.wait_ge(s["ev"], it * 2 + 1)
                        for n in range(2):
                            act.dma_start(g[:, slot, n, :], gates[ds(it * (4 * P) + (n * D + c * P), P), :])\
                                .then_inc(g_in[slot], 16)
                        act.wait_ge(g_in[slot], it * 64 + 32 * (c // 2 + 1))
                        nc.scalar.activation(g[:, slot, :, :], g[:, slot, :, :], ACT.Sigmoid).then_inc(s["sig"], 1)

            @block.vector
            def _(dve):
                dve.sem_inc(s["ev"], 2)
                with dve.Fori(0, TURNS) as it:
                    for c in range(4):
                        dve.wait_ge(s["sig"], it * 4 + (c + 1))
                        dve.wait_ge(s["done"], it * 4 + (c + 1))
                        for n in range(2):
                            dve.wait_ge(s["mm"], it * 8 + (2 * c + n + 1))
                            for b in range(2):
                                t = slice(b * BANK, (b + 1) * BANK)
                                ins = nc.vector.tensor_tensor(y[:, n, t], bank[4 * (c % 2) + 2 * n + b][:, :], g[:, c % 2, n, t],
                                                              ALU.mult)
                            ins.then_inc(s["gated"], 1)
                        if c >= 2:
                            dve.wait_ge(s["gated"], it * 8 + 2 * (c + 1))
                            dve.sem_inc(s["ev"], 1)


def cross_attention(nc, bank, cst, col, w_q, w_kv, hT, mT, oT):
    NM = MEM // P
    with Stage(nc, "cross") as st:
        w = st.sb("w", [P, 3, KD, P])
        qk = st.sb("qk", [P, T + MEM])
        sq = st.sb("sq", [P, T + MEM])
        v = st.sb("v", [P, NM, P])
        g2 = st.sb("g2", [P, 2])
        sm = st.sb("sm", [P, NT, 4])
        e = st.sb("e", [P, NT, MEM])
        eT = st.sb("eT", [P, NM, T])
        names = ("proj", "proj_ev", "squared", "sums", "ms", "root", "chain", "head", "normed", "s_mm", "nm", "exp", "p_ready",
                 "tr", "tr_ev", "o_mm", "o_ev")
        s = {n: st.sem(n) for n in names}
        w_in = [st.sem(f"w_in{n}") for n in range(3)]
        ident, ones = (cst[:, CONST[n]:CONST[n] + P] for n in ("ident", "ones"))
        parts = [(0, BANK), (BANK, T), (T, T + MEM)]
        with nc.Block() as block:
            @block.sync
            def _(sp):
                def load(h, n):
                    src = w_q if n == 0 else w_kv
                    c0 = h * P + (MH * P if n == 2 else 0)
                    sp.dma_start(w[:, n], src[:, ds(c0, P)].rearrange("(k p) n -> p k n", p=P)).then_inc(w_in[n], 16)

                for n in range(3):
                    load(0, n)
                with sp.Fori(0, MH - 1) as h:
                    for n in range(3):
                        sp.wait_ge(s["proj"], h * 5 + (2, 3, 5)[n])
                        load(h + 1, n)

            @block.tensor
            def _(pe):
                with pe.Fori(0, MH) as h:
                    for n, (a, b) in enumerate(parts):
                        m = 1 if n == 2 else 0
                        pe.wait_ge(w_in[m], h * 16 + 16)
                        for k in range(KD):
                            rhs = mT[:, k, :] if m else hT[:, k, a:b]
                            last = nc.tensor.matmul(bank[n][:, 0:b - a], w[:, m, k, :], rhs, start=(k == 0), stop=(k == KD - 1))
                        last.then_inc(s["proj"], 1)
                    pe.wait_ge(w_in[2], h * 16 + 16)
                    for t in range(NM):
                        for k in range(KD):
                            last = nc.tensor.matmul(bank[3][:, t * P:(t + 1) * P], mT[:, k, t * P:(t + 1) * P], w[:, 2, k, :],
                                                    start=(k == 0), stop=(k == KD - 1))
                        last.then_inc(s["proj"], 1)
                    for n, (a, b) in enumerate(parts):
                        pe.wait_ge(s["squared"], h * 3 + (n + 1))
                        nc.tensor.matmul(bank[4 + n][:, 0:b - a], ones, sq[:, a:b], start=True, stop=True).then_inc(s["sums"], 1)
                    pe.wait_ge(s["normed"], h * 3 + 3)
                    for i in range(NT):
                        ins = nc.tensor.matmul(bank[i // 2][:, (i % 2) * MEM:(i % 2 + 1) * MEM], qk[:, i * P:(i + 1) * P],
                                               qk[:, T:T + MEM], start=True, stop=True)
                        if i % 2:
                            ins.then_inc(s["s_mm"], 1)
                    for i in range(NT):
                        pe.wait_ge(s["p_ready"], h * NT + (i + 1))
                        for t in range(NM):
                            ins = nc.tensor.transpose(bank[4 + 2 * (i // 4) + t][:, (i % 4) * P:(i % 4 + 1) * P],
                                                      e[:, i, t * P:(t + 1) * P], ident)
                        if i % 4 == 3:
                            ins.then_inc(s["tr"], 1)
                    for b in range(2):
                        pe.wait_ge(s["tr_ev"], h * 2 + (b + 1))
                        for t in range(NM):
                            last = nc.tensor.matmul(bank[b][:, :], v[:, t, :], eT[:, t, b * BANK:(b + 1) * BANK],
                                                    start=(t == 0), stop=(t == NM - 1))
                        last.then_inc(s["o_mm"], 1)
                    pe.wait_ge(s["o_ev"], h * 2 + 2)

            @block.scalar
            def _(act):
                with act.Fori(0, MH) as h:
                    for n, (a, b) in enumerate(parts):
                        act.wait_ge(s["proj_ev"], h * 4 + (n + 1))
                        nc.scalar.activation(sq[:, a:b], qk[:, a:b], ACT.Square).then_inc(s["squared"], 1)
                    act.wait_ge(s["ms"], h * 3 + 3)
                    nc.scalar.activation(sq[:, :], sq[:, :], ACT.Sqrt).then_inc(s["root"], 1)
                    for i in range(NT):
                        act.wait_ge(s["nm"], h * NT + (i // 2 * 2 + 2))
                        nc.scalar.activation(e[:, i, :], bank[i // 2][:, (i % 2) * MEM:(i % 2 + 1) * MEM], ACT.Exp,
                                             bias=sm[:, i, 1:2], accum_out=sm[:, i, 2:3]).then_inc(s["exp"], 1)
                    for b in range(2):
                        act.wait_ge(s["tr"], h * 2 + (b + 1))
                        for t in range(NM):
                            ins = nc.scalar.activation(eT[:, t, b * BANK:(b + 1) * BANK], bank[4 + 2 * b + t][:, :], ACT.Copy)
                        ins.then_inc(s["tr_ev"], 1)

            @block.vector
            def _(dve):
                head = Steps(s["head"])
                for n, (name, scale) in enumerate((("cqn", float(P) ** -0.5), ("ckn", 1.0))):
                    dve.wait_ge(s["head"], head(nc.vector.tensor_scalar(g2[:, n:n + 1], col[:, COLS[name]:COLS[name] + 1], scale,
                                                                       None, ALU.mult)))
                with dve.Fori(0, MH) as h:
                    link = Loop(s["chain"], h, 1 + 2 * NT)

                    def wait(n):
                        dve.wait_ge(s["chain"], n)

                    for n, (a, b) in enumerate(parts):
                        dve.wait_ge(s["proj"], h * 5 + (n + 1))
                        nc.vector.tensor_copy(qk[:, a:b], bank[n][:, 0:b - a]).then_inc(s["proj_ev"], 1)
                    dve.wait_ge(s["proj"], h * 5 + 5)
                    nc.vector.tensor_copy(v[:, :, :].rearrange("p n d -> p (n d)"), bank[3][:, 0:MEM]).then_inc(s["proj_ev"], 1)
                    for n, (a, b) in enumerate(parts):
                        dve.wait_ge(s["sums"], h * 3 + (n + 1))
                        nc.vector.tensor_scalar(sq[:, a:b], bank[4 + n][:, 0:b - a], 1.0 / P, EPS, ALU.mult, ALU.add)\
                            .then_inc(s["ms"], 1)
                    dve.wait_ge(s["root"], h + 1)
                    wait(link(nc.vector.reciprocal(sq[:, :], sq[:, :])))
                    for n, (a, b) in enumerate(parts):
                        m = 1 if n == 2 else 0
                        nc.vector.scalar_tensor_tensor(qk[:, a:b], qk[:, a:b], g2[:, m:m + 1], sq[:, a:b], ALU.mult, ALU.mult)\
                            .then_inc(s["normed"], 1)
                    for i in range(NT):
                        dve.wait_ge(s["s_mm"], h * (NT // 2) + (i // 2 + 1))
                        if i == 0:
                            dve.wait_ge(s["s_mm"], h * (NT // 2) + NT // 2)
                        wait(link(nc.vector.tensor_reduce(sm[:, i, 0:1], bank[i // 2][:, (i % 2) * MEM:(i % 2 + 1) * MEM], AX_X,
                                                          ALU.max)))
                        nc.vector.tensor_scalar(sm[:, i, 1:2], sm[:, i, 0:1], -1.0, None, ALU.mult).then_inc(s["nm"], 1)
                        if i % 2:
                            for j in (i - 1, i):
                                dve.wait_ge(s["exp"], h * NT + (j + 1))
                                wait(link(nc.vector.reciprocal(sm[:, j, 3:4], sm[:, j, 2:3])))
                                nc.vector.tensor_scalar(e[:, j, :], e[:, j, :], sm[:, j, 3:4], None, ALU.mult)\
                                    .then_inc(s["p_ready"], 1)
                    for b in range(2):
                        dve.wait_ge(s["o_mm"], h * 2 + (b + 1))
                        nc.vector.tensor_copy(oT[:, ds(h, 1), b * BANK:(b + 1) * BANK].rearrange("p o t -> p (o t)"), bank[b][:, :])\
                            .then_inc(s["o_ev"], 1)
                    link.end()


NOVER = (2 * T) // (P + 1) + 1
SLOTS = (E2 + NOVER) * P


def route2(nc, bank, cst, tok, hT, w_group, b_group, w_router, b_router, slot_tok, ye_over, dest, weight, eid, placed):
    G, W = GROUPS, GROUPS + E2
    with Stage(nc, "route2") as st:
        wr = st.sb("wr", [P, KD, W])
        br = st.sb("br", [W, 1])
        lT = st.sb("lT", [W, T])
        lg = st.sb("lg", [P, NT, W])
        gs = st.sb("gs", [P, 6, NT])
        gx, gm = st.sb("gx", [P, NT, G]), st.sb("gm", [P, NT, G])
        el = st.sb("el", [P, NT, G, EPG])
        e8 = st.sb("e8", [P, 2, NT, EPG])
        m8 = st.sb("m8", [P, NT, EPG])
        es = st.sb("es", [P, 8, NT])
        A = st.sb("A", [P, 3, NT, E2])
        B = st.sb("B", [P, NT + 1, E2])
        F = st.sb("F", [P, NT, E2])
        G_ = st.sb("G", [P, NT, E2])
        cn = st.sb("cn", [P, 6, E2])
        ov = st.sb("ov", [P, E2, 8])
        ob = st.sb("ob", [P, NOVER, E2])
        df = st.sb("df", [P, 2, NT])
        ef = st.sb("ef", [P, NOVER + 1])
        zero = st.sb("zero", [P, D])
        names = ("w_in", "l_mm", "l_ev", "tr", "chain", "g_sub", "g_exp", "e_sub", "e_exp", "sums", "r_mm", "zeroed", "cleared", "cleared_ye",
                 "dest_ready", "counted")
        s = {n: st.sem(n) for n in names}
        ident, ones, lower = (cst[:, CONST[n]:CONST[n] + P] for n in ("ident", "ones", "lower"))
        iota = cst[:, CONST["e32"]:CONST["e32"] + E2]
        with nc.Block() as block:
            @block.sync
            def _(sp):
                with nc.allow_non_contiguous_dma("narrow matrices"):
                    sp.dma_start(wr[:, :, 0:G], w_group.rearrange("(k p) e -> p k e", p=P)).then_inc(s["w_in"], 16)
                    sp.dma_start(wr[:, :, G:], w_router.rearrange("(k p) e -> p k e", p=P)).then_inc(s["w_in"], 16)
                    sp.dma_start(br[0:G, :], b_group.rearrange("o e -> e o")).then_inc(s["w_in"], 16)
                    sp.dma_start(br[G:, :], b_router.rearrange("o e -> e o")).then_inc(s["w_in"], 16)
                sp.wait_ge(s["zeroed"], 1)
                sp.dma_start(slot_tok.rearrange("(b p) o -> b (p o)", p=P), zero[0:SLOTS // P, 0:P]).then_inc(s["cleared"], 16)
                for b in range(NOVER):
                    sp.dma_start(ye_over[b * P:(b + 1) * P, :], zero[:, :]).then_inc(s["cleared_ye"], 16)
                sp.wait_ge(s["cleared_ye"], 16 * NOVER)

            @block.gpsimd
            def _(pool):
                nc.gpsimd.memset(zero[:, :], 0.0).then_inc(s["zeroed"], 1)
                pool.wait_ge(s["cleared"], 16)
                pool.wait_ge(s["dest_ready"], 1)
                for k in range(2):
                    for i in range(NT):
                        pool.indirect_dma_start(out=slot_tok[:, :],
                                                out_offset=bass.IndirectOffsetOnAxis(ap=dest[:, k * NT + i:k * NT + i + 1], axis=0),
                                                in_=tok[:, i:i + 1], in_offset=None).then_inc(placed, 16)
                pool.wait_ge(placed, 16 * 2 * NT)

            @block.tensor
            def _(pe):
                pe.wait_ge(s["w_in"], 64)
                for c in range(2):
                    for k in range(KD):
                        last = nc.tensor.matmul(bank[c][0:W, :], wr[:, k, :], hT[:, k, c * BANK:(c + 1) * BANK],
                                                start=(k == 0), stop=(k == KD - 1))
                    last.then_inc(s["l_mm"], 1)
                pe.wait_ge(s["l_ev"], 2)
                for i in range(NT):
                    last = nc.tensor.transpose(bank[2][:, i * W:(i + 1) * W], lT[:, i * P:(i + 1) * P], ident[0:W, 0:W])
                last.then_inc(s["tr"], 1)
                pe.wait_ge(s["sums"], 1)
                both = A[:, 2, :, :].rearrange("p n e -> p (n e)")
                nc.tensor.matmul(bank[3][:, 0:NT * E2], lower, both, start=True, stop=False)
                nc.tensor.matmul(bank[3][:, 0:NT * E2], ones, B[:, 0:NT, :].rearrange("p n e -> p (n e)"), start=False, stop=True)
                nc.tensor.matmul(bank[4][:, 0:E2], ones, B[:, NT, :], start=True, stop=True).then_inc(s["r_mm"], 1)

            @block.scalar
            def _(act):
                act.wait_ge(s["w_in"], 64)
                for c in range(2):
                    act.wait_ge(s["l_mm"], c + 1)
                    nc.scalar.activation(lT[:, c * BANK:(c + 1) * BANK], bank[c][0:W, :], ACT.Identity, bias=br[:, 0:1])\
                        .then_inc(s["l_ev"], 1)
                act.wait_ge(s["g_sub"], 1)
                nc.scalar.activation(gx[:, :, :], gx[:, :, :], ACT.Exp).then_inc(s["g_exp"], 1)
                act.wait_ge(s["e_sub"], 1)
                nc.scalar.activation(es[:, 4, :], es[:, 4, :], ACT.Exp).then_inc(s["e_exp"], 1)

            @block.vector
            def _(dve):
                link = Steps(s["chain"])

                def step(ins):
                    dve.wait_ge(s["chain"], link(ins))

                def over(a, n):
                    return a.unsqueeze(2).to_broadcast([P, NT, n])

                def along(a, n):
                    return a.unsqueeze(1).to_broadcast([P, NT, n])

                V = nc.vector
                dve.wait_ge(s["tr"], 1)
                step(V.tensor_copy(lg[:, :, :].rearrange("p n w -> p (n w)"), bank[2][:, 0:NT * W]))
                step(V.tensor_reduce(gs[:, 0, :], lg[:, :, 0:G], AX_X, ALU.max))
                V.tensor_tensor(gx[:, :, :], lg[:, :, 0:G], over(gs[:, 0, :], G), ALU.subtract).then_inc(s["g_sub"], 1)
                dve.wait_ge(s["g_exp"], 1)
                step(V.tensor_reduce(gs[:, 1, :], gx[:, :, :], AX_X, ALU.add))
                step(V.reciprocal(gs[:, 2, :], gs[:, 1, :]))
                step(V.tensor_tensor(gx[:, :, :], gx[:, :, :], over(gs[:, 2, :], G), ALU.mult))

                def first_greatest(values, n, greatest, index, scratch):
                    step(V.tensor_reduce(greatest, values, AX_X, ALU.max))
                    step(V.tensor_tensor(scratch, values, over(greatest, n), ALU.is_equal))
                    step(V.tensor_scalar(m8[:, 0, 0:n], iota[:, 0:n], -64.0, None, ALU.add))
                    step(V.tensor_tensor(scratch, scratch, along(m8[:, 0, 0:n], n), ALU.mult))
                    step(V.tensor_reduce(index, scratch, AX_X, ALU.min))
                    step(V.tensor_scalar(index, index, 64.0, None, ALU.add))
                    step(V.tensor_tensor(scratch, along(iota[:, 0:n], n), over(index, n), ALU.is_equal))

                first_greatest(gx[:, :, :], G, gs[:, 3, :], gs[:, 4, :], gm[:, :, :])
                step(V.tensor_tensor(el[:, :, :, :], lg[:, :, G:].rearrange("p n (g e) -> p n g e", g=G),
                                     gm[:, :, :].unsqueeze(3).to_broadcast([P, NT, G, EPG]), ALU.mult))
                step(V.tensor_tensor(e8[:, 0], el[:, :, 0, :], el[:, :, 1, :], ALU.add))
                step(V.tensor_tensor(e8[:, 0], e8[:, 0], el[:, :, 2, :], ALU.add))
                step(V.tensor_tensor(e8[:, 0], e8[:, 0], el[:, :, 3, :], ALU.add))
                first_greatest(e8[:, 0], EPG, es[:, 0, :], es[:, 1, :], e8[:, 1])
                step(V.scalar_tensor_tensor(e8[:, 0], e8[:, 1], -3.0e38, e8[:, 0], ALU.mult, ALU.add))
                first_greatest(e8[:, 0], EPG, es[:, 2, :], es[:, 3, :], e8[:, 1])
                V.tensor_tensor(es[:, 4, :], es[:, 2, :], es[:, 0, :], ALU.subtract).then_inc(s["e_sub"], 1)
                dve.wait_ge(s["e_exp"], 1)
                step(V.tensor_scalar(es[:, 5, :], es[:, 4, :], 1.0, None, ALU.add))
                step(V.reciprocal(es[:, 5, :], es[:, 5, :]))
                step(V.tensor_tensor(weight[:, 0:NT], es[:, 5, :], gs[:, 3, :], ALU.mult))
                step(V.tensor_tensor(weight[:, NT:], weight[:, 0:NT], es[:, 4, :], ALU.mult))
                for k in range(2):
                    step(V.scalar_tensor_tensor(es[:, 6 + k, :], gs[:, 4, :], float(EPG), es[:, 1 + 2 * k, :], ALU.mult, ALU.add))
                    step(V.tensor_tensor(A[:, k], along(iota, E2), over(es[:, 6 + k, :], E2), ALU.is_equal))
                step(V.tensor_tensor(A[:, 2], A[:, 0], A[:, 1], ALU.add))
                step(V.memset(B[:, 0, :], 0.0))
                for i in range(NT):
                    ins = V.tensor_tensor(B[:, i + 1, :], B[:, i, :], A[:, 2, i, :], ALU.add)
                    if i < NT - 1:
                        step(ins)
                    else:
                        ins.then_inc(s["sums"], 1)
                dve.wait_ge(s["r_mm"], 1)
                rank, count = bank[3][:, 0:NT * E2].rearrange("p (n e) -> p n e", e=E2), bank[4][:, 0:E2]
                step(V.tensor_scalar(cn[:, 5, 0:8], iota[:, 0:8], float(P), float(P), ALU.mult, ALU.add))
                step(V.tensor_tensor(ov[:, :, :], count.unsqueeze(2).to_broadcast([P, E2, 8]),
                                     cn[:, 5, 0:8].unsqueeze(1).to_broadcast([P, E2, 8]), ALU.is_gt))
                step(V.tensor_reduce(cn[:, 0, :], ov[:, :, :], AX_X, ALU.add))
                step(V.tensor_tensor_scan(cn[:, 1, :], ones[:, 0:E2], cn[:, 0, :], 0.0, ALU.mult, ALU.add))
                step(V.tensor_tensor(cn[:, 2, :], cn[:, 1, :], cn[:, 0, :], ALU.subtract))
                step(V.tensor_scalar(cn[:, 3, :], iota, float(P), None, ALU.mult))
                step(V.tensor_scalar(cn[:, 4, :], cn[:, 2, :], float(P), float((E2 - 1) * P), ALU.mult, ALU.add))
                step(V.tensor_tensor(cn[:, 4, :], cn[:, 4, :], cn[:, 3, :], ALU.subtract))
                step(V.tensor_scalar(F[:, :, :], rank, float(P), None, ALU.is_ge))
                step(V.tensor_tensor(F[:, :, :], F[:, :, :], along(cn[:, 4, :], E2), ALU.mult))
                step(V.tensor_tensor(F[:, :, :], F[:, :, :], along(cn[:, 3, :], E2), ALU.add))
                step(V.tensor_tensor(F[:, :, :], F[:, :, :], rank, ALU.add))
                for k in range(2):
                    step(V.tensor_tensor(G_[:, :, :], F[:, :, :], A[:, k], ALU.mult))
                    step(V.tensor_reduce(df[:, k, :], G_[:, :, :], AX_X, ALU.add))
                V.tensor_copy(dest[:, :], df[:, :, :].rearrange("p k n -> p (k n)")).then_inc(s["dest_ready"], 1)
                step(V.tensor_tensor(ob[:, :, :], cn[:, 1, :].unsqueeze(1).to_broadcast([P, NOVER, E2]),
                                     iota[:, 0:NOVER].unsqueeze(2).to_broadcast([P, NOVER, E2]), ALU.is_le))
                step(V.tensor_reduce(ef[:, 0:NOVER], ob[:, :, :], AX_X, ALU.add))
                step(V.tensor_scalar(ef[:, 0:NOVER], ef[:, 0:NOVER], float(E2 - 1), None, ALU.min))
                step(V.tensor_copy(ef[:, NOVER:NOVER + 1], cn[:, 1, E2 - 1:E2]))
                V.tensor_copy(eid[:, :], ef[:, :]).then_inc(s["counted"], 1)


def slot_tokens(nc, bank, cst, slot_tok, idx):
    NB = SLOTS // P
    with Stage(nc, "slots") as st:
        rows = st.sb("rows", [NB, P])
        loaded, tr, done = st.sem("loaded"), st.sem("tr"), st.sem("done")
        with nc.Block() as block:
            @block.sync
            def _(sp):
                sp.dma_start(rows[:, :], slot_tok.rearrange("(b p) o -> b (p o)", p=P)).then_inc(loaded, 16)

            @block.tensor
            def _(pe):
                pe.wait_ge(loaded, 16)
                nc.tensor.transpose(bank[0][:, 0:NB], rows[:, :], cst[0:NB, CONST["ident"]:CONST["ident"] + NB]).then_inc(tr, 1)

            @block.vector
            def _(dve):
                dve.wait_ge(tr, 1)
                nc.vector.tensor_copy(idx[:, 0:NB], bank[0][:, 0:NB]).then_inc(done, 1)
                nc.vector.tensor_copy(idx[:, NB:NB + 1], bank[0][:, 0:1]).then_inc(done, 1)


def experts2(nc, bank, name, cst, h, w_gate_up, w_down, ye, idx, first, blocks, gathered, before, eid=None):
    LB = 2
    with Stage(nc, name) as st:
        w = st.sb("w", [P, LB, 3, 8 * BANK])
        xs, xT = st.sb("xs", [P, LB, D]), st.sb("xT", [P, LB, KD, P])
        cur = st.sb("cur", [P, LB], U32)
        sg, hid = st.sb("sg", [P, LB, BANK]), st.sb("hid", [P, LB, BANK])
        hidT = st.sb("hidT", [P, LB, 4, P])
        y = st.sb("y", [P, LB, D])
        names = ("turns", "cur_ready", "x_in", "x_tr", "xT_ev", "gu_mm", "sg_ready", "hid_ready", "h_tr", "hT_ev", "y_mm", "y_ready")
        s = {n: st.sem(n) for n in names}
        w_in = [[st.sem(f"w_in{k}{i}") for i in range(3)] for k in range(LB)]
        stored = [st.sem(f"stored{k}") for k in range(LB)]
        ident = cst[:, CONST["ident"]:CONST["ident"] + P]
        TURNS = blocks // LB

        def load(sp, e, k, i):
            if i < 2:
                src = w_gate_up[ds(e, 1), :, i * BANK:(i + 1) * BANK].rearrange("o (k p) n -> p (o k) n", p=P)
                dst = w[:, k, i].rearrange("p (k n) -> p k n", k=8)
            else:
                src = w_down[ds(e, 1), :, :].rearrange("o (k p) n -> p (o k) n", p=P)
                dst = w[:, k, 2].rearrange("p (k n) -> p k n", k=4)
            sp.dma_start(dst, src).then_inc(w_in[k][i], 16)

        def expert(sp, b):
            return b if eid is None else sp.value_load(eid[0:1, ds(b, 1)], min_val=0, max_val=E2 - 1)

        def weights_and_stores(sp):
            for k in range(LB):
                sp.sem_inc(stored[k], 1)
                e = expert(sp, k)
                for i in range(3):
                    load(sp, e, k, i)

            def store(it, k):
                sp.wait_ge(s["y_ready"], it * (2 * LB) + (2 * k + 3))
                sp.sem_inc(s["turns"], 1)
                sp.dma_start(ye[ds(it * (LB * P) + (first + k) * P, P), :], y[:, k, :]).then_inc(stored[k], 16)

            with sp.Fori(0, TURNS - 1) as it:
                for k in range(LB):
                    for i in range(3):
                        if i < 2:
                            sp.wait_ge(s["gu_mm"], it * (2 * LB) + (2 * k + i + 1))
                        else:
                            sp.wait_ge(s["y_mm"], it * (2 * LB) + 2 * (k + 1))
                        sp.sem_inc(s["turns"], 1)
                        if i == 0:
                            e = expert(sp, it * LB + (LB + k))
                        load(sp, e, k, i)
                    store(it, k)
            for k in range(LB):
                store(TURNS - 1, k)
                sp.wait_ge(stored[k], 16 * TURNS + 1)

        def gathers(pool):
            def gather(k):
                pool.indirect_dma_start(out=xs[:, k, :], out_offset=None, in_=h[:, :],
                                        in_offset=bass.IndirectOffsetOnAxis(ap=cur[:, k:k + 1], axis=0)).then_inc(gathered, 16)

            for k in range(LB):
                nc.gpsimd.tensor_copy(cur[:, k:k + 1], idx[:, first + k:first + k + 1]).then_inc(s["cur_ready"], 1)
                pool.wait_ge(s["cur_ready"], k + 1)
                gather(k)
                pool.wait_ge(gathered, 16 * (before + k + 1))
                pool.sem_inc(s["x_in"], 1)
            with pool.Fori(0, TURNS - 1) as it:
                for k in range(LB):
                    pool.wait_ge(s["x_tr"], it * (2 * LB) + 2 * (k + 1))
                    pool.sem_inc(s["turns"], 1)
                    nc.gpsimd.tensor_copy(cur[:, k:k + 1], idx[:, ds(it * LB + (first + LB + k), 1)]).then_inc(s["cur_ready"], 1)
                    pool.wait_ge(s["cur_ready"], it * LB + (LB + k + 1))
                    pool.sem_inc(s["turns"], 1)
                    gather(k)
                    pool.wait_ge(gathered, it * (16 * LB) + 16 * (before + LB + k + 1))
                    pool.sem_inc(s["x_in"], 1)

        def products(pe):
            with pe.Fori(0, TURNS) as it:
                def tokens(k):
                    pe.wait_ge(s["x_in"], it * LB + (k + 1))
                    for j in range(KD):
                        ins = nc.tensor.transpose(bank[6 + j // 4][:, (j % 4) * P:(j % 4 + 1) * P], xs[:, k, j * P:(j + 1) * P], ident)
                        if j % 4 == 3:
                            ins.then_inc(s["x_tr"], 1)

                def gate_up(k):
                    pe.wait_ge(s["xT_ev"], it * (2 * LB) + 2 * (k + 1))
                    for i in range(2):
                        pe.wait_ge(w_in[k][i], it * 16 + 16)
                        wi = w[:, k, i].rearrange("p (k n) -> p k n", k=8)
                        for j in range(KD):
                            last = nc.tensor.matmul(bank[2 * k + i][:, :], xT[:, k, j, :], wi[:, j, :], start=(j == 0), stop=(j == KD - 1))
                        last.then_inc(s["gu_mm"], 1)

                def down(k):
                    pe.wait_ge(s["hid_ready"], it * LB + (k + 1))
                    for j in range(4):
                        ins = nc.tensor.transpose(bank[2 * k][:, j * P:(j + 1) * P], hid[:, k, j * P:(j + 1) * P], ident)
                    ins.then_inc(s["h_tr"], 1)
                    pe.wait_ge(s["hT_ev"], it * LB + (k + 1))
                    pe.wait_ge(w_in[k][2], it * 16 + 16)
                    wi = w[:, k, 2].rearrange("p (k n) -> p k n", k=4)
                    pe.wait_ge(s["y_ready"], it * (2 * LB) + (2 * k + 1))
                    for c in range(2):
                        for j in range(4):
                            last = nc.tensor.matmul(bank[4 + c][:, :], hidT[:, k, j, :], wi[:, j, c * BANK:(c + 1) * BANK],
                                                    start=(j == 0), stop=(j == 3))
                        last.then_inc(s["y_mm"], 1)

                tokens(0)
                gate_up(0)
                tokens(1)
                gate_up(1)
                down(0)
                down(1)

        def rows_T(act):
            with act.Fori(0, TURNS) as it:
                for k in range(LB):
                    for b in range(2):
                        act.wait_ge(s["x_tr"], it * (2 * LB) + (2 * k + b + 1))
                        nc.scalar.activation(xT[:, k, 4 * b:4 * b + 4, :].rearrange("p k t -> p (k t)"), bank[6 + b][:, :], ACT.Copy)\
                            .then_inc(s["xT_ev"], 1)
                    act.wait_ge(s["gu_mm"], it * (2 * LB) + (2 * k + 1))
                    nc.scalar.activation(sg[:, k, :], bank[2 * k][:, :], ACT.Silu).then_inc(s["sg_ready"], 1)

        def hidden(dve):
            dve.sem_inc(s["y_ready"], 1)
            with dve.Fori(0, TURNS) as it:
                def gated(k):
                    dve.wait_ge(s["sg_ready"], it * LB + (k + 1))
                    dve.wait_ge(s["gu_mm"], it * (2 * LB) + 2 * (k + 1))
                    nc.vector.tensor_tensor(hid[:, k, :], sg[:, k, :], bank[2 * k + 1][:, :], ALU.mult).then_inc(s["hid_ready"], 1)

                def turned(k):
                    dve.wait_ge(s["h_tr"], it * LB + (k + 1))
                    nc.vector.tensor_copy(hidT[:, k, :, :].rearrange("p k t -> p (k t)"), bank[2 * k][:, :]).then_inc(s["hT_ev"], 1)

                def out(k):
                    dve.wait_ge(stored[k], it * 16 + 1)
                    for c in range(2):
                        dve.wait_ge(s["y_mm"], it * (2 * LB) + (2 * k + c + 1))
                        nc.vector.tensor_copy(y[:, k, c * BANK:(c + 1) * BANK], bank[4 + c][:, :]).then_inc(s["y_ready"], 1)

                gated(0)
                gated(1)
                for k in range(LB):
                    turned(k)
                    out(k)

        def when_used(engine, body):
            if eid is None:
                body(engine)
                return
            with engine.If(engine.value_load(eid[0:1, NOVER:NOVER + 1], min_val=0, max_val=NOVER) > 0):
                body(engine)

        with nc.Block() as block:
            @block.sync
            def _(sp):
                when_used(sp, weights_and_stores)

            @block.gpsimd
            def _(pool):
                when_used(pool, gathers)

            @block.tensor
            def _(pe):
                when_used(pe, products)

            @block.scalar
            def _(act):
                when_used(act, rows_T)

            @block.vector
            def _(dve):
                when_used(dve, hidden)


def combine2(nc, x, ye, dest, weight, out, gathered, out_stored):
    R = 4
    with Stage(nc, "comb2") as st:
        xt, g = st.sb("x", [P, R, D]), st.sb("g", [P, R, 2, D])
        x_in = [st.sem(f"x_in{i}") for i in range(R)]
        got, first, done = st.sem("got"), st.sem("first"), st.sem("done")
        with nc.Block() as block:
            @block.gpsimd
            def _(pool):
                for i in range(NT):
                    if i >= R:
                        pool.wait_ge(done, i - R + 1)
                    for k in range(2):
                        pool.indirect_dma_start(out=g[:, i % R, k, :], out_offset=None, in_=ye[:, :],
                                                in_offset=bass.IndirectOffsetOnAxis(ap=dest[:, k * NT + i:k * NT + i + 1], axis=0))\
                            .then_inc(gathered[i % R], 16)

            @block.sync
            def _(sp):
                for i in range(NT + 2):
                    if i < NT:
                        if i >= R:
                            sp.wait_ge(out_stored[i % R], 16 * (i // R))
                        sp.dma_start(xt[:, i % R, :], x[i * P:(i + 1) * P, :]).then_inc(x_in[i % R], 16)
                    if i >= 2:
                        sp.wait_ge(done, i - 1)
                        sp.dma_start(out[0, (i - 2) * P:(i - 1) * P, :], xt[:, (i - 2) % R, :])\
                            .then_inc(out_stored[(i - 2) % R], 16)
                for r in range(R):
                    sp.wait_ge(out_stored[r], 16 * (NT // R))

            @block.vector
            def _(dve):
                for i in range(NT):
                    r = i % R
                    dve.wait_ge(gathered[r], 32 * (i // R + 1))
                    dve.wait_ge(x_in[r], 16 * (i // R + 1))
                    nc.vector.scalar_tensor_tensor(xt[:, r, :], g[:, r, 0, :], weight[:, i:i + 1], xt[:, r, :], ALU.mult, ALU.add)\
                        .then_inc(first, 1)
                    dve.wait_ge(first, i + 1)
                    nc.vector.scalar_tensor_tensor(xt[:, r, :], g[:, r, 1, :], weight[:, NT + i:NT + i + 1], xt[:, r, :], ALU.mult,
                                                   ALU.add).then_inc(done, 1)


def program(nc, x, tabs, out, stop=None):
    cst = nc.alloc_sbuf_tensor("cst", [P, CW], F32)
    col = nc.alloc_sbuf_tensor("col", [P, VW], F32)
    bank = [nc.alloc_psum_tensor(f"bank{i}", [P, BANK], F32) for i in range(8)]
    tables_in = nc.alloc_semaphore("tables_in")

    def scratch(name, *shape, dt=F32):
        return nc.dram_tensor(name, shape, dt, kind="Internal").ap()

    mod = scratch("mod", 8, D)
    with nc.Block() as block:
        @block.sync
        def _(sp):
            sp.dma_start(cst[:, :], tabs["cst"]).then_inc(tables_in, 16)
            sp.dma_start(col[:, :], tabs["cols"]).then_inc(tables_in, 16)
            sp.wait_ge(tables_in, 32)

    modulation(nc, bank, x["w_mod"], x["b_mod"], x["c"], x["c_ctx"], x["norm_gains"], mod)
    if stop == "mod":
        return

    uT = scratch("uT", D_IN, TT)
    hold = ExitStack()
    with hold:
        hT = hold.enter_context(nc.sbuf_tensor("hT", [P, KD, TT], F32))
        norm_T(nc, bank, "norm_c", cst, x["ctx"][0], TC, hT, 0, gvec=mod[MOD_CG1:MOD_CG1 + 1, :], svec=mod[MOD_CS1:MOD_CS1 + 1, :])
        norm_T(nc, bank, "norm_x", cst, x["x"][0], T, hT, TC, gvec=mod[MOD_G1:MOD_G1 + 1, :], svec=mod[MOD_S1:MOD_S1 + 1, :])
        gemm_T(nc, bank, "proj1", hT, TT, x["w_in"][0], 0, 8, [P, P, P, 64], uT)
    if stop == "proj1":
        return
    latT = scratch("latT", D, T)
    retention(nc, bank, cst, tabs, uT, latT)
    if stop == "ret":
        return
    rwkv(nc, bank, cst, col, tabs, x, uT, scratch, latT)
    if stop == "rwkv":
        return
    x1, h2, acc, x2 = scratch("x1", T, D), scratch("h2", T, D), scratch("acc", T, D), scratch("x2", T, D)
    with nc.sbuf_tensor("lT", [P, KD, T], F32) as lT:
        load_T(nc, "load_lat", latT, lT)
        gemm_rows(nc, bank, "mix", lT, D, x["w_out"][0], x["x"][0], x1, grow=mod[MOD_GT1:MOD_GT1 + 1, :],
                  exchanged=range(KD // 2, KD))
    tokens_in, rows_added = nc.alloc_semaphore("tokens_in"), nc.alloc_semaphore("rows_added")
    experts = ExitStack()
    with experts:
        idx = experts.enter_context(nc.sbuf_tensor("idx", [P, E1 + 1], U32))
        gates = experts.enter_context(nc.sbuf_tensor("gates", [P, E1], F32))
        with nc.sbuf_tensor("h2T", [P, KD, T], F32) as h2T:
            norm_T(nc, bank, "norm_f", cst, x1, T, h2T, 0, grow=mod[MOD_G2:MOD_G2 + 1, :], srow=mod[MOD_S2:MOD_S2 + 1, :],
                   rows_out=h2)
            route1(nc, bank, cst, h2T, x["w_router"][0], acc, idx, gates)
        experts1(nc, bank, cst, h2, x["w_gate"][0], x["w_up"][0], x["w_down"][0], acc, idx, gates, tokens_in, rows_added)
    add_normed(nc, "add1", x1, acc, mod[MOD_GT2:MOD_GT2 + 1, :], x2)
    if stop == "one":
        return
    second(nc, bank, cst, col, tabs, x, scratch, x2, out, stop)


def second(nc, bank, cst, col, tabs, x, scratch, x2, out, stop=None):
    uT2 = scratch("uT2", PROJ2, T)
    norm_mix = col[:, COLS["norm_mix"]:COLS["norm_mix"] + KD]
    with nc.sbuf_tensor("hT2", [P, KD, T], F32) as hT:
        norm_T(nc, bank, "norm_2", cst, x2, T, hT, 0, gcol=norm_mix)
        gemm_T(nc, bank, "proj2", hT, T, x["w_in_2"][0], 0, PROJ2 // BANK, [], uT2)
    if stop == "proj2":
        return
    gT = scratch("gT", D, T)
    lru(nc, bank, col, x["lru_wa_2"][0], x["lru_wx_2"][0], uT2, gT)
    if stop == "lru":
        return
    qkT, v_rows, oT = scratch("qkT", 2, D, T), scratch("v_rows", T, D), scratch("oT", D, T)
    qkv_heads(nc, bank, cst, col, x["positions_2"], uT2, qkT, v_rows)
    if stop == "heads":
        return
    diff_attention(nc, bank, cst, col, x, qkT, v_rows, oT)
    if stop == "attn":
        return
    x3 = scratch("x3", T, D)
    with nc.sbuf_tensor("mT", [P, KD, T], F32) as mT:
        mixed_T(nc, bank, x["w_lru_o_2"][0], x["w_attn_o_2"][0], gT, oT, uT2[5 * D:7 * D, :], mT)
        gemm_rows(nc, bank, "out2", mT, D, x["w_out_2"][0], x2, x3)
    if stop == "x3":
        return
    x4 = scratch("x4", T, D)
    with nc.sbuf_tensor("cT", [P, MH, T], F32) as cT:
        with nc.sbuf_tensor("xT", [P, KD, T], F32) as xT, nc.sbuf_tensor("memT", [P, KD, MEM], F32) as memT:
            norm_T(nc, bank, "norm_cx", cst, x3, T, xT, 0, gcol=col[:, COLS["norm_cx"]:COLS["norm_cx"] + KD])
            norm_T(nc, bank, "norm_mem", cst, x["mem_2"][0], MEM, memT, 0, gcol=col[:, COLS["norm_mem"]:COLS["norm_mem"] + KD])
            cross_attention(nc, bank, cst, col, x["w_cq_2"][0], x["w_ckv_2"][0], xT, memT, cT)
        gemm_rows(nc, bank, "co", cT, MH * P, x["w_co_2"][0], x3, x4)
    if stop == "x4":
        return
    NB = SLOTS // P
    h4, ye, slot_tok = scratch("h4", T, D), scratch("ye", SLOTS, D), scratch("slot_tok", SLOTS, 1)
    placed, blocks_in = nc.alloc_semaphore("placed"), nc.alloc_semaphore("blocks_in")
    rows_in, out_stored = ([nc.alloc_semaphore(f"{n}{i}") for i in range(4)] for n in ("rows_in", "out_stored"))
    with nc.sbuf_tensor("dest", [P, 2 * NT], U32) as dest, nc.sbuf_tensor("weight", [P, 2 * NT], F32) as weight,\
            nc.sbuf_tensor("eid", [P, NOVER + 1], I32) as eid, nc.sbuf_tensor("slot", [P, NB + 1], U32) as idx:
        with nc.sbuf_tensor("h4T", [P, KD, T], F32) as h4T:
            norm_T(nc, bank, "norm_4", cst, x4, T, h4T, 0, grow=x["norm_ffn_2"], rows_out=h4)
            tok = cst[:, CONST["tok"]:CONST["tok"] + NT]
            route2(nc, bank, cst, tok, h4T, x["w_group_2"][0], x["b_group_2"], x["w_router_2"][0], x["b_router_2"],
                   slot_tok, ye[E2 * P:, :], dest, weight, eid, placed)
        slot_tokens(nc, bank, cst, slot_tok, idx)
        if stop == "route2":
            return
        experts2(nc, bank, "moe2", cst, h4, x["w_gate_up_2"][0], x["w_down_2"][0], ye, idx, 0, E2, blocks_in, 0)
        experts2(nc, bank, "moe2o", cst, h4, x["w_gate_up_2"][0], x["w_down_2"][0], ye, idx, E2, NOVER, blocks_in, E2, eid)
        combine2(nc, x4, ye, dest, weight, out, rows_in, out_stored)


def constants():
    c = np.zeros((P, CW), np.float32)
    msk = np.zeros((2, len(LEVELS) + 1, P, 2 * P), np.int32)

    def put(name, a):
        c[:a.shape[0], CONST[name]:CONST[name] + a.shape[1]] = a

    i = np.arange(P)
    put("ident", np.eye(P))
    put("ident2", np.concatenate([np.eye(P)] * 2, 1))
    put("pair", (i[:, None] // 64 == i[None] // 64) * 1.0)
    put("pairx", (i[:, None] // 64 != i[None] // 64) * 1.0)
    put("ones", np.ones((P, P)))
    put("lower", (i[:, None] < i[None]) * 1.0)
    put("hm", np.concatenate([np.tile((i // 64 == h) * 1.0, (P, 1)) for h in range(2)], 1))
    put("cmask", np.concatenate([np.tile((i[:, None] // CH == h) * 1.0, (1, CH)) for h in range(2)], 1))
    put("idc", (i[:, None] % CH == np.arange(CH)[None]) * 1.0)
    ax, r2 = np.zeros((P, P)), np.zeros((P, P))
    for m in range(P):
        d = m % 64
        ax[m + 32 if d < 32 else m - 32, m] = -1.0 if d < 32 else 1.0
        if d < 16:
            r2[m + 8 if d < 8 else m - 8, m] = -1.0 if d < 8 else 1.0
    put("axrot", ax)
    put("rot2", r2)
    same = i[:, None] // CH == i[None] // CH
    s, t = i[:, None], i[None]
    for name, strict, incl in (("st_f", s < t, s <= t), ("st_b", s > t, s >= t)):
        put(name, np.concatenate([same & strict, same & incl], 1) * 1.0)
    for d in range(2):
        for l, n in enumerate((1,) + LEVELS):
            block = s // (2 * n) == t // (2 * n)
            low = block & ((s // n) % 2 == 1) & ((t // n) % 2 == 0)
            msk[d, l] = np.concatenate([low, low.T] if d == 0 else [low.T, low], 1)
    d = i % 64
    inv = np.exp(-math.log(500000.0) * np.arange(8, dtype=np.float32) / 8).astype(np.float32)
    put("invf", np.where(d < 16, inv[d % 8], 0.0)[:, None])
    put("e32", np.tile(np.arange(32), (P, 1)))
    put("tok", i[:, None] + P * np.arange(NT)[None])
    gam = np.log1p(-np.exp2(-5.0 - np.arange(RET_HEADS, dtype=np.float32))).astype(np.float32)
    idx = np.arange(P, dtype=np.float32)
    rel = idx[None] - idx[:, None]
    din = np.zeros((2, RET_HEADS, P, P), np.float32)
    for h in range(RET_HEADS):
        e = np.exp(np.abs(rel) * gam[h])
        din[0, h], din[1, h] = np.where(rel >= 0, e, 0), np.where(rel <= 0, e, 0)
    qd = np.zeros((2, PAIRS, P, P), np.float32)
    kd = np.zeros((2, PAIRS, P, P), np.float32)
    cd = np.zeros((PAIRS, P, 1), np.float32)
    for p in range(PAIRS):
        for hh in range(2):
            r, g = slice(64 * hh, 64 * hh + 64), gam[2 * p + hh]
            qd[0, p, r], qd[1, p, r] = np.exp((idx + 1) * g), np.exp((P - idx) * g)
            kd[0, p, :, r], kd[1, p, :, r] = (np.exp(e * g)[:, None] for e in (P - 1 - idx, idx))
            cd[p, r] = np.exp(P * g)
    row, col = np.repeat(np.arange(T // GRID_W), GRID_W), np.tile(np.arange(GRID_W), T // GRID_W)
    freq = (10000.0 ** (-np.arange(16, dtype=np.float32) / 16)).astype(np.float32)
    ang = np.concatenate([row[:, None].astype(np.float32) * freq, col[:, None].astype(np.float32) * freq], 1)
    ang = ang.T[np.arange(P) % 32]
    scale = RET_DIM ** -0.5
    return dict(cst=c, msk=msk, din=(din * scale).astype(np.float32), qd=qd, kd=(kd * scale).astype(np.float32), cdec=cd,
                ax=np.stack([np.cos(ang), np.sin(ang)]).astype(np.float32))


def columns(x):
    v = np.zeros((P, VW), np.float32)

    def put(name, a, at=0):
        a = np.asarray(a, np.float32).reshape(-1, P).T
        v[:, COLS[name] + at:COLS[name] + at + a.shape[1]] = a

    def xch(a):
        return np.asarray(a).reshape(PAIRS, 2, 64)[:, ::-1].reshape(-1)

    conv = np.asarray(x["rwkv_conv"])[0]
    for tap in range(3):
        full = np.zeros(16 * P, np.float32)
        full[:conv.shape[1]] = conv[tap]
        full[2 * RW:3 * RW] = xch(full[2 * RW:3 * RW])
        lora = conv[tap][3 * RW:]
        full[3 * RW:3 * RW + 128] = lora[0:128]
        full[3 * RW + 128:3 * RW + 256] = 0
        full[3 * RW + 128:3 * RW + 192] = lora[128:192]
        full[3 * RW + 256:3 * RW + 512] = lora[192:448]
        put("conv", full, 16 * tap)
    put("a0", x["rwkv_a0"])
    put("w0", x["rwkv_w0"])
    for n, k in (("k_k", "rwkv_k_k"), ("k_a", "rwkv_k_a"), ("r_k", "rwkv_r_k")):
        put(n, x[k])
    put("lnw", xch(x["rwkv_lnx_w"]))
    put("lnb", xch(x["rwkv_lnx_b"]))
    for n, k in (("norm_mix", "norm_mix_2"), ("conv2", "conv_w_2"), ("conv2b", "conv_b_2"), ("ba", "lru_ba_2"),
                 ("bx", "lru_bx_2"), ("lam", "lru_lambda_2"), ("subln", "subln_2"), ("norm_cx", "norm_cx_2"),
                 ("norm_mem", "norm_mem_2"), ("cqn", "cq_norm_2"), ("ckn", "ck_norm_2")):
        put(n, x[k])
    put("qn", np.concatenate([np.asarray(x["q_norm_2"])] * 2, -1))
    put("kn", np.concatenate([np.asarray(x["k_norm_2"])] * 2, -1))
    pc = np.zeros((PAIRS, P, PW), np.float32)
    for p in range(PAIRS):
        for tap in range(3):
            for n, name in enumerate(("conv_r", "conv_k", "conv_v")):
                pc[p, :, PCOL[name] + tap] = v[:, COLS["conv"] + 16 * tap + 4 * n + p]
        for name in ("a0", "k_k", "k_a", "r_k", "lnw", "lnb"):
            pc[p, :, PCOL[name]] = v[:, COLS[name] + p]
        for d in range(2):
            pc[p, :, PCOL["w0"] + d] = v[:, COLS["w0"] + 4 * d + p]
    return dict(cols=v, pcols=pc)


WHOLE = ("x", "c", "ctx", "c_ctx", "w_mod", "b_mod", "norm_gains", "w_in", "rwkv_w2", "rwkv_a2", "rwkv_g2",
         "w_out", "w_router", "w_gate", "w_up", "w_down", "mem_2", "positions_2", "w_in_2",
         "lru_wa_2", "lru_wx_2", "w_lru_o_2", "lambda_q1_2", "lambda_k1_2", "lambda_q2_2", "lambda_k2_2",
         "w_attn_o_2", "w_out_2", "w_cq_2", "w_ckv_2", "w_co_2", "norm_ffn_2", "w_group_2", "b_group_2",
         "w_router_2", "b_router_2", "w_gate_up_2", "w_down_2")


def kernel(**inputs):
    import concourse.bacc as bacc
    from concourse.bass_utils import run_bass_kernel_spmd

    nc = bacc.Bacc("TRN2", target_bir_lowering=False, num_devices=1)
    arrays, x, tabs = {}, {}, {}

    def take(name, a, into):
        a = np.ascontiguousarray(a)
        arrays[f"in_{name}"] = a
        into[name] = nc.dram_tensor(f"in_{name}", a.shape, mybir.dt.from_np(a.dtype), kind="ExternalInput").ap()

    for name in WHOLE:
        take(name, inputs[name], x)
    for name, a in {**constants(), **columns(inputs)}.items():
        take(name, a, tabs)
    out = nc.dram_tensor("out", (1, T, D), F32, kind="ExternalOutput").ap()
    program(nc, x, tabs, out)
    r = run_bass_kernel_spmd(nc, [arrays], core_ids=[0])
    return r.results[0]["out"]
```

```python
import math
from contextlib import ExitStack

import numpy as np

import concourse.bass as bass
from concourse import mybir

F32 = mybir.dt.float32
F32R = mybir.dt.float32r
I32 = mybir.dt.int32
U32 = mybir.dt.uint32
ALU = mybir.AluOpType
ACT = mybir.ActivationFunctionType
AX_X = mybir.AxisListType.X
ds = bass.ds

P = 128
BANK = 512
D = 1024
KD = D // P
T = 1024
TC = 256
TT = T + TC
NT, NTC = T // P, TC // P
EPS = 1e-6
HI_MASK = -4096

RET_HEADS, RET_DIM, GRID_W = 8, 64, 64
RW = 512
PAIRS = RW // P
GN_EPS = 64e-5
D_IN = 5 * RW + 3 * RW + 64 * 3 + 128 * 2
CH = 64
LEVELS = (2, 4, 8, 16, 32)
E1, CAP = 16, 128

HEADS2, HD2 = 8, 64
CHUNK2 = 64
MEM, MH = 256, 4
PROJ2 = 7 * D
GROUPS, EPG = 4, 8
E2 = GROUPS * EPG
FF2 = 512


def fill(n, parts):
    at, out = n, {}
    for name, width in parts:
        out[name] = at
        at += width
    return out, at


CONST, CW = fill(0, [("ident", 128), ("pair", 128), ("pairx", 128), ("ones", 128), ("lower", 128),
                     ("axrot", 128), ("st_f", 256), ("st_b", 256),
                     ("ident2", 256), ("hm", 256), ("cmask", 128), ("idc", 64),
                     ("invf", 8), ("e32", 32), ("tok", 8)])
COLS, VW = fill(0, [("conv", 3 * 16), ("a0", 4), ("w0", 8), ("k_k", 4), ("k_a", 4), ("r_k", 4),
                    ("lnw", 4), ("lnb", 4),
                    ("norm_mix", 8), ("conv2", 32), ("conv2b", 8), ("ba", 8), ("bx", 8), ("lam", 8),
                    ("subln", 1), ("norm_cx", 8), ("norm_mem", 8),
                    ("cqn", 1), ("ckn", 1)])
MOD_G1, MOD_S1, MOD_CG1, MOD_CS1, MOD_GT1, MOD_G2, MOD_S2, MOD_GT2 = range(8)


class Stage:

    def __init__(self, nc, name):
        self.nc, self.name, self.ctx, self.sems = nc, name, ExitStack(), []

    def __enter__(self):
        return self

    def sb(self, name, shape, dt=F32):
        return self.ctx.enter_context(self.nc.sbuf_tensor(f"{self.name}_{name}", shape, dt))

    def sem(self, name):
        s = self.ctx.enter_context(self.nc.semaphore(f"{self.name}_{name}"))
        self.sems.append(s)
        return s

    def __exit__(self, *exc):
        if exc[0] is None:
            with self.nc.Block() as block:
                @block.gpsimd
                def _(pool):
                    for s in self.sems:
                        pool.sem_clear(s)
        self.ctx.close()
        return False


class Steps:

    def __init__(self, sem, base=0):
        self.sem, self.n = sem, base

    def __call__(self, instruction):
        instruction.then_inc(self.sem, 1)
        self.n = self.n + 1
        return self.n


def modulation(nc, bank, w_mod, b_mod, c, c_ctx, gains, mod):
    N = 6 * D
    NG = N // BANK
    with Stage(nc, "mod") as st:
        cc = st.sb("cc", [P, KD, 2])
        sc = st.sb("sc", [P, KD, 2])
        w = st.sb("w", [P, 2, KD, BANK])
        bias = st.sb("bias", [2, N])
        m = st.sb("m", [2, N])
        g = st.sb("g", [2, 4 * D])
        o = st.sb("o", [2, 4, D])
        c_in, g_in, w_in = st.sem("c_in"), st.sem("g_in"), [st.sem("w_in0"), st.sem("w_in1")]
        silu, mm, added, vec, out = st.sem("silu"), st.sem("mm"), st.sem("added"), st.sem("vec"), st.sem("out")
        with nc.Block() as block:
            @block.sync
            def _(sp):
                with nc.allow_non_contiguous_dma("vectors as columns"):
                    sp.dma_start(cc[:, :, 0], c.rearrange("o (k p) -> p (o k)", p=P)).then_inc(c_in, 16)
                    sp.dma_start(cc[:, :, 1], c_ctx.rearrange("(k p) -> p k", p=P)).then_inc(c_in, 16)
                for r in range(2):
                    sp.dma_start(bias[r:r + 1, :], b_mod[0:1, :]).then_inc(g_in, 16)
                    sp.dma_start(g[r:r + 1, :], gains.rearrange("o a d -> o (a d)")).then_inc(g_in, 16)
                for n in range(NG):
                    if n >= 2:
                        sp.wait_ge(mm, n - 1)
                    sp.dma_start(w[:, n % 2], w_mod[0, :, n * BANK:(n + 1) * BANK]
                                 .rearrange("(k p) n -> p k n", p=P)).then_inc(w_in[n % 2], 16)
                sp.wait_ge(vec, 4)
                rows = [(MOD_G1, o[0:1, 0]), (MOD_CG1, o[1:2, 0]), (MOD_S1, m[0:1, 0:D]), (MOD_CS1, m[1:2, 0:D]),
                        (MOD_GT1, o[0:1, 1]), (MOD_G2, o[0:1, 2]), (MOD_S2, m[0:1, 3 * D:4 * D]),
                        (MOD_GT2, o[0:1, 3])]
                for r, src in rows:
                    sp.dma_start(mod[r:r + 1, :], src).then_inc(out, 16)
                sp.wait_ge(out, 16 * len(rows))

            @block.scalar
            def _(act):
                act.wait_ge(c_in, 32)
                nc.scalar.activation(sc[:, :, :], cc[:, :, :], ACT.Silu).then_inc(silu, 1)

            @block.tensor
            def _(pe):
                pe.wait_ge(silu, 1)
                for n in range(NG):
                    pe.wait_ge(w_in[n % 2], 16 * (n // 2 + 1))
                    if n >= 2:
                        pe.wait_ge(added, n - 1)
                    for k in range(KD):
                        last = nc.tensor.matmul(bank[n % 2][0:2, :], sc[:, k, :], w[:, n % 2, k, :],
                                                start=(k == 0), stop=(k == KD - 1))
                    last.then_inc(mm, 1)

            @block.vector
            def _(dve):
                dve.wait_ge(g_in, 64)
                for n in range(NG):
                    dve.wait_ge(mm, n + 1)
                    c0 = n * BANK
                    nc.vector.tensor_tensor(m[:, c0:c0 + BANK], bank[n % 2][0:2, :], bias[:, c0:c0 + BANK],
                                            ALU.add).then_inc(added, 1)
                dve.wait_ge(added, NG)
                sh1, sc1, gt1, sh2, sc2, gt2 = (m[:, j * D:(j + 1) * D] for j in range(6))
                gain = [g[:, j * D:(j + 1) * D] for j in range(4)]
                nc.vector.scalar_tensor_tensor(o[:, 0], sc1, 1.0, gain[0], ALU.add, ALU.mult).then_inc(vec, 1)
                nc.vector.tensor_tensor(o[:, 1], gt1, gain[1], ALU.mult).then_inc(vec, 1)
                nc.vector.scalar_tensor_tensor(o[:, 2], sc2, 1.0, gain[2], ALU.add, ALU.mult).then_inc(vec, 1)
                nc.vector.tensor_tensor(o[:, 3], gt2, gain[3], ALU.mult).then_inc(vec, 1)


def norm_T(nc, bank, name, cst, x, ntok, actT, at, gcol=None, scol=None, gvec=None, svec=None,
           grow=None, srow=None, rows_out=None):
    n = ntok // P
    by_rows = grow is not None
    per = 2 if by_rows and srow is not None else 1
    with Stage(nc, name) as st:
        xt = st.sb("x", [P, n, D])
        sq = st.sb("sq", [P, D])
        ss = st.sb("ss", [P, n, 3])
        gs = st.sb("gs", [P, 2, KD])
        gb = st.sb("gb", [P, 2, D]) if by_rows else None
        x_in = [st.sem(f"x_in{i}") for i in range(4)]
        g_in, ssq, ms, root, rstd, scaled, stored = (st.sem(s) for s in
                                                     ("g_in", "ssq", "ms", "root", "rstd", "scaled", "stored"))
        tr, ev = st.sem("transposed"), [st.sem("ev_act"), st.sem("ev_dve")]
        ident = cst[:, CONST["ident"]:CONST["ident"] + P]
        if gcol is None:
            gcol, scol = gs[:, 0, :], gs[:, 1, :]
        has_s = scol is not None
        with nc.Block() as block:
            @block.sync
            def _(sp):
                if gvec is not None:
                    with nc.allow_non_contiguous_dma("vectors as columns"):
                        sp.dma_start(gs[:, 0, :], gvec.rearrange("o (k p) -> p (o k)", p=P)).then_inc(g_in, 16)
                        sp.dma_start(gs[:, 1, :], svec.rearrange("o (k p) -> p (o k)", p=P)).then_inc(g_in, 16)
                if by_rows:
                    sp.dma_start(gb[:, 0, :], grow.partition_broadcast(P).rearrange("p o d -> p (o d)"))\
                        .then_inc(g_in, 16)
                    if srow is not None:
                        sp.dma_start(gb[:, 1, :], srow.partition_broadcast(P).rearrange("p o d -> p (o d)"))\
                            .then_inc(g_in, 16)
                for i in range(n):
                    if i >= 4:
                        sp.wait_ge(ssq, i - 3)
                    sp.dma_start(xt[:, i, :], x[i * P:(i + 1) * P, :]).then_inc(x_in[i % 4], 16)
                if rows_out is not None:
                    for i in range(n):
                        sp.wait_ge(scaled, per * (i + 1))
                        sp.dma_start(rows_out[i * P:(i + 1) * P, :], xt[:, i, :]).then_inc(stored, 16)
                    sp.wait_ge(stored, 16 * n)

            def evac_act(act, i):
                act.wait_ge(tr, 2 * i + 1)
                if i == 0 and gvec is not None:
                    act.wait_ge(g_in, 32)
                for k in range(4):
                    dst, src = actT[:, k, at + i * P:at + (i + 1) * P], bank[2 * (i % 2)][:, k * P:(k + 1) * P]
                    if by_rows:
                        ins = nc.scalar.activation(dst, src, ACT.Copy)
                    elif has_s:
                        ins = nc.scalar.activation(dst, src, ACT.Identity, scale=gcol[:, k:k + 1], bias=scol[:, k:k + 1])
                    else:
                        ins = nc.scalar.activation(dst, src, ACT.Copy, scale=gcol[:, k:k + 1])
                    ins.then_inc(ev[0], 1)

            def evac_dve(dve, i):
                dve.wait_ge(tr, 2 * i + 2)
                if i == 0 and gvec is not None:
                    dve.wait_ge(g_in, 32)
                for k in range(4, 8):
                    dst = actT[:, k, at + i * P:at + (i + 1) * P]
                    src = bank[2 * (i % 2) + 1][:, (k - 4) * P:(k - 3) * P]
                    if by_rows:
                        ins = nc.vector.tensor_copy(dst, src)
                    elif has_s:
                        ins = nc.vector.tensor_scalar(dst, src, gcol[:, k:k + 1], scol[:, k:k + 1], ALU.mult, ALU.add)
                    else:
                        ins = nc.vector.tensor_scalar(dst, src, gcol[:, k:k + 1], None, ALU.mult)
                    ins.then_inc(ev[1], 1)

            @block.scalar
            def _(act):
                for i in range(n):
                    act.wait_ge(x_in[i % 4], 16 * (i // 4 + 1))
                    if i:
                        act.wait_ge(ssq, i)
                    nc.scalar.activation(sq[:, :], xt[:, i, :], ACT.Square, accum_out=ss[:, i, 0:1]).then_inc(ssq, 1)
                    act.wait_ge(ms, i + 1)
                    nc.scalar.activation(ss[:, i, 2:3], ss[:, i, 1:2], ACT.Sqrt).then_inc(root, 1)
                    if i:
                        evac_act(act, i - 1)
                evac_act(act, n - 1)

            @block.vector
            def _(dve):
                for i in range(n):
                    dve.wait_ge(ssq, i + 1)
                    nc.vector.tensor_scalar(ss[:, i, 1:2], ss[:, i, 0:1], 1.0 / D, EPS, ALU.mult, ALU.add)\
                        .then_inc(ms, 1)
                    dve.wait_ge(root, i + 1)
                    nc.vector.reciprocal(ss[:, i, 0:1], ss[:, i, 2:3]).then_inc(rstd, 1)
                    dve.wait_ge(rstd, i + 1)
                    if by_rows:
                        if i == 0:
                            dve.wait_ge(g_in, 32 if srow is not None else 16)
                        nc.vector.scalar_tensor_tensor(xt[:, i, :], xt[:, i, :], ss[:, i, 0:1], gb[:, 0, :],
                                                       ALU.mult, ALU.mult).then_inc(scaled, 1)
                        if srow is not None:
                            dve.wait_ge(scaled, 2 * i + 1)
                            nc.vector.tensor_tensor(xt[:, i, :], xt[:, i, :], gb[:, 1, :], ALU.add).then_inc(scaled, 1)
                    else:
                        nc.vector.tensor_scalar(xt[:, i, :], xt[:, i, :], ss[:, i, 0:1], None, ALU.mult)\
                            .then_inc(scaled, 1)
                    if i:
                        evac_dve(dve, i - 1)
                evac_dve(dve, n - 1)

            @block.tensor
            def _(pe):
                for i in range(n):
                    pe.wait_ge(scaled, per * (i + 1))
                    if i >= 2:
                        pe.wait_ge(ev[0], 4 * (i - 1))
                        pe.wait_ge(ev[1], 4 * (i - 1))
                    for k in range(KD):
                        ins = nc.tensor.transpose(bank[2 * (i % 2) + k // 4][:, (k % 4) * P:(k % 4 + 1) * P],
                                                  xt[:, i, k * P:(k + 1) * P], ident)
                        if k % 4 == 3:
                            ins.then_inc(tr, 1)


def gemm_T(nc, bank, name, actT, tok, w, col0, widths, dst):
    full, last = widths
    chunks = [(a, min(BANK, tok - a)) for a in range(0, tok, BANK)]
    nch = len(chunks)
    GW = 2 * P
    size = [(P, P)] * full + list(last)
    G = len(size)
    with Stage(nc, name) as st:
        raw, top = st.sb("raw", [P, KD, GW]), st.sb("top", [P, KD, GW])
        wt = st.sb("w", [P, 2, 2, KD, GW], F32R)
        hi, lo = st.sb("hi", [P, KD, tok], F32R), st.sb("lo", [P, KD, tok], F32R)
        ob = st.sb("out", [P, 2, tok])
        w_in, topped, hi_ready, lo_ready, turns = (st.sem(n) for n in ("w_in", "topped", "hi_ready", "lo_ready", "turns"))
        x_top, x_hi, x_lo = st.sem("x_top"), st.sem("x_hi"), st.sem("x_lo")
        mm = [st.sem("mm_act"), st.sem("mm_dve")]
        ev = [st.sem("ev_act"), st.sem("ev_dve")]
        stored = [st.sem("stored0"), st.sem("stored1")]
        TURNS = full // 2 - 1

        with nc.Block() as block:
            @block.sync
            def _(sp):
                def load(g, width=GW):
                    sp.dma_start(raw[:, :, 0:width], w[:, ds(g * GW + col0, width)].rearrange("(k p) n -> p k n", p=P))\
                        .then_inc(w_in, 16)

                def group(g, ahead, width=(P, P)):
                    for e in range(2):
                        if ahead and e == 0:
                            sp.wait_ge(lo_ready, g + 2)
                            sp.sem_inc(turns, 1)
                            load(g + 2, ahead)
                        sp.wait_ge(ev[e], g * nch + (nch + 1))
                        sp.sem_inc(turns, 1)
                        sp.dma_start(dst[ds(g * GW + e * P, width[e]), :], ob[0:width[e], e, :]).then_inc(stored[e], 16)

                for e in range(2):
                    sp.sem_inc(stored[e], 1)
                load(0)
                sp.wait_ge(lo_ready, 1)
                load(1)
                with sp.Fori(0, TURNS) as it:
                    for s in range(2):
                        group(it * 2 + s, GW)
                for g in range(2 * TURNS, G):
                    group(g, sum(size[g + 2]) if g + 2 < G else 0, size[g])
                for e in range(2):
                    sp.wait_ge(stored[e], 16 * G + 1)

            @block.tensor
            def _(pe):
                def group(g, slot, width=(P, P)):
                    pe.wait_ge(lo_ready, g + 1)
                    pe.wait_ge(hi_ready, g + 1)
                    for e in range(2):
                        pe.wait_ge(ev[e], g * nch + 1)
                        for c, (a, n) in enumerate(chunks):
                            for k in range(KD):
                                w_hi, w_lo = (wt[:, slot, i, k, e * P:e * P + width[e]] for i in range(2))
                                x_h, x_l = hi[:, k, a:a + n], lo[:, k, a:a + n]
                                for i, (l, r) in enumerate(((w_hi, x_h), (w_lo, x_h), (w_hi, x_l))):
                                    last = nc.tensor.matmul(bank[e * nch + c][0:width[e], 0:n], l, r,
                                                            start=(k == 0 and i == 0), stop=(k == KD - 1 and i == 2))
                            last.then_inc(mm[e], 1)

                pe.wait_ge(x_hi, KD)
                pe.wait_ge(x_lo, KD)
                with pe.Fori(0, TURNS) as it:
                    for s in range(2):
                        group(it * 2 + s, s)
                for g in range(2 * TURNS, G):
                    group(g, g % 2, size[g])

            def drain(eng, e, g, width=P):
                eng.wait_ge(stored[e], g * 16 + 1)
                for c, (a, n) in enumerate(chunks):
                    eng.wait_ge(mm[e], g * nch + (c + 1))
                    o, i = ob[0:width, e, a:a + n], bank[e * nch + c][0:width, 0:n]
                    ins = nc.scalar.activation(o, i, ACT.Copy) if e == 0 else nc.vector.tensor_copy(o, i)
                    ins.then_inc(ev[e], 1)

            def groups_of(eng, e, split):
                with eng.Fori(0, TURNS) as it:
                    for s in range(2):
                        drain(eng, e, it * 2 + s)
                        split(it * 2 + (s + 2), s, GW)
                for g in range(2 * TURNS, G):
                    drain(eng, e, g, size[g][e])
                    if g + 2 < G:
                        split(g + 2, g % 2, sum(size[g + 2]))

            @block.scalar
            def _(act):
                def split(g, slot, width=GW):
                    act.wait_ge(topped, g + 1)
                    nc.scalar.activation(wt[:, slot, 0, :, 0:width], top[:, :, 0:width], ACT.Copy).then_inc(hi_ready, 1)

                act.sem_inc(ev[0], 1)
                for k in range(KD):
                    act.wait_ge(x_top, k + 1)
                    nc.scalar.activation(hi[:, k, :], ob[:, k % 2, :], ACT.Copy).then_inc(x_hi, 1)
                    if k < 2:
                        split(k, k)
                groups_of(act, 0, split)

            @block.vector
            def _(dve):
                def leading(part, whole):
                    return nc.vector.tensor_scalar(part.bitcast(I32), whole.bitcast(I32), HI_MASK, None, ALU.bitwise_and)

                def split(g, slot, width=GW):
                    dve.wait_ge(w_in, g * 16 + 16)
                    if not (isinstance(g, int) and g == 0):
                        dve.wait_ge(hi_ready, g)
                        dve.sem_inc(turns, 1)
                    leading(top[:, :, 0:width], raw[:, :, 0:width]).then_inc(topped, 1)
                    dve.wait_ge(topped, g + 1)
                    nc.vector.tensor_tensor(wt[:, slot, 1, :, 0:width], raw[:, :, 0:width], top[:, :, 0:width], ALU.subtract)\
                        .then_inc(lo_ready, 1)

                dve.sem_inc(ev[1], 1)
                for k in range(KD):
                    if k >= 2:
                        dve.wait_ge(x_hi, k - 1)
                    leading(ob[:, k % 2, :], actT[:, k, :]).then_inc(x_top, 1)
                    dve.wait_ge(x_top, k + 1)
                    nc.vector.tensor_tensor(lo[:, k, :], actT[:, k, :], ob[:, k % 2, :], ALU.subtract).then_inc(x_lo, 1)
                    if k < 2:
                        split(k, k)
                groups_of(dve, 1, split)


class Loop:

    def __init__(self, sem, turn, per):
        self.sem, self.base, self.per, self.k = sem, turn * per, per, 0

    def __call__(self, instruction):
        instruction.then_inc(self.sem, 1)
        self.k += 1
        return self.base + self.k

    def end(self):
        assert self.k == self.per, f"{self.sem}: {self.k} a turn, not {self.per}"


def retention(nc, bank, cst, tabs, uT, latT):
    NB = TT // P
    with Stage(nc, "ret") as st:
        q, k, v = st.sb("q", [P, TT]), st.sb("k", [P, TT]), st.sb("v", [P, TT])
        g = st.sb("g", [P, 2, T])
        din = st.sb("din", [P, 2, 2, P])
        qd, kd, cd = st.sb("qd", [P, 2, P]), st.sb("kd", [P, 2, P]), st.sb("cd", [P, 1])
        ax = st.sb("ax", [P, 2, T])
        kz = st.sb("kz", [P, 2, T])
        vz = st.sb("vz", [P, NB, 2, P])
        vr = st.sb("vr", [P, 2, P])
        tmp = st.sb("tmp", [P, 2, T])
        qs = st.sb("qs", [P, 2, T])
        kfb = st.sb("kfb", [P, 2, 2, P])
        kvm = st.sb("kvm", [P, 2, NB, P])
        S = st.sb("S", [P, 2, NT + 3, P])
        sc = st.sb("sc", [P, 2, 2, 2, P])
        y = st.sb("y", [P, 2, T])
        lat = st.sb("lat", [P, T])
        names = ("tab_in", "q_in", "k_in", "v_in", "g_in", "zeroed", "rot", "cosed", "roped", "halved", "tr",
                 "k_rows", "v_rows", "v_copied", "kv", "kv_kept", "scan", "states", "q_scaled", "scores", "sc_ready",
                 "y_mm", "y_ready", "squared", "sums", "ms", "root", "chain", "silu", "lat_ready", "stored")
        s = {n: st.sem(n) for n in names}
        ident, pair = (cst[:, CONST[n]:CONST[n] + P] for n in ("ident", "pair"))
        axrot = cst[:, CONST["axrot"]:CONST["axrot"] + P]
        LAT = slice(TC, TT)
        CHAIN = 10
        with nc.Block() as block:
            @block.sync
            def _(sp):
                sp.dma_start(ax[:, :, :], tabs["ax"].rearrange("a p t -> p a t")).then_inc(s["tab_in"], 16)
                sp.sem_inc(s["stored"], 1)
                with sp.Fori(0, PAIRS) as p:
                    for n, (t, a) in enumerate(((q, 0), (k, RW), (v, 2 * RW))):
                        sp.dma_start(t[:, :], uT[ds(p * P + a, P), :]).then_inc(s["qkv"[n] + "_in"], 16)
                    for d in range(2):
                        sp.dma_start(g[:, d, :], uT[ds(p * P + (3 + d) * RW, P), LAT]).then_inc(s["g_in"], 16)
                    for d in range(2):
                        sp.dma_start(din[:, d], tabs["din"][d, ds(p * 2, 2)].rearrange("h j i -> j h i"))\
                            .then_inc(s["tab_in"], 16)
                    for t, n in ((qd, "qd"), (kd, "kd")):
                        sp.dma_start(t[:, :, :], tabs[n][:, ds(p, 1)].rearrange("d o p t -> p (d o) t"))\
                            .then_inc(s["tab_in"], 16)
                    sp.dma_start(cd[:, :], tabs["cdec"][ds(p, 1)].rearrange("o p t -> p (o t)"))\
                        .then_inc(s["tab_in"], 16)
                    sp.wait_ge(s["lat_ready"], p + 1)
                    sp.dma_start(latT[ds(p * P, P), :], lat[:, :]).then_inc(s["stored"], 16)
                sp.wait_ge(s["stored"], 16 * PAIRS + 1)

            TAB = 80

            @block.gpsimd
            def _(pool):
                nc.gpsimd.memset(kz[:, :, :], 0.0).then_inc(s["zeroed"], 1)
                nc.gpsimd.memset(vz[:, :, :, :], 0.0).then_inc(s["zeroed"], 1)
                nc.gpsimd.memset(S[:, :, 0, :], 0.0).then_inc(s["zeroed"], 1)
                pool.wait_ge(s["zeroed"], 3)
                with pool.Fori(0, PAIRS) as p:
                    pool.wait_ge(s["tab_in"], p * TAB + (TAB + 16))
                    for i, t in enumerate((q, k)):
                        pool.wait_ge(s["rot"], p * 4 + (2 * i + 2))
                        nc.gpsimd.tensor_tensor(t[:, LAT], t[:, LAT], ax[:, 0, :], ALU.mult).then_inc(s["cosed"], 1)
                    pool.wait_ge(s["roped"], p * 4 + 4)
                    for d in range(2):
                        nc.gpsimd.tensor_tensor(qs[:, d, :].rearrange("p (n t) -> p n t", t=P),
                                                q[:, LAT].rearrange("p (n t) -> p n t", t=P),
                                                qd[:, d, :].unsqueeze(1).to_broadcast([P, NT, P]),
                                                ALU.mult).then_inc(s["q_scaled"], 1)

            @block.tensor
            def _(pe):
                pe.wait_ge(s["zeroed"], 3)
                with pe.Fori(0, PAIRS) as p:
                    for n, (t, nm) in enumerate(((q, "q_in"), (k, "k_in"))):
                        pe.wait_ge(s[nm], p * 16 + 16)
                        for c in range(2):
                            nc.tensor.matmul(bank[2 * n + c][:, :], axrot, t[:, TC + c * BANK:TC + (c + 1) * BANK],
                                             start=True, stop=True).then_inc(s["rot"], 1)
                    pe.wait_ge(s["v_in"], p * 16 + 16)
                    pe.wait_ge(s["roped"], p * 4 + 4)

                    def rows(j):
                        if j >= 2:
                            pe.wait_ge(s["k_rows"], p * (2 * NB) + 2 * (j - 1))
                            pe.wait_ge(s["v_rows"], p * NB + (j - 1))
                        b = bank[4 + j % 2]
                        nc.tensor.transpose(b[:, 0:P], k[:, j * P:(j + 1) * P], ident)
                        nc.tensor.transpose(bank[j % 2][:, 0:P], v[:, j * P:(j + 1) * P], ident).then_inc(s["tr"], 1)

                    rows(0)
                    for j in range(NB):
                        if j + 1 < NB:
                            rows(j + 1)
                        pe.wait_ge(s["k_rows"], p * (2 * NB) + 2 * (j + 1))
                        pe.wait_ge(s["v_rows"], p * NB + (j + 1))
                        if j >= 2:
                            pe.wait_ge(s["kv_kept"], p * NB + (j - 1))
                        for d in range(2):
                            ins = nc.tensor.matmul(bank[6 + j % 2][:, d * P:(d + 1) * P], kfb[:, j % 2, d, :],
                                                   vr[:, j % 2, :], start=True, stop=True)
                        ins.then_inc(s["kv"], 1)
                    pe.wait_ge(s["halved"], p * 2 + 2)
                    pe.wait_ge(s["v_copied"], p * (2 * NB) + 2 * NB)
                    pe.wait_ge(s["q_scaled"], p * 2 + 2)

                    def scores(j):
                        if j >= 2:
                            pe.wait_ge(s["sc_ready"], p * (2 * NT) + 2 * (j - 1))
                        t = slice(j * P, (j + 1) * P)
                        for h in range(2):
                            ins = nc.tensor.matmul(bank[j % 2][:, h * P:(h + 1) * P], kz[:, h, t], q[:, TC + j * P:TC + (j + 1) * P],
                                                   start=True, stop=True)
                        ins.then_inc(s["scores"], 1)

                    scores(0)
                    for j in range(NT):
                        if j + 1 < NT:
                            scores(j + 1)
                        if j == 0:
                            pe.wait_ge(s["states"], p + 1)
                        pe.wait_ge(s["sc_ready"], p * (2 * NT) + 2 * (j + 1))
                        if j >= 2:
                            pe.wait_ge(s["y_ready"], p * NT + (j - 1))
                        for d in range(2):
                            o = bank[2 + j % 2][:, d * P:(d + 1) * P]
                            nc.tensor.matmul(o, S[:, d, 2 + j, :], qs[:, d, j * P:(j + 1) * P], start=True, stop=False)
                            for h in range(2):
                                ins = nc.tensor.matmul(o, vz[:, 2 + j, h, :], sc[:, j % 2, d, h, :],
                                                       start=False, stop=(h == 1))
                        ins.then_inc(s["y_mm"], 1)
                    for d in range(2):
                        pe.wait_ge(s["squared"], p * 2 + (d + 1))
                        for c in range(2):
                            nc.tensor.matmul(bank[4 + 2 * d + c][:, :], pair, tmp[:, d, c * BANK:(c + 1) * BANK],
                                             start=True, stop=True).then_inc(s["sums"], 1)

            @block.scalar
            def _(act):
                act.wait_ge(s["zeroed"], 3)
                with act.Fori(0, PAIRS) as p:
                    act.wait_ge(s["roped"], p * 4 + 4)
                    for h in range(2):
                        r = slice(64 * h, 64 * h + 64)
                        nc.scalar.activation(kz[r, h, :], k[r, LAT], ACT.Copy).then_inc(s["halved"], 1)
                    for j in range(NB):
                        act.wait_ge(s["tr"], p * NB + (j + 1))
                        if j >= 2:
                            act.wait_ge(s["kv"], p * NB + (j - 1))
                        nc.scalar.activation(vr[:, j % 2, :], bank[j % 2][:, 0:P], ACT.Copy)\
                            .then_inc(s["v_rows"], 1)
                        act.wait_ge(s["v_rows"], p * NB + (j + 1))
                        for h in range(2):
                            c = slice(64 * h, 64 * h + 64)
                            nc.scalar.activation(vz[:, j, h, c], vr[:, j % 2, c], ACT.Copy).then_inc(s["v_copied"], 1)
                    for j in range(NT):
                        act.wait_ge(s["y_mm"], p * NT + (j + 1))
                        nc.scalar.activation(y[:, :, j * P:(j + 1) * P],
                                             bank[2 + j % 2][:, 0:2 * P].rearrange("p (d t) -> p d t", d=2),
                                             ACT.Copy).then_inc(s["y_ready"], 1)
                    act.wait_ge(s["y_ready"], p * NT + NT)
                    for d in range(2):
                        nc.scalar.activation(tmp[:, d, :], y[:, d, :], ACT.Square).then_inc(s["squared"], 1)
                    act.wait_ge(s["ms"], p * 4 + 4)
                    nc.scalar.activation(tmp[:, :, :], tmp[:, :, :], ACT.Sqrt).then_inc(s["root"], 1)
                    act.wait_ge(s["g_in"], p * 32 + 32)
                    for d in range(2):
                        nc.scalar.activation(g[:, d, :], g[:, d, :], ACT.Silu).then_inc(s["silu"], 1)

            def keep(dve, p, j):
                dve.wait_ge(s["kv"], p * NB + (j + 1))
                nc.vector.tensor_tensor(kvm[:, :, j, :], bank[6 + j % 2][:, 0:2 * P].rearrange("p (d e) -> p d e", d=2),
                                        pair.unsqueeze(1).to_broadcast([P, 2, P]), ALU.mult).then_inc(s["kv_kept"], 1)

            @block.vector
            def _(dve):
                dve.wait_ge(s["zeroed"], 3)
                with dve.Fori(0, PAIRS) as p:
                    link = Loop(s["chain"], p, CHAIN)
                    dve.wait_ge(s["tab_in"], p * TAB + (TAB + 16))
                    for n, t in enumerate((q, k)):
                        for c in range(2):
                            tc = slice(c * BANK, (c + 1) * BANK)
                            dve.wait_ge(s["rot"], p * 4 + (2 * n + c + 1))
                            dve.wait_ge(s["chain"], link(nc.vector.tensor_tensor(
                                tmp[:, n, tc], bank[2 * n + c][:, :], ax[:, 1, tc], ALU.mult)))
                            dve.wait_ge(s["cosed"], p * 2 + (n + 1))
                            o = t[:, TC + c * BANK:TC + (c + 1) * BANK]
                            nc.vector.tensor_tensor(o, o, tmp[:, n, tc], ALU.add).then_inc(s["roped"], 1)
                    for j in range(NB):
                        dve.wait_ge(s["tr"], p * NB + (j + 1))
                        if j >= 2:
                            dve.wait_ge(s["kv"], p * NB + (j - 1))
                        for d in range(2):
                            nc.vector.tensor_tensor(kfb[:, j % 2, d, :], bank[4 + j % 2][:, 0:P], kd[:, d, :],
                                                    ALU.mult).then_inc(s["k_rows"], 1)
                        if j:
                            keep(dve, p, j - 1)
                    keep(dve, p, NB - 1)
                    dve.wait_ge(s["kv_kept"], p * NB + NB)
                    n = 0
                    for d in range(2):
                        order = list(range(NB)) if d == 0 else [1, 0] + list(range(NB - 1, 1, -1))
                        before = 0
                        for i, j in enumerate(order[:-1]):
                            after = order[i + 1] if i >= 1 else NT + 2
                            nc.vector.scalar_tensor_tensor(S[:, d, after, :], S[:, d, before, :], cd[:, 0:1],
                                                           kvm[:, d, j, :], ALU.mult, ALU.add)\
                                .then_inc(s["scan"] if not (d == 1 and i == NB - 2) else s["states"], 1)
                            if not (d == 1 and i == NB - 2):
                                n += 1
                                dve.wait_ge(s["scan"], p * (2 * NB - 3) + n)
                            before = after
                    for j in range(NT):
                        dve.wait_ge(s["scores"], p * NT + (j + 1))
                        if j >= 2:
                            dve.wait_ge(s["y_mm"], p * NT + (j - 1))
                        for d in range(2):
                            nc.vector.tensor_tensor(sc[:, j % 2, d], bank[j % 2][:, 0:2 * P].rearrange("p (h i) -> p h i", h=2),
                                                    din[:, d], ALU.mult).then_inc(s["sc_ready"], 1)
                    for d in range(2):
                        for c in range(2):
                            dve.wait_ge(s["sums"], p * 4 + (2 * d + c + 1))
                            nc.vector.tensor_scalar(tmp[:, d, c * BANK:(c + 1) * BANK], bank[4 + 2 * d + c][:, :],
                                                    1.0 / RET_DIM, EPS, ALU.mult, ALU.add).then_inc(s["ms"], 1)
                    dve.wait_ge(s["root"], p + 1)
                    for d in range(2):
                        dve.wait_ge(s["chain"], link(nc.vector.reciprocal(tmp[:, d, :], tmp[:, d, :])))
                    for d in range(2):
                        dve.wait_ge(s["chain"], link(nc.vector.tensor_tensor(y[:, d, :], y[:, d, :], tmp[:, d, :], ALU.mult)))
                    for d in range(2):
                        dve.wait_ge(s["silu"], p * 2 + (d + 1))
                        dve.wait_ge(s["chain"], link(nc.vector.tensor_tensor(y[:, d, :], y[:, d, :], g[:, d, :], ALU.mult)))
                    dve.wait_ge(s["stored"], p * 16 + 1)
                    nc.vector.tensor_tensor(lat[:, :], y[:, 0, :], y[:, 1, :], ALU.add).then_inc(s["lat_ready"], 1)
                    link.end()


NC = TT // CH
DECAY = math.exp(-0.5)
PCOL, PW = fill(0, [("conv_r", 3), ("conv_k", 3), ("conv_v", 3), ("a0", 1), ("w0", 2), ("k_k", 1), ("k_a", 1),
                    ("r_k", 1), ("lnw", 1), ("lnb", 1)])


def pcol(pcs, p, name, i=0):
    return pcs[:, ds(p, 1), PCOL[name] + i:PCOL[name] + i + 1].rearrange("q p c -> q (p c)")


def rwkv_prepare(nc, bank, cst, col, tabs, x, uT, prim, vT, wc, bonus, gate):
    U0 = 5 * RW
    NBK = TT // P
    CHS = [(0, BANK), (BANK, BANK), (2 * BANK, TT - 2 * BANK)]
    SEG = ((0, TC), (TC, TT))
    LAT = slice(TC, TT)
    w2, a2, g2 = x["rwkv_w2"][0], x["rwkv_a2"][0], x["rwkv_g2"][0]
    with Stage(nc, "prep") as st:
        rin = st.sb("rin", [P, 3, TT])
        raw = st.sb("raw", [P, 3, TT])
        u = st.sb("u", [P, 3, TT])
        wl, al = st.sb("wl", [P, TT]), st.sb("al", [64, TT])
        gl = st.sb("gl", [P, 2, T])
        keep = st.sb("keep", [P, TT])
        sig = st.sb("sig", [P, 2, TT])
        iclr = st.sb("iclr", [P, TT])
        cum = st.sb("cum", [P, 2, TT])
        ex = st.sb("ex", [P, 3, 2, TT])
        kk = st.sb("kk", [P, TT])
        prod = st.sb("prod", [P, TT])
        out = st.sb("out", [P, 2, 2, TT])
        gt = st.sb("gt", [P, 3, T])
        pcs = st.sb("pcs", [P, PAIRS, PW])
        w2t, a2t, g2t = st.sb("w2t", [P, P]), st.sb("a2t", [64, P]), st.sb("g2t", [P, 2, P])
        names = ("pc_in", "lora_in", "lora", "u_in", "w_in", "z_mm", "sig_ready", "chain", "cum_ready", "exp_ready",
                 "kx_ready", "kx_sq", "ss_mm", "norm", "bonus_in", "bonus_mm", "g_mm", "g_ready", "out0", "out1",
                 "gt_ready", "gt_stored", "vt_stored", "wc_stored", "pair_done", "turns")
        s = {n: st.sem(n) for n in names}
        stored = [[st.sem(f"stored{e}{i}") for i in range(2)] for e in range(2)]
        pair, pairx = (cst[:, CONST[n]:CONST[n] + P] for n in ("pair", "pairx"))
        chunked = [P, NC, CH]

        def conv(dst, src, w, rows, link, wait, segments):
            lo, hi = segments[0][0], segments[-1][1]
            o = lo
            wait(link(nc.vector.tensor_scalar(dst[:, 0:hi - o], src[:, lo:hi], w[1], None, ALU.mult)))
            for a, b in segments:
                wait(link(nc.vector.scalar_tensor_tensor(dst[:, a + 1 - o:b - o], src[:, a:b - 1], w[0],
                                                         dst[:, a + 1 - o:b - o], ALU.mult, ALU.add)))
                wait(link(nc.vector.scalar_tensor_tensor(dst[:, a - o:b - 1 - o], src[:, a + 1:b], w[2],
                                                         dst[:, a - o:b - 1 - o], ALU.mult, ALU.add)))

        with nc.Block() as block:
            @block.sync
            def _(sp):
                l0 = U0 + 3 * RW
                sp.dma_start(raw[:, 0, :], uT[l0:l0 + 128, :]).then_inc(s["lora_in"], 16)
                sp.dma_start(raw[0:64, 1, :], uT[l0 + 128:l0 + 192, :]).then_inc(s["lora_in"], 16)
                sp.dma_start(raw[:, 2, :], uT[l0 + 192:l0 + 320, :]).then_inc(s["lora_in"], 16)
                sp.dma_start(ex[:, 0, 0, :], uT[l0 + 320:l0 + 448, :]).then_inc(s["lora_in"], 16)
                sp.dma_start(pcs[:, :, :], tabs["pcols"].rearrange("q p c -> p q c")).then_inc(s["pc_in"], 16)

            @block.vector
            def _(dve):
                link = Steps(s["lora"])

                def wait(n):
                    dve.wait_ge(s["lora"], n)

                link(nc.vector.memset(keep[:, :], 1.0))
                wait(link.n)
                link(nc.vector.memset(keep[:, :].rearrange("p (n c) -> p n c", c=CH)[:, :, 0:1], 0.0))
                dve.wait_ge(s["lora_in"], 64)
                for n, (dst, src, rows, seg) in enumerate(((wl, raw[:, 0, :], P, SEG), (al, raw[0:64, 1, :], 64, SEG),
                                                           (gl[:, 0, :], raw[:, 2, :], P, SEG[1:]),
                                                           (gl[:, 1, :], ex[:, 0, 0, :], P, SEG[1:]))):
                    c0 = COLS["conv"] + 12 + n
                    conv(dst, src, [col[0:rows, c0 + 16 * t:c0 + 16 * t + 1] for t in range(3)], rows, link, wait, seg)
                assert link.n == LORA

            @block.scalar
            def _(act):
                act.wait_ge(s["lora"], LORA)
                nc.scalar.activation(wl[:, :], wl[:, :], ACT.Tanh).then_inc(s["g_ready"], 1)
                nc.scalar.activation(gl[:, :, :], gl[:, :, :], ACT.Sigmoid).then_inc(s["g_ready"], 1)
                act.wait_ge(s["g_ready"], 2)

        with nc.Block() as block:
            @block.sync
            def _(sp):
                for n in stored[0] + stored[1] + [s["gt_stored"], s["vt_stored"], s["wc_stored"]]:
                    sp.sem_inc(n, 1)

                def load_rkv(p):
                    for n in range(2):
                        sp.dma_start(rin[:, n, :], uT[ds(p * P + (U0 + n * RW), P), :]).then_inc(s["u_in"], 16)
                    for h in range(2):
                        sp.dma_start(rin[64 * h:64 * h + 64, 2, :], uT[ds(p * P + (U0 + 2 * RW + 64 * (1 - h)), 64), :])\
                            .then_inc(s["u_in"], 16)

                def load_weights(p):
                    for h in range(2):
                        r = slice(64 * h, 64 * h + 64)
                        sp.dma_start(w2t[r, :], w2[h, :, ds(p * P, P)]).then_inc(s["w_in"], 16)
                        for d in range(2):
                            sp.dma_start(g2t[:, d, r], g2[d, :, ds(p * P + 64 * (1 - h), 64)]).then_inc(s["w_in"], 16)
                    sp.dma_start(a2t[:, :], a2[:, ds(p * P, P)]).then_inc(s["w_in"], 16)

                def pair_of_heads(p, last):
                    sp.wait_ge(s["kx_ready"], p + 1)
                    sp.sem_inc(s["turns"], 1)
                    sp.dma_start(vT[ds(p * NBK, NBK)].rearrange("b c t -> c b t"),
                                 u[:, 2, :].rearrange("p (b t) -> p b t", t=P)).then_inc(s["vt_stored"], 16)
                    if not last:
                        load_rkv(p + 1)
                    sp.wait_ge(s["g_mm"], p * 4 + 4)
                    sp.sem_inc(s["turns"], 1)
                    if not last:
                        load_weights(p + 1)
                    sp.wait_ge(s["exp_ready"], p * 3 + 3)
                    sp.sem_inc(s["turns"], 1)
                    for d in range(2):
                        at = CH - 1 if d == 0 else 0
                        with nc.allow_non_contiguous_dma("one value in a chunk"):
                            for n in range(2):
                                sp.dma_start(wc[ds(p * NBK, NBK), d, :, n].rearrange("b c -> c b"),
                                             ex[:, 0, d, :].rearrange("p (b n c) -> p b n c", n=2, c=CH)[:, :, n, at])\
                                    .then_inc(s["wc_stored"], 16)
                    for n in range(8):
                        sp.wait_ge(s[f"out{n % 2}"], p * 4 + (n // 2 + 1))
                        sp.sem_inc(s["turns"], 1)
                        sp.dma_start(prim[ds(p * NBK, NBK), n].rearrange("b c t -> c b t"),
                                     out[:, n % 2, n // 2 % 2, :].rearrange("p (b t) -> p b t", t=P))\
                            .then_inc(stored[n % 2][n // 2 % 2], 16)
                    sp.wait_ge(s["gt_ready"], p * 3 + 3)
                    sp.sem_inc(s["turns"], 1)
                    sp.dma_start(bonus[ds(p * P, P), :], gt[:, 2, :]).then_inc(s["gt_stored"], 16)
                    sp.dma_start(gate[:, ds(p * P, P), :].rearrange("d c t -> c d t"), gt[:, 0:2, :])\
                        .then_inc(s["gt_stored"], 16)

                load_rkv(0)
                load_weights(0)
                with sp.Fori(0, PAIRS - 1) as p:
                    pair_of_heads(p, False)
                pair_of_heads(PAIRS - 1, True)
                for n in stored[0] + stored[1]:
                    sp.wait_ge(n, 32 * PAIRS + 1)
                sp.wait_ge(s["vt_stored"], 16 * PAIRS + 1)
                sp.wait_ge(s["wc_stored"], 64 * PAIRS + 1)
                sp.wait_ge(s["gt_stored"], 32 * PAIRS + 1)

            @block.gpsimd
            def _(pool):
                with pool.Fori(0, PAIRS) as p:
                    pool.wait_ge(s["exp_ready"], p * 3 + 3)
                    for i, (src, e, d, ready) in enumerate(((u[:, 0, :], 0, 0, None), (u[:, 0, :], 0, 1, None),
                                                            (iclr[:, :], 1, 1, "b"), (raw[:, 2, :], 1, 1, None))):
                        if ready:
                            pool.wait_ge(s["out0"], p * 4 + 3)
                        pool.wait_ge(stored[1][i % 2], p * 32 + (16 * (i // 2) + 1))
                        nc.gpsimd.tensor_tensor(out[:, 1, i % 2, :], src, ex[:, e, d, :], ALU.mult).then_inc(s["out1"], 1)

            @block.tensor
            def _(pe):
                with pe.Fori(0, PAIRS) as p:
                    pe.wait_ge(s["w_in"], p * 112 + 112)
                    pe.wait_ge(s["pair_done"], p + 1)
                    for n in range(3):
                        for c, (a, m) in enumerate(CHS):
                            if n == 2:
                                pe.wait_ge(s["sig_ready"], p * 9 + (c + 1))
                            lhsT, rhs = ((w2t[0:64, :], wl[0:64, a:a + m]), (w2t[64:128, :], wl[64:128, a:a + m]),
                                         (a2t[:, :], al[:, a:a + m]))[n]
                            nc.tensor.matmul(bank[3 * (n % 2) + c][:, 0:m], lhsT, rhs, start=True, stop=True)\
                                .then_inc(s["z_mm"], 1)
                    pe.wait_ge(s["sig_ready"], p * 9 + 9)
                    pe.wait_ge(s["kx_sq"], p + 1)
                    for c, (a, m) in enumerate(CHS):
                        nc.tensor.matmul(bank[c][:, 0:m], pair, prod[:, a:a + m], start=True, stop=True)\
                            .then_inc(s["ss_mm"], 1)
                    for d in range(2):
                        for c in range(2):
                            nc.tensor.matmul(bank[3 + 2 * d + c][:, :], g2t[:, d, :], gl[:, d, c * BANK:(c + 1) * BANK],
                                             start=True, stop=True).then_inc(s["g_mm"], 1)
                    pe.wait_ge(s["norm"], p * 3 + 3)
                    pe.wait_ge(s["bonus_in"], p + 1)
                    for c in range(2):
                        nc.tensor.matmul(bank[c][:, :], pairx, prod[:, TC + c * BANK:TC + (c + 1) * BANK],
                                         start=True, stop=True).then_inc(s["bonus_mm"], 1)

            @block.scalar
            def _(act):
                with act.Fori(0, PAIRS) as p:
                    for n in range(3):
                        for c, (a, m) in enumerate(CHS):
                            act.wait_ge(s["z_mm"], p * 9 + (3 * n + c + 1))
                            act.sem_inc(s["turns"], 1)
                            o = (sig[:, 0, a:a + m], sig[:, 1, a:a + m], iclr[:, a:a + m])[n]
                            b = pcol(pcs, p, "w0", n) if n < 2 else pcol(pcs, p, "a0")
                            nc.scalar.activation(o, bank[3 * (n % 2) + c][:, 0:m], ACT.Sigmoid, bias=b)\
                                .then_inc(s["sig_ready"], 1)
                    act.wait_ge(s["kx_ready"], p + 1)
                    nc.scalar.activation(prod[:, :], kk[:, :], ACT.Square).then_inc(s["kx_sq"], 1)
                    act.wait_ge(s["gt_stored"], p * 32 + 1)
                    for d in range(2):
                        for c in range(2):
                            act.wait_ge(s["g_mm"], p * 4 + (2 * d + c + 1))
                            nc.scalar.activation(gt[:, d, c * BANK:(c + 1) * BANK], bank[3 + 2 * d + c][:, :], ACT.Copy)\
                                .then_inc(s["g_ready"] if 2 * d + c < 3 else s["gt_ready"], 1)
                    for c, (a, m) in enumerate(CHS):
                        act.wait_ge(s["ss_mm"], p * 3 + (c + 1))
                        nc.scalar.activation(prod[:, a:a + m], bank[c][:, 0:m], ACT.Sqrt).then_inc(s["norm"], 1)
                    act.wait_ge(s["cum_ready"], p + 1)
                    act.wait_ge(s["wc_stored"], p * 64 + 1)
                    nc.scalar.activation(ex[:, 2], cum[:, :, :], ACT.Exp, scale=-DECAY).then_inc(s["exp_ready"], 1)
                    nc.scalar.activation(ex[:, 0], raw[:, 0:2, :], ACT.Exp, scale=-DECAY).then_inc(s["exp_ready"], 1)
                    nc.scalar.activation(ex[:, 1], raw[:, 0:2, :], ACT.Exp, scale=DECAY).then_inc(s["exp_ready"], 1)

            @block.vector
            def _(dve):
                dve.sem_inc(s["pair_done"], 1)
                with dve.Fori(0, PAIRS) as p:
                    link = Loop(s["chain"], p, CHAIN)

                    def wait(n):
                        dve.wait_ge(s["chain"], n)

                    def c_(name, i=0):
                        return pcol(pcs, p, name, i)

                    dve.wait_ge(s["u_in"], p * 64 + 64)
                    dve.wait_ge(s["pc_in"], 16)
                    dve.wait_ge(s["vt_stored"], p * 16 + 1)
                    for n, nm in enumerate(("conv_r", "conv_k", "conv_v")):
                        conv(u[:, n, :], rin[:, n, :], [c_(nm, t) for t in range(3)], P, link, wait, SEG)
                    nc.vector.tensor_scalar(kk[:, :], u[:, 1, :], c_("k_k"), None, ALU.mult).then_inc(s["kx_ready"], 1)
                    dve.wait_ge(s["sig_ready"], p * 9 + 9)
                    wait(link(nc.vector.tensor_tensor_scan(raw[:, 0, :], keep[:, :], sig[:, 0, :], 0.0, ALU.mult, ALU.add)))
                    wait(link(nc.vector.tensor_tensor_scan(raw[:, 2, :], keep[:, :], sig[:, 1, :], 0.0, ALU.mult, ALU.add)))
                    link(nc.vector.tensor_tensor(cum[:, 0, :], raw[:, 0, :], sig[:, 0, :], ALU.subtract))
                    c2 = raw[:, 2, :].rearrange("p (n c) -> p n c", c=CH)
                    wait(link(nc.vector.tensor_tensor(cum[:, 1, :].rearrange("p (n c) -> p n c", c=CH),
                                                      c2[:, :, CH - 1:CH].to_broadcast(chunked), c2, ALU.subtract)))
                    nc.vector.tensor_tensor(raw[:, 1, :], cum[:, 1, :], sig[:, 1, :], ALU.add).then_inc(s["cum_ready"], 1)
                    wait(link(nc.vector.tensor_scalar(raw[:, 2, :], iclr[:, :], 1.0, c_("k_a"), ALU.subtract, ALU.mult)))
                    wait(link(nc.vector.scalar_tensor_tensor(raw[:, 2, :], raw[:, 2, :], 1.0, u[:, 1, :], ALU.add, ALU.mult)))
                    dve.wait_ge(s["norm"], p * 3 + 3)
                    wait(link(nc.vector.tensor_scalar(prod[:, :], prod[:, :], 1e-12, None, ALU.max)))
                    wait(link(nc.vector.reciprocal(prod[:, :], prod[:, :])))
                    wait(link(nc.vector.tensor_tensor(kk[:, :], kk[:, :], prod[:, :], ALU.mult)))
                    nc.vector.scalar_tensor_tensor(prod[:, :], u[:, 0, :], c_("r_k"), raw[:, 2, :], ALU.mult, ALU.mult)\
                        .then_inc(s["bonus_in"], 1)
                    wait(link(nc.vector.tensor_tensor(iclr[:, :], kk[:, :], iclr[:, :], ALU.mult)))
                    dve.wait_ge(s["exp_ready"], p * 3 + 3)
                    for i, (src, e, d) in enumerate(((None, 2, 0), (None, 2, 1), (iclr[:, :], 1, 0), (raw[:, 2, :], 1, 0))):
                        dve.wait_ge(stored[0][i % 2], p * 32 + (16 * (i // 2) + 1))
                        if src is None:
                            ins = nc.vector.scalar_tensor_tensor(out[:, 0, i % 2, :], kk[:, :], -1.0, ex[:, e, d, :], ALU.mult, ALU.mult)
                        else:
                            ins = nc.vector.tensor_tensor(out[:, 0, i % 2, :], src, ex[:, e, d, :], ALU.mult)
                        ins.then_inc(s["out0"], 1)
                    for c in range(2):
                        dve.wait_ge(s["bonus_mm"], p * 2 + (c + 1))
                        nc.vector.tensor_tensor(gt[:, 2, c * BANK:(c + 1) * BANK], bank[c][:, :],
                                                u[:, 2, TC + c * BANK:TC + (c + 1) * BANK], ALU.mult)\
                            .then_inc(s["gt_ready"], 1)
                    link.end()
                    dve.wait_ge(s["gt_ready"], p * 3 + 3)
                    dve.wait_ge(s["out1"], p * 4 + 4)
                    dve.sem_inc(s["pair_done"], 1)


LORA = 18
CHAIN = 25


def rwkv_chunks(nc, bank, cst, tabs, prim, vT, wc, mt, nn, re, yi):
    NBK = TT // P
    UN = 4
    NL = len(LEVELS)
    with Stage(nc, "chunks") as st:
        ar = st.sb("ar", [P, 2, 2, 2, P])
        bk = st.sb("bk", [P, 2, 2, 2, 2, P])
        vt = st.sb("vt", [P, 2, P])
        wct = st.sb("wct", [P, 2, 2, 2])
        msk = st.sb("msk", [P, 2, NL + 1, 2 * P], I32)
        vrow = st.sb("vrow", [P, P])
        vz = st.sb("vz", [P, 2, P])
        vm = st.sb("vm", [P, 2, 2, CH])
        LL = st.sb("LL", [P, UN, 2, 2 * P])
        X = st.sb("X", [P, UN, 2 * P])
        T1 = st.sb("T1", [P, UN, P])
        rows = st.sb("rows", [P, UN, 2, P])
        bm = st.sb("bm", [P, UN, 2, CH])
        Y0 = st.sb("Y0", [P, UN, P])
        TT_ = st.sb("TT", [P, UN, P])
        tvm = st.sb("tvm", [P, UN, 2, CH])
        mts, nns = st.sb("mts", [P, 2, 2, CH]), st.sb("nns", [P, 2, 2, CH])
        res, yis = st.sb("res", [P, 2, P]), st.sb("yis", [P, 2, P])
        names = ("msk_in", "zeroed", "in0", "in1", "v_mm", "v_ev", "vz_ready", "g_mm", "g_ev", "x_init", "lab_mm", "lab_ev",
                 "x_one", "rows_mm", "rows_ev", "a_ev", "bm_ready", "lakv_mm", "lakv_ev", "t1_mm", "t1_ev", "p_mm", "x_ev",
                 "ta_mm", "ta_ev", "tvm_ready", "y_mm", "re_ev", "yi_ev", "m_mm", "mt_ev", "n_ev", "stored", "turns")
        s = {n: st.sem(n) for n in names}
        s_in = [s["in0"], s["in1"]]
        ident = cst[:, CONST["ident"]:CONST["ident"] + P]
        ident2 = cst[:, CONST["ident2"]:CONST["ident2"] + 2 * P]
        hm = [cst[:, CONST["hm"] + P * h:CONST["hm"] + P * (h + 1)] for h in range(2)]
        cmask = cst[:, CONST["cmask"]:CONST["cmask"] + P].rearrange("p (c k) -> p c k", c=2)
        idc = cst[:, CONST["idc"]:CONST["idc"] + CH]
        stm = [cst[:, CONST[n]:CONST[n] + 2 * P] for n in ("st_f", "st_b")]
        A = lambda u_: bank[u_]
        B = lambda u_: bank[4 + u_]
        ITS = PAIRS * NBK // 2

        def each(fn):
            for u_ in range(UN):
                fn(u_, u_ // 2, u_ % 2)

        with nc.Block() as block:
            @block.sync
            def _(sp):
                sp.sem_inc(s["stored"], 1)
                sp.dma_start(msk[:, :, :, :], tabs["msk"].rearrange("d l p c -> p d l c")).then_inc(s["msk_in"], 16)
                sp.wait_ge(s["zeroed"], 1)

                def load(q, k):
                    for d in range(2):
                        sp.dma_start(ar[:, k, d], prim[ds(q, 1), 2 * d:2 * d + 2].rearrange("o n c t -> c (o n) t"))\
                            .then_inc(s_in[k], 16)
                        for h in range(2):
                            r = slice(64 * h, 64 * h + 64)
                            for n in range(2):
                                sp.dma_start(bk[r, k, d, h, n, :], prim[ds(q, 1), 4 + 2 * n + d, r]
                                             .rearrange("o c t -> c (o t)")).then_inc(s_in[k], 16)
                    with nc.allow_non_contiguous_dma("four values a channel"):
                        sp.dma_start(wct[:, k], wc[ds(q, 1)].rearrange("o d c n -> c (o d) n")).then_inc(s_in[k], 16)
                    sp.dma_start(vt[:, k, :], vT[ds(q, 1)].rearrange("o c t -> c (o t)")).then_inc(s_in[k], 16)

                def store(q, k):
                    sp.wait_ge(s["mt_ev"], q * 2 + 3)
                    sp.wait_ge(s["n_ev"], q * 4 + 5)
                    sp.wait_ge(s["re_ev"], q * 4 + 5)
                    sp.wait_ge(s["yi_ev"], q * 4 + 5)
                    for dst, src in ((mt, mts), (nn, nns)):
                        sp.dma_start(dst[ds(q, 1)].rearrange("o d c n k -> n (o d) c k"), src[:, :, :, :])\
                            .then_inc(s["stored"], 16)
                    for dst, src in ((re, res), (yi, yis)):
                        sp.dma_start(dst[ds(q, 1)].rearrange("o d c t -> c (o d) t"), src[:, :, :])\
                            .then_inc(s["stored"], 16)

                for k in range(2):
                    load(k, k)
                with sp.Fori(0, ITS - 1) as it:
                    for k in range(2):
                        store(it * 2 + k, k)
                        load(it * 2 + (2 + k), k)
                for k in range(2):
                    store(2 * (ITS - 1) + k, k)
                sp.wait_ge(s["stored"], 64 * 2 * ITS + 1)

            INC = 16 * 12

            @block.gpsimd
            def _(pool):
                nc.gpsimd.memset(bk[:, :, :, :, :, :], 0.0).then_inc(s["zeroed"], 1)
                with pool.Fori(0, ITS) as it:
                    for k in range(2):
                        q = it * 2 + k
                        pool.wait_ge(s["m_mm"], q * 2 + 1)
                        for u_ in range(UN):
                            nc.gpsimd.tensor_tensor(X[:, u_, :], ident2, ident2, ALU.mult).then_inc(s["x_init"], 1)
                        pool.wait_ge(s["v_ev"], q + 1)
                        for h in range(2):
                            nc.gpsimd.tensor_tensor(vz[:, h, :], vrow[:, :], hm[1 - h], ALU.mult).then_inc(s["vz_ready"], 1)
                            vh = vrow[:, CH * (1 - h):CH * (1 - h) + CH]
                            nc.gpsimd.tensor_tensor(vm[:, h], vh.unsqueeze(1).to_broadcast([P, 2, CH]), cmask, ALU.mult)\
                                .then_inc(s["vz_ready"], 1)
                        for u_ in range(UN):
                            h = u_ % 2
                            pool.wait_ge(s["rows_ev"], q * 4 + (u_ + 1))
                            bh = rows[:, u_, 0, CH * h:CH * h + CH]
                            nc.gpsimd.tensor_tensor(bm[:, u_], bh.unsqueeze(1).to_broadcast([P, 2, CH]), cmask, ALU.mult)\
                                .then_inc(s["bm_ready"], 1)
                        for u_ in range(UN):
                            h = u_ % 2
                            pool.wait_ge(s["ta_ev"], q * 4 + (u_ + 1))
                            tv = TT_[:, u_, CH * (1 - h):CH * (1 - h) + CH]
                            nc.gpsimd.tensor_tensor(tvm[:, u_], tv.unsqueeze(1).to_broadcast([P, 2, CH]), cmask, ALU.mult)\
                                .then_inc(s["tvm_ready"], 1)

            @block.tensor
            def _(pe):
                pe.sem_inc(s["m_mm"], 1)
                with pe.Fori(0, ITS) as it:
                    for k in range(2):
                        q = it * 2 + k
                        pe.wait_ge(s_in[k], it * INC + INC)
                        pe.wait_ge(s["mt_ev"], q * 2 + 1)
                        pe.wait_ge(s["n_ev"], q * 4 + 1)

                        def g(u_, d, h):
                            for n in range(2):
                                ins = nc.tensor.matmul(A(u_)[:, n * 256:n * 256 + 256], bk[:, k, d, h, n, :],
                                                       ar[:, k, d].rearrange("p a t -> p (a t)"), start=True, stop=True)
                            ins.then_inc(s["g_mm"], 1)
                        each(g)
                        pe.wait_ge(s["re_ev"], q * 4 + 1)
                        pe.wait_ge(s["yi_ev"], q * 4 + 1)

                        def lab(u_, d, h):
                            nc.tensor.matmul(B(u_)[:, 0:P], ar[:, k, d, 0, :], bk[:, k, d, h, 0, :], start=True, stop=True)\
                                .then_inc(s["lab_mm"], 1)
                        each(lab)

                        def by_rows(u_, d, h):
                            pe.wait_ge(s["g_ev"], q * 4 + (u_ + 1))
                            nc.tensor.transpose(A(u_)[:, 0:P], bk[:, k, d, h, 0, :], ident)
                            nc.tensor.transpose(A(u_)[:, P:2 * P], bk[:, k, d, h, 1, :], ident)
                            nc.tensor.transpose(A(u_)[:, 2 * P:3 * P], ar[:, k, d, 0, :], ident).then_inc(s["rows_mm"], 1)
                        each(by_rows)
                        pe.wait_ge(s["x_one"], q * 4 + 1)
                        nc.tensor.transpose(B(0)[:, 0:P], vt[:, k, :], ident).then_inc(s["v_mm"], 1)
                        pe.wait_ge(s["v_ev"], q + 1)

                        def lakv(u_, d, h):
                            pe.wait_ge(s["x_one"], q * 4 + (u_ + 1))
                            nc.tensor.matmul(B(u_)[:, 0:P], LL[:, u_, 1, 0:P], vrow[:, :], start=True, stop=True)\
                                .then_inc(s["lakv_mm"], 1)
                        each(lakv)
                        for l in range(NL):
                            def t1(u_, d, h):
                                if l == 0:
                                    pe.wait_ge(s["rows_ev"], q * 4 + (u_ + 1))
                                    pe.wait_ge(s["a_ev"], q * 4 + (u_ + 1))
                                else:
                                    pe.wait_ge(s["x_ev"], q * 20 + (4 * (l - 1) + u_ + 1))
                                nc.tensor.matmul(A(u_)[:, 0:P], LL[:, u_, 0, 0:P], X[:, u_, 0:P], start=True, stop=True)\
                                    .then_inc(s["t1_mm"], 1)
                            each(t1)

                            def pp(u_, d, h):
                                pe.wait_ge(s["t1_ev"], q * 20 + (4 * l + u_ + 1))
                                if l == 0:
                                    pe.wait_ge(s["lakv_ev"], q * 4 + (u_ + 1))
                                if l < NL - 1:
                                    nc.tensor.matmul(B(u_)[:, 0:P], X[:, u_, P:2 * P], T1[:, u_, :], start=True, stop=True)
                                nc.tensor.matmul(B(u_)[:, P:2 * P], T1[:, u_, :], X[:, u_, P:2 * P], start=True, stop=True)\
                                    .then_inc(s["p_mm"], 1)
                            each(pp)

                        def ta(u_, d, h):
                            pe.wait_ge(s["x_ev"], q * 20 + (4 * (NL - 1) + u_ + 1))
                            nc.tensor.matmul(A(u_)[:, 0:P], X[:, u_, P:2 * P], Y0[:, u_, :], start=True, stop=True)\
                                .then_inc(s["ta_mm"], 1)
                        each(ta)
                        pe.wait_ge(s["vz_ready"], q * 4 + 4)

                        def yy(u_, d, h):
                            pe.wait_ge(s["ta_ev"], q * 4 + (u_ + 1))
                            nc.tensor.matmul(B(u_)[:, 0:P], TT_[:, u_, :], LL[:, u_, 0, P:2 * P], start=True, stop=False)
                            nc.tensor.matmul(B(u_)[:, 0:P], vz[:, h, :], LL[:, u_, 1, P:2 * P], start=False, stop=True)\
                                .then_inc(s["y_mm"], 1)
                        each(yy)
                        pe.wait_ge(s["bm_ready"], q * 4 + 4)
                        pe.wait_ge(s["tvm_ready"], q * 4 + 4)
                        for d in range(2):
                            for h in range(2):
                                u_ = 2 * d + h
                                nc.tensor.matmul(A(2 * d)[64 * h:64 * h + 64, 0:P], TT_[:, u_, CH * h:CH * h + CH],
                                                 bm[:, u_].rearrange("p c k -> p (c k)"), start=True, stop=True)
                            for h in range(2):
                                u_ = 2 * d + h
                                nc.tensor.matmul(A(2 * d + 1)[:, 0:P], rows[:, u_, 0, :],
                                                 tvm[:, u_].rearrange("p c k -> p (c k)"), start=(h == 0), stop=False)
                                ins = nc.tensor.matmul(A(2 * d + 1)[:, 0:P], rows[:, u_, 1, :],
                                                       vm[:, h].rearrange("p c k -> p (c k)"), start=False, stop=(h == 1))
                            ins.then_inc(s["m_mm"], 1)

            @block.scalar
            def _(act):
                act.sem_inc(s["n_ev"], 1)
                act.sem_inc(s["yi_ev"], 1)
                with act.Fori(0, ITS) as it:
                    for k in range(2):
                        q = it * 2 + k

                        def by_rows(u_, d, h):
                            act.wait_ge(s["rows_mm"], q * 4 + (u_ + 1))
                            nc.scalar.activation(rows[:, u_].rearrange("p a t -> p (a t)"), A(u_)[:, 0:2 * P], ACT.Copy)\
                                .then_inc(s["rows_ev"], 1)
                            nc.scalar.activation(Y0[:, u_, CH * h:CH * h + CH],
                                                 A(u_)[:, 2 * P + CH * h:2 * P + CH * h + CH], ACT.Copy)\
                                .then_inc(s["a_ev"], 1)
                        each(by_rows)
                        act.wait_ge(s["v_mm"], q + 1)
                        nc.scalar.activation(vrow[:, :], B(0)[:, 0:P], ACT.Copy).then_inc(s["v_ev"], 1)

                        def lakv(u_, d, h):
                            c = slice(CH * (1 - h), CH * (1 - h) + CH)
                            act.wait_ge(s["lakv_mm"], q * 4 + (u_ + 1))
                            nc.scalar.activation(Y0[:, u_, c], B(u_)[:, c], ACT.Copy).then_inc(s["lakv_ev"], 1)
                        each(lakv)
                        for l in range(NL):
                            def t1(u_, d, h):
                                act.wait_ge(s["t1_mm"], q * 20 + (4 * l + u_ + 1))
                                nc.scalar.activation(T1[:, u_, :], A(u_)[:, 0:P], ACT.Copy).then_inc(s["t1_ev"], 1)
                            each(t1)

                        def ta(u_, d, h):
                            act.wait_ge(s["ta_mm"], q * 4 + (u_ + 1))
                            nc.scalar.activation(TT_[:, u_, :], A(u_)[:, 0:P], ACT.Copy).then_inc(s["ta_ev"], 1)
                        each(ta)
                        act.wait_ge(s["stored"], q * 64 + 1)

                        def yy(u_, d, h):
                            r = slice(64 * (1 - h), 64 * (1 - h) + 64)
                            act.wait_ge(s["y_mm"], q * 4 + (u_ + 1))
                            nc.scalar.activation(yis[r, d, :], B(u_)[r, 0:P], ACT.Copy).then_inc(s["yi_ev"], 1)
                        each(yy)
                        for d in range(2):
                            act.wait_ge(s["m_mm"], q * 2 + (d + 2))
                            for c in range(2):
                                nc.scalar.activation(nns[:, d, c, :], A(2 * d + 1)[:, CH * c:CH * c + CH], ACT.Copy,
                                                     scale=wct[:, k, d, c:c + 1]).then_inc(s["n_ev"], 1)

            @block.vector
            def _(dve):
                dve.sem_inc(s["mt_ev"], 1)
                dve.sem_inc(s["re_ev"], 1)
                dve.wait_ge(s["msk_in"], 16)
                with dve.Fori(0, ITS) as it:
                    for k in range(2):
                        q = it * 2 + k

                        def g(u_, d, h):
                            dve.wait_ge(s["g_mm"], q * 4 + (u_ + 1))
                            nc.vector.tensor_tensor(LL[:, u_], A(u_)[:, :].rearrange("p (a t) -> p a t", a=2),
                                                    stm[d].unsqueeze(1).to_broadcast([P, 2, 2 * P]), ALU.mult)\
                                .then_inc(s["g_ev"], 1)
                        each(g)
                        dve.wait_ge(s["x_init"], q * 4 + 4)

                        def one(u_, d, h):
                            dve.wait_ge(s["lab_mm"], q * 4 + (u_ + 1))
                            dve.sem_inc(s["turns"], 1)
                            nc.vector.copy_predicated(X[:, u_, 0:P], msk[:, d, 0, 0:P], B(u_)[:, 0:P]).then_inc(s["lab_ev"], 1)
                            dve.wait_ge(s["g_ev"], q * 4 + (u_ + 1))
                            dve.sem_inc(s["turns"], 1)
                            nc.vector.copy_predicated(X[:, u_, P:2 * P], msk[:, d, 0, P:2 * P], LL[:, u_, 0, 0:P])\
                                .then_inc(s["x_one"], 1)
                        each(one)
                        dve.wait_ge(s["lab_ev"], q * 4 + 4)
                        for l in range(NL):
                            def pp(u_, d, h):
                                dve.wait_ge(s["p_mm"], q * 20 + (4 * l + u_ + 1))
                                if l:
                                    dve.wait_ge(s["x_ev"], q * 20 + (4 * (l - 1) + u_ + 1))
                                dve.sem_inc(s["turns"], 1)
                                c = slice(0 if l < NL - 1 else P, 2 * P)
                                nc.vector.copy_predicated(X[:, u_, c], msk[:, d, 1 + l, c], B(u_)[:, c])\
                                    .then_inc(s["x_ev"], 1)
                            each(pp)
                        dve.wait_ge(s["stored"], q * 64 + 1)

                        def yy(u_, d, h):
                            r = slice(64 * h, 64 * h + 64)
                            dve.wait_ge(s["y_mm"], q * 4 + (u_ + 1))
                            nc.vector.tensor_tensor(res[r, d, :], B(u_)[r, 0:P], ar[r, k, d, 1, :], ALU.add)\
                                .then_inc(s["re_ev"], 1)
                        each(yy)
                        for d in range(2):
                            dve.wait_ge(s["m_mm"], q * 2 + (d + 2))
                            nc.vector.tensor_tensor(mts[:, d], A(2 * d)[:, 0:P].rearrange("p (c k) -> p c k", c=2),
                                                    idc.unsqueeze(1).to_broadcast([P, 2, CH]), ALU.add)\
                                .then_inc(s["mt_ev"], 1)


def rwkv_states(nc, bank, wc, mt, nn, re, yi, yT):
    RING = 4
    NBK = TT // P
    with Stage(nc, "states") as st:
        m = st.sb("m", [P, RING, 2, PAIRS, P])
        n_ = st.sb("n", [P, RING, 2, PAIRS, P])
        w = st.sb("w", [P, 2, PAIRS * NBK, 2])
        S = st.sb("S", [P, 2, 2, PAIRS, P])
        r = st.sb("r", [P, 2, PAIRS, NT, P])
        y = st.sb("y", [P, 2, PAIRS, NT, P])
        mn_in = [st.sem(f"mn_in{i}") for i in range(RING)]
        zeroed, ry_in, w_in = st.sem("zeroed"), st.sem("ry_in"), st.sem("w_in")
        p_mm, s_ready, y_mm, y_ready, stored = (st.sem(x) for x in ("p_mm", "s_ready", "y_mm", "y_ready", "stored"))
        C0 = TC // CH
        order = [list(range(NC)), list(range(C0))[::-1] + list(range(C0, NC))[::-1]]
        with nc.Block() as block:
            @block.gpsimd
            def _(pool):
                nc.gpsimd.memset(m[:, :, :, :, :], 0.0).then_inc(zeroed, 1)
                nc.gpsimd.memset(n_[:, :, :, :, :], 0.0).then_inc(zeroed, 1)
                nc.gpsimd.memset(S[:, :, :, :, :], 0.0).then_inc(zeroed, 1)

            def loads(eng, d, i):
                slot, c = i % RING, order[d][i]
                for h in range(2):
                    rr = slice(64 * h, 64 * h + 64)
                    eng.dma_start(m[rr, slot, d, :, 64 * h:64 * h + 64],
                                  mt[c // 2::NBK, d, c % 2, rr].rearrange("p r k -> r p k")).then_inc(mn_in[slot], 16)
                    eng.dma_start(n_[rr, slot, d, :, 64 * (1 - h):64 * (1 - h) + 64],
                                  nn[c // 2::NBK, d, c % 2, rr].rearrange("p r k -> r p k")).then_inc(mn_in[slot], 16)

            @block.sync
            def _(sp):
                sp.wait_ge(zeroed, 3)
                with nc.allow_non_contiguous_dma("four values a channel"):
                    for d in range(2):
                        sp.dma_start(w[:, d], wc[:, d].rearrange("q c n -> c q n")).then_inc(w_in, 16)
                for i in range(NC - 1):
                    if i >= RING:
                        sp.wait_ge(s_ready, 8 * (i - RING + 1))
                    loads(sp, 0, i)
                    if i == 1:
                        for d in range(2):
                            for p in range(PAIRS):
                                b = slice(p * NBK + NTC, (p + 1) * NBK)
                                sp.dma_start(r[:, d, p], re[b, d].rearrange("b c t -> c b t")).then_inc(ry_in, 16)
                                sp.dma_start(y[:, d, p], yi[b, d].rearrange("b c t -> c b t")).then_inc(ry_in, 16)
                for d in range(2):
                    sp.wait_ge(y_ready, 2 * (NC - C0))
                    for p in range(PAIRS):
                        sp.dma_start(yT[d, p * P:(p + 1) * P, :], y[:, d, p].rearrange("c b t -> c (b t)"))\
                            .then_inc(stored, 16)
                sp.wait_ge(stored, 16 * 2 * PAIRS)

            @block.tensor
            def _(pe):
                pe.wait_ge(zeroed, 3)
                for i in range(NC):
                    for d in range(2):
                        c = order[d][i]
                        if i:
                            pe.wait_ge(s_ready, 8 * (i - 1) + 4 * (d + 1))
                        if i < NC - 1:
                            pe.wait_ge(mn_in[i % RING], 128 * (i // RING + 1))
                            for p in range(PAIRS):
                                ins = nc.tensor.matmul(bank[d][:, p * P:(p + 1) * P], m[:, i % RING, d, p, :],
                                                       S[:, i % 2, d, p, :], start=True, stop=True)
                            ins.then_inc(p_mm, 1)
                        if c >= C0:
                            if i == C0 and d == 0:
                                pe.wait_ge(ry_in, 16 * 4 * PAIRS)
                            if i > C0:
                                pe.wait_ge(y_ready, 2 * (i - C0 - 1) + d + 1)
                            for p in range(PAIRS):
                                ins = nc.tensor.matmul(bank[2 + d][:, p * P:(p + 1) * P], S[:, i % 2, d, p, :],
                                                       r[:, d, p, c // 2 - NTC, :], start=True, stop=True)
                            ins.then_inc(y_mm, 1)

            @block.scalar
            def _(act):
                act.wait_ge(zeroed, 3)
                for i in range(NC - 1):
                    if i >= RING:
                        act.wait_ge(s_ready, 8 * (i - RING + 1))
                    loads(act, 1, i)

            @block.vector
            def _(dve):
                dve.wait_ge(zeroed, 3)
                dve.wait_ge(w_in, 32)
                for i in range(NC):
                    for d in range(2):
                        c = order[d][i]
                        if i < NC - 1:
                            dve.wait_ge(p_mm, 2 * i + d + 1)
                            if i:
                                dve.wait_ge(s_ready, 8 * (i - 1) + 4 * (d + 1))
                            if d == 0 and i > C0:
                                dve.wait_ge(y_mm, 2 * (i - C0))
                            dve.wait_ge(mn_in[i % RING], 128 * (i // RING + 1))
                            for p in range(PAIRS):
                                nc.vector.scalar_tensor_tensor(S[:, (i + 1) % 2, d, p, :], bank[d][:, p * P:(p + 1) * P],
                                                               w[:, d, p * NBK + c // 2, c % 2:c % 2 + 1],
                                                               n_[:, i % RING, d, p, :], ALU.mult, ALU.add)\
                                    .then_inc(s_ready, 1)
                        if c >= C0:
                            dve.wait_ge(y_mm, 2 * (i - C0) + d + 1)
                            if i == C0 and d == 0:
                                dve.wait_ge(ry_in, 16 * 4 * PAIRS)
                            t = slice(CH * (c % 2), CH * (c % 2) + CH)
                            o = y[:, d, :, c // 2 - NTC, t]
                            nc.vector.tensor_tensor(o, bank[2 + d][:, :].rearrange("q (p t) -> q p t", p=PAIRS)[:, :, t], o,
                                                    ALU.add).then_inc(y_ready, 1)


def rwkv_combine(nc, bank, cst, tabs, yT, bonus, gate, latT):
    with Stage(nc, "comb") as st:
        y, g, b = st.sb("y", [P, 2, T]), st.sb("g", [P, 2, T]), st.sb("b", [P, T])
        sq = st.sb("sq", [P, 2, T])
        o = st.sb("o", [P, T])
        pc = st.sb("pc", [P, PW])
        names = ("y_in", "g_in", "mean_mm", "centred", "squared", "var_mm", "var", "root", "chain", "out", "stored")
        s = {n: st.sem(n) for n in names}
        pair = cst[:, CONST["pair"]:CONST["pair"] + P]
        CH_ = 10
        with nc.Block() as block:
            @block.sync
            def _(sp):
                sp.sem_inc(s["stored"], 1)
                with sp.Fori(0, PAIRS) as p:
                    rows = ds(p * P, P)
                    sp.dma_start(y[:, :, :], yT[:, rows, :].rearrange("d c t -> c d t")).then_inc(s["y_in"], 16)
                    sp.dma_start(g[:, :, :], gate[:, rows, :].rearrange("d c t -> c d t")).then_inc(s["g_in"], 16)
                    sp.dma_start(b[:, :], bonus[rows, :]).then_inc(s["g_in"], 16)
                    sp.dma_start(pc[:, :], tabs["pcols"][ds(p, 1)].rearrange("o p c -> p (o c)")).then_inc(s["g_in"], 16)
                    sp.wait_ge(s["out"], p + 1)
                    sp.dma_start(latT[ds(p * P + RW, P), :], o[:, :]).then_inc(s["stored"], 16)
                sp.wait_ge(s["stored"], 16 * PAIRS + 1)

            @block.tensor
            def _(pe):
                with pe.Fori(0, PAIRS) as p:
                    pe.wait_ge(s["y_in"], p * 16 + 16)
                    for d in range(2):
                        for c in range(2):
                            nc.tensor.matmul(bank[2 * d + c][:, :], pair, y[:, d, c * BANK:(c + 1) * BANK],
                                             start=True, stop=True).then_inc(s["mean_mm"], 1)
                    for d in range(2):
                        pe.wait_ge(s["squared"], p * 2 + (d + 1))
                        for c in range(2):
                            nc.tensor.matmul(bank[4 + 2 * d + c][:, :], pair, sq[:, d, c * BANK:(c + 1) * BANK],
                                             start=True, stop=True).then_inc(s["var_mm"], 1)

            @block.scalar
            def _(act):
                with act.Fori(0, PAIRS) as p:
                    for d in range(2):
                        act.wait_ge(s["centred"], p * 4 + 2 * (d + 1))
                        nc.scalar.activation(sq[:, d, :], y[:, d, :], ACT.Square).then_inc(s["squared"], 1)
                    act.wait_ge(s["var"], p * 4 + 4)
                    nc.scalar.activation(sq[:, :, :], sq[:, :, :], ACT.Sqrt).then_inc(s["root"], 1)

            @block.vector
            def _(dve):
                with dve.Fori(0, PAIRS) as p:
                    link = Loop(s["chain"], p, CH_)

                    def wait(n):
                        dve.wait_ge(s["chain"], n)

                    for d in range(2):
                        for c in range(2):
                            t = slice(c * BANK, (c + 1) * BANK)
                            dve.wait_ge(s["mean_mm"], p * 4 + (2 * d + c + 1))
                            nc.vector.scalar_tensor_tensor(y[:, d, t], bank[2 * d + c][:, :], -1.0 / RET_DIM, y[:, d, t],
                                                           ALU.mult, ALU.add).then_inc(s["centred"], 1)
                    for d in range(2):
                        for c in range(2):
                            t = slice(c * BANK, (c + 1) * BANK)
                            dve.wait_ge(s["var_mm"], p * 4 + (2 * d + c + 1))
                            nc.vector.tensor_scalar(sq[:, d, t], bank[4 + 2 * d + c][:, :], 1.0 / RET_DIM, GN_EPS,
                                                    ALU.mult, ALU.add).then_inc(s["var"], 1)
                    dve.wait_ge(s["root"], p + 1)
                    dve.wait_ge(s["g_in"], p * 48 + 48)
                    for d in range(2):
                        wait(link(nc.vector.reciprocal(sq[:, d, :], sq[:, d, :])))
                        wait(link(nc.vector.tensor_tensor(y[:, d, :], y[:, d, :], sq[:, d, :], ALU.mult)))
                        wait(link(nc.vector.tensor_scalar(y[:, d, :], y[:, d, :], pc[:, PCOL["lnw"]:PCOL["lnw"] + 1],
                                                          pc[:, PCOL["lnb"]:PCOL["lnb"] + 1], ALU.mult, ALU.add)))
                        wait(link(nc.vector.tensor_tensor(y[:, d, :], y[:, d, :], b[:, :], ALU.add)))
                        wait(link(nc.vector.tensor_tensor(y[:, d, :], y[:, d, :], g[:, d, :], ALU.mult)))
                    dve.wait_ge(s["stored"], p * 16 + 1)
                    nc.vector.tensor_tensor(o[:, :], y[:, 0, :], y[:, 1, :], ALU.add).then_inc(s["out"], 1)
                    link.end()


def rwkv(nc, bank, cst, col, tabs, x, uT, scratch, latT, upto=9):
    NBK = TT // P
    Q = PAIRS * NBK
    prim, vT = scratch("prim", Q, 8, P, P), scratch("vT", Q, P, P)
    wc, bonus, gate = scratch("wc", Q, 2, P, 2), scratch("bonus", RW, T), scratch("gate", 2, RW, T)
    rwkv_prepare(nc, bank, cst, col, tabs, x, uT, prim, vT, wc, bonus, gate)
    if upto < 2:
        return
    mt, nn = scratch("mt", Q, 2, 2, P, CH), scratch("nn", Q, 2, 2, P, CH)
    re, yi = scratch("re", Q, 2, P, P), scratch("yi", Q, 2, P, P)
    rwkv_chunks(nc, bank, cst, tabs, prim, vT, wc, mt, nn, re, yi)
    if upto < 3:
        return
    yT = scratch("yT", 2, RW, T)
    rwkv_states(nc, bank, wc, mt, nn, re, yi, yT)
    rwkv_combine(nc, bank, cst, tabs, yT, bonus, gate, latT)


def gemm_rows(nc, bank, name, actT, K, w, x, out, grow=None, exchanged=()):
    KK = K // P
    with Stage(nc, name) as st:
        wt = st.sb("w", [P, KK, D])
        xt = st.sb("x", [P, 4, D])
        sq = st.sb("sq", [P, D])
        ss = st.sb("ss", [P, NT, 5])
        gb, yt = st.sb("g", [P, D]), st.sb("y", [P, D])
        w_in, g_in, x_in = [st.sem(f"w_in{c}") for c in range(2)], st.sem("g_in"), [st.sem(f"x_in{i}") for i in range(4)]
        mm, ssq, ms, root, rstd, scaled, out_ready = (st.sem(n) for n in
                                                      ("mm", "ssq", "ms", "root", "rstd", "scaled", "out_ready"))
        stored = [st.sem(f"stored{i}") for i in range(4)]
        WIN = 16 * (KK - len(exchanged) + 2 * len(exchanged))
        with nc.Block() as block:
            @block.sync
            def _(sp):
                for c in range(2):
                    cc = slice(c * BANK, (c + 1) * BANK)
                    for k in range(KK):
                        if k in exchanged:
                            for h in range(2):
                                sp.dma_start(wt[64 * h:64 * h + 64, k, cc],
                                             w[k * P + 64 * (1 - h):k * P + 64 * (1 - h) + 64, cc]).then_inc(w_in[c], 16)
                        else:
                            sp.dma_start(wt[:, k, cc], w[k * P:(k + 1) * P, cc]).then_inc(w_in[c], 16)
                    if c == 0 and grow is not None:
                        sp.dma_start(gb[:, :], grow.partition_broadcast(P).rearrange("p o d -> p (o d)")).then_inc(g_in, 16)
                for i in range(4):
                    sp.dma_start(xt[:, i, :], x[i * P:(i + 1) * P, :]).then_inc(x_in[i], 16)
                for i in range(NT):
                    sp.wait_ge(out_ready, (i + 1) if grow is not None else 2 * (i + 1))
                    sp.dma_start(out[i * P:(i + 1) * P, :], xt[:, i % 4, :]).then_inc(stored[i % 4], 16)
                    if i + 4 < NT:
                        sp.wait_ge(stored[i % 4], 16 * (i // 4 + 1))
                        sp.dma_start(xt[:, i % 4, :], x[(i + 4) * P:(i + 5) * P, :]).then_inc(x_in[i % 4], 16)
                for i in range(4):
                    sp.wait_ge(stored[i], 16 * (NT // 4))

            @block.tensor
            def _(pe):
                for i in range(NT):
                    for c in range(2):
                        if i == 0:
                            pe.wait_ge(w_in[c], WIN)
                        if i >= 2 and c == 0:
                            pe.wait_ge(scaled if grow is not None else out_ready, 2 * (i - 1))
                        for k in range(KK):
                            last = nc.tensor.matmul(bank[2 * (i % 2) + c][:, :], actT[:, k, i * P:(i + 1) * P],
                                                    wt[:, k, c * BANK:(c + 1) * BANK], start=(k == 0), stop=(k == KK - 1))
                        last.then_inc(mm, 1)

            if grow is not None:
                @block.scalar
                def _(act):
                    for i in range(NT):
                        for c in range(2):
                            act.wait_ge(mm, 2 * i + c + 1)
                            if i or c:
                                act.wait_ge(ssq, 2 * i + c)
                            nc.scalar.activation(sq[:, c * BANK:(c + 1) * BANK], bank[2 * (i % 2) + c][:, :], ACT.Square,
                                                 accum_out=ss[:, i, c:c + 1]).then_inc(ssq, 1)
                        act.wait_ge(ms, i + 1)
                        nc.scalar.activation(ss[:, i, 3:4], ss[:, i, 2:3], ACT.Sqrt).then_inc(root, 1)

            @block.vector
            def _(dve):
                for i in range(NT):
                    xs = xt[:, i % 4, :]
                    if grow is not None:
                        dve.wait_ge(ssq, 2 * i + 2)
                        nc.vector.tensor_tensor(ss[:, i, 2:3], ss[:, i, 0:1], ss[:, i, 1:2], ALU.add).then_inc(rstd, 1)
                        dve.wait_ge(rstd, 2 * i + 1)
                        nc.vector.tensor_scalar(ss[:, i, 2:3], ss[:, i, 2:3], 1.0 / D, EPS, ALU.mult, ALU.add)\
                            .then_inc(ms, 1)
                        dve.wait_ge(root, i + 1)
                        nc.vector.reciprocal(ss[:, i, 4:5], ss[:, i, 3:4]).then_inc(rstd, 1)
                        dve.wait_ge(rstd, 2 * i + 2)
                        if i == 0:
                            dve.wait_ge(g_in, 16)
                        for c in range(2):
                            cc = slice(c * BANK, (c + 1) * BANK)
                            nc.vector.scalar_tensor_tensor(yt[:, cc], bank[2 * (i % 2) + c][:, :], ss[:, i, 4:5],
                                                           gb[:, cc], ALU.mult, ALU.mult).then_inc(scaled, 1)
                        dve.wait_ge(scaled, 2 * i + 2)
                        dve.wait_ge(x_in[i % 4], 16 * (i // 4 + 1))
                        nc.vector.tensor_tensor(xs, xs, yt[:, :], ALU.add).then_inc(out_ready, 1)
                        dve.wait_ge(out_ready, i + 1)
                    else:
                        dve.wait_ge(x_in[i % 4], 16 * (i // 4 + 1))
                        for c in range(2):
                            cc = slice(c * BANK, (c + 1) * BANK)
                            dve.wait_ge(mm, 2 * i + c + 1)
                            nc.vector.tensor_tensor(xs[:, cc], xs[:, cc], bank[2 * (i % 2) + c][:, :], ALU.add)\
                                .then_inc(out_ready, 1)


def add_normed(nc, name, x, y, grow, out):
    with Stage(nc, name) as st:
        xt, yt, gb = st.sb("x", [P, NT, D]), st.sb("y", [P, NT, D]), st.sb("g", [P, D])
        sq, ss = st.sb("sq", [P, D]), st.sb("ss", [P, NT, 4])
        x_in, y_in = [st.sem(f"x_in{i}") for i in range(2)], [st.sem(f"y_in{i}") for i in range(2)]
        g_in, ssq, ms, root, rstd, scaled, out_ready, stored = (
            st.sem(n) for n in ("g_in", "ssq", "ms", "root", "rstd", "scaled", "out_ready", "stored"))
        H = NT // 2
        with nc.Block() as block:
            @block.sync
            def _(sp):
                for i in range(2):
                    t = slice(i * H * P, (i + 1) * H * P)
                    sp.dma_start(yt[:, i * H:(i + 1) * H, :], y[t, :].rearrange("(n p) d -> p n d", p=P)).then_inc(y_in[i], 16)
                    if i == 0:
                        sp.dma_start(gb[:, :], grow.partition_broadcast(P).rearrange("p o d -> p (o d)")).then_inc(g_in, 16)
                    sp.dma_start(xt[:, i * H:(i + 1) * H, :], x[t, :].rearrange("(n p) d -> p n d", p=P)).then_inc(x_in[i], 16)
                for i in range(NT):
                    sp.wait_ge(out_ready, i + 1)
                    sp.dma_start(out[i * P:(i + 1) * P, :], xt[:, i, :]).then_inc(stored, 16)
                sp.wait_ge(stored, 16 * NT)

            @block.scalar
            def _(act):
                for i in range(NT):
                    act.wait_ge(y_in[i // H], 16)
                    if i:
                        act.wait_ge(ssq, i)
                    nc.scalar.activation(sq[:, :], yt[:, i, :], ACT.Square, accum_out=ss[:, i, 0:1]).then_inc(ssq, 1)
                    act.wait_ge(ms, i + 1)
                    nc.scalar.activation(ss[:, i, 2:3], ss[:, i, 1:2], ACT.Sqrt).then_inc(root, 1)

            @block.vector
            def _(dve):
                dve.wait_ge(g_in, 16)
                for i in range(NT):
                    dve.wait_ge(ssq, i + 1)
                    nc.vector.tensor_scalar(ss[:, i, 1:2], ss[:, i, 0:1], 1.0 / D, EPS, ALU.mult, ALU.add).then_inc(ms, 1)
                    dve.wait_ge(root, i + 1)
                    nc.vector.reciprocal(ss[:, i, 3:4], ss[:, i, 2:3]).then_inc(rstd, 1)
                    dve.wait_ge(rstd, i + 1)
                    nc.vector.scalar_tensor_tensor(yt[:, i, :], yt[:, i, :], ss[:, i, 3:4], gb[:, :], ALU.mult, ALU.mult)\
                        .then_inc(scaled, 1)
                    dve.wait_ge(scaled, i + 1)
                    dve.wait_ge(x_in[i // H], 16)
                    nc.vector.tensor_tensor(xt[:, i, :], xt[:, i, :], yt[:, i, :], ALU.add).then_inc(out_ready, 1)


def route1(nc, bank, cst, hT, w_router, acc, idx, gates):
    with Stage(nc, "route1") as st:
        wr = st.sb("wr", [P, KD, E1])
        lT = st.sb("lT", [E1, T])
        lg, ex = st.sb("lg", [P, NT, E1]), st.sb("ex", [P, NT, E1])
        mx, sm = st.sb("mx", [P, NT]), st.sb("sm", [P, 2, NT])
        af = [st.sb("af0", [E1, T]), st.sb("af1", [E1, T])]
        va, ix, ixf = st.sb("va", [E1, CAP]), st.sb("ix", [E1, CAP], U32), st.sb("ixf", [E1, CAP])
        zero = st.sb("zero", [P, D])
        w_in, l_mm, l_ev, tr, chain, e_ready, af_mm, af_ev, ixf_ready, fin_mm, fin = (
            st.sem(n) for n in ("w_in", "l_mm", "l_ev", "tr", "chain", "e_ready", "af_mm", "af_ev", "ixf_ready", "fin_mm", "fin"))
        zeroed, cleared, p_ready, d_ready = st.sem("zeroed"), st.sem("cleared"), st.sem("p_ready"), st.sem("d_ready")
        ident = cst[:, CONST["ident"]:CONST["ident"] + P]
        with nc.Block() as block:
            @block.sync
            def _(sp):
                sp.dma_start(wr[:, :, :], w_router.rearrange("(k p) e -> p k e", p=P)).then_inc(w_in, 16)
                sp.wait_ge(zeroed, 1)
                for i in range(NT):
                    sp.dma_start(acc[i * P:(i + 1) * P, :], zero[:, :]).then_inc(cleared, 16)
                sp.wait_ge(cleared, 16 * NT)

            @block.gpsimd
            def _(pool):
                nc.gpsimd.memset(zero[:, :], 0.0).then_inc(zeroed, 1)

            @block.tensor
            def _(pe):
                pe.wait_ge(w_in, 16)
                for c in range(2):
                    for k in range(KD):
                        last = nc.tensor.matmul(bank[c][0:E1, :], wr[:, k, :], hT[:, k, c * BANK:(c + 1) * BANK],
                                                start=(k == 0), stop=(k == KD - 1))
                    last.then_inc(l_mm, 1)
                pe.wait_ge(l_ev, 2)
                for i in range(NT):
                    last = nc.tensor.transpose(bank[2][:, i * E1:(i + 1) * E1], lT[:, i * P:(i + 1) * P], ident[0:E1, 0:E1])
                last.then_inc(tr, 1)
                pe.wait_ge(p_ready, 1)
                for i in range(NT):
                    last = nc.tensor.transpose(bank[3 + i // 4][0:E1, (i % 4) * P:(i % 4 + 1) * P], ex[:, i, :], ident)
                last.then_inc(af_mm, 1)
                pe.wait_ge(ixf_ready, 1)
                nc.tensor.transpose(bank[5][:, 0:E1], va[:, :], ident[0:E1, 0:E1])
                nc.tensor.transpose(bank[5][:, E1:2 * E1], ixf[:, :], ident[0:E1, 0:E1]).then_inc(fin_mm, 1)

            @block.scalar
            def _(act):
                for c in range(2):
                    act.wait_ge(l_mm, c + 1)
                    nc.scalar.activation(lT[:, c * BANK:(c + 1) * BANK], bank[c][0:E1, :], ACT.Copy).then_inc(l_ev, 1)
                act.wait_ge(d_ready, 1)
                nc.scalar.activation(ex[:, :, :], lg[:, :, :], ACT.Exp).then_inc(e_ready, 1)

            @block.vector
            def _(dve):
                link = Steps(chain)
                dve.wait_ge(tr, 1)
                lp = bank[2][:, 0:NT * E1].rearrange("p (n e) -> p n e", e=E1)
                dve.wait_ge(chain, link(nc.vector.tensor_reduce(mx[:, :], lp, AX_X, ALU.max)))
                nc.vector.tensor_tensor(lg[:, :, :], lp, mx[:, :].unsqueeze(2).to_broadcast([P, NT, E1]), ALU.subtract)\
                    .then_inc(d_ready, 1)
                dve.wait_ge(e_ready, 1)
                dve.wait_ge(chain, link(nc.vector.tensor_reduce(sm[:, 0, :], ex[:, :, :], AX_X, ALU.add)))
                dve.wait_ge(chain, link(nc.vector.reciprocal(sm[:, 1, :], sm[:, 0, :])))
                nc.vector.tensor_tensor(ex[:, :, :], ex[:, :, :], sm[:, 1, :].unsqueeze(2).to_broadcast([P, NT, E1]),
                                        ALU.mult).then_inc(p_ready, 1)
                dve.wait_ge(af_mm, 1)
                for c in range(2):
                    dve.wait_ge(chain, link(nc.vector.tensor_copy(af[0][:, c * BANK:(c + 1) * BANK], bank[3 + c][0:E1, :])))
                for r in range(CAP // 8):
                    v8, i8, a, b = va[:, 8 * r:8 * r + 8], ix[:, 8 * r:8 * r + 8], af[r % 2], af[(r + 1) % 2]
                    dve.wait_ge(chain, link(nc.vector.max(v8, a[:, :])))
                    link(nc.vector.max_index(i8, v8, a[:, :]))
                    dve.wait_ge(chain, link(nc.vector.match_replace(b[:, :], v8, a[:, :], -1.0)))
                nc.vector.tensor_copy(ixf[:, :], ix[:, :]).then_inc(ixf_ready, 1)
                dve.wait_ge(fin_mm, 1)
                nc.vector.tensor_copy(gates[:, :], bank[5][:, 0:E1]).then_inc(fin, 1)
                nc.vector.tensor_copy(idx[:, 0:E1], bank[5][:, E1:2 * E1]).then_inc(fin, 1)
                nc.vector.tensor_copy(idx[:, E1:E1 + 1], bank[5][:, E1:E1 + 1]).then_inc(fin, 1)


def experts1(nc, bank, cst, h2, w_gate, w_up, w_down, acc, idx, gates, xs_in, added):
    with Stage(nc, "moe1") as st:
        w = st.sb("w", [P, 6, 8 * BANK])
        xs, xT = st.sb("xs", [P, D]), st.sb("xT", [P, KD, P])
        cur = st.sb("cur", [P, 2], U32)
        sg = st.sb("sg", [P, 2, BANK])
        hid, hidT = st.sb("hid", [P, 2, BANK]), st.sb("hidT", [P, KD, P])
        ye = st.sb("ye", [P, D])
        w_in = [st.sem(f"w_in{i}") for i in range(6)]
        names = ("turns", "cur_ready", "x_tr", "xT_ev", "gu_mm", "sg_ready", "hid_ready", "h_tr", "hT_ev", "y_mm",
                 "ye_ready", "ye_free")
        s = {n: st.sem(n) for n in names}
        ident = cst[:, CONST["ident"]:CONST["ident"] + P]

        def load(sp, e, i):
            m = (w_gate, w_up, w_gate, w_up, w_down, w_down)[i]
            if i < 4:
                c = (i // 2) * BANK
                src = m[ds(e, 1), :, c:c + BANK].rearrange("o (k p) n -> p (o k) n", p=P)
                dst = w[:, i].rearrange("p (k n) -> p k n", k=8)
            else:
                r = (i - 4) * BANK
                src = m[ds(e, 1), r:r + BANK, :].rearrange("o (k p) n -> p (o k) n", p=P)
                dst = w[:, i].rearrange("p (k n) -> p k n", k=4)
            sp.dma_start(dst, src).then_inc(w_in[i], 16)

        with nc.Block() as block:
            @block.sync
            def _(sp):
                for i in range(6):
                    load(sp, 0, i)
                with sp.Fori(0, E1 - 1) as e:
                    for i in range(4):
                        sp.wait_ge(s["gu_mm"], e * 4 + (i + 1))
                        load(sp, e + 1, i)
                    for i in range(2):
                        sp.wait_ge(s["y_mm"], e * 2 + (i + 1))
                        load(sp, e + 1, 4 + i)

            @block.gpsimd
            def _(pool):
                def gather():
                    pool.indirect_dma_start(out=xs[:, :], out_offset=None, in_=h2[:, :],
                                            in_offset=bass.IndirectOffsetOnAxis(ap=cur[:, 0:1], axis=0))\
                        .then_inc(xs_in, 16)

                pool.sem_inc(s["ye_free"], 1)
                nc.gpsimd.tensor_copy(cur[:, 0:1], idx[:, 0:1]).then_inc(s["cur_ready"], 1)
                pool.wait_ge(s["cur_ready"], 1)
                gather()
                with pool.Fori(0, E1) as e:
                    pool.wait_ge(s["x_tr"], e * 2 + 2)
                    pool.sem_inc(s["turns"], 1)
                    nc.gpsimd.tensor_copy(cur[:, 1:2], cur[:, 0:1]).then_inc(s["cur_ready"], 1)
                    pool.wait_ge(s["cur_ready"], e * 2 + 2)
                    pool.sem_inc(s["turns"], 1)
                    nc.gpsimd.tensor_copy(cur[:, 0:1], idx[:, ds(e + 1, 1)]).then_inc(s["cur_ready"], 1)
                    pool.wait_ge(s["cur_ready"], e * 2 + 3)
                    pool.sem_inc(s["turns"], 1)
                    gather()
                    pool.wait_ge(s["ye_ready"], e * 2 + 3)
                    pool.sem_inc(s["turns"], 1)
                    pool.indirect_dma_start(out=acc[:, :], out_offset=bass.IndirectOffsetOnAxis(ap=cur[:, 1:2], axis=0),
                                            in_=ye[:, :], in_offset=None, compute_op=ALU.add).then_inc(added, 16)
                    pool.wait_ge(added, e * 16 + 16)
                    pool.sem_inc(s["ye_free"], 1)
                pool.wait_ge(xs_in, 16 * (E1 + 1))

            @block.tensor
            def _(pe):
                def take_tokens(e):
                    pe.wait_ge(xs_in, e * 16 + 16)
                    for k in range(KD):
                        ins = nc.tensor.transpose(bank[k // 4][:, (k % 4) * P:(k % 4 + 1) * P], xs[:, k * P:(k + 1) * P], ident)
                        if k % 4 == 3:
                            ins.then_inc(s["x_tr"], 1)

                take_tokens(0)
                with pe.Fori(0, E1) as e:
                    pe.wait_ge(s["xT_ev"], e * 2 + 2)
                    for i in range(4):
                        pe.wait_ge(w_in[i], e * 16 + 16)
                        wi = w[:, i].rearrange("p (k n) -> p k n", k=8)
                        for k in range(KD):
                            last = nc.tensor.matmul(bank[i][:, :], xT[:, k, :], wi[:, k, :], start=(k == 0), stop=(k == KD - 1))
                        last.then_inc(s["gu_mm"], 1)
                    for half in range(2):
                        pe.wait_ge(s["hid_ready"], e * 2 + (half + 1))
                        for j in range(4):
                            ins = nc.tensor.transpose(bank[4 + half][:, j * P:(j + 1) * P], hid[:, half, j * P:(j + 1) * P], ident)
                        ins.then_inc(s["h_tr"], 1)
                        if half == 0:
                            take_tokens(e + 1)
                        pe.wait_ge(s["hT_ev"], e * 2 + (half + 1))
                        pe.wait_ge(w_in[4 + half], e * 16 + 16)
                        if half == 0:
                            pe.wait_ge(s["ye_ready"], e * 2 + 1)
                        wi = w[:, 4 + half].rearrange("p (k n) -> p k n", k=4)
                        for c in range(2):
                            for j in range(4):
                                last = nc.tensor.matmul(bank[6 + c][:, :], hidT[:, 4 * half + j, :], wi[:, j, c * BANK:(c + 1) * BANK],
                                                        start=(half == 0 and j == 0), stop=(half == 1 and j == 3),
                                                        skip_group_check=True)
                        last.then_inc(s["y_mm"], 1)

            @block.scalar
            def _(act):
                def xT_evac(e):
                    for i in range(2):
                        act.wait_ge(s["x_tr"], e * 2 + (i + 1))
                        nc.scalar.activation(xT[:, 4 * i:4 * i + 4, :].rearrange("p k t -> p (k t)"), bank[i][:, :], ACT.Copy)\
                            .then_inc(s["xT_ev"], 1)

                xT_evac(0)
                with act.Fori(0, E1) as e:
                    for half in range(2):
                        act.wait_ge(s["gu_mm"], e * 4 + (2 * half + 1))
                        nc.scalar.activation(sg[:, half, :], bank[2 * half][:, :], ACT.Silu).then_inc(s["sg_ready"], 1)
                    xT_evac(e + 1)

            @block.vector
            def _(dve):
                dve.sem_inc(s["ye_ready"], 1)
                with dve.Fori(0, E1) as e:
                    for half in range(2):
                        dve.wait_ge(s["sg_ready"], e * 2 + (half + 1))
                        dve.wait_ge(s["gu_mm"], e * 4 + (2 * half + 2))
                        nc.vector.tensor_tensor(hid[:, half, :], sg[:, half, :], bank[2 * half + 1][:, :], ALU.mult)\
                            .then_inc(s["hid_ready"], 1)
                    for half in range(2):
                        dve.wait_ge(s["h_tr"], e * 2 + (half + 1))
                        nc.vector.tensor_copy(hidT[:, 4 * half:4 * half + 4, :].rearrange("p k t -> p (k t)"), bank[4 + half][:, :])\
                            .then_inc(s["hT_ev"], 1)
                    dve.wait_ge(s["y_mm"], e * 2 + 2)
                    dve.wait_ge(s["ye_free"], e + 1)
                    for c in range(2):
                        nc.vector.tensor_scalar(ye[:, c * BANK:(c + 1) * BANK], bank[6 + c][:, :], gates[:, ds(e, 1)], None,
                                                ALU.mult).then_inc(s["ye_ready"], 1)


def load_T(nc, name, src, dst, tiles=KD):
    with Stage(nc, name) as st:
        loaded = st.sem("loaded")
        with nc.Block() as block:
            @block.sync
            def _(sp):
                for k in range(tiles):
                    sp.dma_start(dst[:, k, :], src[k * P:(k + 1) * P, :]).then_inc(loaded, 16)
                sp.wait_ge(loaded, 16 * tiles)


LAMBDA_INIT = 0.8 - 0.6 * math.exp(-0.3 * 0)


TWO_PI_HI, TWO_PI_MID = 6.28125, 0.00193500518798828125
TWO_PI_LO = 2 * math.pi - TWO_PI_HI - TWO_PI_MID
ROUND = 1.5 * 2.0 ** 23
PI_BELOW = 3.1415925


def qkv_and_lru(nc, bank, cst, col, x, hT, uT, gT, qkT, v_rows):
    STEPS = 3 * NT
    NQK = 2 * NT
    MAPS = D // HD2
    w_in2 = x["w_in_2"][0]
    with Stage(nc, "qkv") as st:
        w = st.sb("w", [P, 2, KD, D])
        sq = st.sb("sq", [P, D])
        y = st.sb("y", [P, 2, D])
        yT = st.sb("yT", [P, 2, KD, P])
        ss = st.sb("ss", [P, 2, 3, MAPS])
        gain = st.sb("gain", [P, 2, HD2])
        pos = st.sb("pos", [P, NT], I32)
        rt = st.sb("rt", [P, 4, NT, 8])
        cos2, sin2 = st.sb("cos2", [P, NT, 2, 8]), st.sb("sin2", [P, NT, 2, 8])
        ro = st.sb("ro", [P, MAPS, 2, 8])
        s = {n: st.sem(n) for n in ("tab_in", "head", "sin", "mm", "squared", "stats", "ms", "root", "scaled", "gained",
                                    "rope", "roped", "tr", "evA", "evD", "vA", "vD")}
        w_in = [st.sem(f"w_in{i}") for i in range(6)]
        stored = [st.sem(f"stored{i}") for i in range(2)]
        ident = cst[:, CONST["ident"]:CONST["ident"] + P]

        lx = st.sb("lx", [P, T + 4])
        lgate, lw = st.sb("lgate", [P, T]), st.sb("lw", [P, 2, P])
        pc, sp4 = st.sb("pc", [P, 3, KD]), st.sb("sp4", [P, 4, KD])
        xc, r, i_, a, t, u, h = (st.sb(n, [P, T]) for n in ("xc", "r", "i", "a", "t", "u", "h"))
        l = {n: st.sem("l_" + n) for n in ("zeroed", "x_in", "w_in", "g_in", "head", "head_act", "hc", "chain", "xc", "r_mm",
                                           "i_mm", "r", "i", "t", "a", "u", "root", "ix", "gelu", "out", "stored")}
        c = lambda name, at: col[:, COLS[name] + at:COLS[name] + at + 1]
        wa, wx = x["lru_wa_2"][0], x["lru_wx_2"][0]

        with nc.Block() as block:
            @block.sync
            def _(sp):
                def load_w(m, c_):
                    src = w_in2[:, (2 + m) * D + c_ * BANK:(2 + m) * D + (c_ + 1) * BANK].rearrange("(k p) n -> p k n", p=P)
                    sp.dma_start(w[:, m % 2, :, c_ * BANK:(c_ + 1) * BANK], src).then_inc(w_in[2 * m + c_], 16)

                def load_block(b, what):
                    rows = slice(b * P, (b + 1) * P)
                    if what == "x":
                        sp.dma_start(lx[:, 4:], uT[rows, :]).then_inc(l["x_in"], 16)
                    elif what == "w":
                        for n, src in enumerate((wa, wx)):
                            sp.dma_start(lw[:, n, :], src[b]).then_inc(l["w_in"], 16)
                    else:
                        sp.dma_start(lgate[:, :], uT[D + b * P:D + (b + 1) * P, :]).then_inc(l["g_in"], 16)

                load_w(0, 0)
                with nc.allow_non_contiguous_dma("positions by tokens"):
                    sp.dma_start(pos[:, :], x["positions_2"].rearrange("o (n p) -> p (o n)", p=P)).then_inc(s["tab_in"], 16)
                for n, name in enumerate(("q_norm_2", "k_norm_2")):
                    sp.dma_start(gain[:, n, :], x[name].partition_broadcast(P)
                                 .rearrange("p o d -> p (o d)")).then_inc(s["tab_in"], 16)
                load_w(0, 1)
                sp.wait_ge(l["zeroed"], 1)
                for what in ("x", "w", "gate"):
                    load_block(0, what)
                load_w(1, 0)
                load_w(1, 1)
                for n in range(STEPS + 1):
                    b = n // 3
                    if n % 3 == 0 and b:
                        sp.wait_ge(l["out"], b)
                        sp.dma_start(gT[(b - 1) * P:b * P, :], h[:, :]).then_inc(l["stored"], 16)
                        if b < KD:
                            load_block(b, "gate")
                    if n % 3 == 0 and b + 1 < KD:
                        sp.wait_ge(l["xc"], b + 1)
                        load_block(b + 1, "x")
                    if n % 3 == 0 and 0 < b < KD:
                        sp.wait_ge(l["i_mm"], b)
                        load_block(b, "w")
                    if n >= 1:
                        j = n - 1
                        m, i = j // NT, j % NT
                        if j < NQK:
                            sp.wait_ge(s["evA"], j + 1)
                            sp.wait_ge(s["evD"], j + 1)
                            sp.dma_start(qkT[m].rearrange("(k p) t -> p k t", p=P)[:, :, i * P:(i + 1) * P], yT[:, j % 2])\
                                .then_inc(stored[j % 2], 16)
                        else:
                            sp.wait_ge(s["vA"], j - NQK + 1)
                            sp.wait_ge(s["vD"], j - NQK + 1)
                            sp.dma_start(v_rows[i * P:(i + 1) * P, :], y[:, j % 2, :]).then_inc(stored[j % 2], 16)
                    if n == NT:
                        for c_ in range(2):
                            load_w(2, c_)
                for i in range(2):
                    sp.wait_ge(stored[i], 16 * (STEPS // 2))
                sp.wait_ge(l["stored"], 16 * KD)

            @block.tensor
            def _(pe):
                def products(n):
                    m, i = n // NT, n % NT
                    j = n - 2
                    if 0 <= j < NQK:
                        pe.wait_ge(s["scaled"], j + 1)
                    elif j >= NQK:
                        pe.wait_ge(s["vA"], j - NQK + 1)
                        pe.wait_ge(s["vD"], j - NQK + 1)
                    for c_ in range(2):
                        if i == 0:
                            pe.wait_ge(w_in[2 * m + c_], 16)
                        for k in range(KD):
                            last = nc.tensor.matmul(bank[2 * (n % 2) + c_][:, :], hT[:, k, i * P:(i + 1) * P],
                                                    w[:, m % 2, k, c_ * BANK:(c_ + 1) * BANK], start=(k == 0), stop=(k == KD - 1))
                    last.then_inc(s["mm"], 1)

                def turn(n):
                    pe.wait_ge(s["roped"], n + 1)
                    if n:
                        pe.wait_ge(s["evA"], n)
                        pe.wait_ge(s["evD"], n)
                    for k in range(KD):
                        ins = nc.tensor.transpose(bank[6 + k // 4][:, (k % 4) * P:(k % 4 + 1) * P], y[:, n % 2, k * P:(k + 1) * P],
                                                  ident)
                    ins.then_inc(s["tr"], 1)

                def gate(b, m):
                    if m == 0:
                        pe.wait_ge(l["w_in"], 32 * (b + 1))
                        pe.wait_ge(l["xc"], b + 1)
                        if b:
                            pe.wait_ge(l["i"], b)
                    else:
                        pe.wait_ge(l["r"], b + 1)
                    for c_ in range(2):
                        ins = nc.tensor.matmul(bank[4 + c_][:, :], lw[:, m, :], xc[:, c_ * BANK:(c_ + 1) * BANK], start=True, stop=True)
                    ins.then_inc(l["i_mm" if m else "r_mm"], 1)

                for n in range(STEPS):
                    products(n)
                    if n % 3:
                        gate(n // 3, n % 3 - 1)
                    if 1 <= n <= NQK:
                        turn(n - 1)

            @block.scalar
            def _(act):
                def halves(n, fn, out, sem):
                    for c_ in range(2):
                        ins = fn(c_)
                    ins.then_inc(sem, 1)

                act.wait_ge(l["head"], 1)
                nc.scalar.activation(sp4[:, 1, :], sp4[:, 0, :], ACT.Exp, scale=-1.0).then_inc(l["head_act"], 1)
                act.wait_ge(l["head"], 2)
                nc.scalar.activation(sp4[:, 0, :], sp4[:, 2, :], ACT.Ln).then_inc(l["head_act"], 1)
                act.wait_ge(s["head"], 1)
                nc.scalar.activation(rt[:, 3], rt[:, 1], ACT.Sin).then_inc(s["sin"], 1)
                act.wait_ge(s["head"], 2)
                nc.scalar.activation(rt[:, 2], rt[:, 0], ACT.Sin).then_inc(s["sin"], 1)
                act.wait_ge(l["head"], 3)

                def square(n):
                    act.wait_ge(s["mm"], n + 1)
                    if n:
                        act.wait_ge(s["ms"], n)
                    for c_ in range(2):
                        ins = nc.scalar.activation(sq[:, c_ * BANK:(c_ + 1) * BANK], bank[2 * (n % 2) + c_][:, :], ACT.Square)
                    ins.then_inc(s["squared"], 1)

                def root(n):
                    act.wait_ge(s["ms"], n + 1)
                    nc.scalar.activation(ss[:, n % 2, 1, :], ss[:, n % 2, 0, :], ACT.Sqrt).then_inc(s["root"], 1)

                def turned(n):
                    act.wait_ge(s["tr"], n + 1)
                    if n >= 2:
                        act.wait_ge(stored[n % 2], 16 * (n // 2))
                    nc.scalar.activation(yT[:, n % 2, 0:4, :].rearrange("p k t -> p (k t)"), bank[6][:, :], ACT.Copy)\
                        .then_inc(s["evA"], 1)

                def values(n):
                    act.wait_ge(s["mm"], n + 1)
                    if n >= NQK + 2:
                        act.wait_ge(stored[n % 2], 16 * (n // 2))
                    else:
                        act.wait_ge(s["tr"], n - 1)
                    nc.scalar.activation(y[:, n % 2, 0:BANK], bank[2 * (n % 2)][:, :], ACT.Copy).then_inc(s["vA"], 1)

                def sigmoid(b, m):
                    act.wait_ge(l["i_mm" if m else "r_mm"], b + 1)
                    if b and m:
                        act.wait_ge(l["u"], b)
                    for c_ in range(2):
                        ins = nc.scalar.activation((i_ if m else r)[:, c_ * BANK:(c_ + 1) * BANK], bank[4 + c_][:, :], ACT.Sigmoid,
                                                   bias=c("bx" if m else "ba", b))
                    ins.then_inc(l["i" if m else "r"], 1)

                def decay(b):
                    act.wait_ge(l["r"], b + 1)
                    if b:
                        act.wait_ge(l["out"], b)
                    nc.scalar.activation(t[:, :], r[:, :], ACT.Tanh, scale=pc[:, 0, b:b + 1]).then_inc(l["t"], 1)
                    nc.scalar.activation(a[:, :], r[:, :], ACT.Exp, scale=pc[:, 1, b:b + 1]).then_inc(l["a"], 1)

                for n in range(STEPS):
                    if n < NQK:
                        square(n)
                        root(n)
                    else:
                        values(n)
                    b = n // 3
                    if n % 3 == 1:
                        sigmoid(b, 0)
                        decay(b)
                    elif n % 3 == 2:
                        act.wait_ge(l["u"], b + 1)
                        nc.scalar.activation(u[:, :], u[:, :], ACT.Sqrt).then_inc(l["root"], 1)
                        sigmoid(b, 1)
                        act.wait_ge(l["g_in"], 16 * (b + 1))
                        nc.scalar.activation(lgate[:, :], lgate[:, :], ACT.Gelu_apprx_tanh).then_inc(l["gelu"], 1)
                    if 1 <= n <= NQK:
                        turned(n - 1)

            @block.gpsimd
            def _(pool):
                nc.gpsimd.memset(lx[:, 0:4], 0.0).then_inc(l["zeroed"], 1)
                link = Steps(s["rope"])
                pool.wait_ge(s["head"], 4)

                def maps(n):
                    return y[:, n % 2, :].rearrange("p (m d) -> p m d", d=HD2)

                def rotate(n):
                    i, yn = n % NT, maps(n)
                    pool.wait_ge(s["scaled"], n + 1)
                    nc.gpsimd.tensor_tensor(yn, yn, gain[:, n // NT, :].unsqueeze(1).to_broadcast([P, MAPS, HD2]), ALU.mult)\
                        .then_inc(s["gained"], 1)
                    pool.wait_ge(s["gained"], n + 1)
                    half = yn[:, :, 0:16].rearrange("p m (h e) -> p m h e", h=2)
                    for k in range(2):
                        last = link(nc.gpsimd.tensor_tensor(ro[:, :, k, :], half[:, :, 1 - k, :],
                                                            sin2[:, i, k, :].unsqueeze(1).to_broadcast([P, MAPS, 8]), ALU.mult))
                    pool.wait_ge(s["rope"], last)
                    pool.wait_ge(s["rope"], link(nc.gpsimd.tensor_tensor(
                        yn[:, :, 0:16], yn[:, :, 0:16],
                        cos2[:, i].rearrange("p h e -> p (h e)").unsqueeze(1).to_broadcast([P, MAPS, 16]), ALU.mult)))
                    nc.gpsimd.tensor_tensor(yn[:, :, 0:16], yn[:, :, 0:16], ro[:, :, :, :].rearrange("p m h e -> p m (h e)"), ALU.add)\
                        .then_inc(s["roped"], 1)

                def gated_x(b):
                    pool.wait_ge(l["i"], b + 1)
                    nc.gpsimd.tensor_tensor(i_[:, :], i_[:, :], xc[:, :], ALU.mult).then_inc(l["ix"], 1)

                for n in range(STEPS + 1):
                    if n % 3 == 0 and n:
                        gated_x(n // 3 - 1)
                    if n < NQK:
                        rotate(n)

            @block.vector
            def _(dve):
                V = nc.vector
                head = Steps(l["hc"])

                def step(ins):
                    dve.wait_ge(l["hc"], head(ins))

                lam = col[:, COLS["lam"]:COLS["lam"] + KD]
                step(V.tensor_scalar(sp4[:, 2, :], lam, -1.0, None, ALU.mult))
                step(V.tensor_scalar(sp4[:, 3, :], sp4[:, 2, :], 0.0, None, ALU.max))
                V.tensor_tensor(sp4[:, 0, :], lam, sp4[:, 2, :], ALU.max).then_inc(l["head"], 1)
                dve.wait_ge(l["head_act"], 1)
                V.tensor_scalar(sp4[:, 2, :], sp4[:, 1, :], 1.0, None, ALU.add).then_inc(l["head"], 1)
                dve.wait_ge(l["head_act"], 2)
                step(V.tensor_scalar(pc[:, 2, :], sp4[:, 2, :], 1.0, None, ALU.is_equal))
                step(V.tensor_tensor(sp4[:, 0, :], sp4[:, 0, :], pc[:, 2, :], ALU.add))
                step(V.scalar_tensor_tensor(pc[:, 2, :], sp4[:, 2, :], -1.0, pc[:, 2, :], ALU.add, ALU.add))
                step(V.reciprocal(pc[:, 2, :], pc[:, 2, :]))
                step(V.tensor_tensor(sp4[:, 0, :], sp4[:, 0, :], sp4[:, 1, :], ALU.mult))
                step(V.tensor_tensor(sp4[:, 0, :], sp4[:, 0, :], pc[:, 2, :], ALU.mult))
                step(V.tensor_tensor(sp4[:, 0, :], sp4[:, 0, :], sp4[:, 3, :], ALU.add))
                step(V.tensor_scalar(pc[:, 0, :], sp4[:, 0, :], 8.0, None, ALU.mult))
                step(V.tensor_scalar(pc[:, 1, :], sp4[:, 0, :], -8.0, None, ALU.mult))
                dve.wait_ge(s["tab_in"], 48)
                ang, turns = rt[:, 0], rt[:, 1]
                step(V.tensor_copy(rt[:, 2, :, 0], pos[:, :]))
                step(V.tensor_tensor(ang, rt[:, 2, :, 0].unsqueeze(2).to_broadcast([P, NT, 8]),
                                     cst[:, CONST["invf"]:CONST["invf"] + 8].unsqueeze(1).to_broadcast([P, NT, 8]), ALU.mult))
                step(V.tensor_scalar(turns, ang, 1.0 / (2 * math.pi), ROUND, ALU.mult, ALU.add))
                step(V.tensor_scalar(turns, turns, -ROUND, None, ALU.add))
                for part in (TWO_PI_HI, TWO_PI_MID, TWO_PI_LO):
                    step(V.scalar_tensor_tensor(ang, turns, -part, ang, ALU.mult, ALU.add))
                V.tensor_scalar(turns, ang, PI_BELOW, -PI_BELOW, ALU.min, ALU.max).then_inc(s["head"], 1)
                step(V.tensor_scalar(rt[:, 2], ang, -1.0, None, ALU.mult))
                step(V.tensor_tensor(ang, ang, rt[:, 2], ALU.max))
                V.tensor_scalar(ang, ang, -1.0, math.pi / 2, ALU.mult, ALU.add).then_inc(s["head"], 1)
                dve.wait_ge(s["sin"], 2)
                for k in range(2):
                    step(V.tensor_copy(cos2[:, :, k, :], rt[:, 2]))
                    step(V.tensor_scalar(sin2[:, :, k, :], rt[:, 3], 2.0 * k - 1.0, None, ALU.mult))
                V.tensor_scalar(gain[:, 0, :], gain[:, 0, :], HD2 ** -0.5, None, ALU.mult).then_inc(s["head"], 2)
                V.memset(rt[:, 2, 0, 0:1], 0.0).then_inc(l["head"], 1)
                link, stats = Steps(l["chain"]), Steps(s["stats"])

                def lstep(ins):
                    dve.wait_ge(l["chain"], link(ins))

                def convolve(b):
                    dve.wait_ge(l["x_in"], 16 * (b + 1))
                    if b:
                        dve.wait_ge(l["ix"], b)
                    for tap in range(4):
                        src = lx[:, 1 + tap:1 + tap + T]
                        if tap == 0:
                            lstep(V.tensor_scalar(xc[:, :], src, c("conv2", b), c("conv2b", b), ALU.mult, ALU.add))
                        else:
                            ins = V.scalar_tensor_tensor(xc[:, :], src, c("conv2", b + 8 * tap), xc[:, :], ALU.mult, ALU.add)
                            if tap < 3:
                                lstep(ins)
                    ins.then_inc(l["xc"], 1)

                def input_scale(b):
                    dve.wait_ge(l["t"], b + 1)
                    lstep(V.tensor_scalar(u[:, :], t[:, :], 1.0, None, ALU.add))
                    lstep(V.reciprocal(u[:, :], u[:, :]))
                    V.scalar_tensor_tensor(u[:, :], t[:, :], 2.0, u[:, :], ALU.mult, ALU.mult).then_inc(l["u"], 1)

                def recur(b):
                    dve.wait_ge(l["root"], b + 1)
                    dve.wait_ge(l["ix"], b + 1)
                    lstep(V.tensor_tensor(u[:, :], u[:, :], i_[:, :], ALU.mult))
                    dve.wait_ge(l["a"], b + 1)
                    if b:
                        dve.wait_ge(l["stored"], 16 * b)
                    lstep(V.tensor_tensor_scan(h[:, :], a[:, :], u[:, :], 0.0, ALU.mult, ALU.add))
                    dve.wait_ge(l["gelu"], b + 1)
                    V.tensor_tensor(h[:, :], h[:, :], lgate[:, :], ALU.mult).then_inc(l["out"], 1)

                def scale(n):
                    sn = ss[:, n % 2]
                    dve.wait_ge(s["squared"], n + 1)
                    dve.wait_ge(s["stats"], stats(V.tensor_reduce(sn[:, 0, :], sq[:, :].rearrange("p (m d) -> p m d", d=HD2), AX_X,
                                                                  ALU.add)))
                    V.tensor_scalar(sn[:, 0, :], sn[:, 0, :], 1.0 / HD2, EPS, ALU.mult, ALU.add).then_inc(s["ms"], 1)
                    dve.wait_ge(s["root"], n + 1)
                    dve.wait_ge(s["stats"], stats(V.reciprocal(sn[:, 2, :], sn[:, 1, :])))
                    if n >= 2:
                        dve.wait_ge(s["tr"], n - 1)
                    m = MAPS // 2
                    for c_ in range(2):
                        ins = V.tensor_tensor(y[:, n % 2, c_ * BANK:(c_ + 1) * BANK].rearrange("p (m d) -> p m d", d=HD2),
                                              bank[2 * (n % 2) + c_][:, :].rearrange("p (m d) -> p m d", d=HD2),
                                              sn[:, 2, c_ * m:(c_ + 1) * m].unsqueeze(2).to_broadcast([P, m, HD2]), ALU.mult)
                    ins.then_inc(s["scaled"], 1)

                def turned(n):
                    dve.wait_ge(s["tr"], n + 1)
                    if n >= 2:
                        dve.wait_ge(stored[n % 2], 16 * (n // 2))
                    V.tensor_copy(yT[:, n % 2, 4:8, :].rearrange("p k t -> p (k t)"), bank[7][:, :]).then_inc(s["evD"], 1)

                def values(n):
                    dve.wait_ge(s["mm"], n + 1)
                    if n >= NQK + 2:
                        dve.wait_ge(stored[n % 2], 16 * (n // 2))
                    else:
                        dve.wait_ge(s["tr"], n - 1)
                    V.tensor_copy(y[:, n % 2, BANK:], bank[2 * (n % 2) + 1][:, :]).then_inc(s["vD"], 1)

                for n in range(STEPS + 1):
                    b = n // 3
                    if n % 3 == 0 and b:
                        recur(b - 1)
                    if n % 3 == 0 and b < KD:
                        convolve(b)
                    if n % 3 == 2:
                        input_scale(b)
                    if n < NQK:
                        scale(n)
                    elif n < STEPS:
                        values(n)
                    if 1 <= n <= NQK:
                        turned(n - 1)


def diff_attention(nc, bank, cst, col, x, qkT, v_rows, oT):
    J = 2 * NT
    with Stage(nc, "attn") as st:
        q = st.sb("q", [P, 2, T])
        kz = st.sb("kz", [P, 2, 2, T])
        v = st.sb("v", [P, 2, NT, P])
        lv = st.sb("lv", [P, 4, HD2])
        lp = st.sb("lp", [P, 2, HD2])
        lm = st.sb("lm", [P, 8])
        sub = st.sb("sub", [P, 1])
        e = st.sb("e", [P, 2, 2, T])
        sm = st.sb("sm", [P, 2, 2, 8])
        w = st.sb("w", [P, 2, T])
        wT = st.sb("wT", [P, 2, NT, P])
        o, rs = st.sb("o", [P, 2, T]), st.sb("rs", [P, 2, T])
        names = ("zeroed", "lam_in", "lam", "lam_exp", "ready", "s_mm", "chain", "nm", "exp", "scaled", "rec", "w_ready",
                 "trA", "trB", "evA", "evB", "o_mm", "o_ev", "squared", "sums", "ms", "root", "out")
        s = {n: st.sem(n) for n in names}
        qkv_in = [st.sem(f"qkv_in{k}") for k in range(2)]
        stored = [st.sem(f"stored{k}") for k in range(2)]
        ident, ones = (cst[:, CONST[n]:CONST[n] + P] for n in ("ident", "ones"))
        TURNS = HEADS2 // 2
        LOADS = 4 * 16
        late = lambda j: (j // NT) * 4 + j % NT - 3

        def banks(i):
            n = (i + 1) * P
            return [(0, 0, min(n, BANK))] + ([(1, BANK, n)] if n > BANK else [])

        with nc.Block() as block:
            @block.sync
            def _(sp):
                for n, name in enumerate(("lambda_q1_2", "lambda_k1_2", "lambda_q2_2", "lambda_k2_2")):
                    sp.dma_start(lv[:, n, :], x[name].partition_broadcast(P).rearrange("p o d -> p (o d)")).then_inc(s["lam_in"], 16)

                def load(it, k):
                    rows = ds(it * (2 * P) + k * P, P)
                    sp.dma_start(q[:, k, :], qkT[0, rows, :]).then_inc(qkv_in[k], 16)
                    for m in range(2):
                        sp.dma_start(kz[64 * m:64 * m + 64, k, m, :], qkT[1, ds(it * (2 * P) + (k * P + 64 * m), 64), :])\
                            .then_inc(qkv_in[k], 16)
                    sp.dma_start(v[:, k, :, :], v_rows[:, rows].rearrange("(n p) d -> p n d", p=P)).then_inc(qkv_in[k], 16)

                def store(it, k):
                    sp.wait_ge(s["out"], it * 2 + (k + 1))
                    sp.dma_start(oT[ds(it * (2 * P) + k * P, P), :], o[:, k, :]).then_inc(stored[k], 16)

                for k in range(2):
                    sp.sem_inc(stored[k], 1)
                sp.wait_ge(s["zeroed"], 1)
                load(0, 0)
                load(0, 1)
                with sp.Fori(0, TURNS - 1) as it:
                    for k in range(2):
                        sp.wait_ge(s["o_mm"], it * J + NT * (k + 1))
                        load(it + 1, k)
                        store(it, k)
                for k in range(2):
                    store(TURNS - 1, k)
                    sp.wait_ge(stored[k], 16 * TURNS + 1)

            @block.gpsimd
            def _(pool):
                nc.gpsimd.memset(kz[:, :, :, :], 0.0).then_inc(s["zeroed"], 1)
                with pool.Fori(0, TURNS) as it:
                    for j in range(J):
                        i = j % NT
                        pool.wait_ge(s["rec"], it * J + (j + 1))
                        pool.sem_inc(s["ready"], 1)
                        nc.gpsimd.tensor_scalar(e[:, j % 2, 0, 0:(i + 1) * P], e[:, j % 2, 0, 0:(i + 1) * P],
                                                sm[:, j % 2, 0, 6:7], None, ALU.mult).then_inc(s["scaled"], 1)

            @block.tensor
            def _(pe):
                with pe.Fori(0, TURNS) as it:
                    def scores(j):
                        i, k = j % NT, j // NT
                        if i == 0:
                            pe.wait_ge(qkv_in[k], it * LOADS + LOADS)
                        for m in range(2):
                            if j:
                                pe.wait_ge(s["exp"], it * (2 * J) + (2 * (j - 1) + m + 1))
                            for b, c0, c1 in banks(i):
                                ins = nc.tensor.matmul(bank[2 * m + b][:, 0:c1 - c0], q[:, k, i * P:(i + 1) * P],
                                                       kz[:, k, m, c0:c1], start=True, stop=True)
                            ins.then_inc(s["s_mm"], 1)

                    def turn(j):
                        i = j % NT
                        pe.wait_ge(s["w_ready"], it * J + (j + 1))
                        for b, c0, c1 in banks(i):
                            for t in range(c0 // P, c1 // P):
                                ins = nc.tensor.transpose(bank[4 + b][:, (t % 4) * P:(t % 4 + 1) * P], w[:, j % 2, t * P:(t + 1) * P],
                                                          ident)
                            ins.then_inc(s["trB" if b else "trA"], 1)

                    def values(j):
                        i, k = j % NT, j // NT
                        if j >= 2:
                            pe.wait_ge(s["o_ev"], it * J + (j - 1))
                        if j == NT + 1:
                            pe.wait_ge(s["ms"], it * 2 + 1)
                        for t in range(i + 1):
                            if t % 4 == 0:
                                pe.wait_ge(*((s["evB"], it * 8 + late(j)) if t else (s["evA"], it * J + (j + 1))))
                            ins = nc.tensor.matmul(bank[6 + j % 2][:, 0:P], v[:, k, t, :], wT[:, j % 2, t, :],
                                                   start=(t == 0), stop=(t == i))
                        ins.then_inc(s["o_mm"], 1)

                    def sums(k, j):
                        pe.wait_ge(s["squared"], it * 2 + (k + 1))
                        pe.wait_ge(s["o_ev"], it * J + (j + 1))
                        for b in range(2):
                            ins = nc.tensor.matmul(bank[6 + b][:, :], ones, rs[:, k, b * BANK:(b + 1) * BANK], start=True, stop=True)
                        ins.then_inc(s["sums"], 1)

                    for j in range(J + 2):
                        if j >= 2:
                            turn(j - 2)
                        if j < J:
                            scores(j)
                        if j >= 2:
                            values(j - 2)
                        if j == NT + 2:
                            sums(0, NT)
                    sums(1, J - 1)

            @block.scalar
            def _(act):
                act.wait_ge(s["lam"], 1)
                nc.scalar.activation(lm[:, 2:4], lm[:, 0:2], ACT.Exp).then_inc(s["lam_exp"], 1)
                with act.Fori(0, TURNS) as it:
                    def evacuate(j):
                        i, k = j % NT, j // NT
                        n = min((i + 1) * P, BANK)
                        act.wait_ge(s["trA"], it * J + (j + 1))
                        nc.scalar.activation(wT[:, j % 2, 0:4, :].rearrange("p n d -> p (n d)")[:, 0:n], bank[4][:, 0:n], ACT.Copy)\
                            .then_inc(s["evA"], 1)

                    def result(j):
                        i, k = j % NT, j // NT
                        act.wait_ge(s["o_mm"], it * J + (j + 1))
                        if i == 0:
                            act.wait_ge(stored[k], it * 16 + 1)
                        nc.scalar.activation(o[:, k, i * P:(i + 1) * P], bank[6 + j % 2][:, 0:P], ACT.Copy).then_inc(s["o_ev"], 1)

                    def exponentials(j):
                        i = j % NT
                        if j >= 2:
                            act.wait_ge(s["w_ready"], it * J + (j - 1))
                        for m in range(2):
                            act.wait_ge(s["nm"], it * (2 * J) + (2 * j + m + 1))
                            for b, c0, c1 in banks(i):
                                ins = nc.scalar.activation(e[:, j % 2, m, c0:c1], bank[2 * m + b][:, 0:c1 - c0], ACT.Exp,
                                                           bias=sm[:, j % 2, m, 2:3], accum_out=sm[:, j % 2, m, 3 + b:4 + b])
                            ins.then_inc(s["exp"], 1)

                    def square(k):
                        act.wait_ge(s["o_ev"], it * J + (k + 1) * NT)
                        nc.scalar.activation(rs[:, k, :], o[:, k, :], ACT.Square).then_inc(s["squared"], 1)

                    def root(k):
                        act.wait_ge(s["ms"], it * 2 + (k + 1))
                        nc.scalar.activation(rs[:, k, :], rs[:, k, :], ACT.Sqrt).then_inc(s["root"], 1)

                    for j in range(J + 2):
                        if j >= 2:
                            evacuate(j - 2)
                        if j < J:
                            exponentials(j)
                        if j >= 2:
                            result(j - 2)
                        if j == NT + 1:
                            square(0)
                        if j == NT + 3:
                            root(0)
                    square(1)
                    root(1)

            @block.vector
            def _(dve):
                head = Steps(s["chain"])
                dve.wait_ge(s["lam_in"], 64)
                for n in range(2):
                    dve.wait_ge(s["chain"], head(nc.vector.tensor_tensor(lp[:, n, :], lv[:, 2 * n, :], lv[:, 2 * n + 1, :], ALU.mult)))
                nc.vector.tensor_reduce(lm[:, 0:2], lp[:, :, :], AX_X, ALU.add).then_inc(s["lam"], 1)
                dve.wait_ge(s["lam_exp"], 1)
                dve.wait_ge(s["chain"], head(nc.vector.tensor_tensor(lm[:, 4:5], lm[:, 2:3], lm[:, 3:4], ALU.subtract)))
                dve.wait_ge(s["chain"], head(nc.vector.tensor_scalar(lm[:, 5:6], lm[:, 4:5], LAMBDA_INIT, -1.0, ALU.add, ALU.mult)))
                dve.wait_ge(s["chain"], head(nc.vector.tensor_scalar(sub[:, :], col[:, COLS["subln"]:COLS["subln"] + 1],
                                                                     1.0 - LAMBDA_INIT, None, ALU.mult)))
                base = head.n
                per_tile = lambda i: 2 * (2 + (i >= 4)) + 1 + (i >= 4)
                CHAIN = 2 * sum(per_tile(i) for i in range(NT)) + 2
                with dve.Fori(0, TURNS) as it:
                    class Link(Loop):
                        def __call__(self, ins):
                            return Loop.__call__(self, ins) + base
                    link = Link(s["chain"], it, CHAIN)

                    def wait(n):
                        dve.wait_ge(s["chain"], n)

                    def maxima(j):
                        i = j % NT
                        for m in range(2):
                            c = sm[:, j % 2, m]
                            dve.wait_ge(s["s_mm"], it * (2 * J) + (2 * j + m + 1))
                            d = i % 4 * P
                            wait(link(nc.vector.memset(bank[2 * m + i // 4][0:CHUNK2, d + CHUNK2:d + P], -1e30)))
                            for b, c0, c1 in banks(i):
                                n = link(nc.vector.tensor_reduce(c[:, b:b + 1], bank[2 * m + b][:, 0:c1 - c0], AX_X, ALU.max))
                            wait(n)
                            if i >= 4:
                                nc.vector.tensor_scalar(c[:, 2:3], c[:, 0:1], c[:, 1:2], -1.0, ALU.max, ALU.mult).then_inc(s["nm"], 1)
                            else:
                                nc.vector.tensor_scalar(c[:, 2:3], c[:, 0:1], -1.0, None, ALU.mult).then_inc(s["nm"], 1)

                    def reciprocals(j):
                        i = j % NT
                        both = sm[:, j % 2]
                        dve.wait_ge(s["exp"], it * (2 * J) + 2 * (j + 1))
                        if i >= 4:
                            wait(link(nc.vector.tensor_tensor(both[:, :, 5:6], both[:, :, 3:4], both[:, :, 4:5], ALU.add)))
                        total = 5 if i >= 4 else 3
                        nc.vector.reciprocal(both[:, :, 6:7], both[:, :, total:total + 1]).then_inc(s["rec"], 1)
                        dve.wait_ge(s["rec"], it * J + (j + 1))
                        link(nc.vector.tensor_tensor(both[:, 1, 7:8], both[:, 1, 6:7], lm[:, 5:6], ALU.mult))

                    def weights(j):
                        i = j % NT
                        both = sm[:, j % 2]
                        dve.wait_ge(s["scaled"], it * J + (j + 1))
                        wait(link.base + link.k + base)
                        if j >= 2:
                            dve.wait_ge(s["trA"], it * J + (j - 1))
                        n = (i + 1) * P
                        nc.vector.scalar_tensor_tensor(w[:, j % 2, 0:n], e[:, j % 2, 1, 0:n], both[:, 1, 7:8], e[:, j % 2, 0, 0:n],
                                                       ALU.mult, ALU.add).then_inc(s["w_ready"], 1)

                    def evacuate(j):
                        i = j % NT
                        if i >= 4:
                            n = (i + 1) * P - BANK
                            dve.wait_ge(s["trB"], it * 8 + late(j))
                            nc.vector.tensor_copy(wT[:, j % 2, 4:8, :].rearrange("p n d -> p (n d)")[:, 0:n], bank[5][:, 0:n])\
                                .then_inc(s["evB"], 1)

                    def mean(k):
                        dve.wait_ge(s["sums"], it * 2 + (k + 1))
                        for b in range(2):
                            ins = nc.vector.tensor_scalar(rs[:, k, b * BANK:(b + 1) * BANK], bank[6 + b][:, :], 1.0 / P, EPS,
                                                          ALU.mult, ALU.add)
                        ins.then_inc(s["ms"], 1)

                    def norm(k):
                        dve.wait_ge(s["root"], it * 2 + (k + 1))
                        wait(link(nc.vector.reciprocal(rs[:, k, :], rs[:, k, :])))
                        nc.vector.scalar_tensor_tensor(o[:, k, :], o[:, k, :], sub[:, 0:1], rs[:, k, :], ALU.mult, ALU.mult)\
                            .then_inc(s["out"], 1)

                    for j in range(J + 2):
                        if j >= 2:
                            evacuate(j - 2)
                        if 1 <= j <= J:
                            reciprocals(j - 1)
                        if j < J:
                            maxima(j)
                        if 1 <= j <= J:
                            weights(j - 1)
                        if j == NT + 2:
                            mean(0)
                        if j == NT + 4:
                            norm(0)
                    mean(1)
                    norm(1)
                    link.end()


def mixed_T(nc, bank, w_a, w_b, aT_dram, bT_dram, gates, mT):
    with Stage(nc, "mixed") as st:
        act_T = st.sb("act", [P, 2, KD, T])
        w = st.sb("w", [P, 2, 2, KD, 2 * P])
        g = st.sb("g", [P, 2, 2, T])
        y = st.sb("y", [P, 2, T])
        names = ("mm", "sig", "gated", "done", "ev")
        s = {n: st.sem(n) for n in names}
        a_in = [st.sem(f"a_in{n}") for n in range(2)]
        w_in, g_in = ([st.sem(f"{n}{k}") for k in range(2)] for n in ("w_in", "g_in"))
        TURNS = KD // 4
        with nc.Block() as block:
            @block.sync
            def _(sp):
                def load_w(slot, c0):
                    for n, m in enumerate((w_a, w_b)):
                        sp.dma_start(w[:, slot, n], m[:, ds(c0, 2 * P)].rearrange("(k p) n -> p k n", p=P)).then_inc(w_in[slot], 16)

                load_w(0, 0)
                for n, src in enumerate((aT_dram, bT_dram)):
                    sp.dma_start(act_T[:, n], src.rearrange("(k p) t -> p k t", p=P)).then_inc(a_in[n], 16)
                load_w(1, 2 * P)
                with sp.Fori(0, TURNS - 1) as it:
                    for k in range(2):
                        sp.wait_ge(s["mm"], it * 8 + 4 * (k + 1))
                        load_w(k, it * (4 * P) + ((4 + 2 * k) * P))

            @block.gpsimd
            def _(pool):
                with pool.Fori(0, TURNS) as it:
                    for c in range(4):
                        pool.wait_ge(s["gated"], it * 8 + 2 * (c + 1))
                        nc.gpsimd.tensor_tensor(mT[:, ds(it * 4 + c, 1), :].rearrange("p o t -> p (o t)"), y[:, 0, :], y[:, 1, :],
                                                ALU.add).then_inc(s["done"], 1)

            @block.tensor
            def _(pe):
                pe.wait_ge(a_in[0], 16)
                pe.wait_ge(a_in[1], 16)
                with pe.Fori(0, TURNS) as it:
                    for c in range(4):
                        if c % 2 == 0:
                            pe.wait_ge(w_in[c // 2], it * 32 + 32)
                        for n in range(2):
                            o = bank[4 * (c % 2) + 2 * n:4 * (c % 2) + 2 * n + 2]
                            if c >= 2:
                                pe.wait_ge(s["gated"], it * 8 + (2 * (c - 2) + n + 1))
                            elif c == 0 and n == 0:
                                pe.wait_ge(s["ev"], it * 2 + 1)
                            elif c == 1 and n == 0:
                                pe.wait_ge(s["ev"], it * 2 + 2)
                            for b in range(2):
                                for k in range(KD):
                                    last = nc.tensor.matmul(o[b][:, :], w[:, c // 2, n, k, (c % 2) * P:(c % 2 + 1) * P],
                                                            act_T[:, n, k, b * BANK:(b + 1) * BANK],
                                                            start=(k == 0), stop=(k == KD - 1))
                            last.then_inc(s["mm"], 1)

            @block.scalar
            def _(act):
                act.sem_inc(s["done"], 1)
                with act.Fori(0, TURNS) as it:
                    for c in range(4):
                        slot = c % 2
                        if c >= 2:
                            act.wait_ge(s["gated"], it * 8 + 2 * (c - 1))
                        elif c == 1:
                            act.wait_ge(s["ev"], it * 2 + 2)
                        else:
                            act.wait_ge(s["ev"], it * 2 + 1)
                        for n in range(2):
                            act.dma_start(g[:, slot, n, :], gates[ds(it * (4 * P) + (n * D + c * P), P), :])\
                                .then_inc(g_in[slot], 16)
                        act.wait_ge(g_in[slot], it * 64 + 32 * (c // 2 + 1))
                        nc.scalar.activation(g[:, slot, :, :], g[:, slot, :, :], ACT.Sigmoid).then_inc(s["sig"], 1)

            @block.vector
            def _(dve):
                dve.sem_inc(s["ev"], 2)
                with dve.Fori(0, TURNS) as it:
                    for c in range(4):
                        dve.wait_ge(s["sig"], it * 4 + (c + 1))
                        dve.wait_ge(s["done"], it * 4 + (c + 1))
                        for n in range(2):
                            dve.wait_ge(s["mm"], it * 8 + (2 * c + n + 1))
                            for b in range(2):
                                t = slice(b * BANK, (b + 1) * BANK)
                                ins = nc.vector.tensor_tensor(y[:, n, t], bank[4 * (c % 2) + 2 * n + b][:, :], g[:, c % 2, n, t],
                                                              ALU.mult)
                            ins.then_inc(s["gated"], 1)
                        if c >= 2:
                            dve.wait_ge(s["gated"], it * 8 + 2 * (c + 1))
                            dve.sem_inc(s["ev"], 1)


def cross_attention(nc, bank, cst, col, w_q, w_kv, hT, mT, oT):
    NM = MEM // P
    with Stage(nc, "cross") as st:
        w = st.sb("w", [P, 3, KD, P])
        qk = st.sb("qk", [P, T + MEM])
        sq = st.sb("sq", [P, T + MEM])
        v = st.sb("v", [P, NM, P])
        g2 = st.sb("g2", [P, 2])
        sm = st.sb("sm", [P, NT, 4])
        e = st.sb("e", [P, NT, MEM])
        eT = st.sb("eT", [P, NM, T])
        names = ("proj", "proj_ev", "squared", "sums", "ms", "root", "chain", "head", "normed", "s_mm", "nm", "exp", "p_ready",
                 "tr", "tr_ev", "o_mm", "o_ev")
        s = {n: st.sem(n) for n in names}
        w_in = [st.sem(f"w_in{n}") for n in range(3)]
        ident, ones = (cst[:, CONST[n]:CONST[n] + P] for n in ("ident", "ones"))
        parts = [(0, BANK), (BANK, T), (T, T + MEM)]
        with nc.Block() as block:
            @block.sync
            def _(sp):
                def load(h, n):
                    src = w_q if n == 0 else w_kv
                    c0 = h * P + (MH * P if n == 2 else 0)
                    sp.dma_start(w[:, n], src[:, ds(c0, P)].rearrange("(k p) n -> p k n", p=P)).then_inc(w_in[n], 16)

                for n in range(3):
                    load(0, n)
                with sp.Fori(0, MH - 1) as h:
                    for n in range(3):
                        sp.wait_ge(s["proj"], h * 5 + (2, 3, 5)[n])
                        load(h + 1, n)

            @block.tensor
            def _(pe):
                with pe.Fori(0, MH) as h:
                    for n, (a, b) in enumerate(parts):
                        m = 1 if n == 2 else 0
                        pe.wait_ge(w_in[m], h * 16 + 16)
                        for k in range(KD):
                            rhs = mT[:, k, :] if m else hT[:, k, a:b]
                            last = nc.tensor.matmul(bank[n][:, 0:b - a], w[:, m, k, :], rhs, start=(k == 0), stop=(k == KD - 1))
                        last.then_inc(s["proj"], 1)
                    pe.wait_ge(w_in[2], h * 16 + 16)
                    for t in range(NM):
                        for k in range(KD):
                            last = nc.tensor.matmul(bank[3][:, t * P:(t + 1) * P], mT[:, k, t * P:(t + 1) * P], w[:, 2, k, :],
                                                    start=(k == 0), stop=(k == KD - 1))
                        last.then_inc(s["proj"], 1)
                    for n, (a, b) in enumerate(parts):
                        pe.wait_ge(s["squared"], h * 3 + (n + 1))
                        nc.tensor.matmul(bank[4 + n][:, 0:b - a], ones, sq[:, a:b], start=True, stop=True).then_inc(s["sums"], 1)
                    pe.wait_ge(s["normed"], h * 3 + 3)
                    for i in range(NT):
                        ins = nc.tensor.matmul(bank[i // 2][:, (i % 2) * MEM:(i % 2 + 1) * MEM], qk[:, i * P:(i + 1) * P],
                                               qk[:, T:T + MEM], start=True, stop=True)
                        if i % 2:
                            ins.then_inc(s["s_mm"], 1)
                    for i in range(NT):
                        pe.wait_ge(s["p_ready"], h * NT + (i + 1))
                        for t in range(NM):
                            ins = nc.tensor.transpose(bank[4 + 2 * (i // 4) + t][:, (i % 4) * P:(i % 4 + 1) * P],
                                                      e[:, i, t * P:(t + 1) * P], ident)
                        if i % 4 == 3:
                            ins.then_inc(s["tr"], 1)
                    for b in range(2):
                        pe.wait_ge(s["tr_ev"], h * 2 + (b + 1))
                        for t in range(NM):
                            last = nc.tensor.matmul(bank[b][:, :], v[:, t, :], eT[:, t, b * BANK:(b + 1) * BANK],
                                                    start=(t == 0), stop=(t == NM - 1))
                        last.then_inc(s["o_mm"], 1)
                    pe.wait_ge(s["o_ev"], h * 2 + 2)

            @block.scalar
            def _(act):
                with act.Fori(0, MH) as h:
                    for n, (a, b) in enumerate(parts):
                        act.wait_ge(s["proj_ev"], h * 4 + (n + 1))
                        nc.scalar.activation(sq[:, a:b], qk[:, a:b], ACT.Square).then_inc(s["squared"], 1)
                    act.wait_ge(s["ms"], h * 3 + 3)
                    nc.scalar.activation(sq[:, :], sq[:, :], ACT.Sqrt).then_inc(s["root"], 1)
                    for i in range(NT):
                        act.wait_ge(s["nm"], h * NT + (i // 2 * 2 + 2))
                        nc.scalar.activation(e[:, i, :], bank[i // 2][:, (i % 2) * MEM:(i % 2 + 1) * MEM], ACT.Exp,
                                             bias=sm[:, i, 1:2], accum_out=sm[:, i, 2:3]).then_inc(s["exp"], 1)
                    for b in range(2):
                        act.wait_ge(s["tr"], h * 2 + (b + 1))
                        for t in range(NM):
                            ins = nc.scalar.activation(eT[:, t, b * BANK:(b + 1) * BANK], bank[4 + 2 * b + t][:, :], ACT.Copy)
                        ins.then_inc(s["tr_ev"], 1)

            @block.vector
            def _(dve):
                head = Steps(s["head"])
                for n, (name, scale) in enumerate((("cqn", float(P) ** -0.5), ("ckn", 1.0))):
                    dve.wait_ge(s["head"], head(nc.vector.tensor_scalar(g2[:, n:n + 1], col[:, COLS[name]:COLS[name] + 1], scale,
                                                                       None, ALU.mult)))
                with dve.Fori(0, MH) as h:
                    link = Loop(s["chain"], h, 1 + 2 * NT)

                    def wait(n):
                        dve.wait_ge(s["chain"], n)

                    for n, (a, b) in enumerate(parts):
                        dve.wait_ge(s["proj"], h * 5 + (n + 1))
                        nc.vector.tensor_copy(qk[:, a:b], bank[n][:, 0:b - a]).then_inc(s["proj_ev"], 1)
                    dve.wait_ge(s["proj"], h * 5 + 5)
                    nc.vector.tensor_copy(v[:, :, :].rearrange("p n d -> p (n d)"), bank[3][:, 0:MEM]).then_inc(s["proj_ev"], 1)
                    for n, (a, b) in enumerate(parts):
                        dve.wait_ge(s["sums"], h * 3 + (n + 1))
                        nc.vector.tensor_scalar(sq[:, a:b], bank[4 + n][:, 0:b - a], 1.0 / P, EPS, ALU.mult, ALU.add)\
                            .then_inc(s["ms"], 1)
                    dve.wait_ge(s["root"], h + 1)
                    wait(link(nc.vector.reciprocal(sq[:, :], sq[:, :])))
                    for n, (a, b) in enumerate(parts):
                        m = 1 if n == 2 else 0
                        nc.vector.scalar_tensor_tensor(qk[:, a:b], qk[:, a:b], g2[:, m:m + 1], sq[:, a:b], ALU.mult, ALU.mult)\
                            .then_inc(s["normed"], 1)
                    for i in range(NT):
                        dve.wait_ge(s["s_mm"], h * (NT // 2) + (i // 2 + 1))
                        if i == 0:
                            dve.wait_ge(s["s_mm"], h * (NT // 2) + NT // 2)
                        wait(link(nc.vector.tensor_reduce(sm[:, i, 0:1], bank[i // 2][:, (i % 2) * MEM:(i % 2 + 1) * MEM], AX_X,
                                                          ALU.max)))
                        nc.vector.tensor_scalar(sm[:, i, 1:2], sm[:, i, 0:1], -1.0, None, ALU.mult).then_inc(s["nm"], 1)
                        if i % 2:
                            for j in (i - 1, i):
                                dve.wait_ge(s["exp"], h * NT + (j + 1))
                                wait(link(nc.vector.reciprocal(sm[:, j, 3:4], sm[:, j, 2:3])))
                                nc.vector.tensor_scalar(e[:, j, :], e[:, j, :], sm[:, j, 3:4], None, ALU.mult)\
                                    .then_inc(s["p_ready"], 1)
                    for b in range(2):
                        dve.wait_ge(s["o_mm"], h * 2 + (b + 1))
                        nc.vector.tensor_copy(oT[:, ds(h, 1), b * BANK:(b + 1) * BANK].rearrange("p o t -> p (o t)"), bank[b][:, :])\
                            .then_inc(s["o_ev"], 1)
                    link.end()


NOVER = (2 * T) // (P + 1) + 1
SLOTS = (E2 + NOVER) * P


def route2(nc, bank, cst, tok, hT, w_group, b_group, w_router, b_router, slot_tok, ye_over, dest, weight, eid, placed):
    G, W = GROUPS, GROUPS + E2
    with Stage(nc, "route2") as st:
        wr = st.sb("wr", [P, KD, W])
        br = st.sb("br", [W, 1])
        lT = st.sb("lT", [W, T])
        lg = st.sb("lg", [P, NT, W])
        gs = st.sb("gs", [P, 6, NT])
        gx, gm = st.sb("gx", [P, NT, G]), st.sb("gm", [P, NT, G])
        el = st.sb("el", [P, NT, G, EPG])
        e8 = st.sb("e8", [P, 2, NT, EPG])
        m8 = st.sb("m8", [P, NT, EPG])
        es = st.sb("es", [P, 8, NT])
        A = st.sb("A", [P, 3, NT, E2])
        B = st.sb("B", [P, NT + 1, E2])
        F = st.sb("F", [P, NT, E2])
        G_ = st.sb("G", [P, NT, E2])
        cn = st.sb("cn", [P, 6, E2])
        ov = st.sb("ov", [P, E2, 8])
        ob = st.sb("ob", [P, NOVER, E2])
        df = st.sb("df", [P, 2, NT])
        ef = st.sb("ef", [P, NOVER + 1])
        zero = st.sb("zero", [P, D])
        names = ("w_in", "l_mm", "l_ev", "tr", "chain", "g_sub", "g_exp", "e_sub", "e_exp", "sums", "r_mm", "zeroed", "cleared", "cleared_ye",
                 "dest_ready", "counted")
        s = {n: st.sem(n) for n in names}
        ident, ones, lower = (cst[:, CONST[n]:CONST[n] + P] for n in ("ident", "ones", "lower"))
        iota = cst[:, CONST["e32"]:CONST["e32"] + E2]
        with nc.Block() as block:
            @block.sync
            def _(sp):
                with nc.allow_non_contiguous_dma("narrow matrices"):
                    sp.dma_start(wr[:, :, 0:G], w_group.rearrange("(k p) e -> p k e", p=P)).then_inc(s["w_in"], 16)
                    sp.dma_start(wr[:, :, G:], w_router.rearrange("(k p) e -> p k e", p=P)).then_inc(s["w_in"], 16)
                    sp.dma_start(br[0:G, :], b_group.rearrange("o e -> e o")).then_inc(s["w_in"], 16)
                    sp.dma_start(br[G:, :], b_router.rearrange("o e -> e o")).then_inc(s["w_in"], 16)
                sp.wait_ge(s["zeroed"], 1)
                sp.dma_start(slot_tok.rearrange("(b p) o -> b (p o)", p=P), zero[0:SLOTS // P, 0:P]).then_inc(s["cleared"], 16)
                for b in range(NOVER):
                    sp.dma_start(ye_over[b * P:(b + 1) * P, :], zero[:, :]).then_inc(s["cleared_ye"], 16)
                sp.wait_ge(s["cleared_ye"], 16 * NOVER)

            @block.gpsimd
            def _(pool):
                nc.gpsimd.memset(zero[:, :], 0.0).then_inc(s["zeroed"], 1)
                pool.wait_ge(s["cleared"], 16)
                pool.wait_ge(s["dest_ready"], 1)
                for k in range(2):
                    for i in range(NT):
                        pool.indirect_dma_start(out=slot_tok[:, :],
                                                out_offset=bass.IndirectOffsetOnAxis(ap=dest[:, k * NT + i:k * NT + i + 1], axis=0),
                                                in_=tok[:, i:i + 1], in_offset=None).then_inc(placed, 16)
                pool.wait_ge(placed, 16 * 2 * NT)

            @block.tensor
            def _(pe):
                pe.wait_ge(s["w_in"], 64)
                for c in range(2):
                    for k in range(KD):
                        last = nc.tensor.matmul(bank[c][0:W, :], wr[:, k, :], hT[:, k, c * BANK:(c + 1) * BANK],
                                                start=(k == 0), stop=(k == KD - 1))
                    last.then_inc(s["l_mm"], 1)
                pe.wait_ge(s["l_ev"], 2)
                for i in range(NT):
                    last = nc.tensor.transpose(bank[2][:, i * W:(i + 1) * W], lT[:, i * P:(i + 1) * P], ident[0:W, 0:W])
                last.then_inc(s["tr"], 1)
                pe.wait_ge(s["sums"], 1)
                both = A[:, 2, :, :].rearrange("p n e -> p (n e)")
                nc.tensor.matmul(bank[3][:, 0:NT * E2], lower, both, start=True, stop=False)
                nc.tensor.matmul(bank[3][:, 0:NT * E2], ones, B[:, 0:NT, :].rearrange("p n e -> p (n e)"), start=False, stop=True)
                nc.tensor.matmul(bank[4][:, 0:E2], ones, B[:, NT, :], start=True, stop=True).then_inc(s["r_mm"], 1)

            @block.scalar
            def _(act):
                act.wait_ge(s["w_in"], 64)
                for c in range(2):
                    act.wait_ge(s["l_mm"], c + 1)
                    nc.scalar.activation(lT[:, c * BANK:(c + 1) * BANK], bank[c][0:W, :], ACT.Identity, bias=br[:, 0:1])\
                        .then_inc(s["l_ev"], 1)
                act.wait_ge(s["g_sub"], 1)
                nc.scalar.activation(gx[:, :, :], gx[:, :, :], ACT.Exp).then_inc(s["g_exp"], 1)
                act.wait_ge(s["e_sub"], 1)
                nc.scalar.activation(es[:, 4, :], es[:, 4, :], ACT.Exp).then_inc(s["e_exp"], 1)

            @block.vector
            def _(dve):
                link = Steps(s["chain"])

                def step(ins):
                    dve.wait_ge(s["chain"], link(ins))

                def over(a, n):
                    return a.unsqueeze(2).to_broadcast([P, NT, n])

                def along(a, n):
                    return a.unsqueeze(1).to_broadcast([P, NT, n])

                V = nc.vector
                dve.wait_ge(s["tr"], 1)
                step(V.tensor_copy(lg[:, :, :].rearrange("p n w -> p (n w)"), bank[2][:, 0:NT * W]))
                step(V.tensor_reduce(gs[:, 0, :], lg[:, :, 0:G], AX_X, ALU.max))
                V.tensor_tensor(gx[:, :, :], lg[:, :, 0:G], over(gs[:, 0, :], G), ALU.subtract).then_inc(s["g_sub"], 1)
                dve.wait_ge(s["g_exp"], 1)
                step(V.tensor_reduce(gs[:, 1, :], gx[:, :, :], AX_X, ALU.add))
                step(V.reciprocal(gs[:, 2, :], gs[:, 1, :]))
                step(V.tensor_tensor(gx[:, :, :], gx[:, :, :], over(gs[:, 2, :], G), ALU.mult))

                def first_greatest(values, n, greatest, index, scratch):
                    step(V.tensor_reduce(greatest, values, AX_X, ALU.max))
                    step(V.tensor_tensor(scratch, values, over(greatest, n), ALU.is_equal))
                    step(V.tensor_scalar(m8[:, 0, 0:n], iota[:, 0:n], -64.0, None, ALU.add))
                    step(V.tensor_tensor(scratch, scratch, along(m8[:, 0, 0:n], n), ALU.mult))
                    step(V.tensor_reduce(index, scratch, AX_X, ALU.min))
                    step(V.tensor_scalar(index, index, 64.0, None, ALU.add))
                    step(V.tensor_tensor(scratch, along(iota[:, 0:n], n), over(index, n), ALU.is_equal))

                first_greatest(gx[:, :, :], G, gs[:, 3, :], gs[:, 4, :], gm[:, :, :])
                step(V.tensor_tensor(el[:, :, :, :], lg[:, :, G:].rearrange("p n (g e) -> p n g e", g=G),
                                     gm[:, :, :].unsqueeze(3).to_broadcast([P, NT, G, EPG]), ALU.mult))
                step(V.tensor_tensor(e8[:, 0], el[:, :, 0, :], el[:, :, 1, :], ALU.add))
                step(V.tensor_tensor(e8[:, 0], e8[:, 0], el[:, :, 2, :], ALU.add))
                step(V.tensor_tensor(e8[:, 0], e8[:, 0], el[:, :, 3, :], ALU.add))
                first_greatest(e8[:, 0], EPG, es[:, 0, :], es[:, 1, :], e8[:, 1])
                step(V.scalar_tensor_tensor(e8[:, 0], e8[:, 1], -3.0e38, e8[:, 0], ALU.mult, ALU.add))
                first_greatest(e8[:, 0], EPG, es[:, 2, :], es[:, 3, :], e8[:, 1])
                V.tensor_tensor(es[:, 4, :], es[:, 2, :], es[:, 0, :], ALU.subtract).then_inc(s["e_sub"], 1)
                dve.wait_ge(s["e_exp"], 1)
                step(V.tensor_scalar(es[:, 5, :], es[:, 4, :], 1.0, None, ALU.add))
                step(V.reciprocal(es[:, 5, :], es[:, 5, :]))
                step(V.tensor_tensor(weight[:, 0:NT], es[:, 5, :], gs[:, 3, :], ALU.mult))
                step(V.tensor_tensor(weight[:, NT:], weight[:, 0:NT], es[:, 4, :], ALU.mult))
                for k in range(2):
                    step(V.scalar_tensor_tensor(es[:, 6 + k, :], gs[:, 4, :], float(EPG), es[:, 1 + 2 * k, :], ALU.mult, ALU.add))
                    step(V.tensor_tensor(A[:, k], along(iota, E2), over(es[:, 6 + k, :], E2), ALU.is_equal))
                step(V.tensor_tensor(A[:, 2], A[:, 0], A[:, 1], ALU.add))
                step(V.memset(B[:, 0, :], 0.0))
                for i in range(NT):
                    ins = V.tensor_tensor(B[:, i + 1, :], B[:, i, :], A[:, 2, i, :], ALU.add)
                    if i < NT - 1:
                        step(ins)
                    else:
                        ins.then_inc(s["sums"], 1)
                dve.wait_ge(s["r_mm"], 1)
                rank, count = bank[3][:, 0:NT * E2].rearrange("p (n e) -> p n e", e=E2), bank[4][:, 0:E2]
                step(V.tensor_scalar(cn[:, 5, 0:8], iota[:, 0:8], float(P), float(P), ALU.mult, ALU.add))
                step(V.tensor_tensor(ov[:, :, :], count.unsqueeze(2).to_broadcast([P, E2, 8]),
                                     cn[:, 5, 0:8].unsqueeze(1).to_broadcast([P, E2, 8]), ALU.is_gt))
                step(V.tensor_reduce(cn[:, 0, :], ov[:, :, :], AX_X, ALU.add))
                step(V.tensor_tensor_scan(cn[:, 1, :], ones[:, 0:E2], cn[:, 0, :], 0.0, ALU.mult, ALU.add))
                step(V.tensor_tensor(cn[:, 2, :], cn[:, 1, :], cn[:, 0, :], ALU.subtract))
                step(V.tensor_scalar(cn[:, 3, :], iota, float(P), None, ALU.mult))
                step(V.tensor_scalar(cn[:, 4, :], cn[:, 2, :], float(P), float((E2 - 1) * P), ALU.mult, ALU.add))
                step(V.tensor_tensor(cn[:, 4, :], cn[:, 4, :], cn[:, 3, :], ALU.subtract))
                step(V.tensor_scalar(F[:, :, :], rank, float(P), None, ALU.is_ge))
                step(V.tensor_tensor(F[:, :, :], F[:, :, :], along(cn[:, 4, :], E2), ALU.mult))
                step(V.tensor_tensor(F[:, :, :], F[:, :, :], along(cn[:, 3, :], E2), ALU.add))
                step(V.tensor_tensor(F[:, :, :], F[:, :, :], rank, ALU.add))
                for k in range(2):
                    step(V.tensor_tensor(G_[:, :, :], F[:, :, :], A[:, k], ALU.mult))
                    step(V.tensor_reduce(df[:, k, :], G_[:, :, :], AX_X, ALU.add))
                V.tensor_copy(dest[:, :], df[:, :, :].rearrange("p k n -> p (k n)")).then_inc(s["dest_ready"], 1)
                step(V.tensor_tensor(ob[:, :, :], cn[:, 1, :].unsqueeze(1).to_broadcast([P, NOVER, E2]),
                                     iota[:, 0:NOVER].unsqueeze(2).to_broadcast([P, NOVER, E2]), ALU.is_le))
                step(V.tensor_reduce(ef[:, 0:NOVER], ob[:, :, :], AX_X, ALU.add))
                step(V.tensor_scalar(ef[:, 0:NOVER], ef[:, 0:NOVER], float(E2 - 1), None, ALU.min))
                step(V.tensor_copy(ef[:, NOVER:NOVER + 1], cn[:, 1, E2 - 1:E2]))
                V.tensor_copy(eid[:, :], ef[:, :]).then_inc(s["counted"], 1)


def slot_tokens(nc, bank, cst, slot_tok, idx):
    NB = SLOTS // P
    with Stage(nc, "slots") as st:
        rows = st.sb("rows", [NB, P])
        loaded, tr, done = st.sem("loaded"), st.sem("tr"), st.sem("done")
        with nc.Block() as block:
            @block.sync
            def _(sp):
                sp.dma_start(rows[:, :], slot_tok.rearrange("(b p) o -> b (p o)", p=P)).then_inc(loaded, 16)

            @block.tensor
            def _(pe):
                pe.wait_ge(loaded, 16)
                nc.tensor.transpose(bank[0][:, 0:NB], rows[:, :], cst[0:NB, CONST["ident"]:CONST["ident"] + NB]).then_inc(tr, 1)

            @block.vector
            def _(dve):
                dve.wait_ge(tr, 1)
                nc.vector.tensor_copy(idx[:, 0:NB], bank[0][:, 0:NB]).then_inc(done, 1)
                nc.vector.tensor_copy(idx[:, NB:NB + 1], bank[0][:, 0:1]).then_inc(done, 1)


def experts2(nc, bank, name, cst, h, w_gate_up, w_down, ye, idx, first, blocks, gathered, before, eid=None):
    LB = 2
    with Stage(nc, name) as st:
        w = st.sb("w", [P, LB, 3, 8 * BANK])
        xs, xT = st.sb("xs", [P, LB, D]), st.sb("xT", [P, LB, KD, P])
        cur = st.sb("cur", [P, LB], U32)
        sg, hid = st.sb("sg", [P, LB, BANK]), st.sb("hid", [P, LB, BANK])
        hidT = st.sb("hidT", [P, LB, 4, P])
        y = st.sb("y", [P, LB, D])
        names = ("turns", "cur_ready", "x_in", "x_tr", "xT_ev", "gu_mm", "sg_ready", "hid_ready", "h_tr", "hT_ev", "y_mm", "y_ready")
        s = {n: st.sem(n) for n in names}
        w_in = [[st.sem(f"w_in{k}{i}") for i in range(3)] for k in range(LB)]
        stored = [st.sem(f"stored{k}") for k in range(LB)]
        ident = cst[:, CONST["ident"]:CONST["ident"] + P]
        TURNS = blocks // LB

        def load(sp, e, k, i):
            if i < 2:
                src = w_gate_up[ds(e, 1), :, i * BANK:(i + 1) * BANK].rearrange("o (k p) n -> p (o k) n", p=P)
                dst = w[:, k, i].rearrange("p (k n) -> p k n", k=8)
            else:
                src = w_down[ds(e, 1), :, :].rearrange("o (k p) n -> p (o k) n", p=P)
                dst = w[:, k, 2].rearrange("p (k n) -> p k n", k=4)
            sp.dma_start(dst, src).then_inc(w_in[k][i], 16)

        def expert(sp, b):
            return b if eid is None else sp.value_load(eid[0:1, ds(b, 1)], min_val=0, max_val=E2 - 1)

        def weights_and_stores(sp):
            for k in range(LB):
                sp.sem_inc(stored[k], 1)
                e = expert(sp, k)
                for i in range(3):
                    load(sp, e, k, i)

            def store(it, k):
                sp.wait_ge(s["y_ready"], it * (2 * LB) + (2 * k + 3))
                sp.sem_inc(s["turns"], 1)
                sp.dma_start(ye[ds(it * (LB * P) + (first + k) * P, P), :], y[:, k, :]).then_inc(stored[k], 16)

            with sp.Fori(0, TURNS - 1) as it:
                for k in range(LB):
                    for i in range(3):
                        if i < 2:
                            sp.wait_ge(s["gu_mm"], it * (2 * LB) + (2 * k + i + 1))
                        else:
                            sp.wait_ge(s["y_mm"], it * (2 * LB) + 2 * (k + 1))
                        sp.sem_inc(s["turns"], 1)
                        if i == 0:
                            e = expert(sp, it * LB + (LB + k))
                        load(sp, e, k, i)
                    store(it, k)
            for k in range(LB):
                store(TURNS - 1, k)
                sp.wait_ge(stored[k], 16 * TURNS + 1)

        def gathers(pool):
            def gather(k):
                pool.indirect_dma_start(out=xs[:, k, :], out_offset=None, in_=h[:, :],
                                        in_offset=bass.IndirectOffsetOnAxis(ap=cur[:, k:k + 1], axis=0)).then_inc(gathered, 16)

            for k in range(LB):
                nc.gpsimd.tensor_copy(cur[:, k:k + 1], idx[:, first + k:first + k + 1]).then_inc(s["cur_ready"], 1)
                pool.wait_ge(s["cur_ready"], k + 1)
                gather(k)
                pool.wait_ge(gathered, 16 * (before + k + 1))
                pool.sem_inc(s["x_in"], 1)
            with pool.Fori(0, TURNS - 1) as it:
                for k in range(LB):
                    pool.wait_ge(s["x_tr"], it * (2 * LB) + 2 * (k + 1))
                    pool.sem_inc(s["turns"], 1)
                    nc.gpsimd.tensor_copy(cur[:, k:k + 1], idx[:, ds(it * LB + (first + LB + k), 1)]).then_inc(s["cur_ready"], 1)
                    pool.wait_ge(s["cur_ready"], it * LB + (LB + k + 1))
                    pool.sem_inc(s["turns"], 1)
                    gather(k)
                    pool.wait_ge(gathered, it * (16 * LB) + 16 * (before + LB + k + 1))
                    pool.sem_inc(s["x_in"], 1)

        def products(pe):
            with pe.Fori(0, TURNS) as it:
                def tokens(k):
                    pe.wait_ge(s["x_in"], it * LB + (k + 1))
                    for j in range(KD):
                        ins = nc.tensor.transpose(bank[6 + j // 4][:, (j % 4) * P:(j % 4 + 1) * P], xs[:, k, j * P:(j + 1) * P], ident)
                        if j % 4 == 3:
                            ins.then_inc(s["x_tr"], 1)

                def gate_up(k):
                    pe.wait_ge(s["xT_ev"], it * (2 * LB) + 2 * (k + 1))
                    for i in range(2):
                        pe.wait_ge(w_in[k][i], it * 16 + 16)
                        wi = w[:, k, i].rearrange("p (k n) -> p k n", k=8)
                        for j in range(KD):
                            last = nc.tensor.matmul(bank[2 * k + i][:, :], xT[:, k, j, :], wi[:, j, :], start=(j == 0), stop=(j == KD - 1))
                        last.then_inc(s["gu_mm"], 1)

                def down(k):
                    pe.wait_ge(s["hid_ready"], it * LB + (k + 1))
                    for j in range(4):
                        ins = nc.tensor.transpose(bank[2 * k][:, j * P:(j + 1) * P], hid[:, k, j * P:(j + 1) * P], ident)
                    ins.then_inc(s["h_tr"], 1)
                    pe.wait_ge(s["hT_ev"], it * LB + (k + 1))
                    pe.wait_ge(w_in[k][2], it * 16 + 16)
                    wi = w[:, k, 2].rearrange("p (k n) -> p k n", k=4)
                    pe.wait_ge(s["y_ready"], it * (2 * LB) + (2 * k + 1))
                    for c in range(2):
                        for j in range(4):
                            last = nc.tensor.matmul(bank[4 + c][:, :], hidT[:, k, j, :], wi[:, j, c * BANK:(c + 1) * BANK],
                                                    start=(j == 0), stop=(j == 3))
                        last.then_inc(s["y_mm"], 1)

                tokens(0)
                gate_up(0)
                tokens(1)
                gate_up(1)
                down(0)
                down(1)

        def rows_T(act):
            with act.Fori(0, TURNS) as it:
                for k in range(LB):
                    for b in range(2):
                        act.wait_ge(s["x_tr"], it * (2 * LB) + (2 * k + b + 1))
                        nc.scalar.activation(xT[:, k, 4 * b:4 * b + 4, :].rearrange("p k t -> p (k t)"), bank[6 + b][:, :], ACT.Copy)\
                            .then_inc(s["xT_ev"], 1)
                    act.wait_ge(s["gu_mm"], it * (2 * LB) + (2 * k + 1))
                    nc.scalar.activation(sg[:, k, :], bank[2 * k][:, :], ACT.Silu).then_inc(s["sg_ready"], 1)

        def hidden(dve):
            dve.sem_inc(s["y_ready"], 1)
            with dve.Fori(0, TURNS) as it:
                def gated(k):
                    dve.wait_ge(s["sg_ready"], it * LB + (k + 1))
                    dve.wait_ge(s["gu_mm"], it * (2 * LB) + 2 * (k + 1))
                    nc.vector.tensor_tensor(hid[:, k, :], sg[:, k, :], bank[2 * k + 1][:, :], ALU.mult).then_inc(s["hid_ready"], 1)

                def turned(k):
                    dve.wait_ge(s["h_tr"], it * LB + (k + 1))
                    nc.vector.tensor_copy(hidT[:, k, :, :].rearrange("p k t -> p (k t)"), bank[2 * k][:, :]).then_inc(s["hT_ev"], 1)

                def out(k):
                    dve.wait_ge(stored[k], it * 16 + 1)
                    for c in range(2):
                        dve.wait_ge(s["y_mm"], it * (2 * LB) + (2 * k + c + 1))
                        nc.vector.tensor_copy(y[:, k, c * BANK:(c + 1) * BANK], bank[4 + c][:, :]).then_inc(s["y_ready"], 1)

                gated(0)
                gated(1)
                for k in range(LB):
                    turned(k)
                    out(k)

        def when_used(engine, body):
            if eid is None:
                body(engine)
                return
            with engine.If(engine.value_load(eid[0:1, NOVER:NOVER + 1], min_val=0, max_val=NOVER) > 0):
                body(engine)

        with nc.Block() as block:
            @block.sync
            def _(sp):
                when_used(sp, weights_and_stores)

            @block.gpsimd
            def _(pool):
                when_used(pool, gathers)

            @block.tensor
            def _(pe):
                when_used(pe, products)

            @block.scalar
            def _(act):
                when_used(act, rows_T)

            @block.vector
            def _(dve):
                when_used(dve, hidden)


def combine2(nc, x, ye, dest, weight, out, gathered, out_stored):
    R = 4
    with Stage(nc, "comb2") as st:
        xt, g = st.sb("x", [P, R, D]), st.sb("g", [P, R, 2, D])
        x_in = [st.sem(f"x_in{i}") for i in range(R)]
        got, first, done = st.sem("got"), st.sem("first"), st.sem("done")
        with nc.Block() as block:
            @block.gpsimd
            def _(pool):
                for i in range(NT):
                    if i >= R:
                        pool.wait_ge(done, i - R + 1)
                    for k in range(2):
                        pool.indirect_dma_start(out=g[:, i % R, k, :], out_offset=None, in_=ye[:, :],
                                                in_offset=bass.IndirectOffsetOnAxis(ap=dest[:, k * NT + i:k * NT + i + 1], axis=0))\
                            .then_inc(gathered[i % R], 16)

            @block.sync
            def _(sp):
                for i in range(NT + 2):
                    if i < NT:
                        if i >= R:
                            sp.wait_ge(out_stored[i % R], 16 * (i // R))
                        sp.dma_start(xt[:, i % R, :], x[i * P:(i + 1) * P, :]).then_inc(x_in[i % R], 16)
                    if i >= 2:
                        sp.wait_ge(done, i - 1)
                        sp.dma_start(out[0, (i - 2) * P:(i - 1) * P, :], xt[:, (i - 2) % R, :])\
                            .then_inc(out_stored[(i - 2) % R], 16)
                for r in range(R):
                    sp.wait_ge(out_stored[r], 16 * (NT // R))

            @block.vector
            def _(dve):
                for i in range(NT):
                    r = i % R
                    dve.wait_ge(gathered[r], 32 * (i // R + 1))
                    dve.wait_ge(x_in[r], 16 * (i // R + 1))
                    nc.vector.scalar_tensor_tensor(xt[:, r, :], g[:, r, 0, :], weight[:, i:i + 1], xt[:, r, :], ALU.mult, ALU.add)\
                        .then_inc(first, 1)
                    dve.wait_ge(first, i + 1)
                    nc.vector.scalar_tensor_tensor(xt[:, r, :], g[:, r, 1, :], weight[:, NT + i:NT + i + 1], xt[:, r, :], ALU.mult,
                                                   ALU.add).then_inc(done, 1)


def program(nc, x, tabs, out, stop=None):
    cst = nc.alloc_sbuf_tensor("cst", [P, CW], F32)
    col = nc.alloc_sbuf_tensor("col", [P, VW], F32)
    bank = [nc.alloc_psum_tensor(f"bank{i}", [P, BANK], F32) for i in range(8)]
    tables_in = nc.alloc_semaphore("tables_in")

    def scratch(name, *shape, dt=F32):
        return nc.dram_tensor(name, shape, dt, kind="Internal").ap()

    mod = scratch("mod", 8, D)
    with nc.Block() as block:
        @block.sync
        def _(sp):
            sp.dma_start(cst[:, :], tabs["cst"]).then_inc(tables_in, 16)
            sp.dma_start(col[:, :], tabs["cols"]).then_inc(tables_in, 16)
            sp.wait_ge(tables_in, 32)

    modulation(nc, bank, x["w_mod"], x["b_mod"], x["c"], x["c_ctx"], x["norm_gains"], mod)
    if stop == "mod":
        return

    uT = scratch("uT", D_IN, TT)
    hold = ExitStack()
    with hold:
        hT = hold.enter_context(nc.sbuf_tensor("hT", [P, KD, TT], F32))
        norm_T(nc, bank, "norm_c", cst, x["ctx"][0], TC, hT, 0, gvec=mod[MOD_CG1:MOD_CG1 + 1, :], svec=mod[MOD_CS1:MOD_CS1 + 1, :])
        norm_T(nc, bank, "norm_x", cst, x["x"][0], T, hT, TC, gvec=mod[MOD_G1:MOD_G1 + 1, :], svec=mod[MOD_S1:MOD_S1 + 1, :])
        gemm_T(nc, bank, "proj1", hT, TT, x["w_in"][0], 0, (D_IN // 512 * 2, ((P, P), (P, 64))), uT)
    if stop == "proj1":
        return
    latT = scratch("latT", D, T)
    retention(nc, bank, cst, tabs, uT, latT)
    if stop == "ret":
        return
    rwkv(nc, bank, cst, col, tabs, x, uT, scratch, latT)
    if stop == "rwkv":
        return
    x1, h2, acc, x2 = scratch("x1", T, D), scratch("h2", T, D), scratch("acc", T, D), scratch("x2", T, D)
    with nc.sbuf_tensor("lT", [P, KD, T], F32) as lT:
        load_T(nc, "load_lat", latT, lT)
        gemm_rows(nc, bank, "mix", lT, D, x["w_out"][0], x["x"][0], x1, grow=mod[MOD_GT1:MOD_GT1 + 1, :],
                  exchanged=range(KD // 2, KD))
    tokens_in, rows_added = nc.alloc_semaphore("tokens_in"), nc.alloc_semaphore("rows_added")
    experts = ExitStack()
    with experts:
        idx = experts.enter_context(nc.sbuf_tensor("idx", [P, E1 + 1], U32))
        gates = experts.enter_context(nc.sbuf_tensor("gates", [P, E1], F32))
        with nc.sbuf_tensor("h2T", [P, KD, T], F32) as h2T:
            norm_T(nc, bank, "norm_f", cst, x1, T, h2T, 0, grow=mod[MOD_G2:MOD_G2 + 1, :], srow=mod[MOD_S2:MOD_S2 + 1, :],
                   rows_out=h2)
            route1(nc, bank, cst, h2T, x["w_router"][0], acc, idx, gates)
        experts1(nc, bank, cst, h2, x["w_gate"][0], x["w_up"][0], x["w_down"][0], acc, idx, gates, tokens_in, rows_added)
    add_normed(nc, "add1", x1, acc, mod[MOD_GT2:MOD_GT2 + 1, :], x2)
    if stop == "one":
        return
    second(nc, bank, cst, col, tabs, x, scratch, x2, out, stop)


def second(nc, bank, cst, col, tabs, x, scratch, x2, out, stop=None):
    uT2 = scratch("uT2", PROJ2, T)
    norm_mix = col[:, COLS["norm_mix"]:COLS["norm_mix"] + KD]
    gT, qkT, v_rows, oT = scratch("gT", D, T), scratch("qkT", 2, D, T), scratch("v_rows", T, D), scratch("oT", D, T)
    with nc.sbuf_tensor("hT2", [P, KD, T], F32) as hT:
        norm_T(nc, bank, "norm_2", cst, x2, T, hT, 0, gcol=norm_mix)
        gemm_T(nc, bank, "proj_lru", hT, T, x["w_in_2"][0], 0, (D // P, ()), uT2[0:2 * D, :])
        qkv_and_lru(nc, bank, cst, col, x, hT, uT2, gT, qkT, v_rows)
        gemm_T(nc, bank, "proj_g", hT, T, x["w_in_2"][0], 5 * D, (D // P, ()), uT2[5 * D:7 * D, :])
    if stop == "heads":
        return
    diff_attention(nc, bank, cst, col, x, qkT, v_rows, oT)
    if stop == "attn":
        return
    x3 = scratch("x3", T, D)
    with nc.sbuf_tensor("mT", [P, KD, T], F32) as mT:
        mixed_T(nc, bank, x["w_lru_o_2"][0], x["w_attn_o_2"][0], gT, oT, uT2[5 * D:7 * D, :], mT)
        gemm_rows(nc, bank, "out2", mT, D, x["w_out_2"][0], x2, x3)
    if stop == "x3":
        return
    x4 = scratch("x4", T, D)
    with nc.sbuf_tensor("cT", [P, MH, T], F32) as cT:
        with nc.sbuf_tensor("xT", [P, KD, T], F32) as xT, nc.sbuf_tensor("memT", [P, KD, MEM], F32) as memT:
            norm_T(nc, bank, "norm_cx", cst, x3, T, xT, 0, gcol=col[:, COLS["norm_cx"]:COLS["norm_cx"] + KD])
            norm_T(nc, bank, "norm_mem", cst, x["mem_2"][0], MEM, memT, 0, gcol=col[:, COLS["norm_mem"]:COLS["norm_mem"] + KD])
            cross_attention(nc, bank, cst, col, x["w_cq_2"][0], x["w_ckv_2"][0], xT, memT, cT)
        gemm_rows(nc, bank, "co", cT, MH * P, x["w_co_2"][0], x3, x4)
    if stop == "x4":
        return
    NB = SLOTS // P
    h4, ye, slot_tok = scratch("h4", T, D), scratch("ye", SLOTS, D), scratch("slot_tok", SLOTS, 1)
    placed, blocks_in = nc.alloc_semaphore("placed"), nc.alloc_semaphore("blocks_in")
    rows_in, out_stored = ([nc.alloc_semaphore(f"{n}{i}") for i in range(4)] for n in ("rows_in", "out_stored"))
    with nc.sbuf_tensor("dest", [P, 2 * NT], U32) as dest, nc.sbuf_tensor("weight", [P, 2 * NT], F32) as weight,\
            nc.sbuf_tensor("eid", [P, NOVER + 1], I32) as eid, nc.sbuf_tensor("slot", [P, NB + 1], U32) as idx:
        with nc.sbuf_tensor("h4T", [P, KD, T], F32) as h4T:
            norm_T(nc, bank, "norm_4", cst, x4, T, h4T, 0, grow=x["norm_ffn_2"], rows_out=h4)
            tok = cst[:, CONST["tok"]:CONST["tok"] + NT]
            route2(nc, bank, cst, tok, h4T, x["w_group_2"][0], x["b_group_2"], x["w_router_2"][0], x["b_router_2"],
                   slot_tok, ye[E2 * P:, :], dest, weight, eid, placed)
        slot_tokens(nc, bank, cst, slot_tok, idx)
        if stop == "route2":
            return
        experts2(nc, bank, "moe2", cst, h4, x["w_gate_up_2"][0], x["w_down_2"][0], ye, idx, 0, E2, blocks_in, 0)
        experts2(nc, bank, "moe2o", cst, h4, x["w_gate_up_2"][0], x["w_down_2"][0], ye, idx, E2, NOVER, blocks_in, E2, eid)
        combine2(nc, x4, ye, dest, weight, out, rows_in, out_stored)


def constants():
    c = np.zeros((P, CW), np.float32)
    msk = np.zeros((2, len(LEVELS) + 1, P, 2 * P), np.int32)

    def put(name, a):
        c[:a.shape[0], CONST[name]:CONST[name] + a.shape[1]] = a

    i = np.arange(P)
    put("ident", np.eye(P))
    put("ident2", np.concatenate([np.eye(P)] * 2, 1))
    put("pair", (i[:, None] // 64 == i[None] // 64) * 1.0)
    put("pairx", (i[:, None] // 64 != i[None] // 64) * 1.0)
    put("ones", np.ones((P, P)))
    put("lower", (i[:, None] < i[None]) * 1.0)
    put("hm", np.concatenate([np.tile((i // 64 == h) * 1.0, (P, 1)) for h in range(2)], 1))
    put("cmask", np.concatenate([np.tile((i[:, None] // CH == h) * 1.0, (1, CH)) for h in range(2)], 1))
    put("idc", (i[:, None] % CH == np.arange(CH)[None]) * 1.0)
    ax = np.zeros((P, P))
    for m in range(P):
        d = m % 64
        ax[m + 32 if d < 32 else m - 32, m] = -1.0 if d < 32 else 1.0
    put("axrot", ax)
    same = i[:, None] // CH == i[None] // CH
    s, t = i[:, None], i[None]
    for name, strict, incl in (("st_f", s < t, s <= t), ("st_b", s > t, s >= t)):
        put(name, np.concatenate([same & strict, same & incl], 1) * 1.0)
    for d in range(2):
        for l, n in enumerate((1,) + LEVELS):
            block = s // (2 * n) == t // (2 * n)
            low = block & ((s // n) % 2 == 1) & ((t // n) % 2 == 0)
            msk[d, l] = np.concatenate([low, low.T] if d == 0 else [low.T, low], 1)
    put("invf", np.tile(np.exp(-math.log(500000.0) * np.arange(8, dtype=np.float32) / 8).astype(np.float32), (P, 1)))
    put("e32", np.tile(np.arange(32), (P, 1)))
    put("tok", i[:, None] + P * np.arange(NT)[None])
    gam = np.log1p(-np.exp2(-5.0 - np.arange(RET_HEADS, dtype=np.float32))).astype(np.float32)
    idx = np.arange(P, dtype=np.float32)
    rel = idx[None] - idx[:, None]
    din = np.zeros((2, RET_HEADS, P, P), np.float32)
    for h in range(RET_HEADS):
        e = np.exp(np.abs(rel) * gam[h])
        din[0, h], din[1, h] = np.where(rel >= 0, e, 0), np.where(rel <= 0, e, 0)
    qd = np.zeros((2, PAIRS, P, P), np.float32)
    kd = np.zeros((2, PAIRS, P, P), np.float32)
    cd = np.zeros((PAIRS, P, 1), np.float32)
    for p in range(PAIRS):
        for hh in range(2):
            r, g = slice(64 * hh, 64 * hh + 64), gam[2 * p + hh]
            qd[0, p, r], qd[1, p, r] = np.exp((idx + 1) * g), np.exp((P - idx) * g)
            kd[0, p, :, r], kd[1, p, :, r] = (np.exp(e * g)[:, None] for e in (P - 1 - idx, idx))
            cd[p, r] = np.exp(P * g)
    row, col = np.repeat(np.arange(T // GRID_W), GRID_W), np.tile(np.arange(GRID_W), T // GRID_W)
    freq = (10000.0 ** (-np.arange(16, dtype=np.float32) / 16)).astype(np.float32)
    ang = np.concatenate([row[:, None].astype(np.float32) * freq, col[:, None].astype(np.float32) * freq], 1)
    ang = ang.T[np.arange(P) % 32]
    scale = RET_DIM ** -0.5
    return dict(cst=c, msk=msk, din=(din * scale).astype(np.float32), qd=qd, kd=(kd * scale).astype(np.float32), cdec=cd,
                ax=np.stack([np.cos(ang), np.sin(ang)]).astype(np.float32))


def columns(x):
    v = np.zeros((P, VW), np.float32)

    def put(name, a, at=0):
        a = np.asarray(a, np.float32).reshape(-1, P).T
        v[:, COLS[name] + at:COLS[name] + at + a.shape[1]] = a

    def xch(a):
        return np.asarray(a).reshape(PAIRS, 2, 64)[:, ::-1].reshape(-1)

    conv = np.asarray(x["rwkv_conv"])[0]
    for tap in range(3):
        full = np.zeros(16 * P, np.float32)
        full[:conv.shape[1]] = conv[tap]
        full[2 * RW:3 * RW] = xch(full[2 * RW:3 * RW])
        lora = conv[tap][3 * RW:]
        full[3 * RW:3 * RW + 128] = lora[0:128]
        full[3 * RW + 128:3 * RW + 256] = 0
        full[3 * RW + 128:3 * RW + 192] = lora[128:192]
        full[3 * RW + 256:3 * RW + 512] = lora[192:448]
        put("conv", full, 16 * tap)
    put("a0", x["rwkv_a0"])
    put("w0", x["rwkv_w0"])
    for n, k in (("k_k", "rwkv_k_k"), ("k_a", "rwkv_k_a"), ("r_k", "rwkv_r_k")):
        put(n, x[k])
    put("lnw", xch(x["rwkv_lnx_w"]))
    put("lnb", xch(x["rwkv_lnx_b"]))
    for n, k in (("norm_mix", "norm_mix_2"), ("conv2", "conv_w_2"), ("conv2b", "conv_b_2"), ("ba", "lru_ba_2"),
                 ("bx", "lru_bx_2"), ("lam", "lru_lambda_2"), ("subln", "subln_2"), ("norm_cx", "norm_cx_2"),
                 ("norm_mem", "norm_mem_2"), ("cqn", "cq_norm_2"), ("ckn", "ck_norm_2")):
        put(n, x[k])
    pc = np.zeros((PAIRS, P, PW), np.float32)
    for p in range(PAIRS):
        for tap in range(3):
            for n, name in enumerate(("conv_r", "conv_k", "conv_v")):
                pc[p, :, PCOL[name] + tap] = v[:, COLS["conv"] + 16 * tap + 4 * n + p]
        for name in ("a0", "k_k", "k_a", "r_k", "lnw", "lnb"):
            pc[p, :, PCOL[name]] = v[:, COLS[name] + p]
        for d in range(2):
            pc[p, :, PCOL["w0"] + d] = v[:, COLS["w0"] + 4 * d + p]
    return dict(cols=v, pcols=pc)


WHOLE = ("x", "c", "ctx", "c_ctx", "w_mod", "b_mod", "norm_gains", "w_in", "rwkv_w2", "rwkv_a2", "rwkv_g2",
         "w_out", "w_router", "w_gate", "w_up", "w_down", "mem_2", "positions_2", "q_norm_2", "k_norm_2", "w_in_2",
         "lru_wa_2", "lru_wx_2", "w_lru_o_2", "lambda_q1_2", "lambda_k1_2", "lambda_q2_2", "lambda_k2_2",
         "w_attn_o_2", "w_out_2", "w_cq_2", "w_ckv_2", "w_co_2", "norm_ffn_2", "w_group_2", "b_group_2",
         "w_router_2", "b_router_2", "w_gate_up_2", "w_down_2")


def kernel(**inputs):
    import concourse.bacc as bacc
    from concourse.bass_utils import run_bass_kernel_spmd

    nc = bacc.Bacc("TRN2", target_bir_lowering=False, num_devices=1)
    arrays, x, tabs = {}, {}, {}

    def take(name, a, into):
        a = np.ascontiguousarray(a)
        arrays[f"in_{name}"] = a
        into[name] = nc.dram_tensor(f"in_{name}", a.shape, mybir.dt.from_np(a.dtype), kind="ExternalInput").ap()

    for name in WHOLE:
        take(name, inputs[name], x)
    for name, a in {**constants(), **columns(inputs)}.items():
        take(name, a, tabs)
    out = nc.dram_tensor("out", (1, T, D), F32, kind="ExternalOutput").ap()
    program(nc, x, tabs, out)
    r = run_bass_kernel_spmd(nc, [arrays], core_ids=[0])
    return r.results[0]["out"]
```

```python
import math
from contextlib import ExitStack

import numpy as np

import concourse.bass as bass
from concourse import mybir

F32 = mybir.dt.float32
F32R = mybir.dt.float32r
I32 = mybir.dt.int32
U32 = mybir.dt.uint32
ALU = mybir.AluOpType
ACT = mybir.ActivationFunctionType
AX_X = mybir.AxisListType.X
ds = bass.ds

P = 128
BANK = 512
D = 1024
KD = D // P
T = 1024
TC = 256
TT = T + TC
NT, NTC = T // P, TC // P
EPS = 1e-6
HI_MASK = -4096

RET_HEADS, RET_DIM, GRID_W = 8, 64, 64
RW = 512
PAIRS = RW // P
GN_EPS = 64e-5
D_IN = 5 * RW + 3 * RW + 64 * 3 + 128 * 2
CH = 64
LEVELS = (2, 4, 8, 16, 32)
E1, CAP = 16, 128

HEADS2, HD2 = 8, 64
CHUNK2 = 64
MEM, MH = 256, 4
PROJ2 = 7 * D
GROUPS, EPG = 4, 8
E2 = GROUPS * EPG
FF2 = 512


def fill(n, parts):
    at, out = n, {}
    for name, width in parts:
        out[name] = at
        at += width
    return out, at


CONST, CW = fill(0, [("ident", 128), ("pair", 128), ("pairx", 128), ("ones", 128), ("lower", 128),
                     ("axrot", 128), ("st_f", 256), ("st_b", 256),
                     ("ident2", 256), ("hm", 256), ("cmask", 128), ("idc", 64),
                     ("invf", 8), ("e32", 32), ("tok", 8)])
COLS, VW = fill(0, [("conv", 3 * 16), ("a0", 4), ("w0", 8), ("k_k", 4), ("k_a", 4), ("r_k", 4),
                    ("lnw", 4), ("lnb", 4),
                    ("norm_mix", 8), ("conv2", 32), ("conv2b", 8), ("ba", 8), ("bx", 8), ("lam", 8),
                    ("subln", 1), ("norm_cx", 8), ("norm_mem", 8),
                    ("cqn", 1), ("ckn", 1)])
MOD_G1, MOD_S1, MOD_CG1, MOD_CS1, MOD_GT1, MOD_G2, MOD_S2, MOD_GT2 = range(8)


class Stage:

    def __init__(self, nc, name):
        self.nc, self.name, self.ctx, self.sems = nc, name, ExitStack(), []

    def __enter__(self):
        return self

    def sb(self, name, shape, dt=F32):
        return self.ctx.enter_context(self.nc.sbuf_tensor(f"{self.name}_{name}", shape, dt))

    def sem(self, name):
        s = self.ctx.enter_context(self.nc.semaphore(f"{self.name}_{name}"))
        self.sems.append(s)
        return s

    def __exit__(self, *exc):
        if exc[0] is None:
            with self.nc.Block() as block:
                @block.gpsimd
                def _(pool):
                    for s in self.sems:
                        pool.sem_clear(s)
        self.ctx.close()
        return False


class Steps:

    def __init__(self, sem, base=0):
        self.sem, self.n = sem, base

    def __call__(self, instruction):
        instruction.then_inc(self.sem, 1)
        self.n = self.n + 1
        return self.n


def modulation(nc, bank, w_mod, b_mod, c, c_ctx, gains, mod):
    N = 6 * D
    NG = N // BANK
    with Stage(nc, "mod") as st:
        cc = st.sb("cc", [P, KD, 2])
        sc = st.sb("sc", [P, KD, 2])
        w = st.sb("w", [P, 2, KD, BANK])
        bias = st.sb("bias", [2, N])
        m = st.sb("m", [2, N])
        g = st.sb("g", [2, 4 * D])
        o = st.sb("o", [2, 4, D])
        c_in, g_in, w_in = st.sem("c_in"), st.sem("g_in"), [st.sem("w_in0"), st.sem("w_in1")]
        silu, mm, added, vec, out = st.sem("silu"), st.sem("mm"), st.sem("added"), st.sem("vec"), st.sem("out")
        with nc.Block() as block:
            @block.sync
            def _(sp):
                with nc.allow_non_contiguous_dma("vectors as columns"):
                    sp.dma_start(cc[:, :, 0], c.rearrange("o (k p) -> p (o k)", p=P)).then_inc(c_in, 16)
                    sp.dma_start(cc[:, :, 1], c_ctx.rearrange("(k p) -> p k", p=P)).then_inc(c_in, 16)
                for r in range(2):
                    sp.dma_start(bias[r:r + 1, :], b_mod[0:1, :]).then_inc(g_in, 16)
                    sp.dma_start(g[r:r + 1, :], gains.rearrange("o a d -> o (a d)")).then_inc(g_in, 16)
                for n in range(NG):
                    if n >= 2:
                        sp.wait_ge(mm, n - 1)
                    sp.dma_start(w[:, n % 2], w_mod[0, :, n * BANK:(n + 1) * BANK]
                                 .rearrange("(k p) n -> p k n", p=P)).then_inc(w_in[n % 2], 16)
                sp.wait_ge(vec, 4)
                rows = [(MOD_G1, o[0:1, 0]), (MOD_CG1, o[1:2, 0]), (MOD_S1, m[0:1, 0:D]), (MOD_CS1, m[1:2, 0:D]),
                        (MOD_GT1, o[0:1, 1]), (MOD_G2, o[0:1, 2]), (MOD_S2, m[0:1, 3 * D:4 * D]),
                        (MOD_GT2, o[0:1, 3])]
                for r, src in rows:
                    sp.dma_start(mod[r:r + 1, :], src).then_inc(out, 16)
                sp.wait_ge(out, 16 * len(rows))

            @block.scalar
            def _(act):
                act.wait_ge(c_in, 32)
                nc.scalar.activation(sc[:, :, :], cc[:, :, :], ACT.Silu).then_inc(silu, 1)

            @block.tensor
            def _(pe):
                pe.wait_ge(silu, 1)
                for n in range(NG):
                    pe.wait_ge(w_in[n % 2], 16 * (n // 2 + 1))
                    if n >= 2:
                        pe.wait_ge(added, n - 1)
                    for k in range(KD):
                        last = nc.tensor.matmul(bank[n % 2][0:2, :], sc[:, k, :], w[:, n % 2, k, :],
                                                start=(k == 0), stop=(k == KD - 1))
                    last.then_inc(mm, 1)

            @block.vector
            def _(dve):
                dve.wait_ge(g_in, 64)
                for n in range(NG):
                    dve.wait_ge(mm, n + 1)
                    c0 = n * BANK
                    nc.vector.tensor_tensor(m[:, c0:c0 + BANK], bank[n % 2][0:2, :], bias[:, c0:c0 + BANK],
                                            ALU.add).then_inc(added, 1)
                dve.wait_ge(added, NG)
                sh1, sc1, gt1, sh2, sc2, gt2 = (m[:, j * D:(j + 1) * D] for j in range(6))
                gain = [g[:, j * D:(j + 1) * D] for j in range(4)]
                nc.vector.scalar_tensor_tensor(o[:, 0], sc1, 1.0, gain[0], ALU.add, ALU.mult).then_inc(vec, 1)
                nc.vector.tensor_tensor(o[:, 1], gt1, gain[1], ALU.mult).then_inc(vec, 1)
                nc.vector.scalar_tensor_tensor(o[:, 2], sc2, 1.0, gain[2], ALU.add, ALU.mult).then_inc(vec, 1)
                nc.vector.tensor_tensor(o[:, 3], gt2, gain[3], ALU.mult).then_inc(vec, 1)


def norm_T(nc, bank, name, cst, x, ntok, actT, at, gcol=None, scol=None, gvec=None, svec=None,
           grow=None, srow=None, rows_out=None):
    n = ntok // P
    by_rows = grow is not None
    per = 2 if by_rows and srow is not None else 1
    with Stage(nc, name) as st:
        xt = st.sb("x", [P, n, D])
        sq = st.sb("sq", [P, D])
        ss = st.sb("ss", [P, n, 3])
        gs = st.sb("gs", [P, 2, KD])
        gb = st.sb("gb", [P, 2, D]) if by_rows else None
        x_in = [st.sem(f"x_in{i}") for i in range(n)]
        g_in, ssq, ms, root, rstd, scaled, stored = (st.sem(s) for s in
                                                     ("g_in", "ssq", "ms", "root", "rstd", "scaled", "stored"))
        tr, ev = st.sem("transposed"), [st.sem("ev_act"), st.sem("ev_dve")]
        ident = cst[:, CONST["ident"]:CONST["ident"] + P]
        if gcol is None:
            gcol, scol = gs[:, 0, :], gs[:, 1, :]
        has_s = scol is not None
        with nc.Block() as block:
            @block.sync
            def _(sp):
                if gvec is not None:
                    with nc.allow_non_contiguous_dma("vectors as columns"):
                        sp.dma_start(gs[:, 0, :], gvec.rearrange("o (k p) -> p (o k)", p=P)).then_inc(g_in, 16)
                        sp.dma_start(gs[:, 1, :], svec.rearrange("o (k p) -> p (o k)", p=P)).then_inc(g_in, 16)
                if by_rows:
                    sp.dma_start(gb[:, 0, :], grow.partition_broadcast(P).rearrange("p o d -> p (o d)"))\
                        .then_inc(g_in, 16)
                    if srow is not None:
                        sp.dma_start(gb[:, 1, :], srow.partition_broadcast(P).rearrange("p o d -> p (o d)"))\
                            .then_inc(g_in, 16)
                for i in range(n):
                    sp.dma_start(xt[:, i, :], x[i * P:(i + 1) * P, :]).then_inc(x_in[i], 16)
                if rows_out is not None:
                    for i in range(n):
                        sp.wait_ge(scaled, per * (i + 1))
                        sp.dma_start(rows_out[i * P:(i + 1) * P, :], xt[:, i, :]).then_inc(stored, 16)
                    sp.wait_ge(stored, 16 * n)

            def evacuate(eng, e, i):
                eng.wait_ge(tr, 2 * i + e + 1)
                if i == 0 and gvec is not None:
                    eng.wait_ge(g_in, 32)
                b, t = bank[2 * (i % 2) + e], slice(at + i * P, at + (i + 1) * P)
                if by_rows:
                    dst, src = actT[:, 4 * e:4 * e + 4, t], b[:, :].rearrange("p (k t) -> p k t", k=4)
                    ins = nc.vector.tensor_copy(dst, src) if e else nc.scalar.activation(dst, src, ACT.Copy)
                    ins.then_inc(ev[e], 4)
                    return
                for j in range(4):
                    k = 4 * e + j
                    dst, src, g = actT[:, k, t], b[:, j * P:(j + 1) * P], gcol[:, k:k + 1]
                    if e and has_s:
                        ins = nc.vector.tensor_scalar(dst, src, g, scol[:, k:k + 1], ALU.mult, ALU.add)
                    elif e:
                        ins = nc.vector.tensor_scalar(dst, src, g, None, ALU.mult)
                    elif has_s:
                        ins = nc.scalar.activation(dst, src, ACT.Identity, scale=g, bias=scol[:, k:k + 1])
                    else:
                        ins = nc.scalar.activation(dst, src, ACT.Copy, scale=g)
                    ins.then_inc(ev[e], 1)

            @block.scalar
            def _(act):
                for i in range(n + 2):
                    if i < n:
                        act.wait_ge(x_in[i], 16)
                        if i:
                            act.wait_ge(ssq, i)
                        nc.scalar.activation(sq[:, :], xt[:, i, :], ACT.Square, accum_out=ss[:, i, 0:1]).then_inc(ssq, 1)
                    if 1 <= i <= n:
                        act.wait_ge(ms, i)
                        nc.scalar.activation(ss[:, i - 1, 2:3], ss[:, i - 1, 1:2], ACT.Sqrt).then_inc(root, 1)
                    if i >= 2:
                        evacuate(act, 0, i - 2)

            @block.vector
            def _(dve):
                def scale(i):
                    dve.wait_ge(root, i + 1)
                    nc.vector.reciprocal(ss[:, i, 0:1], ss[:, i, 2:3]).then_inc(rstd, 1)
                    dve.wait_ge(rstd, i + 1)
                    if not by_rows:
                        nc.vector.tensor_scalar(xt[:, i, :], xt[:, i, :], ss[:, i, 0:1], None, ALU.mult).then_inc(scaled, 1)
                        return
                    if i == 0:
                        dve.wait_ge(g_in, 32 if srow is not None else 16)
                    nc.vector.scalar_tensor_tensor(xt[:, i, :], xt[:, i, :], ss[:, i, 0:1], gb[:, 0, :], ALU.mult, ALU.mult)\
                        .then_inc(scaled, 1)
                    if srow is not None:
                        dve.wait_ge(scaled, 2 * i + 1)
                        nc.vector.tensor_tensor(xt[:, i, :], xt[:, i, :], gb[:, 1, :], ALU.add).then_inc(scaled, 1)

                for i in range(n + 2):
                    if i < n:
                        dve.wait_ge(ssq, i + 1)
                        nc.vector.tensor_scalar(ss[:, i, 1:2], ss[:, i, 0:1], 1.0 / D, EPS, ALU.mult, ALU.add).then_inc(ms, 1)
                    if 1 <= i <= n:
                        scale(i - 1)
                    if i >= 2:
                        evacuate(dve, 1, i - 2)

            @block.tensor
            def _(pe):
                for i in range(n):
                    pe.wait_ge(scaled, per * (i + 1))
                    if i >= 2:
                        pe.wait_ge(ev[0], 4 * (i - 1))
                        pe.wait_ge(ev[1], 4 * (i - 1))
                    for k in range(KD):
                        ins = nc.tensor.transpose(bank[2 * (i % 2) + k // 4][:, (k % 4) * P:(k % 4 + 1) * P],
                                                  xt[:, i, k * P:(k + 1) * P], ident)
                        if k % 4 == 3:
                            ins.then_inc(tr, 1)


def gemm_T(nc, bank, name, actT, tok, w, col0, widths, dst):
    full, last = widths
    chunks = [(a, min(BANK, tok - a)) for a in range(0, tok, BANK)]
    nch = len(chunks)
    GW = 2 * P
    size = [(P, P)] * full + list(last)
    G = len(size)
    with Stage(nc, name) as st:
        raw, top = st.sb("raw", [P, KD, GW]), st.sb("top", [P, KD, GW])
        wt = st.sb("w", [P, 2, 2, KD, GW], F32R)
        hi, lo = st.sb("hi", [P, KD, tok], F32R), st.sb("lo", [P, KD, tok], F32R)
        ob = st.sb("out", [P, 2, tok])
        w_in, topped, hi_ready, lo_ready, turns = (st.sem(n) for n in ("w_in", "topped", "hi_ready", "lo_ready", "turns"))
        x_top, x_hi, x_lo = st.sem("x_top"), st.sem("x_hi"), st.sem("x_lo")
        mm = [st.sem("mm_act"), st.sem("mm_dve")]
        ev = [st.sem("ev_act"), st.sem("ev_dve")]
        stored = [st.sem("stored0"), st.sem("stored1")]
        TURNS = full // 2 - 1

        with nc.Block() as block:
            @block.sync
            def _(sp):
                def load(g, width=GW):
                    sp.dma_start(raw[:, :, 0:width], w[:, ds(g * GW + col0, width)].rearrange("(k p) n -> p k n", p=P))\
                        .then_inc(w_in, 16)

                def group(g, ahead, width=(P, P)):
                    for e in range(2):
                        if ahead and e == 0:
                            sp.wait_ge(lo_ready, g + 2)
                            sp.sem_inc(turns, 1)
                            load(g + 2, ahead)
                        sp.wait_ge(ev[e], g * nch + (nch + 1))
                        sp.sem_inc(turns, 1)
                        sp.dma_start(dst[ds(g * GW + e * P, width[e]), :], ob[0:width[e], e, :]).then_inc(stored[e], 16)

                for e in range(2):
                    sp.sem_inc(stored[e], 1)
                load(0)
                sp.wait_ge(lo_ready, 1)
                load(1)
                with sp.Fori(0, TURNS) as it:
                    for s in range(2):
                        group(it * 2 + s, GW)
                for g in range(2 * TURNS, G):
                    group(g, sum(size[g + 2]) if g + 2 < G else 0, size[g])
                for e in range(2):
                    sp.wait_ge(stored[e], 16 * G + 1)

            @block.tensor
            def _(pe):
                def group(g, slot, width=(P, P)):
                    pe.wait_ge(lo_ready, g + 1)
                    pe.wait_ge(hi_ready, g + 1)
                    for e in range(2):
                        pe.wait_ge(ev[e], g * nch + 1)
                        for c, (a, n) in enumerate(chunks):
                            for k in range(KD):
                                w_hi, w_lo = (wt[:, slot, i, k, e * P:e * P + width[e]] for i in range(2))
                                x_h, x_l = hi[:, k, a:a + n], lo[:, k, a:a + n]
                                for i, (l, r) in enumerate(((w_hi, x_h), (w_lo, x_h), (w_hi, x_l))):
                                    last = nc.tensor.matmul(bank[e * nch + c][0:width[e], 0:n], l, r,
                                                            start=(k == 0 and i == 0), stop=(k == KD - 1 and i == 2))
                            last.then_inc(mm[e], 1)

                pe.wait_ge(x_hi, KD)
                pe.wait_ge(x_lo, KD)
                with pe.Fori(0, TURNS) as it:
                    for s in range(2):
                        group(it * 2 + s, s)
                for g in range(2 * TURNS, G):
                    group(g, g % 2, size[g])

            def drain(eng, e, g, width=P):
                eng.wait_ge(stored[e], g * 16 + 1)
                for c, (a, n) in enumerate(chunks):
                    eng.wait_ge(mm[e], g * nch + (c + 1))
                    o, i = ob[0:width, e, a:a + n], bank[e * nch + c][0:width, 0:n]
                    ins = nc.scalar.activation(o, i, ACT.Copy) if e == 0 else nc.vector.tensor_copy(o, i)
                    ins.then_inc(ev[e], 1)

            def groups_of(eng, e, split):
                with eng.Fori(0, TURNS) as it:
                    for s in range(2):
                        drain(eng, e, it * 2 + s)
                        split(it * 2 + (s + 2), s, GW)
                for g in range(2 * TURNS, G):
                    drain(eng, e, g, size[g][e])
                    if g + 2 < G:
                        split(g + 2, g % 2, sum(size[g + 2]))

            @block.scalar
            def _(act):
                def split(g, slot, width=GW):
                    act.wait_ge(topped, g + 1)
                    nc.scalar.activation(wt[:, slot, 0, :, 0:width], top[:, :, 0:width], ACT.Copy).then_inc(hi_ready, 1)

                act.sem_inc(ev[0], 1)
                for k in range(KD):
                    act.wait_ge(x_top, k + 1)
                    nc.scalar.activation(hi[:, k, :], ob[:, k % 2, :], ACT.Copy).then_inc(x_hi, 1)
                    if k < 2:
                        split(k, k)
                groups_of(act, 0, split)

            @block.vector
            def _(dve):
                def leading(part, whole):
                    return nc.vector.tensor_scalar(part.bitcast(I32), whole.bitcast(I32), HI_MASK, None, ALU.bitwise_and)

                def split(g, slot, width=GW):
                    dve.wait_ge(w_in, g * 16 + 16)
                    if not (isinstance(g, int) and g == 0):
                        dve.wait_ge(hi_ready, g)
                        dve.sem_inc(turns, 1)
                    leading(top[:, :, 0:width], raw[:, :, 0:width]).then_inc(topped, 1)
                    dve.wait_ge(topped, g + 1)
                    nc.vector.tensor_tensor(wt[:, slot, 1, :, 0:width], raw[:, :, 0:width], top[:, :, 0:width], ALU.subtract)\
                        .then_inc(lo_ready, 1)

                dve.sem_inc(ev[1], 1)
                for k in range(KD):
                    if k >= 2:
                        dve.wait_ge(x_hi, k - 1)
                    leading(ob[:, k % 2, :], actT[:, k, :]).then_inc(x_top, 1)
                    dve.wait_ge(x_top, k + 1)
                    nc.vector.tensor_tensor(lo[:, k, :], actT[:, k, :], ob[:, k % 2, :], ALU.subtract).then_inc(x_lo, 1)
                    if k < 2:
                        split(k, k)
                groups_of(dve, 1, split)


class Loop:

    def __init__(self, sem, turn, per):
        self.sem, self.base, self.per, self.k = sem, turn * per, per, 0

    def __call__(self, instruction):
        instruction.then_inc(self.sem, 1)
        self.k += 1
        return self.base + self.k

    def end(self):
        assert self.k == self.per, f"{self.sem}: {self.k} a turn, not {self.per}"


def retention(nc, bank, cst, tabs, uT, latT):
    NB = TT // P
    with Stage(nc, "ret") as st:
        q, k, v = st.sb("q", [P, TT]), st.sb("k", [P, TT]), st.sb("v", [P, TT])
        g = st.sb("g", [P, 2, T])
        din = st.sb("din", [P, 2, 2, P])
        qd, kd, cd = st.sb("qd", [P, 2, P]), st.sb("kd", [P, 2, P]), st.sb("cd", [P, 1])
        ax = st.sb("ax", [P, 2, T])
        kz = st.sb("kz", [P, 2, T])
        vz = st.sb("vz", [P, NB, 2, P])
        vr = st.sb("vr", [P, 2, P])
        tmp = st.sb("tmp", [P, 2, T])
        qs = st.sb("qs", [P, 2, T])
        kfb = st.sb("kfb", [P, 2, 2, P])
        kvm = st.sb("kvm", [P, 2, NB, P])
        S = st.sb("S", [P, 2, NT + 3, P])
        sc = st.sb("sc", [P, 2, 2, 2, P])
        y = st.sb("y", [P, 2, T])
        lat = st.sb("lat", [P, T])
        names = ("turns", "tab_in", "q_in", "k_in", "v_in", "g_in", "zeroed", "rot", "cosed", "roped", "halved", "tr",
                 "k_rows", "v_rows", "v_copied", "kv", "kv_kept", "scan", "states", "q_scaled", "scores", "sc_ready",
                 "y_mm", "y_ready", "squared", "sums", "ms", "root", "chain", "silu", "lat_ready", "stored")
        s = {n: st.sem(n) for n in names}
        ident, pair = (cst[:, CONST[n]:CONST[n] + P] for n in ("ident", "pair"))
        axrot = cst[:, CONST["axrot"]:CONST["axrot"] + P]
        LAT = slice(TC, TT)
        CHAIN = 10
        with nc.Block() as block:
            @block.sync
            def _(sp):
                sp.dma_start(ax[:, :, :], tabs["ax"].rearrange("a p t -> p a t")).then_inc(s["tab_in"], 16)
                sp.sem_inc(s["stored"], 1)

                def load(p):
                    for n, (t, a) in enumerate(((q, 0), (k, RW), (v, 2 * RW))):
                        sp.dma_start(t[:, :], uT[ds(p * P + a, P), :]).then_inc(s["qkv"[n] + "_in"], 16)
                    for d in range(2):
                        sp.dma_start(din[:, d], tabs["din"][d, ds(p * 2, 2)].rearrange("h j i -> j h i"))\
                            .then_inc(s["tab_in"], 16)
                    for t, n in ((qd, "qd"), (kd, "kd")):
                        sp.dma_start(t[:, :, :], tabs[n][:, ds(p, 1)].rearrange("d o p t -> p (d o) t"))\
                            .then_inc(s["tab_in"], 16)
                    sp.dma_start(cd[:, :], tabs["cdec"][ds(p, 1)].rearrange("o p t -> p (o t)"))\
                        .then_inc(s["tab_in"], 16)

                def load_gates(p):
                    for d in range(2):
                        sp.dma_start(g[:, d, :], uT[ds(p * P + (3 + d) * RW, P), LAT]).then_inc(s["g_in"], 16)

                def store(p):
                    sp.wait_ge(s["lat_ready"], p + 1)
                    sp.sem_inc(s["turns"], 1)
                    sp.dma_start(latT[ds(p * P, P), :], lat[:, :]).then_inc(s["stored"], 16)

                load(0)
                load_gates(0)
                with sp.Fori(0, PAIRS - 1) as p:
                    sp.wait_ge(s["y_mm"], p * NT + NT)
                    sp.sem_inc(s["turns"], 1)
                    load(p + 1)
                    store(p)
                    load_gates(p + 1)
                store(PAIRS - 1)
                sp.wait_ge(s["stored"], 16 * PAIRS + 1)

            TAB = 80

            @block.gpsimd
            def _(pool):
                nc.gpsimd.memset(kz[:, :, :], 0.0).then_inc(s["zeroed"], 1)
                nc.gpsimd.memset(vz[:, :, :, :], 0.0).then_inc(s["zeroed"], 1)
                nc.gpsimd.memset(S[:, :, 0, :], 0.0).then_inc(s["zeroed"], 1)
                pool.wait_ge(s["zeroed"], 3)
                with pool.Fori(0, PAIRS) as p:
                    pool.wait_ge(s["tab_in"], p * TAB + (TAB + 16))
                    for i, t in enumerate((q, k)):
                        pool.wait_ge(s["rot"], p * 4 + (2 * i + 2))
                        nc.gpsimd.tensor_tensor(t[:, LAT], t[:, LAT], ax[:, 0, :], ALU.mult).then_inc(s["cosed"], 1)
                    pool.wait_ge(s["roped"], p * 4 + 4)
                    for d in range(2):
                        nc.gpsimd.tensor_tensor(qs[:, d, :].rearrange("p (n t) -> p n t", t=P),
                                                q[:, LAT].rearrange("p (n t) -> p n t", t=P),
                                                qd[:, d, :].unsqueeze(1).to_broadcast([P, NT, P]),
                                                ALU.mult).then_inc(s["q_scaled"], 1)

            @block.tensor
            def _(pe):
                pe.wait_ge(s["zeroed"], 3)
                with pe.Fori(0, PAIRS) as p:
                    for n, (t, nm) in enumerate(((q, "q_in"), (k, "k_in"))):
                        pe.wait_ge(s[nm], p * 16 + 16)
                        for c in range(2):
                            nc.tensor.matmul(bank[2 * n + c][:, :], axrot, t[:, TC + c * BANK:TC + (c + 1) * BANK],
                                             start=True, stop=True).then_inc(s["rot"], 1)
                    pe.wait_ge(s["v_in"], p * 16 + 16)
                    pe.wait_ge(s["roped"], p * 4 + 4)

                    def rows(j):
                        if j >= 2:
                            pe.wait_ge(s["k_rows"], p * (2 * NB) + 2 * (j - 1))
                            pe.wait_ge(s["v_rows"], p * NB + (j - 1))
                        b = bank[4 + j % 2]
                        nc.tensor.transpose(b[:, 0:P], k[:, j * P:(j + 1) * P], ident)
                        nc.tensor.transpose(bank[j % 2][:, 0:P], v[:, j * P:(j + 1) * P], ident).then_inc(s["tr"], 1)

                    rows(0)
                    for j in range(NB):
                        if j + 1 < NB:
                            rows(j + 1)
                        pe.wait_ge(s["k_rows"], p * (2 * NB) + 2 * (j + 1))
                        pe.wait_ge(s["v_rows"], p * NB + (j + 1))
                        if j >= 2:
                            pe.wait_ge(s["kv_kept"], p * NB + (j - 1))
                        for d in range(2):
                            ins = nc.tensor.matmul(bank[6 + j % 2][:, d * P:(d + 1) * P], kfb[:, j % 2, d, :],
                                                   vr[:, j % 2, :], start=True, stop=True)
                        ins.then_inc(s["kv"], 1)
                    pe.wait_ge(s["halved"], p * 2 + 2)
                    pe.wait_ge(s["v_copied"], p * (2 * NB) + 2 * NB)
                    pe.wait_ge(s["q_scaled"], p * 2 + 2)

                    def scores(j):
                        if j >= 2:
                            pe.wait_ge(s["sc_ready"], p * (2 * NT) + 2 * (j - 1))
                        t = slice(j * P, (j + 1) * P)
                        for h in range(2):
                            ins = nc.tensor.matmul(bank[j % 2][:, h * P:(h + 1) * P], kz[:, h, t], q[:, TC + j * P:TC + (j + 1) * P],
                                                   start=True, stop=True)
                        ins.then_inc(s["scores"], 1)

                    scores(0)
                    for j in range(NT):
                        if j + 1 < NT:
                            scores(j + 1)
                        if j == 0:
                            pe.wait_ge(s["states"], p + 1)
                        pe.wait_ge(s["sc_ready"], p * (2 * NT) + 2 * (j + 1))
                        if j >= 2:
                            pe.wait_ge(s["y_ready"], p * NT + (j - 1))
                        for d in range(2):
                            o = bank[2 + j % 2][:, d * P:(d + 1) * P]
                            nc.tensor.matmul(o, S[:, d, 2 + j, :], qs[:, d, j * P:(j + 1) * P], start=True, stop=False)
                            for h in range(2):
                                ins = nc.tensor.matmul(o, vz[:, 2 + j, h, :], sc[:, j % 2, d, h, :],
                                                       start=False, stop=(h == 1))
                        ins.then_inc(s["y_mm"], 1)
                    for d in range(2):
                        pe.wait_ge(s["squared"], p * 2 + (d + 1))
                        for c in range(2):
                            nc.tensor.matmul(bank[4 + 2 * d + c][:, :], pair, tmp[:, d, c * BANK:(c + 1) * BANK],
                                             start=True, stop=True).then_inc(s["sums"], 1)

            @block.scalar
            def _(act):
                act.wait_ge(s["zeroed"], 3)
                with act.Fori(0, PAIRS) as p:
                    act.wait_ge(s["roped"], p * 4 + 4)
                    for h in range(2):
                        r = slice(64 * h, 64 * h + 64)
                        nc.scalar.activation(kz[r, h, :], k[r, LAT], ACT.Copy).then_inc(s["halved"], 1)
                    for j in range(NB):
                        act.wait_ge(s["tr"], p * NB + (j + 1))
                        if j >= 2:
                            act.wait_ge(s["kv"], p * NB + (j - 1))
                        nc.scalar.activation(vr[:, j % 2, :], bank[j % 2][:, 0:P], ACT.Copy)\
                            .then_inc(s["v_rows"], 1)
                        act.wait_ge(s["v_rows"], p * NB + (j + 1))
                        for h in range(2):
                            c = slice(64 * h, 64 * h + 64)
                            nc.scalar.activation(vz[:, j, h, c], vr[:, j % 2, c], ACT.Copy).then_inc(s["v_copied"], 1)
                    for j in range(NT):
                        act.wait_ge(s["y_mm"], p * NT + (j + 1))
                        nc.scalar.activation(y[:, :, j * P:(j + 1) * P],
                                             bank[2 + j % 2][:, 0:2 * P].rearrange("p (d t) -> p d t", d=2),
                                             ACT.Copy).then_inc(s["y_ready"], 1)
                    act.wait_ge(s["y_ready"], p * NT + NT)
                    for d in range(2):
                        nc.scalar.activation(tmp[:, d, :], y[:, d, :], ACT.Square).then_inc(s["squared"], 1)
                    act.wait_ge(s["ms"], p * 4 + 4)
                    nc.scalar.activation(tmp[:, :, :], tmp[:, :, :], ACT.Sqrt).then_inc(s["root"], 1)
                    act.wait_ge(s["g_in"], p * 32 + 32)
                    for d in range(2):
                        nc.scalar.activation(g[:, d, :], g[:, d, :], ACT.Silu).then_inc(s["silu"], 1)

            def keep(dve, p, j):
                dve.wait_ge(s["kv"], p * NB + (j + 1))
                nc.vector.tensor_tensor(kvm[:, :, j, :], bank[6 + j % 2][:, 0:2 * P].rearrange("p (d e) -> p d e", d=2),
                                        pair.unsqueeze(1).to_broadcast([P, 2, P]), ALU.mult).then_inc(s["kv_kept"], 1)

            @block.vector
            def _(dve):
                dve.wait_ge(s["zeroed"], 3)
                with dve.Fori(0, PAIRS) as p:
                    link = Loop(s["chain"], p, CHAIN)
                    dve.wait_ge(s["tab_in"], p * TAB + (TAB + 16))
                    for n, t in enumerate((q, k)):
                        for c in range(2):
                            tc = slice(c * BANK, (c + 1) * BANK)
                            dve.wait_ge(s["rot"], p * 4 + (2 * n + c + 1))
                            dve.wait_ge(s["chain"], link(nc.vector.tensor_tensor(
                                tmp[:, n, tc], bank[2 * n + c][:, :], ax[:, 1, tc], ALU.mult)))
                            dve.wait_ge(s["cosed"], p * 2 + (n + 1))
                            o = t[:, TC + c * BANK:TC + (c + 1) * BANK]
                            nc.vector.tensor_tensor(o, o, tmp[:, n, tc], ALU.add).then_inc(s["roped"], 1)
                    for j in range(NB):
                        dve.wait_ge(s["tr"], p * NB + (j + 1))
                        if j >= 2:
                            dve.wait_ge(s["kv"], p * NB + (j - 1))
                        for d in range(2):
                            nc.vector.tensor_tensor(kfb[:, j % 2, d, :], bank[4 + j % 2][:, 0:P], kd[:, d, :],
                                                    ALU.mult).then_inc(s["k_rows"], 1)
                        if j:
                            keep(dve, p, j - 1)
                    keep(dve, p, NB - 1)
                    dve.wait_ge(s["kv_kept"], p * NB + NB)
                    n = 0
                    for d in range(2):
                        order = list(range(NB)) if d == 0 else [1, 0] + list(range(NB - 1, 1, -1))
                        before = 0
                        for i, j in enumerate(order[:-1]):
                            after = order[i + 1] if i >= 1 else NT + 2
                            nc.vector.scalar_tensor_tensor(S[:, d, after, :], S[:, d, before, :], cd[:, 0:1],
                                                           kvm[:, d, j, :], ALU.mult, ALU.add)\
                                .then_inc(s["scan"] if not (d == 1 and i == NB - 2) else s["states"], 1)
                            if not (d == 1 and i == NB - 2):
                                n += 1
                                dve.wait_ge(s["scan"], p * (2 * NB - 3) + n)
                            before = after
                    for j in range(NT):
                        dve.wait_ge(s["scores"], p * NT + (j + 1))
                        if j >= 2:
                            dve.wait_ge(s["y_mm"], p * NT + (j - 1))
                        for d in range(2):
                            nc.vector.tensor_tensor(sc[:, j % 2, d], bank[j % 2][:, 0:2 * P].rearrange("p (h i) -> p h i", h=2),
                                                    din[:, d], ALU.mult).then_inc(s["sc_ready"], 1)
                    for d in range(2):
                        for c in range(2):
                            dve.wait_ge(s["sums"], p * 4 + (2 * d + c + 1))
                            nc.vector.tensor_scalar(tmp[:, d, c * BANK:(c + 1) * BANK], bank[4 + 2 * d + c][:, :],
                                                    1.0 / RET_DIM, EPS, ALU.mult, ALU.add).then_inc(s["ms"], 1)
                    dve.wait_ge(s["root"], p + 1)
                    for d in range(2):
                        dve.wait_ge(s["chain"], link(nc.vector.reciprocal(tmp[:, d, :], tmp[:, d, :])))
                    for d in range(2):
                        dve.wait_ge(s["chain"], link(nc.vector.tensor_tensor(y[:, d, :], y[:, d, :], tmp[:, d, :], ALU.mult)))
                    for d in range(2):
                        dve.wait_ge(s["silu"], p * 2 + (d + 1))
                        dve.wait_ge(s["chain"], link(nc.vector.tensor_tensor(y[:, d, :], y[:, d, :], g[:, d, :], ALU.mult)))
                    dve.wait_ge(s["stored"], p * 16 + 1)
                    nc.vector.tensor_tensor(lat[:, :], y[:, 0, :], y[:, 1, :], ALU.add).then_inc(s["lat_ready"], 1)
                    link.end()


NC = TT // CH
DECAY = math.exp(-0.5)
PCOL, PW = fill(0, [("conv_r", 3), ("conv_k", 3), ("conv_v", 3), ("a0", 1), ("w0", 2), ("k_k", 1), ("k_a", 1),
                    ("r_k", 1), ("lnw", 1), ("lnb", 1)])


def pcol(pcs, p, name, i=0):
    return pcs[:, ds(p, 1), PCOL[name] + i:PCOL[name] + i + 1].rearrange("q p c -> q (p c)")


def rwkv_prepare(nc, bank, cst, col, tabs, x, uT, prim, vT, wc, bonus, gate):
    U0 = 5 * RW
    NBK = TT // P
    CHS = [(0, BANK), (BANK, BANK), (2 * BANK, TT - 2 * BANK)]
    SEG = ((0, TC), (TC, TT))
    LAT = slice(TC, TT)
    w2, a2, g2 = x["rwkv_w2"][0], x["rwkv_a2"][0], x["rwkv_g2"][0]
    with Stage(nc, "prep") as st:
        rin = st.sb("rin", [P, 3, TT])
        raw = st.sb("raw", [P, 3, TT])
        u = st.sb("u", [P, 3, TT])
        wl, al = st.sb("wl", [P, TT]), st.sb("al", [64, TT])
        gl = st.sb("gl", [P, 2, T])
        keep = st.sb("keep", [P, TT])
        sig = st.sb("sig", [P, 2, TT])
        iclr = st.sb("iclr", [P, TT])
        cum = st.sb("cum", [P, 2, TT])
        ex = st.sb("ex", [P, 3, 2, TT])
        kk = st.sb("kk", [P, TT])
        prod = st.sb("prod", [P, TT])
        out = st.sb("out", [P, 2, 2, TT])
        gt = st.sb("gt", [P, 3, T])
        pcs = st.sb("pcs", [P, PAIRS, PW])
        w2t, a2t, g2t = st.sb("w2t", [P, P]), st.sb("a2t", [64, P]), st.sb("g2t", [P, 2, P])
        names = ("pc_in", "lora_in", "lora", "u_in", "w_in", "z_mm", "sig_ready", "chain", "cum_ready", "exp_ready",
                 "kx_ready", "kx_sq", "ss_mm", "norm", "bonus_in", "bonus_mm", "g_mm", "g_ready", "out0", "out1",
                 "gt_ready", "gt_stored", "vt_stored", "wc_stored", "pair_done", "turns")
        s = {n: st.sem(n) for n in names}
        stored = [[st.sem(f"stored{e}{i}") for i in range(2)] for e in range(2)]
        pair, pairx = (cst[:, CONST[n]:CONST[n] + P] for n in ("pair", "pairx"))
        chunked = [P, NC, CH]

        def conv(dst, src, w, rows, link, wait, segments):
            lo, hi = segments[0][0], segments[-1][1]
            o = lo
            wait(link(nc.vector.tensor_scalar(dst[:, 0:hi - o], src[:, lo:hi], w[1], None, ALU.mult)))
            for a, b in segments:
                wait(link(nc.vector.scalar_tensor_tensor(dst[:, a + 1 - o:b - o], src[:, a:b - 1], w[0],
                                                         dst[:, a + 1 - o:b - o], ALU.mult, ALU.add)))
                wait(link(nc.vector.scalar_tensor_tensor(dst[:, a - o:b - 1 - o], src[:, a + 1:b], w[2],
                                                         dst[:, a - o:b - 1 - o], ALU.mult, ALU.add)))

        with nc.Block() as block:
            @block.sync
            def _(sp):
                l0 = U0 + 3 * RW
                sp.dma_start(raw[:, 0, :], uT[l0:l0 + 128, :]).then_inc(s["lora_in"], 16)
                sp.dma_start(raw[0:64, 1, :], uT[l0 + 128:l0 + 192, :]).then_inc(s["lora_in"], 16)
                sp.dma_start(raw[:, 2, :], uT[l0 + 192:l0 + 320, :]).then_inc(s["lora_in"], 16)
                sp.dma_start(ex[:, 0, 0, :], uT[l0 + 320:l0 + 448, :]).then_inc(s["lora_in"], 16)
                sp.dma_start(pcs[:, :, :], tabs["pcols"].rearrange("q p c -> p q c")).then_inc(s["pc_in"], 16)

            @block.vector
            def _(dve):
                link = Steps(s["lora"])

                def wait(n):
                    dve.wait_ge(s["lora"], n)

                link(nc.vector.memset(keep[:, :], 1.0))
                wait(link.n)
                link(nc.vector.memset(keep[:, :].rearrange("p (n c) -> p n c", c=CH)[:, :, 0:1], 0.0))
                dve.wait_ge(s["lora_in"], 64)
                for n, (dst, src, rows, seg) in enumerate(((wl, raw[:, 0, :], P, SEG), (al, raw[0:64, 1, :], 64, SEG),
                                                           (gl[:, 0, :], raw[:, 2, :], P, SEG[1:]),
                                                           (gl[:, 1, :], ex[:, 0, 0, :], P, SEG[1:]))):
                    c0 = COLS["conv"] + 12 + n
                    conv(dst, src, [col[0:rows, c0 + 16 * t:c0 + 16 * t + 1] for t in range(3)], rows, link, wait, seg)
                assert link.n == LORA

            @block.scalar
            def _(act):
                act.wait_ge(s["lora"], LORA)
                nc.scalar.activation(wl[:, :], wl[:, :], ACT.Tanh).then_inc(s["g_ready"], 1)
                nc.scalar.activation(gl[:, :, :], gl[:, :, :], ACT.Sigmoid).then_inc(s["g_ready"], 1)
                act.wait_ge(s["g_ready"], 2)

        with nc.Block() as block:
            @block.sync
            def _(sp):
                for n in stored[0] + stored[1] + [s["gt_stored"], s["vt_stored"], s["wc_stored"]]:
                    sp.sem_inc(n, 1)

                def load_rkv(p):
                    for n in range(2):
                        sp.dma_start(rin[:, n, :], uT[ds(p * P + (U0 + n * RW), P), :]).then_inc(s["u_in"], 16)
                    for h in range(2):
                        sp.dma_start(rin[64 * h:64 * h + 64, 2, :], uT[ds(p * P + (U0 + 2 * RW + 64 * (1 - h)), 64), :])\
                            .then_inc(s["u_in"], 16)

                def load_weights(p):
                    for h in range(2):
                        r = slice(64 * h, 64 * h + 64)
                        sp.dma_start(w2t[r, :], w2[h, :, ds(p * P, P)]).then_inc(s["w_in"], 16)
                        for d in range(2):
                            sp.dma_start(g2t[:, d, r], g2[d, :, ds(p * P + 64 * (1 - h), 64)]).then_inc(s["w_in"], 16)
                    sp.dma_start(a2t[:, :], a2[:, ds(p * P, P)]).then_inc(s["w_in"], 16)

                def pair_of_heads(p, last):
                    sp.wait_ge(s["kx_ready"], p + 1)
                    sp.sem_inc(s["turns"], 1)
                    sp.dma_start(vT[ds(p * NBK, NBK)].rearrange("b c t -> c b t"),
                                 u[:, 2, :].rearrange("p (b t) -> p b t", t=P)).then_inc(s["vt_stored"], 16)
                    if not last:
                        load_rkv(p + 1)
                    sp.wait_ge(s["g_mm"], p * 4 + 4)
                    sp.sem_inc(s["turns"], 1)
                    if not last:
                        load_weights(p + 1)
                    sp.wait_ge(s["exp_ready"], p * 3 + 3)
                    sp.sem_inc(s["turns"], 1)
                    for d in range(2):
                        at = CH - 1 if d == 0 else 0
                        with nc.allow_non_contiguous_dma("one value in a chunk"):
                            for n in range(2):
                                sp.dma_start(wc[ds(p * NBK, NBK), d, :, n].rearrange("b c -> c b"),
                                             ex[:, 0, d, :].rearrange("p (b n c) -> p b n c", n=2, c=CH)[:, :, n, at])\
                                    .then_inc(s["wc_stored"], 16)
                    for n in range(8):
                        sp.wait_ge(s[f"out{n % 2}"], p * 4 + (n // 2 + 1))
                        sp.sem_inc(s["turns"], 1)
                        sp.dma_start(prim[ds(p * NBK, NBK), n].rearrange("b c t -> c b t"),
                                     out[:, n % 2, n // 2 % 2, :].rearrange("p (b t) -> p b t", t=P))\
                            .then_inc(stored[n % 2][n // 2 % 2], 16)
                    sp.wait_ge(s["gt_ready"], p * 3 + 3)
                    sp.sem_inc(s["turns"], 1)
                    sp.dma_start(bonus[ds(p * P, P), :], gt[:, 2, :]).then_inc(s["gt_stored"], 16)
                    sp.dma_start(gate[:, ds(p * P, P), :].rearrange("d c t -> c d t"), gt[:, 0:2, :])\
                        .then_inc(s["gt_stored"], 16)

                load_rkv(0)
                load_weights(0)
                with sp.Fori(0, PAIRS - 1) as p:
                    pair_of_heads(p, False)
                pair_of_heads(PAIRS - 1, True)
                for n in stored[0] + stored[1]:
                    sp.wait_ge(n, 32 * PAIRS + 1)
                sp.wait_ge(s["vt_stored"], 16 * PAIRS + 1)
                sp.wait_ge(s["wc_stored"], 64 * PAIRS + 1)
                sp.wait_ge(s["gt_stored"], 32 * PAIRS + 1)

            @block.gpsimd
            def _(pool):
                with pool.Fori(0, PAIRS) as p:
                    pool.wait_ge(s["exp_ready"], p * 3 + 3)
                    for i, (src, e, d, ready) in enumerate(((u[:, 0, :], 0, 0, None), (u[:, 0, :], 0, 1, None),
                                                            (iclr[:, :], 1, 1, "b"), (raw[:, 2, :], 1, 1, None))):
                        if ready:
                            pool.wait_ge(s["out0"], p * 4 + 3)
                        pool.wait_ge(stored[1][i % 2], p * 32 + (16 * (i // 2) + 1))
                        nc.gpsimd.tensor_tensor(out[:, 1, i % 2, :], src, ex[:, e, d, :], ALU.mult).then_inc(s["out1"], 1)

            @block.tensor
            def _(pe):
                with pe.Fori(0, PAIRS) as p:
                    pe.wait_ge(s["w_in"], p * 112 + 112)
                    pe.wait_ge(s["pair_done"], p + 1)
                    for n in range(3):
                        for c, (a, m) in enumerate(CHS):
                            if n == 2:
                                pe.wait_ge(s["sig_ready"], p * 9 + (c + 1))
                            lhsT, rhs = ((w2t[0:64, :], wl[0:64, a:a + m]), (w2t[64:128, :], wl[64:128, a:a + m]),
                                         (a2t[:, :], al[:, a:a + m]))[n]
                            nc.tensor.matmul(bank[3 * (n % 2) + c][:, 0:m], lhsT, rhs, start=True, stop=True)\
                                .then_inc(s["z_mm"], 1)
                    pe.wait_ge(s["sig_ready"], p * 9 + 9)
                    pe.wait_ge(s["kx_sq"], p + 1)
                    for c, (a, m) in enumerate(CHS):
                        nc.tensor.matmul(bank[c][:, 0:m], pair, prod[:, a:a + m], start=True, stop=True)\
                            .then_inc(s["ss_mm"], 1)
                    for d in range(2):
                        for c in range(2):
                            nc.tensor.matmul(bank[3 + 2 * d + c][:, :], g2t[:, d, :], gl[:, d, c * BANK:(c + 1) * BANK],
                                             start=True, stop=True).then_inc(s["g_mm"], 1)
                    pe.wait_ge(s["norm"], p * 3 + 3)
                    pe.wait_ge(s["bonus_in"], p + 1)
                    for c in range(2):
                        nc.tensor.matmul(bank[c][:, :], pairx, prod[:, TC + c * BANK:TC + (c + 1) * BANK],
                                         start=True, stop=True).then_inc(s["bonus_mm"], 1)

            @block.scalar
            def _(act):
                with act.Fori(0, PAIRS) as p:
                    for n in range(3):
                        for c, (a, m) in enumerate(CHS):
                            act.wait_ge(s["z_mm"], p * 9 + (3 * n + c + 1))
                            act.sem_inc(s["turns"], 1)
                            o = (sig[:, 0, a:a + m], sig[:, 1, a:a + m], iclr[:, a:a + m])[n]
                            b = pcol(pcs, p, "w0", n) if n < 2 else pcol(pcs, p, "a0")
                            nc.scalar.activation(o, bank[3 * (n % 2) + c][:, 0:m], ACT.Sigmoid, bias=b)\
                                .then_inc(s["sig_ready"], 1)
                    act.wait_ge(s["kx_ready"], p + 1)
                    nc.scalar.activation(prod[:, :], kk[:, :], ACT.Square).then_inc(s["kx_sq"], 1)
                    act.wait_ge(s["gt_stored"], p * 32 + 1)
                    for d in range(2):
                        for c in range(2):
                            act.wait_ge(s["g_mm"], p * 4 + (2 * d + c + 1))
                            nc.scalar.activation(gt[:, d, c * BANK:(c + 1) * BANK], bank[3 + 2 * d + c][:, :], ACT.Copy)\
                                .then_inc(s["g_ready"] if 2 * d + c < 3 else s["gt_ready"], 1)
                    for c, (a, m) in enumerate(CHS):
                        act.wait_ge(s["ss_mm"], p * 3 + (c + 1))
                        nc.scalar.activation(prod[:, a:a + m], bank[c][:, 0:m], ACT.Sqrt).then_inc(s["norm"], 1)
                    act.wait_ge(s["cum_ready"], p + 1)
                    act.wait_ge(s["wc_stored"], p * 64 + 1)
                    nc.scalar.activation(ex[:, 2], cum[:, :, :], ACT.Exp, scale=-DECAY).then_inc(s["exp_ready"], 1)
                    nc.scalar.activation(ex[:, 0], raw[:, 0:2, :], ACT.Exp, scale=-DECAY).then_inc(s["exp_ready"], 1)
                    nc.scalar.activation(ex[:, 1], raw[:, 0:2, :], ACT.Exp, scale=DECAY).then_inc(s["exp_ready"], 1)

            @block.vector
            def _(dve):
                dve.sem_inc(s["pair_done"], 1)
                with dve.Fori(0, PAIRS) as p:
                    link = Loop(s["chain"], p, CHAIN)

                    def wait(n):
                        dve.wait_ge(s["chain"], n)

                    def c_(name, i=0):
                        return pcol(pcs, p, name, i)

                    dve.wait_ge(s["u_in"], p * 64 + 64)
                    dve.wait_ge(s["pc_in"], 16)
                    dve.wait_ge(s["vt_stored"], p * 16 + 1)
                    for n, nm in enumerate(("conv_r", "conv_k", "conv_v")):
                        conv(u[:, n, :], rin[:, n, :], [c_(nm, t) for t in range(3)], P, link, wait, SEG)
                    nc.vector.tensor_scalar(kk[:, :], u[:, 1, :], c_("k_k"), None, ALU.mult).then_inc(s["kx_ready"], 1)
                    dve.wait_ge(s["sig_ready"], p * 9 + 9)
                    wait(link(nc.vector.tensor_tensor_scan(raw[:, 0, :], keep[:, :], sig[:, 0, :], 0.0, ALU.mult, ALU.add)))
                    wait(link(nc.vector.tensor_tensor_scan(raw[:, 2, :], keep[:, :], sig[:, 1, :], 0.0, ALU.mult, ALU.add)))
                    link(nc.vector.tensor_tensor(cum[:, 0, :], raw[:, 0, :], sig[:, 0, :], ALU.subtract))
                    c2 = raw[:, 2, :].rearrange("p (n c) -> p n c", c=CH)
                    wait(link(nc.vector.tensor_tensor(cum[:, 1, :].rearrange("p (n c) -> p n c", c=CH),
                                                      c2[:, :, CH - 1:CH].to_broadcast(chunked), c2, ALU.subtract)))
                    nc.vector.tensor_tensor(raw[:, 1, :], cum[:, 1, :], sig[:, 1, :], ALU.add).then_inc(s["cum_ready"], 1)
                    wait(link(nc.vector.tensor_scalar(raw[:, 2, :], iclr[:, :], 1.0, c_("k_a"), ALU.subtract, ALU.mult)))
                    wait(link(nc.vector.scalar_tensor_tensor(raw[:, 2, :], raw[:, 2, :], 1.0, u[:, 1, :], ALU.add, ALU.mult)))
                    dve.wait_ge(s["norm"], p * 3 + 3)
                    wait(link(nc.vector.tensor_scalar(prod[:, :], prod[:, :], 1e-12, None, ALU.max)))
                    wait(link(nc.vector.reciprocal(prod[:, :], prod[:, :])))
                    wait(link(nc.vector.tensor_tensor(kk[:, :], kk[:, :], prod[:, :], ALU.mult)))
                    nc.vector.scalar_tensor_tensor(prod[:, :], u[:, 0, :], c_("r_k"), raw[:, 2, :], ALU.mult, ALU.mult)\
                        .then_inc(s["bonus_in"], 1)
                    wait(link(nc.vector.tensor_tensor(iclr[:, :], kk[:, :], iclr[:, :], ALU.mult)))
                    dve.wait_ge(s["exp_ready"], p * 3 + 3)
                    for i, (src, e, d) in enumerate(((None, 2, 0), (None, 2, 1), (iclr[:, :], 1, 0), (raw[:, 2, :], 1, 0))):
                        dve.wait_ge(stored[0][i % 2], p * 32 + (16 * (i // 2) + 1))
                        if src is None:
                            ins = nc.vector.scalar_tensor_tensor(out[:, 0, i % 2, :], kk[:, :], -1.0, ex[:, e, d, :], ALU.mult, ALU.mult)
                        else:
                            ins = nc.vector.tensor_tensor(out[:, 0, i % 2, :], src, ex[:, e, d, :], ALU.mult)
                        ins.then_inc(s["out0"], 1)
                    for c in range(2):
                        dve.wait_ge(s["bonus_mm"], p * 2 + (c + 1))
                        nc.vector.tensor_tensor(gt[:, 2, c * BANK:(c + 1) * BANK], bank[c][:, :],
                                                u[:, 2, TC + c * BANK:TC + (c + 1) * BANK], ALU.mult)\
                            .then_inc(s["gt_ready"], 1)
                    link.end()
                    dve.wait_ge(s["gt_ready"], p * 3 + 3)
                    dve.wait_ge(s["out1"], p * 4 + 4)
                    dve.sem_inc(s["pair_done"], 1)


LORA = 18
CHAIN = 25


def rwkv_chunks(nc, bank, cst, tabs, prim, vT, wc, mt, nn, re, yi):
    NBK = TT // P
    UN = 4
    NL = len(LEVELS)
    with Stage(nc, "chunks") as st:
        ar = st.sb("ar", [P, 2, 2, 2, P])
        bk = st.sb("bk", [P, 2, 2, 2, 2, P])
        vt = st.sb("vt", [P, 2, P])
        wct = st.sb("wct", [P, 2, 2, 2])
        msk = st.sb("msk", [P, 2, NL + 1, 2 * P], I32)
        vrow = st.sb("vrow", [P, P])
        vz = st.sb("vz", [P, 2, P])
        vm = st.sb("vm", [P, 2, 2, CH])
        LL = st.sb("LL", [P, UN, 2, 2 * P])
        X = st.sb("X", [P, UN, 2 * P])
        T1 = st.sb("T1", [P, UN, P])
        rows = st.sb("rows", [P, UN, 2, P])
        bm = st.sb("bm", [P, UN, 2, CH])
        Y0 = st.sb("Y0", [P, UN, P])
        TT_ = st.sb("TT", [P, UN, P])
        tvm = st.sb("tvm", [P, UN, 2, CH])
        mts, nns = st.sb("mts", [P, 2, 2, CH]), st.sb("nns", [P, 2, 2, CH])
        res, yis = st.sb("res", [P, 2, P]), st.sb("yis", [P, 2, P])
        names = ("msk_in", "zeroed", "in0", "in1", "v_mm", "v_ev", "vz_ready", "g_mm", "g_ev", "x_init", "lab_mm", "lab_ev",
                 "x_one", "rows_mm", "rows_ev", "a_ev", "bm_ready", "lakv_mm", "lakv_ev", "t1_mm", "t1_ev", "p_mm", "x_ev",
                 "ta_mm", "ta_ev", "tvm_ready", "y_mm", "re_ev", "yi_ev", "m_mm", "mt_ev", "n_ev", "stored", "turns")
        s = {n: st.sem(n) for n in names}
        s_in = [s["in0"], s["in1"]]
        ident = cst[:, CONST["ident"]:CONST["ident"] + P]
        ident2 = cst[:, CONST["ident2"]:CONST["ident2"] + 2 * P]
        hm = [cst[:, CONST["hm"] + P * h:CONST["hm"] + P * (h + 1)] for h in range(2)]
        cmask = cst[:, CONST["cmask"]:CONST["cmask"] + P].rearrange("p (c k) -> p c k", c=2)
        idc = cst[:, CONST["idc"]:CONST["idc"] + CH]
        stm = [cst[:, CONST[n]:CONST[n] + 2 * P] for n in ("st_f", "st_b")]
        A = lambda u_: bank[u_]
        B = lambda u_: bank[4 + u_]
        ITS = PAIRS * NBK // 2

        def each(fn):
            for u_ in range(UN):
                fn(u_, u_ // 2, u_ % 2)

        with nc.Block() as block:
            @block.sync
            def _(sp):
                sp.sem_inc(s["stored"], 1)
                sp.dma_start(msk[:, :, :, :], tabs["msk"].rearrange("d l p c -> p d l c")).then_inc(s["msk_in"], 16)
                sp.wait_ge(s["zeroed"], 1)

                def load(q, k):
                    for d in range(2):
                        sp.dma_start(ar[:, k, d], prim[ds(q, 1), 2 * d:2 * d + 2].rearrange("o n c t -> c (o n) t"))\
                            .then_inc(s_in[k], 16)
                        for h in range(2):
                            r = slice(64 * h, 64 * h + 64)
                            for n in range(2):
                                sp.dma_start(bk[r, k, d, h, n, :], prim[ds(q, 1), 4 + 2 * n + d, r]
                                             .rearrange("o c t -> c (o t)")).then_inc(s_in[k], 16)
                    with nc.allow_non_contiguous_dma("four values a channel"):
                        sp.dma_start(wct[:, k], wc[ds(q, 1)].rearrange("o d c n -> c (o d) n")).then_inc(s_in[k], 16)
                    sp.dma_start(vt[:, k, :], vT[ds(q, 1)].rearrange("o c t -> c (o t)")).then_inc(s_in[k], 16)

                def store(q, k):
                    sp.wait_ge(s["mt_ev"], q * 2 + 3)
                    sp.wait_ge(s["n_ev"], q * 4 + 5)
                    sp.wait_ge(s["re_ev"], q * 4 + 5)
                    sp.wait_ge(s["yi_ev"], q * 4 + 5)
                    for dst, src in ((mt, mts), (nn, nns)):
                        sp.dma_start(dst[ds(q, 1)].rearrange("o d c n k -> n (o d) c k"), src[:, :, :, :])\
                            .then_inc(s["stored"], 16)
                    for dst, src in ((re, res), (yi, yis)):
                        sp.dma_start(dst[ds(q, 1)].rearrange("o d c t -> c (o d) t"), src[:, :, :])\
                            .then_inc(s["stored"], 16)

                for k in range(2):
                    load(k, k)
                with sp.Fori(0, ITS - 1) as it:
                    for k in range(2):
                        store(it * 2 + k, k)
                        load(it * 2 + (2 + k), k)
                for k in range(2):
                    store(2 * (ITS - 1) + k, k)
                sp.wait_ge(s["stored"], 64 * 2 * ITS + 1)

            INC = 16 * 12

            @block.gpsimd
            def _(pool):
                nc.gpsimd.memset(bk[:, :, :, :, :, :], 0.0).then_inc(s["zeroed"], 1)
                with pool.Fori(0, ITS) as it:
                    for k in range(2):
                        q = it * 2 + k
                        pool.wait_ge(s["m_mm"], q * 2 + 1)
                        for u_ in range(UN):
                            nc.gpsimd.tensor_tensor(X[:, u_, :], ident2, ident2, ALU.mult).then_inc(s["x_init"], 1)
                        pool.wait_ge(s["v_ev"], q + 1)
                        for h in range(2):
                            nc.gpsimd.tensor_tensor(vz[:, h, :], vrow[:, :], hm[1 - h], ALU.mult).then_inc(s["vz_ready"], 1)
                            vh = vrow[:, CH * (1 - h):CH * (1 - h) + CH]
                            nc.gpsimd.tensor_tensor(vm[:, h], vh.unsqueeze(1).to_broadcast([P, 2, CH]), cmask, ALU.mult)\
                                .then_inc(s["vz_ready"], 1)
                        for u_ in range(UN):
                            h = u_ % 2
                            pool.wait_ge(s["rows_ev"], q * 4 + (u_ + 1))
                            bh = rows[:, u_, 0, CH * h:CH * h + CH]
                            nc.gpsimd.tensor_tensor(bm[:, u_], bh.unsqueeze(1).to_broadcast([P, 2, CH]), cmask, ALU.mult)\
                                .then_inc(s["bm_ready"], 1)
                        for u_ in range(UN):
                            h = u_ % 2
                            pool.wait_ge(s["ta_ev"], q * 4 + (u_ + 1))
                            tv = TT_[:, u_, CH * (1 - h):CH * (1 - h) + CH]
                            nc.gpsimd.tensor_tensor(tvm[:, u_], tv.unsqueeze(1).to_broadcast([P, 2, CH]), cmask, ALU.mult)\
                                .then_inc(s["tvm_ready"], 1)

            @block.tensor
            def _(pe):
                pe.sem_inc(s["m_mm"], 1)
                with pe.Fori(0, ITS) as it:
                    for k in range(2):
                        q = it * 2 + k
                        pe.wait_ge(s_in[k], it * INC + INC)
                        pe.wait_ge(s["mt_ev"], q * 2 + 1)
                        pe.wait_ge(s["n_ev"], q * 4 + 1)

                        def g(u_, d, h):
                            for n in range(2):
                                ins = nc.tensor.matmul(A(u_)[:, n * 256:n * 256 + 256], bk[:, k, d, h, n, :],
                                                       ar[:, k, d].rearrange("p a t -> p (a t)"), start=True, stop=True)
                            ins.then_inc(s["g_mm"], 1)
                        each(g)
                        pe.wait_ge(s["re_ev"], q * 4 + 1)
                        pe.wait_ge(s["yi_ev"], q * 4 + 1)

                        def lab(u_, d, h):
                            nc.tensor.matmul(B(u_)[:, 0:P], ar[:, k, d, 0, :], bk[:, k, d, h, 0, :], start=True, stop=True)\
                                .then_inc(s["lab_mm"], 1)
                        each(lab)

                        def by_rows(u_, d, h):
                            pe.wait_ge(s["g_ev"], q * 4 + (u_ + 1))
                            nc.tensor.transpose(A(u_)[:, 0:P], bk[:, k, d, h, 0, :], ident)
                            nc.tensor.transpose(A(u_)[:, P:2 * P], bk[:, k, d, h, 1, :], ident)
                            nc.tensor.transpose(A(u_)[:, 2 * P:3 * P], ar[:, k, d, 0, :], ident).then_inc(s["rows_mm"], 1)
                        each(by_rows)
                        pe.wait_ge(s["x_one"], q * 4 + 1)
                        nc.tensor.transpose(B(0)[:, 0:P], vt[:, k, :], ident).then_inc(s["v_mm"], 1)
                        pe.wait_ge(s["v_ev"], q + 1)

                        def lakv(u_, d, h):
                            pe.wait_ge(s["x_one"], q * 4 + (u_ + 1))
                            nc.tensor.matmul(B(u_)[:, 0:P], LL[:, u_, 1, 0:P], vrow[:, :], start=True, stop=True)\
                                .then_inc(s["lakv_mm"], 1)
                        each(lakv)
                        for l in range(NL):
                            def t1(u_, d, h):
                                if l == 0:
                                    pe.wait_ge(s["rows_ev"], q * 4 + (u_ + 1))
                                    pe.wait_ge(s["a_ev"], q * 4 + (u_ + 1))
                                else:
                                    pe.wait_ge(s["x_ev"], q * 20 + (4 * (l - 1) + u_ + 1))
                                nc.tensor.matmul(A(u_)[:, 0:P], LL[:, u_, 0, 0:P], X[:, u_, 0:P], start=True, stop=True)\
                                    .then_inc(s["t1_mm"], 1)
                            each(t1)

                            def pp(u_, d, h):
                                pe.wait_ge(s["t1_ev"], q * 20 + (4 * l + u_ + 1))
                                if l == 0:
                                    pe.wait_ge(s["lakv_ev"], q * 4 + (u_ + 1))
                                if l < NL - 1:
                                    nc.tensor.matmul(B(u_)[:, 0:P], X[:, u_, P:2 * P], T1[:, u_, :], start=True, stop=True)
                                nc.tensor.matmul(B(u_)[:, P:2 * P], T1[:, u_, :], X[:, u_, P:2 * P], start=True, stop=True)\
                                    .then_inc(s["p_mm"], 1)
                            each(pp)

                        def ta(u_, d, h):
                            pe.wait_ge(s["x_ev"], q * 20 + (4 * (NL - 1) + u_ + 1))
                            nc.tensor.matmul(A(u_)[:, 0:P], X[:, u_, P:2 * P], Y0[:, u_, :], start=True, stop=True)\
                                .then_inc(s["ta_mm"], 1)
                        each(ta)
                        pe.wait_ge(s["vz_ready"], q * 4 + 4)

                        def yy(u_, d, h):
                            pe.wait_ge(s["ta_ev"], q * 4 + (u_ + 1))
                            nc.tensor.matmul(B(u_)[:, 0:P], TT_[:, u_, :], LL[:, u_, 0, P:2 * P], start=True, stop=False)
                            nc.tensor.matmul(B(u_)[:, 0:P], vz[:, h, :], LL[:, u_, 1, P:2 * P], start=False, stop=True)\
                                .then_inc(s["y_mm"], 1)
                        each(yy)
                        pe.wait_ge(s["bm_ready"], q * 4 + 4)
                        pe.wait_ge(s["tvm_ready"], q * 4 + 4)
                        for d in range(2):
                            for h in range(2):
                                u_ = 2 * d + h
                                nc.tensor.matmul(A(2 * d)[64 * h:64 * h + 64, 0:P], TT_[:, u_, CH * h:CH * h + CH],
                                                 bm[:, u_].rearrange("p c k -> p (c k)"), start=True, stop=True)
                            for h in range(2):
                                u_ = 2 * d + h
                                nc.tensor.matmul(A(2 * d + 1)[:, 0:P], rows[:, u_, 0, :],
                                                 tvm[:, u_].rearrange("p c k -> p (c k)"), start=(h == 0), stop=False)
                                ins = nc.tensor.matmul(A(2 * d + 1)[:, 0:P], rows[:, u_, 1, :],
                                                       vm[:, h].rearrange("p c k -> p (c k)"), start=False, stop=(h == 1))
                            ins.then_inc(s["m_mm"], 1)

            @block.scalar
            def _(act):
                act.sem_inc(s["n_ev"], 1)
                act.sem_inc(s["yi_ev"], 1)
                with act.Fori(0, ITS) as it:
                    for k in range(2):
                        q = it * 2 + k

                        def by_rows(u_, d, h):
                            act.wait_ge(s["rows_mm"], q * 4 + (u_ + 1))
                            nc.scalar.activation(rows[:, u_].rearrange("p a t -> p (a t)"), A(u_)[:, 0:2 * P], ACT.Copy)\
                                .then_inc(s["rows_ev"], 1)
                            nc.scalar.activation(Y0[:, u_, CH * h:CH * h + CH],
                                                 A(u_)[:, 2 * P + CH * h:2 * P + CH * h + CH], ACT.Copy)\
                                .then_inc(s["a_ev"], 1)
                        each(by_rows)
                        act.wait_ge(s["v_mm"], q + 1)
                        nc.scalar.activation(vrow[:, :], B(0)[:, 0:P], ACT.Copy).then_inc(s["v_ev"], 1)

                        def lakv(u_, d, h):
                            c = slice(CH * (1 - h), CH * (1 - h) + CH)
                            act.wait_ge(s["lakv_mm"], q * 4 + (u_ + 1))
                            nc.scalar.activation(Y0[:, u_, c], B(u_)[:, c], ACT.Copy).then_inc(s["lakv_ev"], 1)
                        each(lakv)
                        for l in range(NL):
                            def t1(u_, d, h):
                                act.wait_ge(s["t1_mm"], q * 20 + (4 * l + u_ + 1))
                                nc.scalar.activation(T1[:, u_, :], A(u_)[:, 0:P], ACT.Copy).then_inc(s["t1_ev"], 1)
                            each(t1)

                        def ta(u_, d, h):
                            act.wait_ge(s["ta_mm"], q * 4 + (u_ + 1))
                            nc.scalar.activation(TT_[:, u_, :], A(u_)[:, 0:P], ACT.Copy).then_inc(s["ta_ev"], 1)
                        each(ta)
                        act.wait_ge(s["stored"], q * 64 + 1)

                        def yy(u_, d, h):
                            r = slice(64 * (1 - h), 64 * (1 - h) + 64)
                            act.wait_ge(s["y_mm"], q * 4 + (u_ + 1))
                            nc.scalar.activation(yis[r, d, :], B(u_)[r, 0:P], ACT.Copy).then_inc(s["yi_ev"], 1)
                        each(yy)
                        for d in range(2):
                            act.wait_ge(s["m_mm"], q * 2 + (d + 2))
                            for c in range(2):
                                nc.scalar.activation(nns[:, d, c, :], A(2 * d + 1)[:, CH * c:CH * c + CH], ACT.Copy,
                                                     scale=wct[:, k, d, c:c + 1]).then_inc(s["n_ev"], 1)

            @block.vector
            def _(dve):
                dve.sem_inc(s["mt_ev"], 1)
                dve.sem_inc(s["re_ev"], 1)
                dve.wait_ge(s["msk_in"], 16)
                with dve.Fori(0, ITS) as it:
                    for k in range(2):
                        q = it * 2 + k

                        def g(u_, d, h):
                            dve.wait_ge(s["g_mm"], q * 4 + (u_ + 1))
                            nc.vector.tensor_tensor(LL[:, u_], A(u_)[:, :].rearrange("p (a t) -> p a t", a=2),
                                                    stm[d].unsqueeze(1).to_broadcast([P, 2, 2 * P]), ALU.mult)\
                                .then_inc(s["g_ev"], 1)
                        each(g)
                        dve.wait_ge(s["x_init"], q * 4 + 4)

                        def one(u_, d, h):
                            dve.wait_ge(s["lab_mm"], q * 4 + (u_ + 1))
                            dve.sem_inc(s["turns"], 1)
                            nc.vector.copy_predicated(X[:, u_, 0:P], msk[:, d, 0, 0:P], B(u_)[:, 0:P]).then_inc(s["lab_ev"], 1)
                            dve.wait_ge(s["g_ev"], q * 4 + (u_ + 1))
                            dve.sem_inc(s["turns"], 1)
                            nc.vector.copy_predicated(X[:, u_, P:2 * P], msk[:, d, 0, P:2 * P], LL[:, u_, 0, 0:P])\
                                .then_inc(s["x_one"], 1)
                        each(one)
                        dve.wait_ge(s["lab_ev"], q * 4 + 4)
                        for l in range(NL):
                            def pp(u_, d, h):
                                dve.wait_ge(s["p_mm"], q * 20 + (4 * l + u_ + 1))
                                if l:
                                    dve.wait_ge(s["x_ev"], q * 20 + (4 * (l - 1) + u_ + 1))
                                dve.sem_inc(s["turns"], 1)
                                c = slice(0 if l < NL - 1 else P, 2 * P)
                                nc.vector.copy_predicated(X[:, u_, c], msk[:, d, 1 + l, c], B(u_)[:, c])\
                                    .then_inc(s["x_ev"], 1)
                            each(pp)
                        dve.wait_ge(s["stored"], q * 64 + 1)

                        def yy(u_, d, h):
                            r = slice(64 * h, 64 * h + 64)
                            dve.wait_ge(s["y_mm"], q * 4 + (u_ + 1))
                            nc.vector.tensor_tensor(res[r, d, :], B(u_)[r, 0:P], ar[r, k, d, 1, :], ALU.add)\
                                .then_inc(s["re_ev"], 1)
                        each(yy)
                        for d in range(2):
                            dve.wait_ge(s["m_mm"], q * 2 + (d + 2))
                            nc.vector.tensor_tensor(mts[:, d], A(2 * d)[:, 0:P].rearrange("p (c k) -> p c k", c=2),
                                                    idc.unsqueeze(1).to_broadcast([P, 2, CH]), ALU.add)\
                                .then_inc(s["mt_ev"], 1)


def rwkv_states(nc, bank, wc, mt, nn, re, yi, yT):
    RING = 4
    NBK = TT // P
    with Stage(nc, "states") as st:
        m = st.sb("m", [P, RING, 2, PAIRS, P])
        n_ = st.sb("n", [P, RING, 2, PAIRS, P])
        w = st.sb("w", [P, 2, PAIRS * NBK, 2])
        S = st.sb("S", [P, 2, 2, PAIRS, P])
        r = st.sb("r", [P, 2, PAIRS, NT, P])
        y = st.sb("y", [P, 2, PAIRS, NT, P])
        mn_in = [st.sem(f"mn_in{i}") for i in range(RING)]
        zeroed, ry_in, w_in = st.sem("zeroed"), st.sem("ry_in"), st.sem("w_in")
        p_mm, s_ready, y_mm, y_ready, stored = (st.sem(x) for x in ("p_mm", "s_ready", "y_mm", "y_ready", "stored"))
        C0 = TC // CH
        order = [list(range(NC)), list(range(C0))[::-1] + list(range(C0, NC))[::-1]]
        with nc.Block() as block:
            @block.gpsimd
            def _(pool):
                nc.gpsimd.memset(m[:, :, :, :, :], 0.0).then_inc(zeroed, 1)
                nc.gpsimd.memset(n_[:, :, :, :, :], 0.0).then_inc(zeroed, 1)
                nc.gpsimd.memset(S[:, :, :, :, :], 0.0).then_inc(zeroed, 1)

            def loads(eng, d, i):
                slot, c = i % RING, order[d][i]
                for h in range(2):
                    rr = slice(64 * h, 64 * h + 64)
                    eng.dma_start(m[rr, slot, d, :, 64 * h:64 * h + 64],
                                  mt[c // 2::NBK, d, c % 2, rr].rearrange("p r k -> r p k")).then_inc(mn_in[slot], 16)
                    eng.dma_start(n_[rr, slot, d, :, 64 * (1 - h):64 * (1 - h) + 64],
                                  nn[c // 2::NBK, d, c % 2, rr].rearrange("p r k -> r p k")).then_inc(mn_in[slot], 16)

            @block.sync
            def _(sp):
                sp.wait_ge(zeroed, 3)
                with nc.allow_non_contiguous_dma("four values a channel"):
                    for d in range(2):
                        sp.dma_start(w[:, d], wc[:, d].rearrange("q c n -> c q n")).then_inc(w_in, 16)
                for i in range(NC - 1):
                    if i >= RING:
                        sp.wait_ge(s_ready, 8 * (i - RING + 1))
                    loads(sp, 0, i)
                    if i == 1:
                        for d in range(2):
                            for p in range(PAIRS):
                                b = slice(p * NBK + NTC, (p + 1) * NBK)
                                sp.dma_start(r[:, d, p], re[b, d].rearrange("b c t -> c b t")).then_inc(ry_in, 16)
                                sp.dma_start(y[:, d, p], yi[b, d].rearrange("b c t -> c b t")).then_inc(ry_in, 16)
                for d in range(2):
                    sp.wait_ge(y_ready, 2 * (NC - C0))
                    for p in range(PAIRS):
                        sp.dma_start(yT[d, p * P:(p + 1) * P, :], y[:, d, p].rearrange("c b t -> c (b t)"))\
                            .then_inc(stored, 16)
                sp.wait_ge(stored, 16 * 2 * PAIRS)

            @block.tensor
            def _(pe):
                pe.wait_ge(zeroed, 3)
                for i in range(NC):
                    for d in range(2):
                        c = order[d][i]
                        if i:
                            pe.wait_ge(s_ready, 8 * (i - 1) + 4 * (d + 1))
                        if i < NC - 1:
                            pe.wait_ge(mn_in[i % RING], 128 * (i // RING + 1))
                            for p in range(PAIRS):
                                ins = nc.tensor.matmul(bank[d][:, p * P:(p + 1) * P], m[:, i % RING, d, p, :],
                                                       S[:, i % 2, d, p, :], start=True, stop=True)
                            ins.then_inc(p_mm, 1)
                        if c >= C0:
                            if i == C0 and d == 0:
                                pe.wait_ge(ry_in, 16 * 4 * PAIRS)
                            if i > C0:
                                pe.wait_ge(y_ready, 2 * (i - C0 - 1) + d + 1)
                            for p in range(PAIRS):
                                ins = nc.tensor.matmul(bank[2 + d][:, p * P:(p + 1) * P], S[:, i % 2, d, p, :],
                                                       r[:, d, p, c // 2 - NTC, :], start=True, stop=True)
                            ins.then_inc(y_mm, 1)

            @block.scalar
            def _(act):
                act.wait_ge(zeroed, 3)
                for i in range(NC - 1):
                    if i >= RING:
                        act.wait_ge(s_ready, 8 * (i - RING + 1))
                    loads(act, 1, i)

            @block.vector
            def _(dve):
                dve.wait_ge(zeroed, 3)
                dve.wait_ge(w_in, 32)
                for i in range(NC):
                    for d in range(2):
                        c = order[d][i]
                        if i < NC - 1:
                            dve.wait_ge(p_mm, 2 * i + d + 1)
                            if i:
                                dve.wait_ge(s_ready, 8 * (i - 1) + 4 * (d + 1))
                            if d == 0 and i > C0:
                                dve.wait_ge(y_mm, 2 * (i - C0))
                            dve.wait_ge(mn_in[i % RING], 128 * (i // RING + 1))
                            for p in range(PAIRS):
                                nc.vector.scalar_tensor_tensor(S[:, (i + 1) % 2, d, p, :], bank[d][:, p * P:(p + 1) * P],
                                                               w[:, d, p * NBK + c // 2, c % 2:c % 2 + 1],
                                                               n_[:, i % RING, d, p, :], ALU.mult, ALU.add)\
                                    .then_inc(s_ready, 1)
                        if c >= C0:
                            dve.wait_ge(y_mm, 2 * (i - C0) + d + 1)
                            if i == C0 and d == 0:
                                dve.wait_ge(ry_in, 16 * 4 * PAIRS)
                            t = slice(CH * (c % 2), CH * (c % 2) + CH)
                            o = y[:, d, :, c // 2 - NTC, t]
                            nc.vector.tensor_tensor(o, bank[2 + d][:, :].rearrange("q (p t) -> q p t", p=PAIRS)[:, :, t], o,
                                                    ALU.add).then_inc(y_ready, 1)


def rwkv_combine(nc, bank, cst, tabs, yT, bonus, gate, latT):
    L = 2
    with Stage(nc, "comb") as st:
        y, g, b = st.sb("y", [P, L, 2, T]), st.sb("g", [P, L, 2, T]), st.sb("b", [P, L, T])
        sq = st.sb("sq", [P, L, 2, T])
        o = st.sb("o", [P, L, T])
        pcs = st.sb("pcs", [P, PAIRS, PW])
        names = ("turns", "pc_in", "y_in", "g_in", "mean_mm", "centred", "squared", "var_mm", "var", "root", "rstd", "scaled",
                 "affine", "with_bonus", "gated", "out")
        s = {n: st.sem(n) for n in names}
        stored = [st.sem(f"stored{k}") for k in range(L)]
        pair = cst[:, CONST["pair"]:CONST["pair"] + P]
        N = 2 * L
        units = [(k, d) for k in range(L) for d in range(2)]
        with nc.Block() as block:
            @block.sync
            def _(sp):
                sp.dma_start(pcs[:, :, :], tabs["pcols"].rearrange("q p c -> p q c")).then_inc(s["pc_in"], 16)
                for k in range(L):
                    sp.sem_inc(stored[k], 1)

                def load(it):
                    for k in range(L):
                        rows = ds(it * (L * P) + k * P, P)
                        sp.dma_start(y[:, k], yT[:, rows, :].rearrange("d c t -> c d t")).then_inc(s["y_in"], 16)
                    for k in range(L):
                        rows = ds(it * (L * P) + k * P, P)
                        sp.dma_start(g[:, k], gate[:, rows, :].rearrange("d c t -> c d t")).then_inc(s["g_in"], 16)
                        sp.dma_start(b[:, k], bonus[rows, :]).then_inc(s["g_in"], 16)

                def store(it):
                    for k in range(L):
                        sp.wait_ge(s["out"], it * L + (k + 1))
                        sp.sem_inc(s["turns"], 1)
                        sp.dma_start(latT[ds(it * (L * P) + (RW + k * P), P), :], o[:, k]).then_inc(stored[k], 16)

                load(0)
                with sp.Fori(0, PAIRS // L - 1) as it:
                    store(it)
                    load(it + 1)
                store(PAIRS // L - 1)
                for k in range(L):
                    sp.wait_ge(stored[k], 16 * (PAIRS // L) + 1)

            @block.tensor
            def _(pe):
                with pe.Fori(0, PAIRS // L) as it:
                    pe.wait_ge(s["y_in"], it * (16 * L) + 16 * L)
                    for u_, (k, d) in enumerate(units):
                        for c in range(2):
                            ins = nc.tensor.matmul(bank[2 * u_ + c][:, :], pair, y[:, k, d, c * BANK:(c + 1) * BANK],
                                                   start=True, stop=True)
                        ins.then_inc(s["mean_mm"], 1)
                    for u_, (k, d) in enumerate(units):
                        pe.wait_ge(s["squared"], it * N + (u_ + 1))
                        for c in range(2):
                            ins = nc.tensor.matmul(bank[2 * u_ + c][:, :], pair, sq[:, k, d, c * BANK:(c + 1) * BANK],
                                                   start=True, stop=True)
                        ins.then_inc(s["var_mm"], 1)

            @block.scalar
            def _(act):
                with act.Fori(0, PAIRS // L) as it:
                    for u_, (k, d) in enumerate(units):
                        act.wait_ge(s["centred"], it * N + (u_ + 1))
                        nc.scalar.activation(sq[:, k, d, :], y[:, k, d, :], ACT.Square).then_inc(s["squared"], 1)
                    for u_, (k, d) in enumerate(units):
                        act.wait_ge(s["var"], it * N + (u_ + 1))
                        nc.scalar.activation(sq[:, k, d, :], sq[:, k, d, :], ACT.Sqrt).then_inc(s["root"], 1)
                    for u_, (k, d) in enumerate(units):
                        act.wait_ge(s["scaled"], it * N + (u_ + 1))
                        act.sem_inc(s["turns"], 1)
                        nc.scalar.activation(y[:, k, d, :], y[:, k, d, :], ACT.Identity, scale=pcol(pcs, it * L + k, "lnw"),
                                             bias=pcol(pcs, it * L + k, "lnb")).then_inc(s["affine"], 1)

            @block.gpsimd
            def _(pool):
                with pool.Fori(0, PAIRS // L) as it:
                    for u_, (k, d) in enumerate(units):
                        pool.wait_ge(s["affine"], it * N + (u_ + 1))
                        nc.gpsimd.tensor_tensor(y[:, k, d, :], y[:, k, d, :], b[:, k, :], ALU.add).then_inc(s["with_bonus"], 1)

            @block.vector
            def _(dve):
                dve.wait_ge(s["pc_in"], 16)
                with dve.Fori(0, PAIRS // L) as it:
                    for u_, (k, d) in enumerate(units):
                        dve.wait_ge(s["mean_mm"], it * N + (u_ + 1))
                        for c in range(2):
                            t = slice(c * BANK, (c + 1) * BANK)
                            ins = nc.vector.scalar_tensor_tensor(y[:, k, d, t], bank[2 * u_ + c][:, :], -1.0 / RET_DIM, y[:, k, d, t],
                                                                 ALU.mult, ALU.add)
                        ins.then_inc(s["centred"], 1)
                    for u_, (k, d) in enumerate(units):
                        dve.wait_ge(s["var_mm"], it * N + (u_ + 1))
                        for c in range(2):
                            ins = nc.vector.tensor_scalar(sq[:, k, d, c * BANK:(c + 1) * BANK], bank[2 * u_ + c][:, :], 1.0 / RET_DIM,
                                                          GN_EPS, ALU.mult, ALU.add)
                        ins.then_inc(s["var"], 1)
                    dve.wait_ge(s["g_in"], it * (32 * L) + 32 * L)

                    def gated(u_):
                        k, d = units[u_]
                        dve.wait_ge(s["with_bonus"], it * N + (u_ + 1))
                        nc.vector.tensor_tensor(g[:, k, d, :], y[:, k, d, :], g[:, k, d, :], ALU.mult).then_inc(s["gated"], 1)
                        if d:
                            dve.wait_ge(s["gated"], it * N + (u_ + 1))
                            dve.wait_ge(stored[k], it * 16 + 1)
                            nc.vector.tensor_tensor(o[:, k, :], g[:, k, 0, :], g[:, k, 1, :], ALU.add).then_inc(s["out"], 1)

                    for u_, (k, d) in enumerate(units):
                        dve.wait_ge(s["root"], it * N + (u_ + 1))
                        nc.vector.reciprocal(sq[:, k, d, :], sq[:, k, d, :]).then_inc(s["rstd"], 1)
                        dve.wait_ge(s["rstd"], it * N + (u_ + 1))
                        nc.vector.tensor_tensor(y[:, k, d, :], y[:, k, d, :], sq[:, k, d, :], ALU.mult).then_inc(s["scaled"], 1)
                        if u_:
                            gated(u_ - 1)
                    gated(N - 1)


def rwkv(nc, bank, cst, col, tabs, x, uT, scratch, latT, upto=9):
    NBK = TT // P
    Q = PAIRS * NBK
    prim, vT = scratch("prim", Q, 8, P, P), scratch("vT", Q, P, P)
    wc, bonus, gate = scratch("wc", Q, 2, P, 2), scratch("bonus", RW, T), scratch("gate", 2, RW, T)
    rwkv_prepare(nc, bank, cst, col, tabs, x, uT, prim, vT, wc, bonus, gate)
    if upto < 2:
        return
    mt, nn = scratch("mt", Q, 2, 2, P, CH), scratch("nn", Q, 2, 2, P, CH)
    re, yi = scratch("re", Q, 2, P, P), scratch("yi", Q, 2, P, P)
    rwkv_chunks(nc, bank, cst, tabs, prim, vT, wc, mt, nn, re, yi)
    if upto < 3:
        return
    yT = scratch("yT", 2, RW, T)
    rwkv_states(nc, bank, wc, mt, nn, re, yi, yT)
    rwkv_combine(nc, bank, cst, tabs, yT, bonus, gate, latT)


def gemm_rows(nc, bank, name, cst, actT, K, w, x, out, hT, grow=None, exchanged=(), h_col=None, h_rows=None, h_out=None):
    KK = K // P
    per = 1 if h_rows is None else len(h_rows)
    with Stage(nc, name) as st:
        wt = st.sb("w", [P, KK, D])
        xt = st.sb("x", [P, 4, D])
        sq = st.sb("sq", [P, D])
        ss = st.sb("ss", [P, NT, 5])
        gb, yt = st.sb("g", [P, D]), st.sb("y", [P, D])
        w_in, g_in, x_in = [st.sem(f"w_in{c}") for c in range(2)], st.sem("g_in"), [st.sem(f"x_in{i}") for i in range(4)]
        mm, ssq, ms, root, rstd, scaled, out_ready = (st.sem(n) for n in
                                                      ("mm", "ssq", "ms", "root", "rstd", "scaled", "out_ready"))
        stored = [st.sem(f"stored{i}") for i in range(4)]
        sq2 = st.sb("sq2", [P, D])
        ht, hg = st.sb("h", [P, 2, D]), st.sb("hg", [P, per, D])
        hs = st.sb("hs", [P, NT, 4])
        hg_in, hsq, hms, hroot, hrstd, normed, tr = (st.sem(n) for n in
                                                     ("hg_in", "hsq", "hms", "hroot", "hrstd", "normed", "tr"))
        ev, h_stored = ([st.sem(f"{n}{i}") for i in range(2)] for n in ("ev", "h_stored"))
        ident = cst[:, CONST["ident"]:CONST["ident"] + P]
        WIN = 16 * (KK - len(exchanged) + 2 * len(exchanged))
        with nc.Block() as block:
            @block.sync
            def _(sp):
                for c in range(2):
                    cc = slice(c * BANK, (c + 1) * BANK)
                    for k in range(KK):
                        if k in exchanged:
                            for h in range(2):
                                sp.dma_start(wt[64 * h:64 * h + 64, k, cc],
                                             w[k * P + 64 * (1 - h):k * P + 64 * (1 - h) + 64, cc]).then_inc(w_in[c], 16)
                        else:
                            sp.dma_start(wt[:, k, cc], w[k * P:(k + 1) * P, cc]).then_inc(w_in[c], 16)
                    if c == 0 and grow is not None:
                        sp.dma_start(gb[:, :], grow.partition_broadcast(P).rearrange("p o d -> p (o d)")).then_inc(g_in, 16)
                for i in range(4):
                    sp.dma_start(xt[:, i, :], x[i * P:(i + 1) * P, :]).then_inc(x_in[i], 16)
                for i, row in enumerate(h_rows or ()):
                    sp.dma_start(hg[:, i, :], row.partition_broadcast(P).rearrange("p o d -> p (o d)")).then_inc(hg_in, 16)
                for i in range(NT):
                    sp.wait_ge(out_ready, (i + 1) if grow is not None else 2 * (i + 1))
                    sp.dma_start(out[i * P:(i + 1) * P, :], xt[:, i % 4, :]).then_inc(stored[i % 4], 16)
                    sp.wait_ge(normed, per * (i + 1))
                    if h_out is not None:
                        sp.dma_start(h_out[i * P:(i + 1) * P, :], ht[:, i % 2, :]).then_inc(h_stored[i % 2], 16)
                    if i + 4 < NT:
                        sp.wait_ge(stored[i % 4], 16 * (i // 4 + 1))
                        sp.dma_start(xt[:, i % 4, :], x[(i + 4) * P:(i + 5) * P, :]).then_inc(x_in[i % 4], 16)
                for i in range(4):
                    sp.wait_ge(stored[i], 16 * (NT // 4))
                if h_out is not None:
                    for i in range(2):
                        sp.wait_ge(h_stored[i], 16 * (NT // 2))

            @block.tensor
            def _(pe):
                def turn(i):
                    pe.wait_ge(normed, per * (i + 1))
                    if i >= 2:
                        for e in range(2):
                            pe.wait_ge(ev[e], i - 1)
                    for k in range(KD):
                        ins = nc.tensor.transpose(bank[4 + 2 * (i % 2) + k // 4][:, (k % 4) * P:(k % 4 + 1) * P],
                                                  ht[:, i % 2, k * P:(k + 1) * P], ident)
                    ins.then_inc(tr, 1)

                for i in range(NT):
                    for c in range(2):
                        if i == 0:
                            pe.wait_ge(w_in[c], WIN)
                        if i >= 2 and c == 0:
                            pe.wait_ge(scaled if grow is not None else out_ready, 2 * (i - 1))
                        for k in range(KK):
                            last = nc.tensor.matmul(bank[2 * (i % 2) + c][:, :], actT[:, k, i * P:(i + 1) * P],
                                                    wt[:, k, c * BANK:(c + 1) * BANK], start=(k == 0), stop=(k == KK - 1))
                        last.then_inc(mm, 1)
                    if i:
                        turn(i - 1)
                turn(NT - 1)

            def evacuate(eng, e, i):
                eng.wait_ge(tr, i + 1)
                b, t = bank[4 + 2 * (i % 2) + e], slice(i * P, (i + 1) * P)
                if h_col is None:
                    dst, src = hT[:, 4 * e:4 * e + 4, t], b[:, :].rearrange("p (k t) -> p k t", k=4)
                    ins = nc.vector.tensor_copy(dst, src) if e else nc.scalar.activation(dst, src, ACT.Copy)
                else:
                    for j in range(4):
                        k = 4 * e + j
                        dst, src = hT[:, k, t], b[:, j * P:(j + 1) * P]
                        ins = (nc.vector.tensor_scalar(dst, src, h_col[:, k:k + 1], None, ALU.mult) if e else
                               nc.scalar.activation(dst, src, ACT.Copy, scale=h_col[:, k:k + 1]))
                ins.then_inc(ev[e], 1)

            @block.scalar
            def _(act):
                for i in range(NT + 2):
                    if 1 <= i <= NT:
                        j = i - 1
                        act.wait_ge(out_ready, i if grow is not None else 2 * i)
                        if j:
                            act.wait_ge(hsq, j)
                        nc.scalar.activation(sq2[:, :], xt[:, j % 4, :], ACT.Square, accum_out=hs[:, j, 0:1]).then_inc(hsq, 1)
                        act.wait_ge(hms, i)
                        nc.scalar.activation(hs[:, j, 2:3], hs[:, j, 1:2], ACT.Sqrt).then_inc(hroot, 1)
                    if i >= 2:
                        evacuate(act, 0, i - 2)
                    if i < NT and grow is not None:
                        for c in range(2):
                            act.wait_ge(mm, 2 * i + c + 1)
                            if i or c:
                                act.wait_ge(ssq, 2 * i + c)
                            nc.scalar.activation(sq[:, c * BANK:(c + 1) * BANK], bank[2 * (i % 2) + c][:, :], ACT.Square,
                                                 accum_out=ss[:, i, c:c + 1]).then_inc(ssq, 1)
                        act.wait_ge(ms, i + 1)
                        nc.scalar.activation(ss[:, i, 3:4], ss[:, i, 2:3], ACT.Sqrt).then_inc(root, 1)

            @block.vector
            def _(dve):
                def norm(i):
                    dve.wait_ge(hsq, i + 1)
                    nc.vector.tensor_scalar(hs[:, i, 1:2], hs[:, i, 0:1], 1.0 / D, EPS, ALU.mult, ALU.add).then_inc(hms, 1)
                    dve.wait_ge(hroot, i + 1)
                    nc.vector.reciprocal(hs[:, i, 3:4], hs[:, i, 2:3]).then_inc(hrstd, 1)
                    dve.wait_ge(hrstd, i + 1)
                    if i >= 2:
                        dve.wait_ge(tr, i - 1)
                        if h_out is not None:
                            dve.wait_ge(h_stored[i % 2], 16 * (i // 2))
                    h, xs = ht[:, i % 2, :], xt[:, i % 4, :]
                    if h_rows is None:
                        nc.vector.tensor_scalar(h, xs, hs[:, i, 3:4], None, ALU.mult).then_inc(normed, 1)
                        return
                    if i == 0:
                        dve.wait_ge(hg_in, 16 * per)
                    nc.vector.scalar_tensor_tensor(h, xs, hs[:, i, 3:4], hg[:, 0, :], ALU.mult, ALU.mult).then_inc(normed, 1)
                    if per == 2:
                        dve.wait_ge(normed, 2 * i + 1)
                        nc.vector.tensor_tensor(h, h, hg[:, 1, :], ALU.add).then_inc(normed, 1)

                for i in range(NT + 2):
                    if 1 <= i <= NT:
                        norm(i - 1)
                    if i >= 2:
                        evacuate(dve, 1, i - 2)
                    if i >= NT:
                        continue
                    xs = xt[:, i % 4, :]
                    if grow is not None:
                        dve.wait_ge(ssq, 2 * i + 2)
                        nc.vector.tensor_tensor(ss[:, i, 2:3], ss[:, i, 0:1], ss[:, i, 1:2], ALU.add).then_inc(rstd, 1)
                        dve.wait_ge(rstd, 2 * i + 1)
                        nc.vector.tensor_scalar(ss[:, i, 2:3], ss[:, i, 2:3], 1.0 / D, EPS, ALU.mult, ALU.add)\
                            .then_inc(ms, 1)
                        dve.wait_ge(root, i + 1)
                        nc.vector.reciprocal(ss[:, i, 4:5], ss[:, i, 3:4]).then_inc(rstd, 1)
                        dve.wait_ge(rstd, 2 * i + 2)
                        if i == 0:
                            dve.wait_ge(g_in, 16)
                        for c in range(2):
                            cc = slice(c * BANK, (c + 1) * BANK)
                            nc.vector.scalar_tensor_tensor(yt[:, cc], bank[2 * (i % 2) + c][:, :], ss[:, i, 4:5],
                                                           gb[:, cc], ALU.mult, ALU.mult).then_inc(scaled, 1)
                        dve.wait_ge(scaled, 2 * i + 2)
                        dve.wait_ge(x_in[i % 4], 16 * (i // 4 + 1))
                        nc.vector.tensor_tensor(xs, xs, yt[:, :], ALU.add).then_inc(out_ready, 1)
                        dve.wait_ge(out_ready, i + 1)
                    else:
                        dve.wait_ge(x_in[i % 4], 16 * (i // 4 + 1))
                        for c in range(2):
                            cc = slice(c * BANK, (c + 1) * BANK)
                            dve.wait_ge(mm, 2 * i + c + 1)
                            nc.vector.tensor_tensor(xs[:, cc], xs[:, cc], bank[2 * (i % 2) + c][:, :], ALU.add)\
                                .then_inc(out_ready, 1)


def add_normed(nc, name, x, y, grow, out):
    with Stage(nc, name) as st:
        xt, yt, gb = st.sb("x", [P, NT, D]), st.sb("y", [P, NT, D]), st.sb("g", [P, D])
        sq, ss = st.sb("sq", [P, D]), st.sb("ss", [P, NT, 4])
        x_in, y_in = [st.sem(f"x_in{i}") for i in range(2)], [st.sem(f"y_in{i}") for i in range(2)]
        g_in, ssq, ms, root, rstd, scaled, out_ready, stored = (
            st.sem(n) for n in ("g_in", "ssq", "ms", "root", "rstd", "scaled", "out_ready", "stored"))
        H = NT // 2
        with nc.Block() as block:
            @block.sync
            def _(sp):
                for i in range(2):
                    t = slice(i * H * P, (i + 1) * H * P)
                    sp.dma_start(yt[:, i * H:(i + 1) * H, :], y[t, :].rearrange("(n p) d -> p n d", p=P)).then_inc(y_in[i], 16)
                    if i == 0:
                        sp.dma_start(gb[:, :], grow.partition_broadcast(P).rearrange("p o d -> p (o d)")).then_inc(g_in, 16)
                    sp.dma_start(xt[:, i * H:(i + 1) * H, :], x[t, :].rearrange("(n p) d -> p n d", p=P)).then_inc(x_in[i], 16)
                for i in range(NT):
                    sp.wait_ge(out_ready, i + 1)
                    sp.dma_start(out[i * P:(i + 1) * P, :], xt[:, i, :]).then_inc(stored, 16)
                sp.wait_ge(stored, 16 * NT)

            @block.scalar
            def _(act):
                for i in range(NT):
                    act.wait_ge(y_in[i // H], 16)
                    if i:
                        act.wait_ge(ssq, i)
                    nc.scalar.activation(sq[:, :], yt[:, i, :], ACT.Square, accum_out=ss[:, i, 0:1]).then_inc(ssq, 1)
                    act.wait_ge(ms, i + 1)
                    nc.scalar.activation(ss[:, i, 2:3], ss[:, i, 1:2], ACT.Sqrt).then_inc(root, 1)

            @block.vector
            def _(dve):
                dve.wait_ge(g_in, 16)
                for i in range(NT):
                    dve.wait_ge(ssq, i + 1)
                    nc.vector.tensor_scalar(ss[:, i, 1:2], ss[:, i, 0:1], 1.0 / D, EPS, ALU.mult, ALU.add).then_inc(ms, 1)
                    dve.wait_ge(root, i + 1)
                    nc.vector.reciprocal(ss[:, i, 3:4], ss[:, i, 2:3]).then_inc(rstd, 1)
                    dve.wait_ge(rstd, i + 1)
                    nc.vector.scalar_tensor_tensor(yt[:, i, :], yt[:, i, :], ss[:, i, 3:4], gb[:, :], ALU.mult, ALU.mult)\
                        .then_inc(scaled, 1)
                    dve.wait_ge(scaled, i + 1)
                    dve.wait_ge(x_in[i // H], 16)
                    nc.vector.tensor_tensor(xt[:, i, :], xt[:, i, :], yt[:, i, :], ALU.add).then_inc(out_ready, 1)


def route1(nc, bank, cst, hT, w_router, acc, idx, gates):
    with Stage(nc, "route1") as st:
        wr = st.sb("wr", [P, KD, E1])
        lT = st.sb("lT", [E1, T])
        lg, ex = st.sb("lg", [P, NT, E1]), st.sb("ex", [P, NT, E1])
        mx, sm = st.sb("mx", [P, NT]), st.sb("sm", [P, 2, NT])
        af = [st.sb("af0", [E1, T]), st.sb("af1", [E1, T])]
        va, ix, ixf = st.sb("va", [E1, CAP]), st.sb("ix", [E1, CAP], U32), st.sb("ixf", [E1, CAP])
        zero = st.sb("zero", [P, D])
        w_in, l_mm, l_ev, tr, chain, e_ready, af_mm, af_ev, ixf_ready, fin_mm, fin = (
            st.sem(n) for n in ("w_in", "l_mm", "l_ev", "tr", "chain", "e_ready", "af_mm", "af_ev", "ixf_ready", "fin_mm", "fin"))
        zeroed, cleared, p_ready, d_ready = st.sem("zeroed"), st.sem("cleared"), st.sem("p_ready"), st.sem("d_ready")
        ident = cst[:, CONST["ident"]:CONST["ident"] + P]
        with nc.Block() as block:
            @block.sync
            def _(sp):
                sp.dma_start(wr[:, :, :], w_router.rearrange("(k p) e -> p k e", p=P)).then_inc(w_in, 16)
                sp.wait_ge(zeroed, 1)
                for i in range(NT):
                    sp.dma_start(acc[i * P:(i + 1) * P, :], zero[:, :]).then_inc(cleared, 16)
                sp.wait_ge(cleared, 16 * NT)

            @block.gpsimd
            def _(pool):
                nc.gpsimd.memset(zero[:, :], 0.0).then_inc(zeroed, 1)

            @block.tensor
            def _(pe):
                pe.wait_ge(w_in, 16)
                for c in range(2):
                    for k in range(KD):
                        last = nc.tensor.matmul(bank[c][0:E1, :], wr[:, k, :], hT[:, k, c * BANK:(c + 1) * BANK],
                                                start=(k == 0), stop=(k == KD - 1))
                    last.then_inc(l_mm, 1)
                pe.wait_ge(l_ev, 2)
                for i in range(NT):
                    last = nc.tensor.transpose(bank[2][:, i * E1:(i + 1) * E1], lT[:, i * P:(i + 1) * P], ident[0:E1, 0:E1])
                last.then_inc(tr, 1)
                pe.wait_ge(p_ready, 1)
                for i in range(NT):
                    last = nc.tensor.transpose(bank[3 + i // 4][0:E1, (i % 4) * P:(i % 4 + 1) * P], ex[:, i, :], ident)
                last.then_inc(af_mm, 1)
                pe.wait_ge(ixf_ready, 1)
                nc.tensor.transpose(bank[5][:, 0:E1], va[:, :], ident[0:E1, 0:E1])
                nc.tensor.transpose(bank[5][:, E1:2 * E1], ixf[:, :], ident[0:E1, 0:E1]).then_inc(fin_mm, 1)

            @block.scalar
            def _(act):
                for c in range(2):
                    act.wait_ge(l_mm, c + 1)
                    nc.scalar.activation(lT[:, c * BANK:(c + 1) * BANK], bank[c][0:E1, :], ACT.Copy).then_inc(l_ev, 1)
                act.wait_ge(d_ready, 1)
                nc.scalar.activation(ex[:, :, :], lg[:, :, :], ACT.Exp).then_inc(e_ready, 1)

            @block.vector
            def _(dve):
                link = Steps(chain)
                dve.wait_ge(tr, 1)
                lp = bank[2][:, 0:NT * E1].rearrange("p (n e) -> p n e", e=E1)
                dve.wait_ge(chain, link(nc.vector.tensor_reduce(mx[:, :], lp, AX_X, ALU.max)))
                nc.vector.tensor_tensor(lg[:, :, :], lp, mx[:, :].unsqueeze(2).to_broadcast([P, NT, E1]), ALU.subtract)\
                    .then_inc(d_ready, 1)
                dve.wait_ge(e_ready, 1)
                dve.wait_ge(chain, link(nc.vector.tensor_reduce(sm[:, 0, :], ex[:, :, :], AX_X, ALU.add)))
                dve.wait_ge(chain, link(nc.vector.reciprocal(sm[:, 1, :], sm[:, 0, :])))
                nc.vector.tensor_tensor(ex[:, :, :], ex[:, :, :], sm[:, 1, :].unsqueeze(2).to_broadcast([P, NT, E1]),
                                        ALU.mult).then_inc(p_ready, 1)
                dve.wait_ge(af_mm, 1)
                for c in range(2):
                    dve.wait_ge(chain, link(nc.vector.tensor_copy(af[0][:, c * BANK:(c + 1) * BANK], bank[3 + c][0:E1, :])))
                for r in range(CAP // 8):
                    v8, i8, a, b = va[:, 8 * r:8 * r + 8], ix[:, 8 * r:8 * r + 8], af[r % 2], af[(r + 1) % 2]
                    dve.wait_ge(chain, link(nc.vector.max(v8, a[:, :])))
                    link(nc.vector.max_index(i8, v8, a[:, :]))
                    dve.wait_ge(chain, link(nc.vector.match_replace(b[:, :], v8, a[:, :], -1.0)))
                nc.vector.tensor_copy(ixf[:, :], ix[:, :]).then_inc(ixf_ready, 1)
                dve.wait_ge(fin_mm, 1)
                nc.vector.tensor_copy(gates[:, :], bank[5][:, 0:E1]).then_inc(fin, 1)
                nc.vector.tensor_copy(idx[:, 0:E1], bank[5][:, E1:2 * E1]).then_inc(fin, 1)
                nc.vector.tensor_copy(idx[:, E1:E1 + 1], bank[5][:, E1:E1 + 1]).then_inc(fin, 1)


def experts1(nc, bank, cst, h2, w_gate, w_up, w_down, acc, idx, gates, xs_in, added):
    with Stage(nc, "moe1") as st:
        w = st.sb("w", [P, 6, 8 * BANK])
        xs, xT = st.sb("xs", [P, D]), st.sb("xT", [P, KD, P])
        cur = st.sb("cur", [P, 2], U32)
        sg = st.sb("sg", [P, 2, BANK])
        hid, hidT = st.sb("hid", [P, 2, BANK]), st.sb("hidT", [P, KD, P])
        ye = st.sb("ye", [P, D])
        w_in = [st.sem(f"w_in{i}") for i in range(6)]
        names = ("turns", "cur_ready", "x_tr", "xT_ev", "gu_mm", "sg_ready", "hid_ready", "h_tr", "hT_ev", "y_mm",
                 "ye_ready", "ye_free")
        s = {n: st.sem(n) for n in names}
        ident = cst[:, CONST["ident"]:CONST["ident"] + P]

        def load(sp, e, i):
            m = (w_gate, w_up, w_gate, w_up, w_down, w_down)[i]
            if i < 4:
                c = (i // 2) * BANK
                src = m[ds(e, 1), :, c:c + BANK].rearrange("o (k p) n -> p (o k) n", p=P)
                dst = w[:, i].rearrange("p (k n) -> p k n", k=8)
            else:
                r = (i - 4) * BANK
                src = m[ds(e, 1), r:r + BANK, :].rearrange("o (k p) n -> p (o k) n", p=P)
                dst = w[:, i].rearrange("p (k n) -> p k n", k=4)
            sp.dma_start(dst, src).then_inc(w_in[i], 16)

        with nc.Block() as block:
            @block.sync
            def _(sp):
                for i in range(6):
                    load(sp, 0, i)
                with sp.Fori(0, E1 - 1) as e:
                    for i in range(4):
                        sp.wait_ge(s["gu_mm"], e * 4 + (i + 1))
                        load(sp, e + 1, i)
                    for i in range(2):
                        sp.wait_ge(s["y_mm"], e * 2 + (i + 1))
                        load(sp, e + 1, 4 + i)

            @block.gpsimd
            def _(pool):
                def gather():
                    pool.indirect_dma_start(out=xs[:, :], out_offset=None, in_=h2[:, :],
                                            in_offset=bass.IndirectOffsetOnAxis(ap=cur[:, 0:1], axis=0))\
                        .then_inc(xs_in, 16)

                pool.sem_inc(s["ye_free"], 1)
                nc.gpsimd.tensor_copy(cur[:, 0:1], idx[:, 0:1]).then_inc(s["cur_ready"], 1)
                pool.wait_ge(s["cur_ready"], 1)
                gather()
                with pool.Fori(0, E1) as e:
                    pool.wait_ge(s["x_tr"], e * 2 + 2)
                    pool.sem_inc(s["turns"], 1)
                    nc.gpsimd.tensor_copy(cur[:, 1:2], cur[:, 0:1]).then_inc(s["cur_ready"], 1)
                    pool.wait_ge(s["cur_ready"], e * 2 + 2)
                    pool.sem_inc(s["turns"], 1)
                    nc.gpsimd.tensor_copy(cur[:, 0:1], idx[:, ds(e + 1, 1)]).then_inc(s["cur_ready"], 1)
                    pool.wait_ge(s["cur_ready"], e * 2 + 3)
                    pool.sem_inc(s["turns"], 1)
                    gather()
                    pool.wait_ge(s["ye_ready"], e * 2 + 3)
                    pool.sem_inc(s["turns"], 1)
                    pool.indirect_dma_start(out=acc[:, :], out_offset=bass.IndirectOffsetOnAxis(ap=cur[:, 1:2], axis=0),
                                            in_=ye[:, :], in_offset=None, compute_op=ALU.add).then_inc(added, 16)
                    pool.wait_ge(added, e * 16 + 16)
                    pool.sem_inc(s["ye_free"], 1)
                pool.wait_ge(xs_in, 16 * (E1 + 1))

            @block.tensor
            def _(pe):
                def take_tokens(e):
                    pe.wait_ge(xs_in, e * 16 + 16)
                    for k in range(KD):
                        ins = nc.tensor.transpose(bank[k // 4][:, (k % 4) * P:(k % 4 + 1) * P], xs[:, k * P:(k + 1) * P], ident)
                        if k % 4 == 3:
                            ins.then_inc(s["x_tr"], 1)

                take_tokens(0)
                with pe.Fori(0, E1) as e:
                    pe.wait_ge(s["xT_ev"], e * 2 + 2)
                    for i in range(4):
                        pe.wait_ge(w_in[i], e * 16 + 16)
                        wi = w[:, i].rearrange("p (k n) -> p k n", k=8)
                        for k in range(KD):
                            last = nc.tensor.matmul(bank[i][:, :], xT[:, k, :], wi[:, k, :], start=(k == 0), stop=(k == KD - 1))
                        last.then_inc(s["gu_mm"], 1)
                    for half in range(2):
                        pe.wait_ge(s["hid_ready"], e * 2 + (half + 1))
                        for j in range(4):
                            ins = nc.tensor.transpose(bank[4 + half][:, j * P:(j + 1) * P], hid[:, half, j * P:(j + 1) * P], ident)
                        ins.then_inc(s["h_tr"], 1)
                        if half == 0:
                            take_tokens(e + 1)
                        pe.wait_ge(s["hT_ev"], e * 2 + (half + 1))
                        pe.wait_ge(w_in[4 + half], e * 16 + 16)
                        if half == 0:
                            pe.wait_ge(s["ye_ready"], e * 2 + 1)
                        wi = w[:, 4 + half].rearrange("p (k n) -> p k n", k=4)
                        for c in range(2):
                            for j in range(4):
                                last = nc.tensor.matmul(bank[6 + c][:, :], hidT[:, 4 * half + j, :], wi[:, j, c * BANK:(c + 1) * BANK],
                                                        start=(half == 0 and j == 0), stop=(half == 1 and j == 3),
                                                        skip_group_check=True)
                        last.then_inc(s["y_mm"], 1)

            @block.scalar
            def _(act):
                def xT_evac(e):
                    for i in range(2):
                        act.wait_ge(s["x_tr"], e * 2 + (i + 1))
                        nc.scalar.activation(xT[:, 4 * i:4 * i + 4, :].rearrange("p k t -> p (k t)"), bank[i][:, :], ACT.Copy)\
                            .then_inc(s["xT_ev"], 1)

                xT_evac(0)
                with act.Fori(0, E1) as e:
                    for half in range(2):
                        act.wait_ge(s["gu_mm"], e * 4 + (2 * half + 1))
                        nc.scalar.activation(sg[:, half, :], bank[2 * half][:, :], ACT.Silu).then_inc(s["sg_ready"], 1)
                    xT_evac(e + 1)

            @block.vector
            def _(dve):
                dve.sem_inc(s["ye_ready"], 1)
                with dve.Fori(0, E1) as e:
                    for half in range(2):
                        dve.wait_ge(s["sg_ready"], e * 2 + (half + 1))
                        dve.wait_ge(s["gu_mm"], e * 4 + (2 * half + 2))
                        nc.vector.tensor_tensor(hid[:, half, :], sg[:, half, :], bank[2 * half + 1][:, :], ALU.mult)\
                            .then_inc(s["hid_ready"], 1)
                    for half in range(2):
                        dve.wait_ge(s["h_tr"], e * 2 + (half + 1))
                        nc.vector.tensor_copy(hidT[:, 4 * half:4 * half + 4, :].rearrange("p k t -> p (k t)"), bank[4 + half][:, :])\
                            .then_inc(s["hT_ev"], 1)
                    dve.wait_ge(s["y_mm"], e * 2 + 2)
                    dve.wait_ge(s["ye_free"], e + 1)
                    for c in range(2):
                        nc.vector.tensor_scalar(ye[:, c * BANK:(c + 1) * BANK], bank[6 + c][:, :], gates[:, ds(e, 1)], None,
                                                ALU.mult).then_inc(s["ye_ready"], 1)


def load_T(nc, name, src, dst, tiles=KD):
    with Stage(nc, name) as st:
        loaded = st.sem("loaded")
        with nc.Block() as block:
            @block.sync
            def _(sp):
                for k in range(tiles):
                    sp.dma_start(dst[:, k, :], src[k * P:(k + 1) * P, :]).then_inc(loaded, 16)
                sp.wait_ge(loaded, 16 * tiles)


LAMBDA_INIT = 0.8 - 0.6 * math.exp(-0.3 * 0)


TWO_PI_HI, TWO_PI_MID = 6.28125, 0.00193500518798828125
TWO_PI_LO = 2 * math.pi - TWO_PI_HI - TWO_PI_MID
ROUND = 1.5 * 2.0 ** 23
PI_BELOW = 3.1415925


def qkv_and_lru(nc, bank, cst, col, x, hT, uT, gT, qkT, v_rows):
    STEPS = 3 * NT
    NQK = 2 * NT
    MAPS = D // HD2
    w_in2 = x["w_in_2"][0]
    with Stage(nc, "qkv") as st:
        w = st.sb("w", [P, 2, KD, D])
        sq = st.sb("sq", [P, D])
        y = st.sb("y", [P, 2, D])
        yT = st.sb("yT", [P, 2, KD, P])
        ss = st.sb("ss", [P, 2, 3, MAPS])
        gain = st.sb("gain", [P, 2, HD2])
        pos = st.sb("pos", [P, NT], I32)
        rt = st.sb("rt", [P, 4, NT, 8])
        cos2, sin2 = st.sb("cos2", [P, NT, 2, 8]), st.sb("sin2", [P, NT, 2, 8])
        ro = st.sb("ro", [P, MAPS, 2, 8])
        s = {n: st.sem(n) for n in ("tab_in", "head", "sin", "mm", "squared", "stats", "ms", "root", "scaled", "gained",
                                    "rope", "roped", "tr", "evA", "evD", "vA", "vD")}
        w_in = [st.sem(f"w_in{i}") for i in range(6)]
        stored = [st.sem(f"stored{i}") for i in range(2)]
        ident = cst[:, CONST["ident"]:CONST["ident"] + P]

        lx = st.sb("lx", [P, T + 4])
        lgate, lw = st.sb("lgate", [P, T]), st.sb("lw", [P, 2, P])
        pc, sp4 = st.sb("pc", [P, 3, KD]), st.sb("sp4", [P, 4, KD])
        xc, r, i_, a, t, u, h = (st.sb(n, [P, T]) for n in ("xc", "r", "i", "a", "t", "u", "h"))
        l = {n: st.sem("l_" + n) for n in ("zeroed", "x_in", "w_in", "g_in", "head", "head_act", "hc", "chain", "xc", "r_mm",
                                           "i_mm", "r", "i", "t", "a", "u", "root", "ix", "gelu", "out", "stored")}
        c = lambda name, at: col[:, COLS[name] + at:COLS[name] + at + 1]
        wa, wx = x["lru_wa_2"][0], x["lru_wx_2"][0]

        with nc.Block() as block:
            @block.sync
            def _(sp):
                def load_w(m, c_):
                    src = w_in2[:, (2 + m) * D + c_ * BANK:(2 + m) * D + (c_ + 1) * BANK].rearrange("(k p) n -> p k n", p=P)
                    sp.dma_start(w[:, m % 2, :, c_ * BANK:(c_ + 1) * BANK], src).then_inc(w_in[2 * m + c_], 16)

                def load_block(b, what):
                    rows = slice(b * P, (b + 1) * P)
                    if what == "x":
                        sp.dma_start(lx[:, 4:], uT[rows, :]).then_inc(l["x_in"], 16)
                    elif what == "w":
                        for n, src in enumerate((wa, wx)):
                            sp.dma_start(lw[:, n, :], src[b]).then_inc(l["w_in"], 16)
                    else:
                        sp.dma_start(lgate[:, :], uT[D + b * P:D + (b + 1) * P, :]).then_inc(l["g_in"], 16)

                load_w(0, 0)
                with nc.allow_non_contiguous_dma("positions by tokens"):
                    sp.dma_start(pos[:, :], x["positions_2"].rearrange("o (n p) -> p (o n)", p=P)).then_inc(s["tab_in"], 16)
                for n, name in enumerate(("q_norm_2", "k_norm_2")):
                    sp.dma_start(gain[:, n, :], x[name].partition_broadcast(P)
                                 .rearrange("p o d -> p (o d)")).then_inc(s["tab_in"], 16)
                load_w(0, 1)
                sp.wait_ge(l["zeroed"], 1)
                for what in ("x", "w", "gate"):
                    load_block(0, what)
                load_w(1, 0)
                load_w(1, 1)
                for n in range(STEPS + 1):
                    b = n // 3
                    if n % 3 == 0 and b:
                        sp.wait_ge(l["out"], b)
                        sp.dma_start(gT[(b - 1) * P:b * P, :], h[:, :]).then_inc(l["stored"], 16)
                        if b < KD:
                            load_block(b, "gate")
                    if n % 3 == 0 and b + 1 < KD:
                        sp.wait_ge(l["xc"], b + 1)
                        load_block(b + 1, "x")
                    if n % 3 == 0 and 0 < b < KD:
                        sp.wait_ge(l["i_mm"], b)
                        load_block(b, "w")
                    if n >= 1:
                        j = n - 1
                        m, i = j // NT, j % NT
                        if j < NQK:
                            sp.wait_ge(s["evA"], j + 1)
                            sp.wait_ge(s["evD"], j + 1)
                            sp.dma_start(qkT[m].rearrange("(k p) t -> p k t", p=P)[:, :, i * P:(i + 1) * P], yT[:, j % 2])\
                                .then_inc(stored[j % 2], 16)
                        else:
                            sp.wait_ge(s["vA"], j - NQK + 1)
                            sp.wait_ge(s["vD"], j - NQK + 1)
                            sp.dma_start(v_rows[i * P:(i + 1) * P, :], y[:, j % 2, :]).then_inc(stored[j % 2], 16)
                    if n == NT:
                        for c_ in range(2):
                            load_w(2, c_)
                for i in range(2):
                    sp.wait_ge(stored[i], 16 * (STEPS // 2))
                sp.wait_ge(l["stored"], 16 * KD)

            @block.tensor
            def _(pe):
                def products(n):
                    m, i = n // NT, n % NT
                    j = n - 2
                    if 0 <= j < NQK:
                        pe.wait_ge(s["scaled"], j + 1)
                    elif j >= NQK:
                        pe.wait_ge(s["vA"], j - NQK + 1)
                        pe.wait_ge(s["vD"], j - NQK + 1)
                    for c_ in range(2):
                        if i == 0:
                            pe.wait_ge(w_in[2 * m + c_], 16)
                        for k in range(KD):
                            last = nc.tensor.matmul(bank[2 * (n % 2) + c_][:, :], hT[:, k, i * P:(i + 1) * P],
                                                    w[:, m % 2, k, c_ * BANK:(c_ + 1) * BANK], start=(k == 0), stop=(k == KD - 1))
                    last.then_inc(s["mm"], 1)

                def turn(n):
                    pe.wait_ge(s["roped"], n + 1)
                    if n:
                        pe.wait_ge(s["evA"], n)
                        pe.wait_ge(s["evD"], n)
                    for k in range(KD):
                        ins = nc.tensor.transpose(bank[6 + k // 4][:, (k % 4) * P:(k % 4 + 1) * P], y[:, n % 2, k * P:(k + 1) * P],
                                                  ident)
                    ins.then_inc(s["tr"], 1)

                def gate(b, m):
                    if m == 0:
                        pe.wait_ge(l["w_in"], 32 * (b + 1))
                        pe.wait_ge(l["xc"], b + 1)
                        if b:
                            pe.wait_ge(l["i"], b)
                    else:
                        pe.wait_ge(l["r"], b + 1)
                    for c_ in range(2):
                        ins = nc.tensor.matmul(bank[4 + c_][:, :], lw[:, m, :], xc[:, c_ * BANK:(c_ + 1) * BANK], start=True, stop=True)
                    ins.then_inc(l["i_mm" if m else "r_mm"], 1)

                for n in range(STEPS):
                    products(n)
                    if n % 3:
                        gate(n // 3, n % 3 - 1)
                    if 1 <= n <= NQK:
                        turn(n - 1)

            @block.scalar
            def _(act):
                def halves(n, fn, out, sem):
                    for c_ in range(2):
                        ins = fn(c_)
                    ins.then_inc(sem, 1)

                act.wait_ge(l["head"], 1)
                nc.scalar.activation(sp4[:, 1, :], sp4[:, 0, :], ACT.Exp, scale=-1.0).then_inc(l["head_act"], 1)
                act.wait_ge(l["head"], 2)
                nc.scalar.activation(sp4[:, 0, :], sp4[:, 2, :], ACT.Ln).then_inc(l["head_act"], 1)
                act.wait_ge(s["head"], 1)
                nc.scalar.activation(rt[:, 3], rt[:, 1], ACT.Sin).then_inc(s["sin"], 1)
                act.wait_ge(s["head"], 2)
                nc.scalar.activation(rt[:, 2], rt[:, 0], ACT.Sin).then_inc(s["sin"], 1)
                act.wait_ge(l["head"], 3)

                def square(n):
                    act.wait_ge(s["mm"], n + 1)
                    if n:
                        act.wait_ge(s["ms"], n)
                    for c_ in range(2):
                        ins = nc.scalar.activation(sq[:, c_ * BANK:(c_ + 1) * BANK], bank[2 * (n % 2) + c_][:, :], ACT.Square)
                    ins.then_inc(s["squared"], 1)

                def root(n):
                    act.wait_ge(s["ms"], n + 1)
                    nc.scalar.activation(ss[:, n % 2, 1, :], ss[:, n % 2, 0, :], ACT.Sqrt).then_inc(s["root"], 1)

                def turned(n):
                    act.wait_ge(s["tr"], n + 1)
                    if n >= 2:
                        act.wait_ge(stored[n % 2], 16 * (n // 2))
                    nc.scalar.activation(yT[:, n % 2, 0:4, :].rearrange("p k t -> p (k t)"), bank[6][:, :], ACT.Copy)\
                        .then_inc(s["evA"], 1)

                def values(n):
                    act.wait_ge(s["mm"], n + 1)
                    if n >= NQK + 2:
                        act.wait_ge(stored[n % 2], 16 * (n // 2))
                    else:
                        act.wait_ge(s["tr"], n - 1)
                    nc.scalar.activation(y[:, n % 2, 0:BANK], bank[2 * (n % 2)][:, :], ACT.Copy).then_inc(s["vA"], 1)

                def sigmoid(b, m):
                    act.wait_ge(l["i_mm" if m else "r_mm"], b + 1)
                    if b and m:
                        act.wait_ge(l["u"], b)
                    for c_ in range(2):
                        ins = nc.scalar.activation((i_ if m else r)[:, c_ * BANK:(c_ + 1) * BANK], bank[4 + c_][:, :], ACT.Sigmoid,
                                                   bias=c("bx" if m else "ba", b))
                    ins.then_inc(l["i" if m else "r"], 1)

                def decay(b):
                    act.wait_ge(l["r"], b + 1)
                    if b:
                        act.wait_ge(l["out"], b)
                    nc.scalar.activation(t[:, :], r[:, :], ACT.Tanh, scale=pc[:, 0, b:b + 1]).then_inc(l["t"], 1)
                    nc.scalar.activation(a[:, :], r[:, :], ACT.Exp, scale=pc[:, 1, b:b + 1]).then_inc(l["a"], 1)

                for n in range(STEPS):
                    if n < NQK:
                        square(n)
                        root(n)
                    else:
                        values(n)
                    b = n // 3
                    if n % 3 == 1:
                        sigmoid(b, 0)
                        decay(b)
                    elif n % 3 == 2:
                        act.wait_ge(l["u"], b + 1)
                        nc.scalar.activation(u[:, :], u[:, :], ACT.Sqrt).then_inc(l["root"], 1)
                        sigmoid(b, 1)
                        act.wait_ge(l["g_in"], 16 * (b + 1))
                        nc.scalar.activation(lgate[:, :], lgate[:, :], ACT.Gelu_apprx_tanh).then_inc(l["gelu"], 1)
                    if 1 <= n <= NQK:
                        turned(n - 1)

            @block.gpsimd
            def _(pool):
                nc.gpsimd.memset(lx[:, 0:4], 0.0).then_inc(l["zeroed"], 1)
                link = Steps(s["rope"])
                pool.wait_ge(s["head"], 4)

                def maps(n):
                    return y[:, n % 2, :].rearrange("p (m d) -> p m d", d=HD2)

                def rotate(n):
                    i, yn = n % NT, maps(n)
                    pool.wait_ge(s["scaled"], n + 1)
                    nc.gpsimd.tensor_tensor(yn, yn, gain[:, n // NT, :].unsqueeze(1).to_broadcast([P, MAPS, HD2]), ALU.mult)\
                        .then_inc(s["gained"], 1)
                    pool.wait_ge(s["gained"], n + 1)
                    half = yn[:, :, 0:16].rearrange("p m (h e) -> p m h e", h=2)
                    for k in range(2):
                        last = link(nc.gpsimd.tensor_tensor(ro[:, :, k, :], half[:, :, 1 - k, :],
                                                            sin2[:, i, k, :].unsqueeze(1).to_broadcast([P, MAPS, 8]), ALU.mult))
                    pool.wait_ge(s["rope"], last)
                    pool.wait_ge(s["rope"], link(nc.gpsimd.tensor_tensor(
                        yn[:, :, 0:16], yn[:, :, 0:16],
                        cos2[:, i].rearrange("p h e -> p (h e)").unsqueeze(1).to_broadcast([P, MAPS, 16]), ALU.mult)))
                    nc.gpsimd.tensor_tensor(yn[:, :, 0:16], yn[:, :, 0:16], ro[:, :, :, :].rearrange("p m h e -> p m (h e)"), ALU.add)\
                        .then_inc(s["roped"], 1)

                def gated_x(b):
                    pool.wait_ge(l["i"], b + 1)
                    nc.gpsimd.tensor_tensor(i_[:, :], i_[:, :], xc[:, :], ALU.mult).then_inc(l["ix"], 1)

                for n in range(STEPS + 1):
                    if n % 3 == 0 and n:
                        gated_x(n // 3 - 1)
                    if n < NQK:
                        rotate(n)

            @block.vector
            def _(dve):
                V = nc.vector
                head = Steps(l["hc"])

                def step(ins):
                    dve.wait_ge(l["hc"], head(ins))

                lam = col[:, COLS["lam"]:COLS["lam"] + KD]
                step(V.tensor_scalar(sp4[:, 2, :], lam, -1.0, None, ALU.mult))
                step(V.tensor_scalar(sp4[:, 3, :], sp4[:, 2, :], 0.0, None, ALU.max))
                V.tensor_tensor(sp4[:, 0, :], lam, sp4[:, 2, :], ALU.max).then_inc(l["head"], 1)
                dve.wait_ge(l["head_act"], 1)
                V.tensor_scalar(sp4[:, 2, :], sp4[:, 1, :], 1.0, None, ALU.add).then_inc(l["head"], 1)
                dve.wait_ge(l["head_act"], 2)
                step(V.tensor_scalar(pc[:, 2, :], sp4[:, 2, :], 1.0, None, ALU.is_equal))
                step(V.tensor_tensor(sp4[:, 0, :], sp4[:, 0, :], pc[:, 2, :], ALU.add))
                step(V.scalar_tensor_tensor(pc[:, 2, :], sp4[:, 2, :], -1.0, pc[:, 2, :], ALU.add, ALU.add))
                step(V.reciprocal(pc[:, 2, :], pc[:, 2, :]))
                step(V.tensor_tensor(sp4[:, 0, :], sp4[:, 0, :], sp4[:, 1, :], ALU.mult))
                step(V.tensor_tensor(sp4[:, 0, :], sp4[:, 0, :], pc[:, 2, :], ALU.mult))
                step(V.tensor_tensor(sp4[:, 0, :], sp4[:, 0, :], sp4[:, 3, :], ALU.add))
                step(V.tensor_scalar(pc[:, 0, :], sp4[:, 0, :], 8.0, None, ALU.mult))
                step(V.tensor_scalar(pc[:, 1, :], sp4[:, 0, :], -8.0, None, ALU.mult))
                dve.wait_ge(s["tab_in"], 48)
                ang, turns = rt[:, 0], rt[:, 1]
                step(V.tensor_copy(rt[:, 2, :, 0], pos[:, :]))
                step(V.tensor_tensor(ang, rt[:, 2, :, 0].unsqueeze(2).to_broadcast([P, NT, 8]),
                                     cst[:, CONST["invf"]:CONST["invf"] + 8].unsqueeze(1).to_broadcast([P, NT, 8]), ALU.mult))
                step(V.tensor_scalar(turns, ang, 1.0 / (2 * math.pi), ROUND, ALU.mult, ALU.add))
                step(V.tensor_scalar(turns, turns, -ROUND, None, ALU.add))
                for part in (TWO_PI_HI, TWO_PI_MID, TWO_PI_LO):
                    step(V.scalar_tensor_tensor(ang, turns, -part, ang, ALU.mult, ALU.add))
                V.tensor_scalar(turns, ang, PI_BELOW, -PI_BELOW, ALU.min, ALU.max).then_inc(s["head"], 1)
                step(V.tensor_scalar(rt[:, 2], ang, -1.0, None, ALU.mult))
                step(V.tensor_tensor(ang, ang, rt[:, 2], ALU.max))
                V.tensor_scalar(ang, ang, -1.0, math.pi / 2, ALU.mult, ALU.add).then_inc(s["head"], 1)
                dve.wait_ge(s["sin"], 2)
                for k in range(2):
                    step(V.tensor_copy(cos2[:, :, k, :], rt[:, 2]))
                    step(V.tensor_scalar(sin2[:, :, k, :], rt[:, 3], 2.0 * k - 1.0, None, ALU.mult))
                V.tensor_scalar(gain[:, 0, :], gain[:, 0, :], HD2 ** -0.5, None, ALU.mult).then_inc(s["head"], 2)
                V.memset(rt[:, 2, 0, 0:1], 0.0).then_inc(l["head"], 1)
                link, stats = Steps(l["chain"]), Steps(s["stats"])

                def lstep(ins):
                    dve.wait_ge(l["chain"], link(ins))

                def convolve(b):
                    dve.wait_ge(l["x_in"], 16 * (b + 1))
                    if b:
                        dve.wait_ge(l["ix"], b)
                    for tap in range(4):
                        src = lx[:, 1 + tap:1 + tap + T]
                        if tap == 0:
                            lstep(V.tensor_scalar(xc[:, :], src, c("conv2", b), c("conv2b", b), ALU.mult, ALU.add))
                        else:
                            ins = V.scalar_tensor_tensor(xc[:, :], src, c("conv2", b + 8 * tap), xc[:, :], ALU.mult, ALU.add)
                            if tap < 3:
                                lstep(ins)
                    ins.then_inc(l["xc"], 1)

                def input_scale(b):
                    dve.wait_ge(l["t"], b + 1)
                    lstep(V.tensor_scalar(u[:, :], t[:, :], 1.0, None, ALU.add))
                    lstep(V.reciprocal(u[:, :], u[:, :]))
                    V.scalar_tensor_tensor(u[:, :], t[:, :], 2.0, u[:, :], ALU.mult, ALU.mult).then_inc(l["u"], 1)

                def recur(b):
                    dve.wait_ge(l["root"], b + 1)
                    dve.wait_ge(l["ix"], b + 1)
                    lstep(V.tensor_tensor(u[:, :], u[:, :], i_[:, :], ALU.mult))
                    dve.wait_ge(l["a"], b + 1)
                    if b:
                        dve.wait_ge(l["stored"], 16 * b)
                    lstep(V.tensor_tensor_scan(h[:, :], a[:, :], u[:, :], 0.0, ALU.mult, ALU.add))
                    dve.wait_ge(l["gelu"], b + 1)
                    V.tensor_tensor(h[:, :], h[:, :], lgate[:, :], ALU.mult).then_inc(l["out"], 1)

                def scale(n):
                    sn = ss[:, n % 2]
                    dve.wait_ge(s["squared"], n + 1)
                    dve.wait_ge(s["stats"], stats(V.tensor_reduce(sn[:, 0, :], sq[:, :].rearrange("p (m d) -> p m d", d=HD2), AX_X,
                                                                  ALU.add)))
                    V.tensor_scalar(sn[:, 0, :], sn[:, 0, :], 1.0 / HD2, EPS, ALU.mult, ALU.add).then_inc(s["ms"], 1)
                    dve.wait_ge(s["root"], n + 1)
                    dve.wait_ge(s["stats"], stats(V.reciprocal(sn[:, 2, :], sn[:, 1, :])))
                    if n >= 2:
                        dve.wait_ge(s["tr"], n - 1)
                    m = MAPS // 2
                    for c_ in range(2):
                        ins = V.tensor_tensor(y[:, n % 2, c_ * BANK:(c_ + 1) * BANK].rearrange("p (m d) -> p m d", d=HD2),
                                              bank[2 * (n % 2) + c_][:, :].rearrange("p (m d) -> p m d", d=HD2),
                                              sn[:, 2, c_ * m:(c_ + 1) * m].unsqueeze(2).to_broadcast([P, m, HD2]), ALU.mult)
                    ins.then_inc(s["scaled"], 1)

                def turned(n):
                    dve.wait_ge(s["tr"], n + 1)
                    if n >= 2:
                        dve.wait_ge(stored[n % 2], 16 * (n // 2))
                    V.tensor_copy(yT[:, n % 2, 4:8, :].rearrange("p k t -> p (k t)"), bank[7][:, :]).then_inc(s["evD"], 1)

                def values(n):
                    dve.wait_ge(s["mm"], n + 1)
                    if n >= NQK + 2:
                        dve.wait_ge(stored[n % 2], 16 * (n // 2))
                    else:
                        dve.wait_ge(s["tr"], n - 1)
                    V.tensor_copy(y[:, n % 2, BANK:], bank[2 * (n % 2) + 1][:, :]).then_inc(s["vD"], 1)

                for n in range(STEPS + 1):
                    b = n // 3
                    if n % 3 == 0 and b:
                        recur(b - 1)
                    if n % 3 == 0 and b < KD:
                        convolve(b)
                    if n % 3 == 2:
                        input_scale(b)
                    if n < NQK:
                        scale(n)
                    elif n < STEPS:
                        values(n)
                    if 1 <= n <= NQK:
                        turned(n - 1)


def diff_attention(nc, bank, cst, col, x, qkT, v_rows, oT):
    J = 2 * NT
    with Stage(nc, "attn") as st:
        q = st.sb("q", [P, 2, T])
        kz = st.sb("kz", [P, 2, 2, T])
        v = st.sb("v", [P, 2, NT, P])
        lv = st.sb("lv", [P, 4, HD2])
        lp = st.sb("lp", [P, 2, HD2])
        lm = st.sb("lm", [P, 8])
        sub = st.sb("sub", [P, 1])
        e = st.sb("e", [P, 2, 2, T])
        sm = st.sb("sm", [P, 2, 2, 8])
        w = st.sb("w", [P, 2, T])
        wT = st.sb("wT", [P, 2, NT, P])
        o, rs = st.sb("o", [P, 2, T]), st.sb("rs", [P, 2, T])
        names = ("zeroed", "lam_in", "lam", "lam_exp", "ready", "s_mm", "chain", "nm", "exp", "scaled", "rec", "w_ready",
                 "trA", "trB", "evA", "evB", "o_mm", "o_ev", "squared", "sums", "ms", "root", "out")
        s = {n: st.sem(n) for n in names}
        qkv_in = [st.sem(f"qkv_in{k}") for k in range(2)]
        ident, ones = (cst[:, CONST[n]:CONST[n] + P] for n in ("ident", "ones"))
        TURNS = HEADS2 // 2
        LOADS = 4 * 16
        late = lambda j: (j // NT) * 4 + j % NT - 3

        def banks(i):
            n = (i + 1) * P
            return [(0, 0, min(n, BANK))] + ([(1, BANK, n)] if n > BANK else [])

        with nc.Block() as block:
            @block.sync
            def _(sp):
                for n, name in enumerate(("lambda_q1_2", "lambda_k1_2", "lambda_q2_2", "lambda_k2_2")):
                    sp.dma_start(lv[:, n, :], x[name].partition_broadcast(P).rearrange("p o d -> p (o d)")).then_inc(s["lam_in"], 16)

                def load(it, k):
                    rows = ds(it * (2 * P) + k * P, P)
                    sp.dma_start(q[:, k, :], qkT[0, rows, :]).then_inc(qkv_in[k], 16)
                    for m in range(2):
                        sp.dma_start(kz[64 * m:64 * m + 64, k, m, :], qkT[1, ds(it * (2 * P) + (k * P + 64 * m), 64), :])\
                            .then_inc(qkv_in[k], 16)
                    sp.dma_start(v[:, k, :, :], v_rows[:, rows].rearrange("(n p) d -> p n d", p=P)).then_inc(qkv_in[k], 16)

                sp.wait_ge(s["zeroed"], 1)
                load(0, 0)
                load(0, 1)
                with sp.Fori(0, TURNS - 1) as it:
                    for k in range(2):
                        sp.wait_ge(s["o_mm"], it * J + NT * (k + 1))
                        load(it + 1, k)

            @block.gpsimd
            def _(pool):
                nc.gpsimd.memset(kz[:, :, :, :], 0.0).then_inc(s["zeroed"], 1)
                with pool.Fori(0, TURNS) as it:
                    for j in range(J):
                        i = j % NT
                        pool.wait_ge(s["rec"], it * J + (j + 1))
                        pool.sem_inc(s["ready"], 1)
                        nc.gpsimd.tensor_scalar(e[:, j % 2, 0, 0:(i + 1) * P], e[:, j % 2, 0, 0:(i + 1) * P],
                                                sm[:, j % 2, 0, 6:7], None, ALU.mult).then_inc(s["scaled"], 1)

            @block.tensor
            def _(pe):
                def tiles(it, first=False, last=False):
                    def scores(j):
                        i, k = j % NT, j // NT
                        if i == 0:
                            pe.wait_ge(qkv_in[k], it * LOADS + LOADS)
                        for m in range(2):
                            if j or not first:
                                pe.wait_ge(s["exp"], it * (2 * J) + (2 * (j - 1) + m + 1))
                            for b, c0, c1 in banks(i):
                                ins = nc.tensor.matmul(bank[2 * m + b][:, 0:c1 - c0], q[:, k, i * P:(i + 1) * P],
                                                       kz[:, k, m, c0:c1], start=True, stop=True)
                            ins.then_inc(s["s_mm"], 1)

                    def turn(j):
                        i = j % NT
                        pe.wait_ge(s["w_ready"], it * J + (j + 1))
                        for b, c0, c1 in banks(i):
                            for t in range(c0 // P, c1 // P):
                                ins = nc.tensor.transpose(bank[4 + b][:, (t % 4) * P:(t % 4 + 1) * P], w[:, j % 2, t * P:(t + 1) * P],
                                                          ident)
                            ins.then_inc(s["trB" if b else "trA"], 1)

                    def values(j):
                        i, k = j % NT, j // NT % 2
                        if j >= 2 or not first:
                            pe.wait_ge(s["o_ev"], it * J + (j - 1))
                        if j == NT + 1 or j == 1 and not first:
                            pe.wait_ge(s["ms"], it * 2 + j // NT)
                        for t in range(i + 1):
                            if t % 4 == 0:
                                pe.wait_ge(*((s["evB"], it * 8 + late(j)) if t else (s["evA"], it * J + (j + 1))))
                            ins = nc.tensor.matmul(bank[6 + j % 2][:, 0:P], v[:, k, t, :], wT[:, j % 2, t, :],
                                                   start=(t == 0), stop=(t == i))
                        ins.then_inc(s["o_mm"], 1)

                    def sums(k):
                        pe.wait_ge(s["squared"], it * 2 + (k + 1))
                        pe.wait_ge(s["o_ev"], it * J + ((k + 1) * NT + (0 if last else 1)))
                        for b in range(2):
                            ins = nc.tensor.matmul(bank[6 + b][:, :], ones, rs[:, k % 2, b * BANK:(b + 1) * BANK], start=True, stop=True)
                        ins.then_inc(s["sums"], 1)

                    for j in range(2 if last else J):
                        before = j >= 2 or not first
                        if before:
                            turn(j - 2)
                        if not last:
                            scores(j)
                        if before:
                            values(j - 2)
                        if j == NT + 2 or j == 2 and not first:
                            sums(j // NT - 1)
                    if last:
                        sums(-1)

                tiles(0, first=True)
                with pe.Fori(1, TURNS) as it:
                    tiles(it)
                tiles(TURNS, last=True)

            @block.scalar
            def _(act):
                act.wait_ge(s["lam"], 1)
                nc.scalar.activation(lm[:, 2:4], lm[:, 0:2], ACT.Exp).then_inc(s["lam_exp"], 1)
                def tiles(it, first=False, last=False):
                    def evacuate(j):
                        i = j % NT
                        n = min((i + 1) * P, BANK)
                        act.wait_ge(s["trA"], it * J + (j + 1))
                        nc.scalar.activation(wT[:, j % 2, 0:4, :].rearrange("p n d -> p (n d)")[:, 0:n], bank[4][:, 0:n], ACT.Copy)\
                            .then_inc(s["evA"], 1)

                    def result(j):
                        i, k = j % NT, j // NT % 2
                        act.wait_ge(s["o_mm"], it * J + (j + 1))
                        if i == 0 and not first:
                            act.wait_ge(s["out"], it * 2 + (k - 1))
                        nc.scalar.activation(o[:, k, i * P:(i + 1) * P], bank[6 + j % 2][:, 0:P], ACT.Copy).then_inc(s["o_ev"], 1)

                    def exponentials(j):
                        i = j % NT
                        if j >= 2 or not first:
                            act.wait_ge(s["w_ready"], it * J + (j - 1))
                        for m in range(2):
                            act.wait_ge(s["nm"], it * (2 * J) + (2 * j + m + 1))
                            for b, c0, c1 in banks(i):
                                ins = nc.scalar.activation(e[:, j % 2, m, c0:c1], bank[2 * m + b][:, 0:c1 - c0], ACT.Exp,
                                                           bias=sm[:, j % 2, m, 2:3], accum_out=sm[:, j % 2, m, 3 + b:4 + b])
                            ins.then_inc(s["exp"], 1)

                    def square(k):
                        act.wait_ge(s["o_ev"], it * J + (k + 1) * NT)
                        nc.scalar.activation(rs[:, k % 2, :], o[:, k % 2, :], ACT.Square).then_inc(s["squared"], 1)

                    def root(k):
                        act.wait_ge(s["ms"], it * 2 + (k + 1))
                        nc.scalar.activation(rs[:, k % 2, :], rs[:, k % 2, :], ACT.Sqrt).then_inc(s["root"], 1)

                    for j in range(2 if last else J):
                        before = j >= 2 or not first
                        if before:
                            evacuate(j - 2)
                        if not last:
                            exponentials(j)
                        if before:
                            result(j - 2)
                        if j == NT + 1 or j == 1 and not first:
                            square(j // NT - 1)
                        if j == NT + 3 or j == 3 and not first:
                            root(j // NT - 1)
                    if last:
                        root(-1)

                tiles(0, first=True)
                with act.Fori(1, TURNS) as it:
                    tiles(it)
                tiles(TURNS, last=True)

            @block.vector
            def _(dve):
                head = Steps(s["chain"])
                dve.wait_ge(s["lam_in"], 64)
                for n in range(2):
                    dve.wait_ge(s["chain"], head(nc.vector.tensor_tensor(lp[:, n, :], lv[:, 2 * n, :], lv[:, 2 * n + 1, :], ALU.mult)))
                nc.vector.tensor_reduce(lm[:, 0:2], lp[:, :, :], AX_X, ALU.add).then_inc(s["lam"], 1)
                dve.wait_ge(s["lam_exp"], 1)
                dve.wait_ge(s["chain"], head(nc.vector.tensor_tensor(lm[:, 4:5], lm[:, 2:3], lm[:, 3:4], ALU.subtract)))
                dve.wait_ge(s["chain"], head(nc.vector.tensor_scalar(lm[:, 5:6], lm[:, 4:5], LAMBDA_INIT, -1.0, ALU.add, ALU.mult)))
                dve.wait_ge(s["chain"], head(nc.vector.tensor_scalar(sub[:, :], col[:, COLS["subln"]:COLS["subln"] + 1],
                                                                     1.0 - LAMBDA_INIT, None, ALU.mult)))
                base = head.n
                per_tile = lambda i: 2 * (2 + (i >= 4)) + 1 + (i >= 4)
                CHAIN = 2 * sum(per_tile(i) for i in range(NT)) + 2
                FIRST = CHAIN - 3

                def tiles(it, first=False, last=False):
                    link = Loop(s["chain"], 0 if first else it - 1, CHAIN)
                    link.base = link.base + (base if first else base + FIRST)

                    def wait(n):
                        dve.wait_ge(s["chain"], n)

                    def maxima(j):
                        i = j % NT
                        for m in range(2):
                            c = sm[:, j % 2, m]
                            dve.wait_ge(s["s_mm"], it * (2 * J) + (2 * j + m + 1))
                            d = i % 4 * P
                            wait(link(nc.vector.memset(bank[2 * m + i // 4][0:CHUNK2, d + CHUNK2:d + P], -1e30)))
                            for b, c0, c1 in banks(i):
                                n = link(nc.vector.tensor_reduce(c[:, b:b + 1], bank[2 * m + b][:, 0:c1 - c0], AX_X, ALU.max))
                            wait(n)
                            if i >= 4:
                                nc.vector.tensor_scalar(c[:, 2:3], c[:, 0:1], c[:, 1:2], -1.0, ALU.max, ALU.mult).then_inc(s["nm"], 1)
                            else:
                                nc.vector.tensor_scalar(c[:, 2:3], c[:, 0:1], -1.0, None, ALU.mult).then_inc(s["nm"], 1)

                    def reciprocals(j):
                        i = j % NT
                        both = sm[:, j % 2]
                        dve.wait_ge(s["exp"], it * (2 * J) + 2 * (j + 1))
                        if i >= 4:
                            wait(link(nc.vector.tensor_tensor(both[:, :, 5:6], both[:, :, 3:4], both[:, :, 4:5], ALU.add)))
                        total = 5 if i >= 4 else 3
                        nc.vector.reciprocal(both[:, :, 6:7], both[:, :, total:total + 1]).then_inc(s["rec"], 1)
                        dve.wait_ge(s["rec"], it * J + (j + 1))
                        link(nc.vector.tensor_tensor(both[:, 1, 7:8], both[:, 1, 6:7], lm[:, 5:6], ALU.mult))

                    def weights(j):
                        i = j % NT
                        both = sm[:, j % 2]
                        dve.wait_ge(s["scaled"], it * J + (j + 1))
                        wait(link.base + link.k)
                        if j >= 2 or not first:
                            dve.wait_ge(s["trA"], it * J + (j - 1))
                        n = (i + 1) * P
                        nc.vector.scalar_tensor_tensor(w[:, j % 2, 0:n], e[:, j % 2, 1, 0:n], both[:, 1, 7:8], e[:, j % 2, 0, 0:n],
                                                       ALU.mult, ALU.add).then_inc(s["w_ready"], 1)

                    def evacuate(j):
                        i = j % NT
                        if i >= 4:
                            n = (i + 1) * P - BANK
                            dve.wait_ge(s["trB"], it * 8 + late(j))
                            nc.vector.tensor_copy(wT[:, j % 2, 4:8, :].rearrange("p n d -> p (n d)")[:, 0:n], bank[5][:, 0:n])\
                                .then_inc(s["evB"], 1)

                    def mean(k):
                        dve.wait_ge(s["sums"], it * 2 + (k + 1))
                        for b in range(2):
                            ins = nc.vector.tensor_scalar(rs[:, k % 2, b * BANK:(b + 1) * BANK], bank[6 + b][:, :], 1.0 / P, EPS,
                                                          ALU.mult, ALU.add)
                        ins.then_inc(s["ms"], 1)

                    def norm(k):
                        dve.wait_ge(s["root"], it * 2 + (k + 1))
                        ok, rk = o[:, k % 2, :], rs[:, k % 2, :]
                        wait(link(nc.vector.reciprocal(rk, rk)))
                        nc.vector.scalar_tensor_tensor(oT[:, ds(it * 2 + k, 1), :].rearrange("p o t -> p (o t)"), ok, sub[:, 0:1],
                                                       rk, ALU.mult, ALU.mult)\
                            .then_inc(s["out"], 1)

                    for j in range(2 if last else J):
                        if j >= 2 or not first:
                            evacuate(j - 2)
                        weigh = j == 0 if last else j >= 1 or not first
                        if weigh:
                            reciprocals(j - 1)
                        if not last:
                            maxima(j)
                        if weigh:
                            weights(j - 1)
                        if j == NT + 2 or j == 2 and not first:
                            mean(j // NT - 1)
                        if j == NT + 4 or j == 4 and not first:
                            norm(j // NT - 1)
                    if last:
                        mean(-1)
                        norm(-1)
                    return link.k

                n = tiles(0, first=True)
                assert n == FIRST
                with dve.Fori(1, TURNS) as it:
                    n = tiles(it)
                    assert n == CHAIN
                tiles(TURNS, last=True)


def mixed_T(nc, bank, w_a, w_b, act_T, a_in, gates, mT):
    with Stage(nc, "mixed") as st:
        w = st.sb("w", [P, 2, 2, KD, 2 * P])
        g = st.sb("g", [P, 2, 2, T])
        y = st.sb("y", [P, 2, T])
        names = ("mm", "sig", "gated", "done", "ev")
        s = {n: st.sem(n) for n in names}
        w_in, g_in = ([st.sem(f"{n}{k}") for k in range(2)] for n in ("w_in", "g_in"))
        TURNS = KD // 4
        with nc.Block() as block:
            @block.sync
            def _(sp):
                def load_w(slot, c0):
                    for n, m in enumerate((w_a, w_b)):
                        sp.dma_start(w[:, slot, n], m[:, ds(c0, 2 * P)].rearrange("(k p) n -> p k n", p=P)).then_inc(w_in[slot], 16)

                load_w(0, 0)
                load_w(1, 2 * P)
                with sp.Fori(0, TURNS - 1) as it:
                    for k in range(2):
                        sp.wait_ge(s["mm"], it * 8 + 4 * (k + 1))
                        load_w(k, it * (4 * P) + ((4 + 2 * k) * P))

            @block.gpsimd
            def _(pool):
                with pool.Fori(0, TURNS) as it:
                    for c in range(4):
                        pool.wait_ge(s["gated"], it * 8 + 2 * (c + 1))
                        nc.gpsimd.tensor_tensor(mT[:, ds(it * 4 + c, 1), :].rearrange("p o t -> p (o t)"), y[:, 0, :], y[:, 1, :],
                                                ALU.add).then_inc(s["done"], 1)

            @block.tensor
            def _(pe):
                pe.wait_ge(a_in, 16)
                with pe.Fori(0, TURNS) as it:
                    for c in range(4):
                        if c % 2 == 0:
                            pe.wait_ge(w_in[c // 2], it * 32 + 32)
                        for n in range(2):
                            o = bank[4 * (c % 2) + 2 * n:4 * (c % 2) + 2 * n + 2]
                            if c >= 2:
                                pe.wait_ge(s["gated"], it * 8 + (2 * (c - 2) + n + 1))
                            elif c == 0 and n == 0:
                                pe.wait_ge(s["ev"], it * 2 + 1)
                            elif c == 1 and n == 0:
                                pe.wait_ge(s["ev"], it * 2 + 2)
                            for b in range(2):
                                for k in range(KD):
                                    last = nc.tensor.matmul(o[b][:, :], w[:, c // 2, n, k, (c % 2) * P:(c % 2 + 1) * P],
                                                            act_T[:, n, k, b * BANK:(b + 1) * BANK],
                                                            start=(k == 0), stop=(k == KD - 1))
                            last.then_inc(s["mm"], 1)

            @block.scalar
            def _(act):
                act.sem_inc(s["done"], 1)
                with act.Fori(0, TURNS) as it:
                    for c in range(4):
                        slot = c % 2
                        if c >= 2:
                            act.wait_ge(s["gated"], it * 8 + 2 * (c - 1))
                        elif c == 1:
                            act.wait_ge(s["ev"], it * 2 + 2)
                        else:
                            act.wait_ge(s["ev"], it * 2 + 1)
                        for n in range(2):
                            act.dma_start(g[:, slot, n, :], gates[ds(it * (4 * P) + (n * D + c * P), P), :])\
                                .then_inc(g_in[slot], 16)
                        act.wait_ge(g_in[slot], it * 64 + 32 * (c // 2 + 1))
                        nc.scalar.activation(g[:, slot, :, :], g[:, slot, :, :], ACT.Sigmoid).then_inc(s["sig"], 1)

            @block.vector
            def _(dve):
                dve.sem_inc(s["ev"], 2)
                with dve.Fori(0, TURNS) as it:
                    for c in range(4):
                        dve.wait_ge(s["sig"], it * 4 + (c + 1))
                        dve.wait_ge(s["done"], it * 4 + (c + 1))
                        for n in range(2):
                            dve.wait_ge(s["mm"], it * 8 + (2 * c + n + 1))
                            for b in range(2):
                                t = slice(b * BANK, (b + 1) * BANK)
                                ins = nc.vector.tensor_tensor(y[:, n, t], bank[4 * (c % 2) + 2 * n + b][:, :], g[:, c % 2, n, t],
                                                              ALU.mult)
                            ins.then_inc(s["gated"], 1)
                        if c >= 2:
                            dve.wait_ge(s["gated"], it * 8 + 2 * (c + 1))
                            dve.sem_inc(s["ev"], 1)


def cross_attention(nc, bank, cst, col, w_q, w_kv, hT, mT, oT):
    NM = MEM // P
    with Stage(nc, "cross") as st:
        w = st.sb("w", [P, 2, 3, KD, P])
        qk = st.sb("qk", [P, 2, T + MEM])
        sq = st.sb("sq", [P, 2, T + MEM])
        v = st.sb("v", [P, 2, NM, P])
        g2 = st.sb("g2", [P, 2])
        sm = st.sb("sm", [P, 2, NT, 4])
        e = st.sb("e", [P, NT, MEM])
        eT = st.sb("eT", [P, NM, T])
        names = ("proj", "proj_ev", "v_ev", "squared", "sums", "ms", "root", "chain", "head", "normed", "s_mm", "nm", "exp",
                 "p_ready", "tr", "tr_ev", "o_mm", "o_ev")
        s = {n: st.sem(n) for n in names}
        w_in = [[st.sem(f"w_in{k}{n}") for n in range(3)] for k in range(2)]
        ident, ones = (cst[:, CONST[n]:CONST[n] + P] for n in ("ident", "ones"))
        parts = [(0, BANK), (BANK, T), (T, T + MEM)]
        TURNS = MH // 2
        with nc.Block() as block:
            @block.sync
            def _(sp):
                def load(it, k, n):
                    src = w_q if n == 0 else w_kv
                    sp.dma_start(w[:, k, n], src[:, ds(it * (2 * P) + (k * P + (MH * P if n == 2 else 0)), P)]
                                 .rearrange("(k p) n -> p k n", p=P)).then_inc(w_in[k][n], 16)

                for k in range(2):
                    for n in range(3):
                        load(0, k, n)
                for it in range(TURNS - 1):
                    for k in range(2):
                        for n in range(3):
                            sp.wait_ge(s["proj"], it * 10 + 5 * k + (2, 3, 5)[n])
                            load(it + 1, k, n)

            @block.tensor
            def _(pe):
                def project(h, k, which):
                    if h >= 2 and which[0] == 0:
                        pe.wait_ge(s["o_ev"], 2 * (h - 1))
                    for n in which:
                        a, b = parts[n]
                        m = 1 if n == 2 else 0
                        pe.wait_ge(w_in[k][m], 16 * (h // 2 + 1))
                        for j in range(KD):
                            rhs = mT[:, j, :] if m else hT[:, j, a:b]
                            last = nc.tensor.matmul(bank[n][:, 0:b - a], w[:, k, m, j, :], rhs, start=(j == 0), stop=(j == KD - 1))
                        last.then_inc(s["proj"], 1)
                    if which[-1] < 2:
                        return
                    pe.wait_ge(w_in[k][2], 16 * (h // 2 + 1))
                    for t in range(NM):
                        for j in range(KD):
                            last = nc.tensor.matmul(bank[3][:, t * P:(t + 1) * P], mT[:, j, t * P:(t + 1) * P], w[:, k, 2, j, :],
                                                    start=(j == 0), stop=(j == KD - 1))
                        last.then_inc(s["proj"], 1)

                def sums(h, k):
                    for n, (a, b) in enumerate(parts):
                        pe.wait_ge(s["squared"], h * 3 + (n + 1))
                        nc.tensor.matmul(bank[4 + n][:, 0:b - a], ones, sq[:, k, a:b], start=True, stop=True).then_inc(s["sums"], 1)

                def scores(h, k):
                    pe.wait_ge(s["normed"], h * 3 + 3)
                    for i in range(NT):
                        ins = nc.tensor.matmul(bank[4 + i // 2][:, (i % 2) * MEM:(i % 2 + 1) * MEM], qk[:, k, i * P:(i + 1) * P],
                                               qk[:, k, T:T + MEM], start=True, stop=True)
                        if i % 2:
                            ins.then_inc(s["s_mm"], 1)

                def results(h, k):
                    pe.wait_ge(s["exp"], h * NT + NT)
                    for i in range(NT):
                        pe.wait_ge(s["p_ready"], h * NT + (i + 1))
                        for t in range(NM):
                            ins = nc.tensor.transpose(bank[4 + 2 * (i // 4) + t][:, (i % 4) * P:(i % 4 + 1) * P],
                                                      e[:, i, t * P:(t + 1) * P], ident)
                        if i % 4 == 3:
                            ins.then_inc(s["tr"], 1)
                    if h + 1 < MH:
                        pe.wait_ge(s["proj_ev"], 3 * (h + 1) + 2)
                    for b in range(2):
                        pe.wait_ge(s["tr_ev"], h * 2 + (b + 1))
                        for t in range(NM):
                            last = nc.tensor.matmul(bank[b][:, :], v[:, k, t, :], eT[:, t, b * BANK:(b + 1) * BANK],
                                                    start=(t == 0), stop=(t == NM - 1))
                        last.then_inc(s["o_mm"], 1)

                project(0, 0, (0, 1, 2))
                for h in range(MH):
                    k = h % 2
                    sums(h, k)
                    if h + 1 < MH:
                        project(h + 1, 1 - k, (0, 1))
                    scores(h, k)
                    if h + 1 < MH:
                        if h:
                            pe.wait_ge(s["v_ev"], h + 1)
                        project(h + 1, 1 - k, (2,))
                    results(h, k)

            @block.scalar
            def _(act):
                def evacuate(h, k, which):
                    for n in which:
                        a, b = parts[n]
                        act.wait_ge(s["proj"], h * 5 + (n + 1))
                        nc.scalar.activation(qk[:, k, a:b], bank[n][:, 0:b - a], ACT.Copy).then_inc(s["proj_ev"], 1)
                    if which[-1] == 2:
                        act.wait_ge(s["proj"], h * 5 + 5)
                        nc.scalar.activation(v[:, k, :, :].rearrange("p n d -> p (n d)"), bank[3][:, 0:MEM], ACT.Copy)\
                            .then_inc(s["v_ev"], 1)
                    for n in which:
                        a, b = parts[n]
                        act.wait_ge(s["proj_ev"], h * 3 + (n + 1))
                        nc.scalar.activation(sq[:, k, a:b], qk[:, k, a:b], ACT.Square).then_inc(s["squared"], 1)

                evacuate(0, 0, (0, 1, 2))
                for h in range(MH):
                    k = h % 2
                    act.wait_ge(s["ms"], h * 3 + 3)
                    nc.scalar.activation(sq[:, k, :], sq[:, k, :], ACT.Sqrt).then_inc(s["root"], 1)
                    if h + 1 < MH:
                        evacuate(h + 1, 1 - k, (0, 1))
                    for i in range(NT):
                        act.wait_ge(s["nm"], h * NT + (i // 2 * 2 + 2))
                        nc.scalar.activation(e[:, i, :], bank[4 + i // 2][:, (i % 2) * MEM:(i % 2 + 1) * MEM], ACT.Exp,
                                             bias=sm[:, k, i, 1:2], accum_out=sm[:, k, i, 2:3]).then_inc(s["exp"], 1)
                    if h + 1 < MH:
                        evacuate(h + 1, 1 - k, (2,))
                    for b in range(2):
                        act.wait_ge(s["tr"], h * 2 + (b + 1))
                        for t in range(NM):
                            ins = nc.scalar.activation(eT[:, t, b * BANK:(b + 1) * BANK], bank[4 + 2 * b + t][:, :], ACT.Copy)
                        ins.then_inc(s["tr_ev"], 1)

            @block.vector
            def _(dve):
                head, link = Steps(s["head"]), Steps(s["chain"])
                for n, (name, scale) in enumerate((("cqn", float(P) ** -0.5), ("ckn", 1.0))):
                    dve.wait_ge(s["head"], head(nc.vector.tensor_scalar(g2[:, n:n + 1], col[:, COLS[name]:COLS[name] + 1], scale,
                                                                       None, ALU.mult)))

                def step(ins):
                    dve.wait_ge(s["chain"], link(ins))

                for h in range(MH):
                    k = h % 2
                    for n, (a, b) in enumerate(parts):
                        dve.wait_ge(s["sums"], h * 3 + (n + 1))
                        nc.vector.tensor_scalar(sq[:, k, a:b], bank[4 + n][:, 0:b - a], 1.0 / P, EPS, ALU.mult, ALU.add)\
                            .then_inc(s["ms"], 1)
                    dve.wait_ge(s["root"], h + 1)
                    step(nc.vector.reciprocal(sq[:, k, :], sq[:, k, :]))
                    for n, (a, b) in enumerate(parts):
                        m = 1 if n == 2 else 0
                        nc.vector.scalar_tensor_tensor(qk[:, k, a:b], qk[:, k, a:b], g2[:, m:m + 1], sq[:, k, a:b], ALU.mult, ALU.mult)\
                            .then_inc(s["normed"], 1)

                    def weights(i):
                        dve.wait_ge(s["exp"], h * NT + (i + 1))
                        step(nc.vector.reciprocal(sm[:, k, i, 3:4], sm[:, k, i, 2:3]))
                        nc.vector.tensor_scalar(e[:, i, :], e[:, i, :], sm[:, k, i, 3:4], None, ALU.mult).then_inc(s["p_ready"], 1)

                    dve.wait_ge(s["s_mm"], h * (NT // 2) + NT // 2)
                    for i in range(NT):
                        step(nc.vector.tensor_reduce(sm[:, k, i, 0:1], bank[4 + i // 2][:, (i % 2) * MEM:(i % 2 + 1) * MEM], AX_X,
                                                     ALU.max))
                        nc.vector.tensor_scalar(sm[:, k, i, 1:2], sm[:, k, i, 0:1], -1.0, None, ALU.mult).then_inc(s["nm"], 1)
                        if i >= 2:
                            weights(i - 2)
                    weights(NT - 2)
                    weights(NT - 1)
                    for b in range(2):
                        dve.wait_ge(s["o_mm"], h * 2 + (b + 1))
                        nc.vector.tensor_copy(oT[:, h, b * BANK:(b + 1) * BANK], bank[b][:, :]).then_inc(s["o_ev"], 1)


NOVER = (2 * T) // (P + 1) + 1
SLOTS = (E2 + NOVER) * P


def route2(nc, bank, cst, tok, hT, w_group, b_group, w_router, b_router, slot_tok, ye_over, dest, weight, eid, placed):
    G, W = GROUPS, GROUPS + E2
    with Stage(nc, "route2") as st:
        wr = st.sb("wr", [P, KD, W])
        br = st.sb("br", [W, 1])
        lT = st.sb("lT", [W, T])
        lg = st.sb("lg", [P, NT, W])
        gs = st.sb("gs", [P, 6, NT])
        gx, gm = st.sb("gx", [P, NT, G]), st.sb("gm", [P, NT, G])
        el = st.sb("el", [P, NT, G, EPG])
        e8 = st.sb("e8", [P, 2, NT, EPG])
        m8 = st.sb("m8", [P, NT, EPG])
        es = st.sb("es", [P, 8, NT])
        A = st.sb("A", [P, 3, NT, E2])
        B = st.sb("B", [P, NT + 1, E2])
        F = st.sb("F", [P, NT, E2])
        G_ = st.sb("G", [P, NT, E2])
        cn = st.sb("cn", [P, 6, E2])
        ov = st.sb("ov", [P, E2, 8])
        ob = st.sb("ob", [P, NOVER, E2])
        df = st.sb("df", [P, 2, NT])
        ef = st.sb("ef", [P, NOVER + 1])
        zero = st.sb("zero", [P, D])
        names = ("w_in", "l_mm", "l_ev", "tr", "chain", "g_sub", "g_exp", "e_sub", "e_exp", "sums", "r_mm", "zeroed", "cleared", "cleared_ye",
                 "dest_ready", "counted")
        s = {n: st.sem(n) for n in names}
        ident, ones, lower = (cst[:, CONST[n]:CONST[n] + P] for n in ("ident", "ones", "lower"))
        iota = cst[:, CONST["e32"]:CONST["e32"] + E2]
        with nc.Block() as block:
            @block.sync
            def _(sp):
                with nc.allow_non_contiguous_dma("narrow matrices"):
                    sp.dma_start(wr[:, :, 0:G], w_group.rearrange("(k p) e -> p k e", p=P)).then_inc(s["w_in"], 16)
                    sp.dma_start(wr[:, :, G:], w_router.rearrange("(k p) e -> p k e", p=P)).then_inc(s["w_in"], 16)
                    sp.dma_start(br[0:G, :], b_group.rearrange("o e -> e o")).then_inc(s["w_in"], 16)
                    sp.dma_start(br[G:, :], b_router.rearrange("o e -> e o")).then_inc(s["w_in"], 16)
                sp.wait_ge(s["zeroed"], 1)
                sp.dma_start(slot_tok.rearrange("(b p) o -> b (p o)", p=P), zero[0:SLOTS // P, 0:P]).then_inc(s["cleared"], 16)
                for b in range(NOVER):
                    sp.dma_start(ye_over[b * P:(b + 1) * P, :], zero[:, :]).then_inc(s["cleared_ye"], 16)
                sp.wait_ge(s["cleared_ye"], 16 * NOVER)

            @block.gpsimd
            def _(pool):
                nc.gpsimd.memset(zero[:, :], 0.0).then_inc(s["zeroed"], 1)
                pool.wait_ge(s["cleared"], 16)
                pool.wait_ge(s["dest_ready"], 1)
                for k in range(2):
                    for i in range(NT):
                        pool.indirect_dma_start(out=slot_tok[:, :],
                                                out_offset=bass.IndirectOffsetOnAxis(ap=dest[:, k * NT + i:k * NT + i + 1], axis=0),
                                                in_=tok[:, i:i + 1], in_offset=None).then_inc(placed, 16)
                pool.wait_ge(placed, 16 * 2 * NT)

            @block.tensor
            def _(pe):
                pe.wait_ge(s["w_in"], 64)
                for c in range(2):
                    for k in range(KD):
                        last = nc.tensor.matmul(bank[c][0:W, :], wr[:, k, :], hT[:, k, c * BANK:(c + 1) * BANK],
                                                start=(k == 0), stop=(k == KD - 1))
                    last.then_inc(s["l_mm"], 1)
                pe.wait_ge(s["l_ev"], 2)
                for i in range(NT):
                    last = nc.tensor.transpose(bank[2][:, i * W:(i + 1) * W], lT[:, i * P:(i + 1) * P], ident[0:W, 0:W])
                last.then_inc(s["tr"], 1)
                pe.wait_ge(s["sums"], 1)
                both = A[:, 2, :, :].rearrange("p n e -> p (n e)")
                nc.tensor.matmul(bank[3][:, 0:NT * E2], lower, both, start=True, stop=False)
                nc.tensor.matmul(bank[3][:, 0:NT * E2], ones, B[:, 0:NT, :].rearrange("p n e -> p (n e)"), start=False, stop=True)
                nc.tensor.matmul(bank[4][:, 0:E2], ones, B[:, NT, :], start=True, stop=True).then_inc(s["r_mm"], 1)

            @block.scalar
            def _(act):
                act.wait_ge(s["w_in"], 64)
                for c in range(2):
                    act.wait_ge(s["l_mm"], c + 1)
                    nc.scalar.activation(lT[:, c * BANK:(c + 1) * BANK], bank[c][0:W, :], ACT.Identity, bias=br[:, 0:1])\
                        .then_inc(s["l_ev"], 1)
                act.wait_ge(s["g_sub"], 1)
                nc.scalar.activation(gx[:, :, :], gx[:, :, :], ACT.Exp).then_inc(s["g_exp"], 1)
                act.wait_ge(s["e_sub"], 1)
                nc.scalar.activation(es[:, 4, :], es[:, 4, :], ACT.Exp).then_inc(s["e_exp"], 1)

            @block.vector
            def _(dve):
                link = Steps(s["chain"])

                def step(ins):
                    dve.wait_ge(s["chain"], link(ins))

                def over(a, n):
                    return a.unsqueeze(2).to_broadcast([P, NT, n])

                def along(a, n):
                    return a.unsqueeze(1).to_broadcast([P, NT, n])

                V = nc.vector
                dve.wait_ge(s["tr"], 1)
                step(V.tensor_copy(lg[:, :, :].rearrange("p n w -> p (n w)"), bank[2][:, 0:NT * W]))
                step(V.tensor_reduce(gs[:, 0, :], lg[:, :, 0:G], AX_X, ALU.max))
                V.tensor_tensor(gx[:, :, :], lg[:, :, 0:G], over(gs[:, 0, :], G), ALU.subtract).then_inc(s["g_sub"], 1)
                dve.wait_ge(s["g_exp"], 1)
                step(V.tensor_reduce(gs[:, 1, :], gx[:, :, :], AX_X, ALU.add))
                step(V.reciprocal(gs[:, 2, :], gs[:, 1, :]))
                step(V.tensor_tensor(gx[:, :, :], gx[:, :, :], over(gs[:, 2, :], G), ALU.mult))

                def first_greatest(values, n, greatest, index, scratch):
                    step(V.tensor_reduce(greatest, values, AX_X, ALU.max))
                    step(V.tensor_tensor(scratch, values, over(greatest, n), ALU.is_equal))
                    step(V.tensor_scalar(m8[:, 0, 0:n], iota[:, 0:n], -64.0, None, ALU.add))
                    step(V.tensor_tensor(scratch, scratch, along(m8[:, 0, 0:n], n), ALU.mult))
                    step(V.tensor_reduce(index, scratch, AX_X, ALU.min))
                    step(V.tensor_scalar(index, index, 64.0, None, ALU.add))
                    step(V.tensor_tensor(scratch, along(iota[:, 0:n], n), over(index, n), ALU.is_equal))

                first_greatest(gx[:, :, :], G, gs[:, 3, :], gs[:, 4, :], gm[:, :, :])
                step(V.tensor_tensor(el[:, :, :, :], lg[:, :, G:].rearrange("p n (g e) -> p n g e", g=G),
                                     gm[:, :, :].unsqueeze(3).to_broadcast([P, NT, G, EPG]), ALU.mult))
                step(V.tensor_tensor(e8[:, 0], el[:, :, 0, :], el[:, :, 1, :], ALU.add))
                step(V.tensor_tensor(e8[:, 0], e8[:, 0], el[:, :, 2, :], ALU.add))
                step(V.tensor_tensor(e8[:, 0], e8[:, 0], el[:, :, 3, :], ALU.add))
                first_greatest(e8[:, 0], EPG, es[:, 0, :], es[:, 1, :], e8[:, 1])
                step(V.scalar_tensor_tensor(e8[:, 0], e8[:, 1], -3.0e38, e8[:, 0], ALU.mult, ALU.add))
                first_greatest(e8[:, 0], EPG, es[:, 2, :], es[:, 3, :], e8[:, 1])
                V.tensor_tensor(es[:, 4, :], es[:, 2, :], es[:, 0, :], ALU.subtract).then_inc(s["e_sub"], 1)
                dve.wait_ge(s["e_exp"], 1)
                step(V.tensor_scalar(es[:, 5, :], es[:, 4, :], 1.0, None, ALU.add))
                step(V.reciprocal(es[:, 5, :], es[:, 5, :]))
                step(V.tensor_tensor(weight[:, 0:NT], es[:, 5, :], gs[:, 3, :], ALU.mult))
                step(V.tensor_tensor(weight[:, NT:], weight[:, 0:NT], es[:, 4, :], ALU.mult))
                for k in range(2):
                    step(V.scalar_tensor_tensor(es[:, 6 + k, :], gs[:, 4, :], float(EPG), es[:, 1 + 2 * k, :], ALU.mult, ALU.add))
                    step(V.tensor_tensor(A[:, k], along(iota, E2), over(es[:, 6 + k, :], E2), ALU.is_equal))
                step(V.tensor_tensor(A[:, 2], A[:, 0], A[:, 1], ALU.add))
                step(V.memset(B[:, 0, :], 0.0))
                for i in range(NT):
                    ins = V.tensor_tensor(B[:, i + 1, :], B[:, i, :], A[:, 2, i, :], ALU.add)
                    if i < NT - 1:
                        step(ins)
                    else:
                        ins.then_inc(s["sums"], 1)
                dve.wait_ge(s["r_mm"], 1)
                rank, count = bank[3][:, 0:NT * E2].rearrange("p (n e) -> p n e", e=E2), bank[4][:, 0:E2]
                step(V.tensor_scalar(cn[:, 5, 0:8], iota[:, 0:8], float(P), float(P), ALU.mult, ALU.add))
                step(V.tensor_tensor(ov[:, :, :], count.unsqueeze(2).to_broadcast([P, E2, 8]),
                                     cn[:, 5, 0:8].unsqueeze(1).to_broadcast([P, E2, 8]), ALU.is_gt))
                step(V.tensor_reduce(cn[:, 0, :], ov[:, :, :], AX_X, ALU.add))
                step(V.tensor_tensor_scan(cn[:, 1, :], ones[:, 0:E2], cn[:, 0, :], 0.0, ALU.mult, ALU.add))
                step(V.tensor_tensor(cn[:, 2, :], cn[:, 1, :], cn[:, 0, :], ALU.subtract))
                step(V.tensor_scalar(cn[:, 3, :], iota, float(P), None, ALU.mult))
                step(V.tensor_scalar(cn[:, 4, :], cn[:, 2, :], float(P), float((E2 - 1) * P), ALU.mult, ALU.add))
                step(V.tensor_tensor(cn[:, 4, :], cn[:, 4, :], cn[:, 3, :], ALU.subtract))
                step(V.tensor_scalar(F[:, :, :], rank, float(P), None, ALU.is_ge))
                step(V.tensor_tensor(F[:, :, :], F[:, :, :], along(cn[:, 4, :], E2), ALU.mult))
                step(V.tensor_tensor(F[:, :, :], F[:, :, :], along(cn[:, 3, :], E2), ALU.add))
                step(V.tensor_tensor(F[:, :, :], F[:, :, :], rank, ALU.add))
                for k in range(2):
                    step(V.tensor_tensor(G_[:, :, :], F[:, :, :], A[:, k], ALU.mult))
                    step(V.tensor_reduce(df[:, k, :], G_[:, :, :], AX_X, ALU.add))
                V.tensor_copy(dest[:, :], df[:, :, :].rearrange("p k n -> p (k n)")).then_inc(s["dest_ready"], 1)
                step(V.tensor_tensor(ob[:, :, :], cn[:, 1, :].unsqueeze(1).to_broadcast([P, NOVER, E2]),
                                     iota[:, 0:NOVER].unsqueeze(2).to_broadcast([P, NOVER, E2]), ALU.is_le))
                step(V.tensor_reduce(ef[:, 0:NOVER], ob[:, :, :], AX_X, ALU.add))
                step(V.tensor_scalar(ef[:, 0:NOVER], ef[:, 0:NOVER], float(E2 - 1), None, ALU.min))
                step(V.tensor_copy(ef[:, NOVER:NOVER + 1], cn[:, 1, E2 - 1:E2]))
                V.tensor_copy(eid[:, :], ef[:, :]).then_inc(s["counted"], 1)


def slot_tokens(nc, bank, cst, slot_tok, idx):
    NB = SLOTS // P
    with Stage(nc, "slots") as st:
        rows = st.sb("rows", [NB, P])
        loaded, tr, done = st.sem("loaded"), st.sem("tr"), st.sem("done")
        with nc.Block() as block:
            @block.sync
            def _(sp):
                sp.dma_start(rows[:, :], slot_tok.rearrange("(b p) o -> b (p o)", p=P)).then_inc(loaded, 16)

            @block.tensor
            def _(pe):
                pe.wait_ge(loaded, 16)
                nc.tensor.transpose(bank[0][:, 0:NB], rows[:, :], cst[0:NB, CONST["ident"]:CONST["ident"] + NB]).then_inc(tr, 1)

            @block.vector
            def _(dve):
                dve.wait_ge(tr, 1)
                nc.vector.tensor_copy(idx[:, 0:NB], bank[0][:, 0:NB]).then_inc(done, 1)
                nc.vector.tensor_copy(idx[:, NB:NB + 1], bank[0][:, 0:1]).then_inc(done, 1)


def experts2(nc, bank, name, cst, h, w_gate_up, w_down, ye, idx, first, blocks, gathered, before, eid=None):
    LB = 2
    with Stage(nc, name) as st:
        w = st.sb("w", [P, LB, 3, 8 * BANK])
        xs, xT = st.sb("xs", [P, LB, D]), st.sb("xT", [P, LB, KD, P])
        cur = st.sb("cur", [P, LB], U32)
        sg, hid = st.sb("sg", [P, LB, BANK]), st.sb("hid", [P, LB, BANK])
        hidT = st.sb("hidT", [P, LB, 4, P])
        y = st.sb("y", [P, LB, D])
        names = ("turns", "cur_ready", "x_in", "x_tr", "xT_ev", "gu_mm", "sg_ready", "hid_ready", "h_tr", "hT_ev", "y_mm", "y_ready")
        s = {n: st.sem(n) for n in names}
        w_in = [[st.sem(f"w_in{k}{i}") for i in range(3)] for k in range(LB)]
        stored = [st.sem(f"stored{k}") for k in range(LB)]
        ident = cst[:, CONST["ident"]:CONST["ident"] + P]
        TURNS = blocks // LB

        def load(sp, e, k, i):
            if i < 2:
                src = w_gate_up[ds(e, 1), :, i * BANK:(i + 1) * BANK].rearrange("o (k p) n -> p (o k) n", p=P)
                dst = w[:, k, i].rearrange("p (k n) -> p k n", k=8)
            else:
                src = w_down[ds(e, 1), :, :].rearrange("o (k p) n -> p (o k) n", p=P)
                dst = w[:, k, 2].rearrange("p (k n) -> p k n", k=4)
            sp.dma_start(dst, src).then_inc(w_in[k][i], 16)

        def expert(sp, b):
            return b if eid is None else sp.value_load(eid[0:1, ds(b, 1)], min_val=0, max_val=E2 - 1)

        def weights_and_stores(sp):
            for k in range(LB):
                sp.sem_inc(stored[k], 1)
                e = expert(sp, k)
                for i in range(3):
                    load(sp, e, k, i)

            def store(it, k):
                sp.wait_ge(s["y_ready"], it * (2 * LB) + (2 * k + 3))
                sp.sem_inc(s["turns"], 1)
                sp.dma_start(ye[ds(it * (LB * P) + (first + k) * P, P), :], y[:, k, :]).then_inc(stored[k], 16)

            with sp.Fori(0, TURNS - 1) as it:
                for k in range(LB):
                    for i in range(3):
                        if i < 2:
                            sp.wait_ge(s["gu_mm"], it * (2 * LB) + (2 * k + i + 1))
                        else:
                            sp.wait_ge(s["y_mm"], it * (2 * LB) + 2 * (k + 1))
                        sp.sem_inc(s["turns"], 1)
                        if i == 0:
                            e = expert(sp, it * LB + (LB + k))
                        load(sp, e, k, i)
                    store(it, k)
            for k in range(LB):
                store(TURNS - 1, k)
                sp.wait_ge(stored[k], 16 * TURNS + 1)

        def gathers(pool):
            def gather(k):
                pool.indirect_dma_start(out=xs[:, k, :], out_offset=None, in_=h[:, :],
                                        in_offset=bass.IndirectOffsetOnAxis(ap=cur[:, k:k + 1], axis=0)).then_inc(gathered, 16)

            for k in range(LB):
                nc.gpsimd.tensor_copy(cur[:, k:k + 1], idx[:, first + k:first + k + 1]).then_inc(s["cur_ready"], 1)
                pool.wait_ge(s["cur_ready"], k + 1)
                gather(k)
                pool.wait_ge(gathered, 16 * (before + k + 1))
                pool.sem_inc(s["x_in"], 1)
            with pool.Fori(0, TURNS - 1) as it:
                for k in range(LB):
                    pool.wait_ge(s["x_tr"], it * (2 * LB) + 2 * (k + 1))
                    pool.sem_inc(s["turns"], 1)
                    nc.gpsimd.tensor_copy(cur[:, k:k + 1], idx[:, ds(it * LB + (first + LB + k), 1)]).then_inc(s["cur_ready"], 1)
                    pool.wait_ge(s["cur_ready"], it * LB + (LB + k + 1))
                    pool.sem_inc(s["turns"], 1)
                    gather(k)
                    pool.wait_ge(gathered, it * (16 * LB) + 16 * (before + LB + k + 1))
                    pool.sem_inc(s["x_in"], 1)

        def products(pe):
            with pe.Fori(0, TURNS) as it:
                def tokens(k):
                    pe.wait_ge(s["x_in"], it * LB + (k + 1))
                    for j in range(KD):
                        ins = nc.tensor.transpose(bank[6 + j // 4][:, (j % 4) * P:(j % 4 + 1) * P], xs[:, k, j * P:(j + 1) * P], ident)
                        if j % 4 == 3:
                            ins.then_inc(s["x_tr"], 1)

                def gate_up(k):
                    pe.wait_ge(s["xT_ev"], it * (2 * LB) + 2 * (k + 1))
                    for i in range(2):
                        pe.wait_ge(w_in[k][i], it * 16 + 16)
                        wi = w[:, k, i].rearrange("p (k n) -> p k n", k=8)
                        for j in range(KD):
                            last = nc.tensor.matmul(bank[2 * k + i][:, :], xT[:, k, j, :], wi[:, j, :], start=(j == 0), stop=(j == KD - 1))
                        last.then_inc(s["gu_mm"], 1)

                def down(k):
                    pe.wait_ge(s["hid_ready"], it * LB + (k + 1))
                    for j in range(4):
                        ins = nc.tensor.transpose(bank[2 * k][:, j * P:(j + 1) * P], hid[:, k, j * P:(j + 1) * P], ident)
                    ins.then_inc(s["h_tr"], 1)
                    pe.wait_ge(s["hT_ev"], it * LB + (k + 1))
                    pe.wait_ge(w_in[k][2], it * 16 + 16)
                    wi = w[:, k, 2].rearrange("p (k n) -> p k n", k=4)
                    pe.wait_ge(s["y_ready"], it * (2 * LB) + (2 * k + 1))
                    for c in range(2):
                        for j in range(4):
                            last = nc.tensor.matmul(bank[4 + c][:, :], hidT[:, k, j, :], wi[:, j, c * BANK:(c + 1) * BANK],
                                                    start=(j == 0), stop=(j == 3))
                        last.then_inc(s["y_mm"], 1)

                tokens(0)
                gate_up(0)
                tokens(1)
                gate_up(1)
                down(0)
                down(1)

        def rows_T(act):
            with act.Fori(0, TURNS) as it:
                for k in range(LB):
                    for b in range(2):
                        act.wait_ge(s["x_tr"], it * (2 * LB) + (2 * k + b + 1))
                        nc.scalar.activation(xT[:, k, 4 * b:4 * b + 4, :].rearrange("p k t -> p (k t)"), bank[6 + b][:, :], ACT.Copy)\
                            .then_inc(s["xT_ev"], 1)
                    act.wait_ge(s["gu_mm"], it * (2 * LB) + (2 * k + 1))
                    nc.scalar.activation(sg[:, k, :], bank[2 * k][:, :], ACT.Silu).then_inc(s["sg_ready"], 1)

        def hidden(dve):
            dve.sem_inc(s["y_ready"], 1)
            with dve.Fori(0, TURNS) as it:
                def gated(k):
                    dve.wait_ge(s["sg_ready"], it * LB + (k + 1))
                    dve.wait_ge(s["gu_mm"], it * (2 * LB) + 2 * (k + 1))
                    nc.vector.tensor_tensor(hid[:, k, :], sg[:, k, :], bank[2 * k + 1][:, :], ALU.mult).then_inc(s["hid_ready"], 1)

                def turned(k):
                    dve.wait_ge(s["h_tr"], it * LB + (k + 1))
                    nc.vector.tensor_copy(hidT[:, k, :, :].rearrange("p k t -> p (k t)"), bank[2 * k][:, :]).then_inc(s["hT_ev"], 1)

                def out(k):
                    dve.wait_ge(stored[k], it * 16 + 1)
                    for c in range(2):
                        dve.wait_ge(s["y_mm"], it * (2 * LB) + (2 * k + c + 1))
                        nc.vector.tensor_copy(y[:, k, c * BANK:(c + 1) * BANK], bank[4 + c][:, :]).then_inc(s["y_ready"], 1)

                gated(0)
                gated(1)
                for k in range(LB):
                    turned(k)
                    out(k)

        def when_used(engine, body):
            if eid is None:
                body(engine)
                return
            with engine.If(engine.value_load(eid[0:1, NOVER:NOVER + 1], min_val=0, max_val=NOVER) > 0):
                body(engine)

        with nc.Block() as block:
            @block.sync
            def _(sp):
                when_used(sp, weights_and_stores)

            @block.gpsimd
            def _(pool):
                when_used(pool, gathers)

            @block.tensor
            def _(pe):
                when_used(pe, products)

            @block.scalar
            def _(act):
                when_used(act, rows_T)

            @block.vector
            def _(dve):
                when_used(dve, hidden)


def combine2(nc, x, ye, dest, weight, out, gathered, out_stored):
    R = 4
    with Stage(nc, "comb2") as st:
        xt, g = st.sb("x", [P, R, D]), st.sb("g", [P, R, 2, D])
        x_in = [st.sem(f"x_in{i}") for i in range(R)]
        got, first, done = st.sem("got"), st.sem("first"), st.sem("done")
        with nc.Block() as block:
            @block.gpsimd
            def _(pool):
                for i in range(NT):
                    if i >= R:
                        pool.wait_ge(done, i - R + 1)
                    for k in range(2):
                        pool.indirect_dma_start(out=g[:, i % R, k, :], out_offset=None, in_=ye[:, :],
                                                in_offset=bass.IndirectOffsetOnAxis(ap=dest[:, k * NT + i:k * NT + i + 1], axis=0))\
                            .then_inc(gathered[i % R], 16)

            @block.sync
            def _(sp):
                for i in range(NT + 2):
                    if i < NT:
                        if i >= R:
                            sp.wait_ge(out_stored[i % R], 16 * (i // R))
                        sp.dma_start(xt[:, i % R, :], x[i * P:(i + 1) * P, :]).then_inc(x_in[i % R], 16)
                    if i >= 2:
                        sp.wait_ge(done, i - 1)
                        sp.dma_start(out[0, (i - 2) * P:(i - 1) * P, :], xt[:, (i - 2) % R, :])\
                            .then_inc(out_stored[(i - 2) % R], 16)
                for r in range(R):
                    sp.wait_ge(out_stored[r], 16 * (NT // R))

            @block.vector
            def _(dve):
                for i in range(NT):
                    r = i % R
                    dve.wait_ge(gathered[r], 32 * (i // R + 1))
                    dve.wait_ge(x_in[r], 16 * (i // R + 1))
                    nc.vector.scalar_tensor_tensor(xt[:, r, :], g[:, r, 0, :], weight[:, i:i + 1], xt[:, r, :], ALU.mult, ALU.add)\
                        .then_inc(first, 1)
                    dve.wait_ge(first, i + 1)
                    nc.vector.scalar_tensor_tensor(xt[:, r, :], g[:, r, 1, :], weight[:, NT + i:NT + i + 1], xt[:, r, :], ALU.mult,
                                                   ALU.add).then_inc(done, 1)


def program(nc, x, tabs, out, stop=None):
    cst = nc.alloc_sbuf_tensor("cst", [P, CW], F32)
    col = nc.alloc_sbuf_tensor("col", [P, VW], F32)
    bank = [nc.alloc_psum_tensor(f"bank{i}", [P, BANK], F32) for i in range(8)]
    tables_in = nc.alloc_semaphore("tables_in")

    def scratch(name, *shape, dt=F32):
        return nc.dram_tensor(name, shape, dt, kind="Internal").ap()

    mod = scratch("mod", 8, D)
    with nc.Block() as block:
        @block.sync
        def _(sp):
            sp.dma_start(cst[:, :], tabs["cst"]).then_inc(tables_in, 16)
            sp.dma_start(col[:, :], tabs["cols"]).then_inc(tables_in, 16)
            sp.wait_ge(tables_in, 32)

    modulation(nc, bank, x["w_mod"], x["b_mod"], x["c"], x["c_ctx"], x["norm_gains"], mod)
    if stop == "mod":
        return

    uT = scratch("uT", D_IN, TT)
    hold = ExitStack()
    with hold:
        hT = hold.enter_context(nc.sbuf_tensor("hT", [P, KD, TT], F32))
        norm_T(nc, bank, "norm_c", cst, x["ctx"][0], TC, hT, 0, gvec=mod[MOD_CG1:MOD_CG1 + 1, :], svec=mod[MOD_CS1:MOD_CS1 + 1, :])
        norm_T(nc, bank, "norm_x", cst, x["x"][0], T, hT, TC, gvec=mod[MOD_G1:MOD_G1 + 1, :], svec=mod[MOD_S1:MOD_S1 + 1, :])
        gemm_T(nc, bank, "proj1", hT, TT, x["w_in"][0], 0, (D_IN // 512 * 2, ((P, P), (P, 64))), uT)
    if stop == "proj1":
        return
    latT = scratch("latT", D, T)
    retention(nc, bank, cst, tabs, uT, latT)
    if stop == "ret":
        return
    rwkv(nc, bank, cst, col, tabs, x, uT, scratch, latT)
    if stop == "rwkv":
        return
    x1, h2, acc, x2 = scratch("x1", T, D), scratch("h2", T, D), scratch("acc", T, D), scratch("x2", T, D)
    tokens_in, rows_added = nc.alloc_semaphore("tokens_in"), nc.alloc_semaphore("rows_added")
    experts = ExitStack()
    with experts:
        idx = experts.enter_context(nc.sbuf_tensor("idx", [P, E1 + 1], U32))
        gates = experts.enter_context(nc.sbuf_tensor("gates", [P, E1], F32))
        with nc.sbuf_tensor("h2T", [P, KD, T], F32) as h2T:
            with nc.sbuf_tensor("lT", [P, KD, T], F32) as lT:
                load_T(nc, "load_lat", latT, lT)
                gemm_rows(nc, bank, "mix", cst, lT, D, x["w_out"][0], x["x"][0], x1, h2T,
                          grow=mod[MOD_GT1:MOD_GT1 + 1, :], exchanged=range(KD // 2, KD),
                          h_rows=[mod[MOD_G2:MOD_G2 + 1, :], mod[MOD_S2:MOD_S2 + 1, :]], h_out=h2)
            route1(nc, bank, cst, h2T, x["w_router"][0], acc, idx, gates)
        experts1(nc, bank, cst, h2, x["w_gate"][0], x["w_up"][0], x["w_down"][0], acc, idx, gates, tokens_in, rows_added)
    add_normed(nc, "add1", x1, acc, mod[MOD_GT2:MOD_GT2 + 1, :], x2)
    if stop == "one":
        return
    second(nc, bank, cst, col, tabs, x, scratch, x2, out, stop)


def second(nc, bank, cst, col, tabs, x, scratch, x2, out, stop=None):
    uT2 = scratch("uT2", PROJ2, T)
    norm_mix = col[:, COLS["norm_mix"]:COLS["norm_mix"] + KD]
    gT, qkT, v_rows = scratch("gT", D, T), scratch("qkT", 2, D, T), scratch("v_rows", T, D)
    with nc.sbuf_tensor("hT2", [P, KD, T], F32) as hT:
        norm_T(nc, bank, "norm_2", cst, x2, T, hT, 0, gcol=norm_mix)
        gemm_T(nc, bank, "proj_lru", hT, T, x["w_in_2"][0], 0, (D // P, ()), uT2[0:2 * D, :])
        qkv_and_lru(nc, bank, cst, col, x, hT, uT2, gT, qkT, v_rows)
        gemm_T(nc, bank, "proj_g", hT, T, x["w_in_2"][0], 5 * D, (D // P, ()), uT2[5 * D:7 * D, :])
    if stop == "heads":
        return
    x3 = scratch("x3", T, D)
    NB = SLOTS // P
    x4, h4 = scratch("x4", T, D), scratch("h4", T, D)
    ye, slot_tok = scratch("ye", SLOTS, D), scratch("slot_tok", SLOTS, 1)
    placed, blocks_in = nc.alloc_semaphore("placed"), nc.alloc_semaphore("blocks_in")
    rows_in, out_stored = ([nc.alloc_semaphore(f"{n}{i}") for i in range(4)] for n in ("rows_in", "out_stored"))
    with nc.sbuf_tensor("dest", [P, 2 * NT], U32) as dest, nc.sbuf_tensor("weight", [P, 2 * NT], F32) as weight,\
            nc.sbuf_tensor("eid", [P, NOVER + 1], I32) as eid, nc.sbuf_tensor("slot", [P, NB + 1], U32) as idx:
        with nc.sbuf_tensor("mT", [P, KD, T], F32) as mT:
            with Stage(nc, "branches") as st:
                branches, lru_in = st.sb("T", [P, 2, KD, T]), st.sem("lru_in")
                with nc.Block() as block:
                    @block.sync
                    def _(sp):
                        sp.dma_start(branches[:, 0], gT.rearrange("(k p) t -> p k t", p=P)).then_inc(lru_in, 16)
                diff_attention(nc, bank, cst, col, x, qkT, v_rows, branches[:, 1])
                mixed_T(nc, bank, x["w_lru_o_2"][0], x["w_attn_o_2"][0], branches, lru_in, uT2[5 * D:7 * D, :], mT)
            xT = mT
            gemm_rows(nc, bank, "out2", cst, mT, D, x["w_out_2"][0], x2, x3, xT, h_col=col[:, COLS["norm_cx"]:COLS["norm_cx"] + KD])
            if stop == "x3":
                return
            with nc.sbuf_tensor("cT", [P, MH, T], F32) as cT:
                with nc.sbuf_tensor("memT", [P, KD, MEM], F32) as memT:
                    norm_T(nc, bank, "norm_mem", cst, x["mem_2"][0], MEM, memT, 0,
                           gcol=col[:, COLS["norm_mem"]:COLS["norm_mem"] + KD])
                    cross_attention(nc, bank, cst, col, x["w_cq_2"][0], x["w_ckv_2"][0], xT, memT, cT)
                h4T = xT
                gemm_rows(nc, bank, "co", cst, cT, MH * P, x["w_co_2"][0], x3, x4, h4T, h_rows=[x["norm_ffn_2"]], h_out=h4)
            if stop == "x4":
                return
            tok = cst[:, CONST["tok"]:CONST["tok"] + NT]
            route2(nc, bank, cst, tok, h4T, x["w_group_2"][0], x["b_group_2"], x["w_router_2"][0], x["b_router_2"],
                   slot_tok, ye[E2 * P:, :], dest, weight, eid, placed)
        slot_tokens(nc, bank, cst, slot_tok, idx)
        if stop == "route2":
            return
        experts2(nc, bank, "moe2", cst, h4, x["w_gate_up_2"][0], x["w_down_2"][0], ye, idx, 0, E2, blocks_in, 0)
        experts2(nc, bank, "moe2o", cst, h4, x["w_gate_up_2"][0], x["w_down_2"][0], ye, idx, E2, NOVER, blocks_in, E2, eid)
        combine2(nc, x4, ye, dest, weight, out, rows_in, out_stored)


def constants():
    c = np.zeros((P, CW), np.float32)
    msk = np.zeros((2, len(LEVELS) + 1, P, 2 * P), np.int32)

    def put(name, a):
        c[:a.shape[0], CONST[name]:CONST[name] + a.shape[1]] = a

    i = np.arange(P)
    put("ident", np.eye(P))
    put("ident2", np.concatenate([np.eye(P)] * 2, 1))
    put("pair", (i[:, None] // 64 == i[None] // 64) * 1.0)
    put("pairx", (i[:, None] // 64 != i[None] // 64) * 1.0)
    put("ones", np.ones((P, P)))
    put("lower", (i[:, None] < i[None]) * 1.0)
    put("hm", np.concatenate([np.tile((i // 64 == h) * 1.0, (P, 1)) for h in range(2)], 1))
    put("cmask", np.concatenate([np.tile((i[:, None] // CH == h) * 1.0, (1, CH)) for h in range(2)], 1))
    put("idc", (i[:, None] % CH == np.arange(CH)[None]) * 1.0)
    ax = np.zeros((P, P))
    for m in range(P):
        d = m % 64
        ax[m + 32 if d < 32 else m - 32, m] = -1.0 if d < 32 else 1.0
    put("axrot", ax)
    same = i[:, None] // CH == i[None] // CH
    s, t = i[:, None], i[None]
    for name, strict, incl in (("st_f", s < t, s <= t), ("st_b", s > t, s >= t)):
        put(name, np.concatenate([same & strict, same & incl], 1) * 1.0)
    for d in range(2):
        for l, n in enumerate((1,) + LEVELS):
            block = s // (2 * n) == t // (2 * n)
            low = block & ((s // n) % 2 == 1) & ((t // n) % 2 == 0)
            msk[d, l] = np.concatenate([low, low.T] if d == 0 else [low.T, low], 1)
    put("invf", np.tile(np.exp(-math.log(500000.0) * np.arange(8, dtype=np.float32) / 8).astype(np.float32), (P, 1)))
    put("e32", np.tile(np.arange(32), (P, 1)))
    put("tok", i[:, None] + P * np.arange(NT)[None])
    gam = np.log1p(-np.exp2(-5.0 - np.arange(RET_HEADS, dtype=np.float32))).astype(np.float32)
    idx = np.arange(P, dtype=np.float32)
    rel = idx[None] - idx[:, None]
    din = np.zeros((2, RET_HEADS, P, P), np.float32)
    for h in range(RET_HEADS):
        e = np.exp(np.abs(rel) * gam[h])
        din[0, h], din[1, h] = np.where(rel >= 0, e, 0), np.where(rel <= 0, e, 0)
    qd = np.zeros((2, PAIRS, P, P), np.float32)
    kd = np.zeros((2, PAIRS, P, P), np.float32)
    cd = np.zeros((PAIRS, P, 1), np.float32)
    for p in range(PAIRS):
        for hh in range(2):
            r, g = slice(64 * hh, 64 * hh + 64), gam[2 * p + hh]
            qd[0, p, r], qd[1, p, r] = np.exp((idx + 1) * g), np.exp((P - idx) * g)
            kd[0, p, :, r], kd[1, p, :, r] = (np.exp(e * g)[:, None] for e in (P - 1 - idx, idx))
            cd[p, r] = np.exp(P * g)
    row, col = np.repeat(np.arange(T // GRID_W), GRID_W), np.tile(np.arange(GRID_W), T // GRID_W)
    freq = (10000.0 ** (-np.arange(16, dtype=np.float32) / 16)).astype(np.float32)
    ang = np.concatenate([row[:, None].astype(np.float32) * freq, col[:, None].astype(np.float32) * freq], 1)
    ang = ang.T[np.arange(P) % 32]
    scale = RET_DIM ** -0.5
    return dict(cst=c, msk=msk, din=(din * scale).astype(np.float32), qd=qd, kd=(kd * scale).astype(np.float32), cdec=cd,
                ax=np.stack([np.cos(ang), np.sin(ang)]).astype(np.float32))


def columns(x):
    v = np.zeros((P, VW), np.float32)

    def put(name, a, at=0):
        a = np.asarray(a, np.float32).reshape(-1, P).T
        v[:, COLS[name] + at:COLS[name] + at + a.shape[1]] = a

    def xch(a):
        return np.asarray(a).reshape(PAIRS, 2, 64)[:, ::-1].reshape(-1)

    conv = np.asarray(x["rwkv_conv"])[0]
    for tap in range(3):
        full = np.zeros(16 * P, np.float32)
        full[:conv.shape[1]] = conv[tap]
        full[2 * RW:3 * RW] = xch(full[2 * RW:3 * RW])
        lora = conv[tap][3 * RW:]
        full[3 * RW:3 * RW + 128] = lora[0:128]
        full[3 * RW + 128:3 * RW + 256] = 0
        full[3 * RW + 128:3 * RW + 192] = lora[128:192]
        full[3 * RW + 256:3 * RW + 512] = lora[192:448]
        put("conv", full, 16 * tap)
    put("a0", x["rwkv_a0"])
    put("w0", x["rwkv_w0"])
    for n, k in (("k_k", "rwkv_k_k"), ("k_a", "rwkv_k_a"), ("r_k", "rwkv_r_k")):
        put(n, x[k])
    put("lnw", xch(x["rwkv_lnx_w"]))
    put("lnb", xch(x["rwkv_lnx_b"]))
    for n, k in (("norm_mix", "norm_mix_2"), ("conv2", "conv_w_2"), ("conv2b", "conv_b_2"), ("ba", "lru_ba_2"),
                 ("bx", "lru_bx_2"), ("lam", "lru_lambda_2"), ("subln", "subln_2"), ("norm_cx", "norm_cx_2"),
                 ("norm_mem", "norm_mem_2"), ("cqn", "cq_norm_2"), ("ckn", "ck_norm_2")):
        put(n, x[k])
    pc = np.zeros((PAIRS, P, PW), np.float32)
    for p in range(PAIRS):
        for tap in range(3):
            for n, name in enumerate(("conv_r", "conv_k", "conv_v")):
                pc[p, :, PCOL[name] + tap] = v[:, COLS["conv"] + 16 * tap + 4 * n + p]
        for name in ("a0", "k_k", "k_a", "r_k", "lnw", "lnb"):
            pc[p, :, PCOL[name]] = v[:, COLS[name] + p]
        for d in range(2):
            pc[p, :, PCOL["w0"] + d] = v[:, COLS["w0"] + 4 * d + p]
    return dict(cols=v, pcols=pc)


WHOLE = ("x", "c", "ctx", "c_ctx", "w_mod", "b_mod", "norm_gains", "w_in", "rwkv_w2", "rwkv_a2", "rwkv_g2",
         "w_out", "w_router", "w_gate", "w_up", "w_down", "mem_2", "positions_2", "q_norm_2", "k_norm_2", "w_in_2",
         "lru_wa_2", "lru_wx_2", "w_lru_o_2", "lambda_q1_2", "lambda_k1_2", "lambda_q2_2", "lambda_k2_2",
         "w_attn_o_2", "w_out_2", "w_cq_2", "w_ckv_2", "w_co_2", "norm_ffn_2", "w_group_2", "b_group_2",
         "w_router_2", "b_router_2", "w_gate_up_2", "w_down_2")


def kernel(**inputs):
    import concourse.bacc as bacc
    from concourse.bass_utils import run_bass_kernel_spmd

    nc = bacc.Bacc("TRN2", target_bir_lowering=False, num_devices=1)
    arrays, x, tabs = {}, {}, {}

    def take(name, a, into):
        a = np.ascontiguousarray(a)
        arrays[f"in_{name}"] = a
        into[name] = nc.dram_tensor(f"in_{name}", a.shape, mybir.dt.from_np(a.dtype), kind="ExternalInput").ap()

    for name in WHOLE:
        take(name, inputs[name], x)
    for name, a in {**constants(), **columns(inputs)}.items():
        take(name, a, tabs)
    out = nc.dram_tensor("out", (1, T, D), F32, kind="ExternalOutput").ap()
    program(nc, x, tabs, out)
    r = run_bass_kernel_spmd(nc, [arrays], core_ids=[0])
    return r.results[0]["out"]
```
